# Optimizing a Trainium2 kernel written in Bass

```python
import math
import jax, jax.numpy as jnp
from jax import lax
import numpy as np

D_MODEL = 1024
BATCH = 1
SEQ = 1024
DEPTH = 2
DEC_BATCH = 8
DEC_SEQ = 1
PAST_LEN = 8192
PAGE_SIZE = 128

N_AB_LAYERS = (DEPTH + 1) // 2
N_C_LAYERS = DEPTH // 2
DH_A = 64
H_A = (D_MODEL // 2) // DH_A
D_A = H_A * DH_A
SB_BLOCK = 128
N_B = 64
H_B = (D_MODEL // 2) // N_B
D_B = H_B * N_B
R_W = 64
R_A = 64
R_G = 128
NB_COLS = 3 * D_B + R_W + R_A + R_G
N_IN_EVEN = 3 * D_A + NB_COLS
DK_C = 128
DV_C = 128
H_C = D_MODEL // DK_C
DQK_C = H_C * DK_C
DVV_C = H_C * DV_C
DN_CONV_W = 4
DN_CONV_DIM = 2 * DQK_C + DVV_C
N_IN_ODD = DN_CONV_DIM + DVV_C + 2 * H_C
GDN_CHUNK = 64
D_FF = ((8 * D_MODEL // 3 + 127) // 128) * 128
FFN_CONV_W = 3
RMS_EPS = 1e-6
GN_EPS = 64e-5
POOL_SLACK_NUM = 5
POOL_SLACK_DEN = 4

kernel_name = 'hybrid_stickbreak_rwkv7_gdn_convffn_step'

def rmsnorm(x, g):
    xf = x.astype(jnp.float32)
    y = xf * lax.rsqrt(jnp.mean(xf * xf, axis=-1, keepdims=True) + RMS_EPS)
    return (y * g.astype(jnp.float32)).astype(x.dtype)

def l2norm(x):
    xf = x.astype(jnp.float32)
    return xf * lax.rsqrt(jnp.sum(xf * xf, axis=-1, keepdims=True) + 1e-6)

def causal_dwconv(x, buf, w):
    width = w.shape[0]
    t = x.shape[1]
    xp = jnp.concatenate([buf.astype(x.dtype), x], axis=1)
    y = sum(xp[:, i:i + t] * w[i] for i in range(width))
    return y, xp[:, t:]

def gather_pages(pool, layer, page_table):
    b, n = page_table.shape
    rows = pool[layer, page_table]
    return rows.reshape(b, n * pool.shape[2], pool.shape[3], pool.shape[4])

def sb_weights(z, q_pos, k_pos):
    causal = k_pos[None, :] < q_pos[:, None]
    u = jnp.where(causal, jax.nn.log_sigmoid(-z), 0.0)
    after = lax.cumsum(u, axis=z.ndim - 1, reverse=True) - u
    return jnp.where(causal, jnp.exp(jax.nn.log_sigmoid(z) + after), 0.0)

def stick_breaking(q, k, v, past_k, past_v, bias):
    t = q.shape[1]
    p_len = 0 if past_k is None else past_k.shape[1]
    scale = DH_A ** -0.5
    bias_h = bias.astype(jnp.float32)[None, :, None, None]

    def score(qb, kb):
        return jnp.einsum('bthd,bshd->bhts', qb, kb, preferred_element_type=jnp.float32) * scale + bias_h

    def read(wb, vb):
        return jnp.einsum('bhts,bshd->bthd', wb.astype(vb.dtype), vb, preferred_element_type=jnp.float32)

    outs = []
    for start in range(0, t, SB_BLOCK):
        end = min(start + SB_BLOCK, t)
        qb = q[:, start:end]
        z = score(qb, k[:, :end])
        if p_len:
            z = jnp.concatenate([score(qb, past_k), z], axis=-1)
        w = sb_weights(z, p_len + jnp.arange(start, end), jnp.arange(p_len + end))
        o = read(w[..., p_len:], v[:, :end])
        if p_len:
            o = o + read(w[..., :p_len], past_v)
        outs.append(o)
    return jnp.concatenate(outs, axis=1).astype(q.dtype)

def rwkv7_mix(pb, shift0, s0, mu, w0, w_up, a0, a_up, g_up, k_k, k_a, r_k, ln_w, ln_b):
    f32 = jnp.float32
    b, t, _ = pb.shape
    prev = jnp.concatenate([shift0[:, None].astype(pb.dtype), pb[:, :-1]], axis=1)
    xs = pb + (prev - pb) * mu
    r, k, v, xw, xa, xg = jnp.split(
        xs, [D_B, 2 * D_B, 3 * D_B, 3 * D_B + R_W, 3 * D_B + R_W + R_A], axis=-1)
    w_log = -jax.nn.softplus(-(w0 + jnp.tanh(xw) @ w_up).astype(f32)) - 0.5
    decay = jnp.exp(-jnp.exp(w_log))
    a = jax.nn.sigmoid((a0 + xa @ a_up).astype(f32))
    g = jax.nn.sigmoid(xg) @ g_up

    def heads(x):
        return x.astype(f32).reshape(b, t, H_B, N_B)

    kk = l2norm(heads(k * k_k))
    k_mod = k.astype(f32) * (1.0 + (a - 1.0) * k_a)
    r_h, k_h, v_h, w_h, a_h = heads(r), heads(k_mod), heads(v), heads(decay), heads(a)

    def step(s, inp):
        r_t, w_t, k_t, v_t, kk_t, a_t = inp
        sa = jnp.einsum('bhvk,bhk->bhv', s, kk_t)
        s = (s * w_t[:, :, None, :] - sa[..., None] * (kk_t * a_t)[:, :, None, :]
             + v_t[..., None] * k_t[:, :, None, :])
        return s, jnp.einsum('bhvk,bhk->bhv', s, r_t)

    seq = tuple(jnp.moveaxis(x, 1, 0) for x in (r_h, w_h, k_h, v_h, kk, a_h))
    s_fin, o = lax.scan(step, s0.astype(f32), seq)
    o = jnp.moveaxis(o, 0, 1)
    mean = jnp.mean(o, axis=-1, keepdims=True)
    var = jnp.mean(jnp.square(o - mean), axis=-1, keepdims=True)
    o = ((o - mean) * lax.rsqrt(var + GN_EPS)).reshape(b, t, D_B) * ln_w + ln_b
    bonus = jnp.sum(r_h * k_h * r_k.reshape(H_B, N_B), axis=-1, keepdims=True) * v_h
    o = (o + bonus.reshape(b, t, D_B)) * g
    return o.astype(pb.dtype), s_fin, pb[:, -1]

def gated_delta(q, k, v, beta, g, s0):
    b, t, h, _ = q.shape
    c = min(GDN_CHUNK, t)
    n = -(-t // c)
    pad = n * c - t

    def chunks(x):
        x = jnp.pad(x, [(0, 0), (0, pad)] + [(0, 0)] * (x.ndim - 2))
        x = x.reshape(b, n, c, *x.shape[2:])
        return jnp.moveaxis(x, (1, 3), (0, 2))

    qc, kc, vc, bc, gc = (chunks(x) for x in (q, k, v, beta, g))
    gcum = jnp.cumsum(gc, axis=-1)
    incl = jnp.tril(jnp.ones((c, c), bool))
    strict = jnp.tril(jnp.ones((c, c), bool), -1)
    diff = gcum[..., :, None] - gcum[..., None, :]
    lmask = jnp.where(incl, jnp.exp(jnp.where(incl, diff, 0.0)), 0.0)
    kb = kc * bc[..., None]
    m = jnp.where(strict, jnp.einsum('nbhik,nbhjk->nbhij', kb, kc) * lmask, 0.0)
    eye = jnp.broadcast_to(jnp.eye(c, dtype=m.dtype), m.shape)
    tinv = lax.linalg.triangular_solve(eye + m, eye, left_side=True, lower=True)
    u = tinv @ (vc * bc[..., None])
    wmat = tinv @ (kb * jnp.exp(gcum)[..., None])
    aqk = jnp.where(incl, jnp.einsum('nbhik,nbhjk->nbhij', qc, kc) * lmask, 0.0)

    def step(s, inp):
        q_i, k_i, u_i, w_i, g_i, a_i = inp
        v_new = u_i - jnp.einsum('bhck,bhkv->bhcv', w_i, s)
        o = (jnp.einsum('bhck,bhkv->bhcv', q_i * jnp.exp(g_i)[..., None], s)
             + jnp.einsum('bhij,bhjv->bhiv', a_i, v_new))
        g_last = g_i[..., -1:]
        s = (s * jnp.exp(g_last)[..., None]
             + jnp.einsum('bhck,bhcv->bhkv', k_i * jnp.exp(g_last - g_i)[..., None], v_new))
        return s, o

    s_fin, o = lax.scan(step, s0, (qc, kc, u, wmat, gcum, aqk))
    o = jnp.moveaxis(o, (0, 2), (1, 3)).reshape(b, n * c, h, -1)[:, :t]
    return o, s_fin

def mix_even(h, past_kv, wkv0, shift0, p, i):
    b, t, _ = h.shape
    proj = h @ p['w_in_even'][i]
    q, k, v, pb = jnp.split(proj, [D_A, 2 * D_A, 3 * D_A], axis=-1)
    q = rmsnorm(q.reshape(b, t, H_A, DH_A), p['qnorm_a'][i])
    k = rmsnorm(k.reshape(b, t, H_A, DH_A), p['knorm_a'][i])
    v = v.reshape(b, t, H_A, DH_A)
    if past_kv is None:
        o_a = stick_breaking(q, k, v, None, None, p['sb_bias'][i])
    else:
        o_a = stick_breaking(q, k, v, past_kv[0].astype(k.dtype), past_kv[1].astype(v.dtype),
                             p['sb_bias'][i])
    o_a = o_a.reshape(b, t, D_A)
    o_b, wkv, shift = rwkv7_mix(pb, shift0, wkv0, p['mu_b'][i], p['w0_b'][i], p['w_up_b'][i],
                                p['a0_b'][i], p['a_up_b'][i], p['g_up_b'][i], p['kk_b'][i],
                                p['ka_b'][i], p['rk_b'][i], p['lnx_w_b'][i], p['lnx_b_b'][i])
    y = jnp.concatenate([o_a, o_b.astype(o_a.dtype)], axis=-1) @ p['w_out_even'][i]
    return y, k, v, wkv, shift

def mix_odd(h, s0, conv0, p, i):
    f32 = jnp.float32
    b, t, _ = h.shape
    proj = h @ p['w_in_odd'][i]
    qkv, z, b_raw, a_raw = jnp.split(
        proj, [DN_CONV_DIM, DN_CONV_DIM + DVV_C, DN_CONV_DIM + DVV_C + H_C], axis=-1)
    qkv_c, conv_new = causal_dwconv(qkv, conv0, p['conv_dn'][i])
    qkv_c = jax.nn.silu(qkv_c)
    q, k, v = jnp.split(qkv_c, [DQK_C, 2 * DQK_C], axis=-1)
    q = l2norm(q.reshape(b, t, H_C, DK_C)) * (DK_C ** -0.5)
    k = l2norm(k.reshape(b, t, H_C, DK_C))
    v = v.astype(f32).reshape(b, t, H_C, DV_C)
    beta = jax.nn.sigmoid(b_raw.astype(f32))
    g = -jnp.exp(p['a_log_dn'][i].astype(f32)) * jax.nn.softplus(a_raw.astype(f32) + p['dt_bias_dn'][i])
    o, s_fin = gated_delta(q, k, v, beta, g, s0.astype(f32))
    o = rmsnorm(o, p['onorm_dn'][i]) * jax.nn.silu(z.astype(f32)).reshape(b, t, H_C, DV_C)
    y = o.reshape(b, t, DVV_C).astype(h.dtype) @ p['w_out_odd'][i]
    return y, s_fin, conv_new

def conv_ffn(h, buf, p, l):
    gate = h @ p['w_gate'][l]
    up = h @ p['w_up'][l]
    gate, buf_new = causal_dwconv(gate, buf, p['conv_ffn'][l])
    y = (jax.nn.silu(gate + p['conv_ffn_b'][l]) * up) @ p['w_down'][l]
    return y, buf_new

def trunk(x, kv, wkv0, shift0, dn0, dnconv0, ffnconv0, p):
    new_k, new_v, new_wkv, new_shift, new_dn, new_dnconv, new_ffn = [], [], [], [], [], [], []
    for l in range(DEPTH):
        i = l // 2
        if l % 2 == 0:
            h = rmsnorm(x, p['norm_mix_even'][i])
            if kv is None:
                past_kv = None
            else:
                past_kv = (gather_pages(kv[0], i, kv[2]), gather_pages(kv[1], i, kv[2]))
            y, k_rows, v_rows, wkv, shift = mix_even(h, past_kv, wkv0[i], shift0[i], p, i)
            new_k.append(k_rows)
            new_v.append(v_rows)
            new_wkv.append(wkv)
            new_shift.append(shift)
        else:
            h = rmsnorm(x, p['norm_mix_odd'][i])
            y, s_fin, cbuf = mix_odd(h, dn0[i], dnconv0[i], p, i)
            new_dn.append(s_fin)
            new_dnconv.append(cbuf)
        x = x + y
        h = rmsnorm(x, p['norm_ffn'][l])
        y, fbuf = conv_ffn(h, ffnconv0[l], p, l)
        new_ffn.append(fbuf)
        x = x + y
    dt = x.dtype
    states = (jnp.stack(new_k).astype(dt), jnp.stack(new_v).astype(dt), jnp.stack(new_wkv).astype(dt),
              jnp.stack(new_shift).astype(dt), jnp.stack(new_dn).astype(dt),
              jnp.stack(new_dnconv).astype(dt), jnp.stack(new_ffn).astype(dt))
    return x, states

def setup_inputs(seed: int = 0) -> dict:
    key = jax.random.key(seed)
    ks = iter(jax.random.split(key, 64))
    f32 = jnp.float32

    def nrm(shape, scale):
        return jax.random.normal(next(ks), shape, f32) * scale

    def uni(shape, lo, hi):
        return jax.random.uniform(next(ks), shape, f32, lo, hi)

    n_pages = PAST_LEN // PAGE_SIZE
    n_phys = (POOL_SLACK_NUM * DEC_BATCH * n_pages) // POOL_SLACK_DEN
    perm = jax.random.permutation(next(ks), n_phys)
    page_table = perm[:DEC_BATCH * n_pages].reshape(DEC_BATCH, n_pages).astype(jnp.int32)
    dt = jnp.exp(uni((N_C_LAYERS, H_C), math.log(1e-3), math.log(1e-1)))
    dt_bias = dt + jnp.log(-jnp.expm1(-dt))
    return {
        'x_prompt': nrm((BATCH, SEQ, D_MODEL), 1.0),
        'x_sample': nrm((DEC_BATCH, DEC_SEQ, D_MODEL), 1.0),
        'cache_k': nrm((N_AB_LAYERS, n_phys, PAGE_SIZE, H_A, DH_A), 1.0),
        'cache_v': nrm((N_AB_LAYERS, n_phys, PAGE_SIZE, H_A, DH_A), 1.0),
        'page_table': page_table,
        'state_wkv': nrm((N_AB_LAYERS, DEC_BATCH, H_B, N_B, N_B), 0.3),
        'state_shift': nrm((N_AB_LAYERS, DEC_BATCH, NB_COLS), 1.0),
        'state_dn': nrm((N_C_LAYERS, DEC_BATCH, H_C, DK_C, DV_C), 0.1),
        'state_dn_conv': nrm((N_C_LAYERS, DEC_BATCH, DN_CONV_W - 1, DN_CONV_DIM), 1.0),
        'state_ffn_conv': nrm((DEPTH, DEC_BATCH, FFN_CONV_W - 1, D_FF), 1.0),
        'norm_mix_even': 1.0 + nrm((N_AB_LAYERS, D_MODEL), 0.02),
        'w_in_even': nrm((N_AB_LAYERS, D_MODEL, N_IN_EVEN), D_MODEL ** -0.5),
        'qnorm_a': 1.0 + nrm((N_AB_LAYERS, DH_A), 0.02),
        'knorm_a': 1.0 + nrm((N_AB_LAYERS, DH_A), 0.02),
        'sb_bias': uni((N_AB_LAYERS, H_A), -7.0, -6.0),
        'mu_b': uni((N_AB_LAYERS, NB_COLS), 0.0, 1.0),
        'w0_b': uni((N_AB_LAYERS, D_B), -6.0, -1.0),
        'w_up_b': nrm((N_AB_LAYERS, R_W, D_B), 0.1),
        'a0_b': nrm((N_AB_LAYERS, D_B), 0.1),
        'a_up_b': nrm((N_AB_LAYERS, R_A, D_B), 0.1),
        'g_up_b': nrm((N_AB_LAYERS, R_G, D_B), R_G ** -0.5),
        'kk_b': 0.85 + nrm((N_AB_LAYERS, D_B), 0.05),
        'ka_b': 1.0 + nrm((N_AB_LAYERS, D_B), 0.05),
        'rk_b': nrm((N_AB_LAYERS, D_B), 0.1),
        'lnx_w_b': 1.0 + nrm((N_AB_LAYERS, D_B), 0.02),
        'lnx_b_b': nrm((N_AB_LAYERS, D_B), 0.02),
        'w_out_even': nrm((N_AB_LAYERS, D_A + D_B, D_MODEL), (D_A + D_B) ** -0.5),
        'norm_mix_odd': 1.0 + nrm((N_C_LAYERS, D_MODEL), 0.02),
        'w_in_odd': nrm((N_C_LAYERS, D_MODEL, N_IN_ODD), D_MODEL ** -0.5),
        'conv_dn': nrm((N_C_LAYERS, DN_CONV_W, DN_CONV_DIM), DN_CONV_W ** -0.5),
        'a_log_dn': jnp.log(uni((N_C_LAYERS, H_C), 1.0, 16.0)),
        'dt_bias_dn': dt_bias,
        'onorm_dn': 1.0 + nrm((N_C_LAYERS, DV_C), 0.02),
        'w_out_odd': nrm((N_C_LAYERS, DVV_C, D_MODEL), DVV_C ** -0.5),
        'norm_ffn': 1.0 + nrm((DEPTH, D_MODEL), 0.02),
        'w_gate': nrm((DEPTH, D_MODEL, D_FF), D_MODEL ** -0.5),
        'w_up': nrm((DEPTH, D_MODEL, D_FF), D_MODEL ** -0.5),
        'conv_ffn': nrm((DEPTH, FFN_CONV_W, D_FF), FFN_CONV_W ** -0.5),
        'conv_ffn_b': nrm((DEPTH, D_FF), 0.02),
        'w_down': nrm((DEPTH, D_FF, D_MODEL), D_FF ** -0.5),
    }

def reference(x_prompt, x_sample, cache_k, cache_v, page_table, state_wkv, state_shift, state_dn,
              state_dn_conv, state_ffn_conv, norm_mix_even, w_in_even, qnorm_a, knorm_a, sb_bias,
              mu_b, w0_b, w_up_b, a0_b, a_up_b, g_up_b, kk_b, ka_b, rk_b, lnx_w_b, lnx_b_b,
              w_out_even, norm_mix_odd, w_in_odd, conv_dn, a_log_dn, dt_bias_dn, onorm_dn, w_out_odd,
              norm_ffn, w_gate, w_up, conv_ffn, conv_ffn_b, w_down):
    p = dict(norm_mix_even=norm_mix_even, w_in_even=w_in_even, qnorm_a=qnorm_a, knorm_a=knorm_a,
             sb_bias=sb_bias, mu_b=mu_b, w0_b=w0_b, w_up_b=w_up_b, a0_b=a0_b, a_up_b=a_up_b,
             g_up_b=g_up_b, kk_b=kk_b, ka_b=ka_b, rk_b=rk_b, lnx_w_b=lnx_w_b, lnx_b_b=lnx_b_b,
             w_out_even=w_out_even, norm_mix_odd=norm_mix_odd, w_in_odd=w_in_odd, conv_dn=conv_dn,
             a_log_dn=a_log_dn, dt_bias_dn=dt_bias_dn, onorm_dn=onorm_dn, w_out_odd=w_out_odd,
             norm_ffn=norm_ffn, w_gate=w_gate, w_up=w_up, conv_ffn=conv_ffn,
             conv_ffn_b=conv_ffn_b, w_down=w_down)
    f32 = jnp.float32
    b = x_prompt.shape[0]
    y_prompt, prompt_states = trunk(
        x_prompt, None,
        jnp.zeros((N_AB_LAYERS, b, H_B, N_B, N_B), f32),
        jnp.zeros((N_AB_LAYERS, b, NB_COLS), x_prompt.dtype),
        jnp.zeros((N_C_LAYERS, b, H_C, DK_C, DV_C), f32),
        jnp.zeros((N_C_LAYERS, b, DN_CONV_W - 1, DN_CONV_DIM), x_prompt.dtype),
        jnp.zeros((DEPTH, b, FFN_CONV_W - 1, D_FF), x_prompt.dtype), p)
    k_prompt, v_prompt, wkv_prompt, shift_prompt, dn_prompt, dnconv_prompt, ffnconv_prompt = prompt_states
    y_sample, sample_states = trunk(
        x_sample, (cache_k, cache_v, page_table), state_wkv, state_shift, state_dn,
        state_dn_conv, state_ffn_conv, p)
    k_sample, v_sample, wkv_sample, shift_sample, dn_sample, dnconv_sample, ffnconv_sample = sample_states
    return (y_prompt, y_sample, k_prompt, v_prompt, k_sample, v_sample, wkv_prompt, wkv_sample,
            shift_prompt, shift_sample, dn_prompt, dn_sample, dnconv_prompt, dnconv_sample,
            ffnconv_prompt, ffnconv_sample)


_drawn_inputs = setup_inputs


def setup_inputs(seed=0):
    import zlib

    import numpy as np

    out = dict(_drawn_inputs(seed))
    spreads = {}
    factors = {'qnorm_a': 8.0,
     'knorm_a': 2.927,
     'sb_bias': 7.029,
     'lnx_w_b': 3.973,
     'lnx_b_b': 4.842,
     'onorm_dn': 20.265,
     'conv_ffn_b': 3.524,
     'cache_k': 8.0,
     'cache_v': 8.0}
    for name, (base, spread) in spreads.items():
        noise = np.random.default_rng([zlib.crc32(name.encode()), seed]).standard_normal(out[name].shape)
        drawn = base * np.exp(spread * noise) if base else spread * noise
        out[name] = __import__('jax').numpy.asarray(drawn.astype(out[name].dtype))
    for name, factor in factors.items():
        out[name] = (out[name] * factor).astype(out[name].dtype)
    return out
```

```python
from contextlib import ExitStack

import concourse.bass as bass
import numpy as np
from concourse import mybir

F32 = mybir.dt.float32
I32 = mybir.dt.int32
ALU = mybir.AluOpType
ACT = mybir.ActivationFunctionType
AX = mybir.AxisListType

P = 128
D_MODEL = 1024
SEQ = 1024
NS = 8
TOK = SEQ + NS
GRP = 3
GC = TOK // GRP
KT = D_MODEL // P
H_A, DH = 8, 64
D_A = H_A * DH
PAST, PAGE = 8192, 128
NPG = PAST // PAGE
D_B = 512
NB_COLS = 3 * D_B + 256
NB_T = NB_COLS // P
H_C = 8
QKV_T = 24
ODD_T = QKV_T + 8 + 1
BETA_ROW, A_ROW = 0, 32
D_FF = 2816
FT = D_FF // P
C = 64
NPAIR = SEQ // (2 * C)
RMS_EPS = 1e-6
GN_EPS = 64e-5
DECAY = float(np.exp(-0.5))

QK_BLK = KT * P + 1
PB_BLK = KT * P + 1 + NS
ODD_BLK = KT * P + 4 + 3 * NS
FF_BLK = 2 * KT * P + 4 + 2 * NS

CONST_COLS = {}


def _constants():
    parts = {}
    r = np.arange(P)
    parts["ident"] = np.eye(P)
    parts["ones"] = np.ones((P, P))
    parts["halves"] = (r[:, None] // 64 == r[None, :] // 64) * 1.0
    parts["later"] = (r[:, None] >= r[None, :]) * 1.0
    parts["earlier"] = (r[:, None] < r[None, :]) * 1.0
    parts["dcap"] = np.where(r[:, None] < r[None, :], 3e38, -1e30)
    j, i = r[:, None] % C, np.arange(C)[None, :]
    parts["strictT"] = (j < i) * 1.0
    parts["inclT"] = (j <= i) * 1.0
    parts["ninclT"] = (j <= i) * -1.0
    parts["eye64"] = (j == i) * 1.0
    for lv in range(6):
        b = 1 << lv
        parts[f"lev{lv}T"] = ((j // (2 * b) == i // (2 * b)) & (j % (2 * b) < b) & (i % (2 * b) >= b)) * 1.0
    b = 1
    parts["lev0"] = ((j // 2 == i // 2) & (i % 2 < 1) & (j % 2 >= 1)) * 1.0
    sel = np.zeros((P, 8 * P))
    for h in range(8):
        sel[A_ROW + h, h * P:(h + 1) * P] = 1.0
        sel[BETA_ROW + h, h * P:(h + 1) * P] = 1.0
    parts["sel"] = sel
    parts["scan64"] = np.broadcast_to((np.arange(SEQ) % C != 0) * 1.0, (P, SEQ))
    parts["scanhead"] = np.broadcast_to((np.arange(512) % NPG != 0) * 1.0, (P, 512))
    at = 0
    for n, a in parts.items():
        CONST_COLS[n] = (at, a.shape[1])
        at += a.shape[1]
    return np.concatenate(list(parts.values()), axis=1).astype(np.float32)


CONSTS = _constants()
VEC_COLS = {}
for _n, _w in (("norm_even", 8), ("norm_ffn0", 8), ("norm_odd", 8), ("norm_ffn1", 8), ("w0", 4), ("a0", 4),
               ("kk", 4), ("ka", 4), ("rk", 4), ("lnw", 4), ("lnb", 4), ("onorm", 1), ("sb_bias", 8),
               ("a_log", 1), ("dt_bias", 1), ("eps_rms", 1), ("eps_gn", 1)):
    VEC_COLS[_n] = (sum(w for _, w in VEC_COLS.values()), _w)
NVEC = sum(w for _, w in VEC_COLS.values())


class Sems:

    def __init__(self, nc, phase):
        self.nc, self.phase, self.all = nc, phase, []

    def __call__(self, name):
        s = self.nc.alloc_semaphore(f"{self.phase}_{name}")
        self.all.append(s)
        return s

    def clear(self):
        self.nc.clear_and_free_semaphores(self.all)
        self.nc.all_engine_barrier()


class Steps:

    def __init__(self, eng, sem, at=0):
        self.eng, self.sem, self.at, self.n = eng, sem, at, 0

    def do(self, ins):
        ins.then_inc(self.sem, 1)
        self.n += 1

    def settle(self):
        self.eng.wait_ge(self.sem, self.at + self.n)

    def link(self, ins):
        self.do(ins)
        self.settle()


class Trunk:

    def __init__(self, nc, io, ctx):
        self.nc, self.io = nc, io
        sb = lambda n, s, d=F32: ctx.enter_context(nc.sbuf_tensor(n, s, d))
        self.x = sb("x", [P, KT, TOK])
        self.h = sb("h", [P, KT, TOK])
        self.consts = sb("consts_sb", [P, CONSTS.shape[1]])
        self.vecs = sb("vecs_sb", [P, NVEC])
        self.ps = ctx.enter_context(nc.psum_tensor("ps", [P, 8, 512], F32))

    def const(self, name):
        a, w = CONST_COLS[name]
        return self.consts[:, a:a + w]

    def vec(self, name):
        a, w = VEC_COLS[name]
        return self.vecs[:, a:a + w]


def load_phase(T):
    nc, io = T.nc, T.io
    sems = Sems(nc, "load")
    x_in = sems("x_in")
    with nc.Block() as block:
        @block.sync
        def _(sp):
            sp.dma_start(T.consts[:, :], io["consts"]).then_inc(x_in, 16)
            sp.dma_start(T.vecs[:, :], io["vecs"]).then_inc(x_in, 16)
            sp.dma_start(T.x[:, :, :], io["x"].rearrange("(k p) t -> p k t", p=P)).then_inc(x_in, 16)
            sp.dma_start(io["dnconv_old"], io["dn_conv_rows"]).then_inc(x_in, 16)
            sp.dma_start(io["ffnconv_old"], io["ffn_conv_rows"]).then_inc(x_in, 16)
            sp.wait_ge(x_in, 80)
    sems.clear()


def norm_phase(T, name, gain):
    nc, x, h, ps = T.nc, T.x, T.h, T.ps
    sems = Sems(nc, name)
    squared, summed, rooted, sq_used, step = (sems(n) for n in ("squared", "summed", "rooted", "sq_used", "step"))
    ones, g = T.const("ones"), T.vec(gain)
    with nc.sbuf_tensor(name + "_sq", [P, 2, TOK], F32) as sq, nc.sbuf_tensor(name + "_r", [P, TOK], F32) as rinv, \
            nc.Block() as block:
        @block.scalar
        def _(act):
            for k in range(KT):
                if k >= 2:
                    act.wait_ge(sq_used, k - 1)
                act.activation(sq[:, k % 2, :], x[:, k, :], ACT.Square).then_inc(squared, 1)
            act.wait_ge(summed, 1)
            for c in range(GRP):
                act.activation(rinv[:, c * GC:(c + 1) * GC], ps[:, c, 0:GC], ACT.Sqrt, scale=1.0 / D_MODEL,
                               bias=T.vec("eps_rms")).then_inc(rooted, 1)

        @block.tensor
        def _(pe):
            for k in range(KT):
                pe.wait_ge(squared, k + 1)
                for c in range(GRP):
                    mm = pe.matmul(ps[:, c, 0:GC], ones, sq[:, k % 2, c * GC:(c + 1) * GC], start=(k == 0),
                                   stop=(k == KT - 1))
                mm.then_inc(sq_used, 1)
            pe.wait_ge(sq_used, KT)
            pe.sem_inc(summed, 1)

        @block.vector
        def _(dve):
            dve.wait_ge(rooted, GRP)
            dve.reciprocal(rinv[:, :], rinv[:, :]).then_inc(step, 1)
            dve.wait_ge(step, 1)
            for k in range(KT):
                dve.scalar_tensor_tensor(out=h[:, k, :], in0=x[:, k, :], scalar=g[:, k:k + 1], in1=rinv[:, :],
                                         op0=ALU.mult, op1=ALU.mult)
    sems.clear()


def group_products(pe, T, bank, w, src, kt, c):
    for k in range(kt):
        mm = pe.matmul(T.ps[:, bank, 0:GC], w[:, k * P:(k + 1) * P], src[:, k, c * GC:(c + 1) * GC],
                       start=(k == 0), stop=(k == kt - 1))
    return mm


def residual_phase(T, name, w_dram, src, kt):
    nc, x, ps = T.nc, T.x, T.ps
    sems = Sems(nc, name)
    w_in = [sems("w_in0"), sems("w_in1")]
    product, added = sems("product"), sems("added")
    with nc.sbuf_tensor(name + "_w", [P, 2, kt * P], F32) as w, nc.Block() as block:
        @block.sync
        def _(sp):
            with sp.Fori(0, KT // 2) as i:
                for j in range(2):
                    sp.wait_ge(product, 6 * i + 3 * j + 3)
                    sp.dma_start(w[:, j, :], w_dram[bass.ds(2 * i + j, 1), :, :].rearrange("a p n -> (a p) n"))\
                      .then_inc(w_in[j], 16)

        @block.tensor
        def _(pe):
            pe.sem_inc(product, 6)
            with pe.Fori(0, KT // 2) as i:
                for j in range(2):
                    pe.wait_ge(w_in[j], 16 * i + 16)
                    for c in range(GRP):
                        pe.wait_ge(added, 6 * i + 3 * j + c + 1)
                        group_products(pe, T, 3 * j + c, w[:, j, :], src, kt, c).then_inc(product, 1)

        @block.vector
        def _(dve):
            dve.sem_inc(added, 6)
            with dve.Fori(0, KT // 2) as i:
                for j in range(2):
                    for c in range(GRP):
                        dve.wait_ge(product, 6 * i + 3 * j + c + 7)
                        row = x[:, bass.ds(2 * i + j, 1), c * GC:(c + 1) * GC].rearrange("p a t -> p (a t)")
                        dve.tensor_tensor(row, ps[:, 3 * j + c, 0:GC], row, ALU.add).then_inc(added, 1)
    sems.clear()


def ffn_up_phase(T, name, l, a):
    nc, h, ps, io = T.nc, T.h, T.ps, T.io
    sems = Sems(nc, name)
    w_in = [sems("w_in0"), sems("w_in1")]
    tail_out, tail_free = sems("tail_out"), sems("tail_free")
    gate_done, up_done, row_in, conv_done, silu_done, multiplied, step, cleared = (
        sems(n) for n in ("gate_done", "up_done", "row_in", "conv_done", "silu_done", "multiplied", "step", "cleared"))
    w_dram, tail = io["w_ff"][l], io["ffnconv_new"][l]
    UP, PAR = KT * P, 2 * KT * P
    with ExitStack() as ctx:
        sb = lambda n, s: ctx.enter_context(nc.sbuf_tensor(name + n, s, F32))
        w = sb("_w", [P, 2, FF_BLK])
        row = sb("_row", [P, 2, 2 + TOK])
        cv = sb("_cv", [P, 2, TOK])
        block = ctx.enter_context(nc.Block())

        def span(c):
            return c * GC, min((c + 1) * GC, SEQ)

        @block.sync
        def _(sp):
            with sp.Fori(0, FT // 2) as i:
                for j in range(2):
                    sp.wait_ge(multiplied, 6 * i + 3 * j + 3)
                    sp.dma_start(w[:, j, :], w_dram[bass.ds(2 * i + j, 1), :, :].rearrange("a p n -> (a p) n"))\
                      .then_inc(w_in[j], 16)

        @block.gpsimd
        def _(pool):
            pool.memset(row[:, :, 0:2], 0.0).then_inc(cleared, 1)
            pool.sem_inc(tail_free, 2)
            with pool.Fori(0, FT // 2) as i:
                for j in range(2):
                    pool.wait_ge(row_in, 6 * i + 3 * j + 3 + 3)
                    pool.dma_start(tail[bass.ds(2 * i + j, 1), :, :].rearrange("a p n -> (a p) n"),
                                   row[:, j, SEQ:SEQ + 2 + NS]).then_inc(tail_out, 16)
                    pool.wait_ge(tail_out, 32 * i + 16 * j + 16)
                    pool.sem_inc(tail_free, 1)

        @block.tensor
        def _(pe):
            with pe.Fori(0, FT // 2) as i:
                for j in range(2):
                    pe.wait_ge(w_in[j], 16 * i + 16)
                    for c in range(GRP):
                        n = 6 * i + 3 * j + c
                        pe.wait_ge(row_in, n + 1)
                        group_products(pe, T, c, w[:, j, 0:UP], h, KT, c).then_inc(gate_done, 1)
                        pe.wait_ge(multiplied, n + 4)
                        group_products(pe, T, 3 + c, w[:, j, UP:PAR], h, KT, c).then_inc(up_done, 1)

        @block.scalar
        def _(act):
            act.sem_inc(row_in, 3)
            with act.Fori(0, FT // 2) as i:
                for j in range(2):
                    for c in range(GRP):
                        n = 6 * i + 3 * j + c
                        act.wait_ge(gate_done, n + 1)
                        act.wait_ge(conv_done, n + (2 if c < 2 else 1))
                        if c == 2:
                            act.wait_ge(tail_free, 2 * i + j + 1)
                        act.activation(row[:, j, 2 + c * GC:2 + (c + 1) * GC], ps[:, c, 0:GC], ACT.Copy)\
                           .then_inc(row_in, 1)
                        act.wait_ge(conv_done, n + 7)
                        act.activation(cv[:, j, c * GC:(c + 1) * GC], cv[:, j, c * GC:(c + 1) * GC], ACT.Silu,
                                       bias=w[:, j, PAR + 3:PAR + 4]).then_inc(silu_done, 1)

        @block.vector
        def _(dve):
            dve.sem_inc(multiplied, 6)
            dve.sem_inc(conv_done, 6)
            dve.wait_ge(cleared, 1)
            per = 2 * (2 * GRP + 3)
            with dve.Fori(0, FT // 2) as i:
                st = Steps(dve, step, i * per)
                for j in range(2):
                    tap = [w[:, j, PAR + n:PAR + n + 1] for n in range(3)]
                    kept = w[:, j, PAR + 4:PAR + 4 + 2 * NS].rearrange("p (r b) -> p r b", r=2)
                    for c in range(GRP):
                        n = 6 * i + 3 * j + c
                        a0, a1 = c * GC, min((c + 1) * GC, SEQ)
                        dve.wait_ge(row_in, n + 4)
                        dve.wait_ge(multiplied, n + 1)
                        o = cv[:, j, a0:a1]
                        st.link(dve.tensor_scalar(o, row[:, j, a0:a1], tap[0], None, ALU.mult))
                        st.link(dve.scalar_tensor_tensor(out=o, in0=row[:, j, a0 + 1:a1 + 1], scalar=tap[1],
                                                         in1=o, op0=ALU.mult, op1=ALU.add))
                        if c == 2:
                            s = cv[:, j, SEQ:TOK]
                            st.link(dve.tensor_scalar(s, kept[:, 0, :], tap[0], None, ALU.mult))
                            st.link(dve.scalar_tensor_tensor(out=s, in0=kept[:, 1, :], scalar=tap[1], in1=s,
                                                             op0=ALU.mult, op1=ALU.add))
                            st.link(dve.scalar_tensor_tensor(out=s, in0=row[:, j, 2 + SEQ:2 + TOK], scalar=tap[2],
                                                             in1=s, op0=ALU.mult, op1=ALU.add))
                        dve.scalar_tensor_tensor(out=o, in0=row[:, j, a0 + 2:a1 + 2], scalar=tap[2], in1=o,
                                                 op0=ALU.mult, op1=ALU.add).then_inc(conv_done, 1)
                        dve.wait_ge(silu_done, n + 1)
                        dve.wait_ge(up_done, n + 1)
                        dve.tensor_tensor(a[:, bass.ds(2 * i + j, 1), c * GC:(c + 1) * GC].rearrange("p a t -> p (a t)"),
                                          cv[:, j, c * GC:(c + 1) * GC], ps[:, 3 + c, 0:GC], ALU.mult)\
                           .then_inc(multiplied, 1)
                assert st.n == per
    sems.clear()


def qk_phase(T):
    nc, h, ps, io = T.nc, T.h, T.ps, T.io
    sems = Sems(nc, "qk")
    w_in = [sems("w_in0"), sems("w_in1")]
    row_out, row_free, product, raw_in, squared, summed, rooted, scaled, step = (
        sems(n) for n in ("row_out", "row_free", "product", "raw_in", "squared", "summed", "rooted", "scaled", "step"))
    halves = T.const("halves")
    with ExitStack() as ctx:
        sb = lambda n, s: ctx.enter_context(nc.sbuf_tensor("qk" + n, s, F32))
        w, raw, sq, rt = sb("_w", [P, 2, QK_BLK]), sb("_raw", [P, 2, TOK]), sb("_sq", [P, 2, TOK]), sb("_rt", [P, 2, TOK])
        block = ctx.enter_context(nc.Block())

        @block.sync
        def _(sp):
            with sp.Fori(0, 4) as i:
                for j in range(2):
                    sp.wait_ge(scaled, 2 * i + j + 1)
                    sp.dma_start(w[:, j, :], io["w_qk"][bass.ds(2 * i + j, 1), :, :].rearrange("a p n -> (a p) n"))\
                      .then_inc(w_in[j], 16)

        @block.tensor
        def _(pe):
            def sums(i, j):
                for c in range(GRP):
                    pe.wait_ge(squared, 6 * i + 3 * j + c + 1)
                    pe.matmul(ps[:, 3 * j + c, 0:GC], halves, sq[:, j, c * GC:(c + 1) * GC], start=True, stop=True)\
                      .then_inc(summed, 1)

            with pe.Fori(0, 4) as i:
                for j in range(2):
                    pe.wait_ge(w_in[j], 16 * i + 16)
                    pe.wait_ge(rooted, 2 * i + j + 1)
                    for c in range(GRP):
                        group_products(pe, T, 3 * j + c, w[:, j, :], h, KT, c).then_inc(product, 1)
                    sums(i, j)

        @block.scalar
        def _(act):
            act.sem_inc(rooted, 2)
            with act.Fori(0, 4) as i:
                for j in range(2):
                    act.wait_ge(row_free, 2 * i + j + 1)
                    for c in range(GRP):
                        act.wait_ge(product, 6 * i + 3 * j + c + 1)
                        act.activation(raw[:, j, c * GC:(c + 1) * GC], ps[:, 3 * j + c, 0:GC], ACT.Copy)\
                           .then_inc(raw_in, 1)
                        act.activation(sq[:, j, c * GC:(c + 1) * GC], ps[:, 3 * j + c, 0:GC], ACT.Square)\
                           .then_inc(squared, 1)
                    act.wait_ge(summed, 6 * i + 3 * j + 3)
                    act.activation(rt[:, j, :].rearrange("p (c n) -> p c n", c=GRP), ps[:, 3 * j:3 * j + 3, 0:GC],
                                   ACT.Sqrt, scale=1.0 / DH, bias=T.vec("eps_rms")).then_inc(rooted, 1)

        @block.vector
        def _(dve):
            dve.sem_inc(scaled, 2)
            with dve.Fori(0, 4) as i:
                for j in range(2):
                    dve.wait_ge(rooted, 2 * i + j + 3)
                    dve.reciprocal(rt[:, j, :], rt[:, j, :]).then_inc(step, 1)
                    dve.wait_ge(step, 2 * i + j + 1)
                    dve.wait_ge(raw_in, 6 * i + 3 * j + 3)
                    dve.scalar_tensor_tensor(out=raw[:, j, :], in0=raw[:, j, :], scalar=w[:, j, KT * P:KT * P + 1],
                                             in1=rt[:, j, :], op0=ALU.mult, op1=ALU.mult).then_inc(scaled, 1)

        @block.gpsimd
        def _(pool):
            pool.sem_inc(row_free, 2)
            with pool.Fori(0, 4) as i:
                for j in range(2):
                    pool.wait_ge(scaled, 2 * i + j + 3)
                    pool.dma_start(io["qk_rows"][bass.ds(2 * i + j, 1), :, :].rearrange("a p n -> (a p) n"),
                                   raw[:, j, :]).then_inc(row_out, 16)
                    pool.wait_ge(row_out, 32 * i + 16 * j + 16)
                    pool.sem_inc(row_free, 1)
    sems.clear()


def v_phase(T):
    nc, h, ps, io = T.nc, T.h, T.ps, T.io
    sems = Sems(nc, "v")
    w_in, product, copied, out = (sems(n) for n in ("w_in", "product", "copied", "out"))
    with nc.sbuf_tensor("v_w", [P, KT, D_A], F32) as w, nc.sbuf_tensor("v_sb", [P, 9, D_A], F32) as v, nc.Block() as block:
        rows = [P] * 8 + [NS]

        @block.sync
        def _(sp):
            sp.dma_start(w[:, :, :], io["w_v"]).then_inc(w_in, 16)
            sp.wait_ge(copied, 8)
            sp.dma_start(io["v_rows"][0:SEQ, :].rearrange("(s p) n -> p s n", p=P), v[:, 0:8, :]).then_inc(out, 16)
            sp.wait_ge(copied, 9)
            sp.dma_start(io["v_rows"][SEQ:TOK, :], v[0:NS, 8, :]).then_inc(out, 16)
            sp.wait_ge(out, 32)

        @block.tensor
        def _(pe):
            pe.wait_ge(w_in, 16)
            for s in range(9):
                if s >= 8:
                    pe.wait_ge(copied, s - 7)
                for k in range(KT):
                    mm = pe.matmul(ps[0:rows[s], s % 8, :], h[:, k, s * P:s * P + rows[s]], w[:, k, :], start=(k == 0),
                                   stop=(k == KT - 1))
                mm.then_inc(product, 1)

        @block.scalar
        def _(act):
            for s in range(9):
                act.wait_ge(product, s + 1)
                act.activation(v[0:rows[s], s, :], ps[0:rows[s], s % 8, :], ACT.Copy).then_inc(copied, 1)
    sems.clear()


def pb_phase(T):
    nc, h, ps, io = T.nc, T.h, T.ps, T.io
    sems = Sems(nc, "pb")
    w_in = [sems("w_in0"), sems("w_in1")]
    out_sem, row_free, product, row_in, mixed, step, cleared = (
        sems(n) for n in ("out", "row_free", "product", "row_in", "mixed", "step", "cleared"))
    MU = KT * P
    with ExitStack() as ctx:
        sb = lambda n, s: ctx.enter_context(nc.sbuf_tensor("pb" + n, s, F32))
        w, row, xs = sb("_w", [P, 2, PB_BLK]), sb("_row", [P, 2, 1 + TOK]), sb("_xs", [P, 2, TOK])
        block = ctx.enter_context(nc.Block())

        @block.sync
        def _(sp):
            with sp.Fori(0, NB_T // 2) as i:
                for j in range(2):
                    sp.wait_ge(mixed, 2 * i + j + 1)
                    sp.dma_start(w[:, j, :], io["w_pb"][bass.ds(2 * i + j, 1), :, :].rearrange("a p n -> (a p) n"))\
                      .then_inc(w_in[j], 16)

        @block.tensor
        def _(pe):
            with pe.Fori(0, NB_T // 2) as i:
                for j in range(2):
                    pe.wait_ge(w_in[j], 16 * i + 16)
                    for c in range(GRP):
                        pe.wait_ge(row_in, 6 * i + 3 * j + c + 1)
                        group_products(pe, T, 3 * j + c, w[:, j, :], h, KT, c).then_inc(product, 1)

        @block.scalar
        def _(act):
            act.sem_inc(row_in, 6)
            with act.Fori(0, NB_T // 2) as i:
                for j in range(2):
                    act.wait_ge(row_free, 2 * i + j + 1)
                    for c in range(GRP):
                        act.wait_ge(product, 6 * i + 3 * j + c + 1)
                        act.activation(row[:, j, 1 + c * GC:1 + (c + 1) * GC], ps[:, 3 * j + c, 0:GC], ACT.Copy)\
                           .then_inc(row_in, 1)

        @block.vector
        def _(dve):
            dve.sem_inc(mixed, 2)
            dve.wait_ge(cleared, 1)
            with dve.Fori(0, NB_T // 2) as i:
                st = Steps(dve, step, 4 * i)
                for j in range(2):
                    dve.wait_ge(row_in, 6 * i + 3 * j + 3 + 6)
                    st.do(dve.tensor_tensor(xs[:, j, 0:SEQ], row[:, j, 0:SEQ], row[:, j, 1:1 + SEQ], ALU.subtract))
                    st.link(dve.tensor_tensor(xs[:, j, SEQ:TOK], w[:, j, MU + 1:MU + 1 + NS], row[:, j, 1 + SEQ:1 + TOK],
                                              ALU.subtract))
                    dve.scalar_tensor_tensor(out=xs[:, j, :], in0=xs[:, j, :], scalar=w[:, j, MU:MU + 1],
                                             in1=row[:, j, 1:1 + TOK], op0=ALU.mult, op1=ALU.add).then_inc(mixed, 1)

        @block.gpsimd
        def _(pool):
            pool.memset(row[:, :, 0:1], 0.0).then_inc(cleared, 1)
            pool.sem_inc(row_free, 2)
            with pool.Fori(0, NB_T // 2) as i:
                for j in range(2):
                    pool.wait_ge(mixed, 2 * i + j + 3)
                    pool.dma_start(T.xs_rows[bass.ds(2 * i + j, 1), :, :].rearrange("a p n -> (a p) n"),
                                   xs[:, j, :]).then_inc(out_sem, 16)
                    pool.dma_start(io["shift_new"][bass.ds(2 * i + j, 1), :, :].rearrange("a p n -> (a p) n"),
                                   row[:, j, SEQ:SEQ + 1 + NS]).then_inc(out_sem, 16)
                    pool.wait_ge(out_sem, 64 * i + 32 * j + 32)
                    pool.sem_inc(row_free, 1)
    sems.clear()


def pages_phase(T):
    nc, h, ps, io = T.nc, T.h, T.ps, T.io
    sems = Sems(nc, "pages")
    RING = 8
    k_in = [sems(f"k_in{n}") for n in range(RING)]
    v_in = [sems(f"v_in{n}") for n in range(RING)]
    (q_in, q_spread, q_ready, table_in, vtable_in, k_used, v_used, multiplied, biased, logged, softplus_ready, summed,
     z_ready, w_ready, read, picked, step, act_step) = (
        sems(n) for n in ("q_in", "q_spread", "q_ready", "table_in", "vtable_in", "k_used", "v_used", "multiplied",
                          "biased", "logged", "softplus_ready", "summed", "z_ready", "w_ready", "read", "picked",
                          "step", "act_step"))
    later, ones, ident = T.const("later"), T.const("ones"), T.const("ident")
    NH = NPG * H_A
    with ExitStack() as ctx:
        sb = lambda n, s, d=F32: ctx.enter_context(nc.sbuf_tensor("pg" + n, s, d))
        kp, vp = sb("_k", [P, RING, D_A]), sb("_v", [P, RING, D_A])
        qc, q = sb("_qc", [P, 4, NS]), sb("_q", [P, NS, D_A])
        prod = sb("_prod", [P, 2, D_A])
        z = sb("_z", [P, H_A, NPG])
        zb, sp_, tmp, run, cum, wts = (sb(n, [P, H_A, NPG]) for n in ("_zb", "_sp", "_tmp", "_run", "_cum", "_w"))
        table, vtable = sb("_table", [1, NS * NPG], I32), sb("_vtable", [1, NS * NPG], I32)
        block = ctx.enter_context(nc.Block())
        flat = lambda t: t[:, :, :].rearrange("p h n -> p (h n)")

        @block.sync
        def _(sp):
            sp.dma_start(table[:, :], io["page_table"]).then_inc(table_in, 16)
            sp.dma_start(qc[:, :, :], io["qk_rows"][0:4, :, SEQ:TOK].rearrange("t p b -> p t b")).then_inc(q_in, 16)
            sp.wait_ge(table_in, 16)
            with sp.Fori(0, NS * NPG // RING) as i:
                for n in range(RING):
                    sp.wait_ge(k_used, RING * i + n + 1)
                    page = sp.value_load(table[0:1, bass.ds(RING * i + n, 1)], min_val=0, max_val=T.n_phys - 1)
                    sp.dma_start(kp[:, n, :], io["k_pages"][bass.ds(page, 1), :, :].rearrange("a p n -> (a p) n"))\
                      .then_inc(k_in[n], 16)

        @block.gpsimd
        def _(pool):
            pool.wait_ge(picked, NS)

        @block.tensor
        def _(pe):
            pe.wait_ge(q_in, 16)
            for b in range(NS):
                for t in range(4):
                    mm = pe.matmul(ps[:, b, t * P:(t + 1) * P], qc[:, t, b:b + 1].to_broadcast([P, P]), ident,
                                   start=True, stop=True)
                mm.then_inc(q_spread, 1)
            pe.sem_inc(v_used, RING)
            pe.wait_ge(q_ready, NS)
            with pe.Fori(0, NS) as b:
                pe.wait_ge(softplus_ready, b + 1)
                pe.matmul(ps[:, 0, :], later, flat(sp_), start=True, stop=True).then_inc(summed, 1)
                pe.matmul(ps[:, 1, :], ones, flat(sp_), start=True, stop=True).then_inc(summed, 1)
                pe.wait_ge(w_ready, b + 1)
                pe.wait_ge(picked, b + 1)
                for n in range(RING):
                    pe.wait_ge(v_in[n], 16 * (NPG // RING) * b + 16)
                    for t in range(4):
                        mm = pe.matmul(ps[:, 2, 2 * t:2 * t + 2], vp[:, n, t * P:(t + 1) * P], wts[:, 2 * t:2 * t + 2, n],
                                       start=(n == 0 and t == 0), stop=False, skip_group_check=True)
                    mm.then_inc(v_used, 1)
                with pe.Fori(1, NPG // RING) as m:
                    for n in range(RING):
                        pe.wait_ge(v_in[n], 16 * (NPG // RING) * b + 16 * m + 16)
                        for t in range(4):
                            mm = pe.matmul(ps[:, 2, 2 * t:2 * t + 2], vp[:, n, t * P:(t + 1) * P],
                                           wts[:, 2 * t:2 * t + 2, bass.ds(RING * m + n, 1)].rearrange("p h a -> p (h a)"),
                                           start=False, stop=False, skip_group_check=True)
                        mm.then_inc(v_used, 1)
                pe.wait_ge(v_used, RING + NPG * b + NPG)
                pe.sem_inc(read, 1)

        @block.scalar
        def _(act):
            act.dma_start(vtable[:, :], io["page_table"]).then_inc(vtable_in, 16)
            for b in range(NS):
                act.wait_ge(q_spread, b + 1)
                act.activation(q[:, b, :], ps[:, b, :], ACT.Copy, scale=DH ** -0.5).then_inc(q_ready, 1)
            act.wait_ge(vtable_in, 16)
            act.sem_inc(picked, 1)
            with act.Fori(0, NS) as b:
                st = Steps(act, act_step, 2 * b)
                act.wait_ge(biased, b + 1)
                st.link(act.activation(flat(tmp), flat(zb), ACT.Abs))
                st.link(act.activation(flat(tmp), flat(tmp), ACT.Exp, scale=-1.0))
                act.activation(flat(tmp), flat(tmp), ACT.Ln, bias=1.0).then_inc(logged, 1)
                act.wait_ge(z_ready, b + 1)
                act.activation(flat(wts), flat(cum), ACT.Exp).then_inc(w_ready, 1)
                with act.Fori(0, NPG // RING) as m:
                    for n in range(RING):
                        g = NPG * b + RING * m + n
                        act.wait_ge(v_used, g + 1)
                        page = act.value_load(vtable[0:1, bass.ds(g, 1)], min_val=0, max_val=T.n_phys - 1)
                        act.dma_start(vp[:, n, :], io["v_pages"][bass.ds(page, 1), :, :].rearrange("a p n -> (a p) n"))\
                           .then_inc(v_in[n], 16)
                act.wait_ge(read, b + 1)
                for e in range(2):
                    r = slice(64 * e, 64 * e + 64)
                    last = act.activation(h[r, 0:4, bass.ds(SEQ + b, 1)].rearrange("p t a -> p (t a)"),
                                          ps[r, 2, e:8:2], ACT.Copy)
                last.then_inc(picked, 1)

        @block.vector
        def _(dve):
            dve.sem_inc(k_used, RING)
            dve.wait_ge(q_ready, NS)
            with dve.Fori(0, NS) as b:
                with dve.Fori(0, NPG // RING) as m:
                    for n in range(RING):
                        g = NPG * b + RING * m + n
                        dve.wait_ge(k_in[n], 16 * (NPG // RING) * b + 16 * m + 16)
                        dve.tensor_tensor(prod[:, n % 2, :], kp[:, n, :],
                                          q[:, bass.ds(b, 1), :].rearrange("p a n -> p (a n)"), ALU.mult)\
                           .then_inc(k_used, 1)
                        dve.wait_ge(k_used, RING + g + 1)
                        dve.tensor_reduce(z[:, :, bass.ds(RING * m + n, 1)].rearrange("p h a -> p (h a)"),
                                          prod[:, n % 2, :].rearrange("p (h d) -> p h d", h=H_A), AX.X, ALU.add)\
                           .then_inc(multiplied, 1)
                st = Steps(dve, step, 3 * b)
                dve.wait_ge(multiplied, NPG * b + NPG)
                dve.tensor_tensor(zb[:, :, :], z[:, :, :], T.vec("sb_bias").unsqueeze(2).to_broadcast([P, H_A, NPG]),
                                  ALU.add).then_inc(biased, 1)
                dve.wait_ge(logged, b + 1)
                dve.scalar_tensor_tensor(out=flat(sp_), in0=flat(zb), scalar=0.0, in1=flat(tmp), op0=ALU.max,
                                         op1=ALU.add).then_inc(softplus_ready, 1)
                dve.wait_ge(summed, 2 * b + 2)
                st.do(dve.tensor_tensor(flat(cum), flat(zb), ps[:, 0, :], ALU.subtract))
                st.link(dve.tensor_tensor_scan(flat(run), T.const("scanhead"), ps[:, 1, :], 0.0, ALU.mult, ALU.add))
                st.link(dve.tensor_tensor(flat(run), flat(run), ps[:, 1, :], ALU.subtract))
                dve.tensor_tensor(flat(cum), flat(cum), flat(run), ALU.subtract).then_inc(z_ready, 1)
                assert st.n == 3
    sems.clear()


def attention_phase(T):
    nc, h, ps, io = T.nc, T.h, T.ps, T.io
    sems = Sems(nc, "attn")
    later, earlier = T.const("later"), T.const("earlier")
    HALF = 512
    ticks = []
    for j in range(2):
        for g in range(2):
            for s in reversed(range(4 * g + 4)):
                q0 = max(s * P, g * HALF)
                ticks.append((j, g, s, q0, (g + 1) * HALF - q0, s == 0, 2 * j + g))
    NT = len(ticks)
    k_in = [sems("heads_in0"), sems("heads_in1")]
    (z_done, zb_done, na_done, log_done, sp_done, cum_done, d_done, w_done, read_done, carried, out_done, step) = (
        sems(n) for n in ("z_done", "zb_done", "na_done", "log_done", "sp_done", "cum_done", "d_done", "w_done",
                          "read_done", "carried", "out_done", "step"))
    exp_done = sems("exp_done")
    with ExitStack() as ctx:
        sb = lambda n, s: ctx.enter_context(nc.sbuf_tensor("at" + n, s, F32))
        kh, qh, vh = sb("_k", [64, 2, SEQ]), sb("_q", [64, 2, SEQ]), sb("_v", [P, 2, 8, DH])
        zb, na, sp_, d, w = sb("_zb", [P, 3, HALF]), sb("_na", [P, 2, HALF]), sb("_sp", [P, 2, HALF]), \
            sb("_d", [P, 2, HALF]), sb("_w", [P, 2, HALF])
        block = ctx.enter_context(nc.Block())
        qk = io["qk_rows"].rearrange("(a t) (e p) n -> a (t e) p n", a=2, e=2)
        vr = io["v_rows"][0:SEQ, :].rearrange("(s p) (h n) -> h p s n", p=P, n=DH)

        @block.sync
        def _(sp):
            with sp.Fori(0, 4) as i:
                for j in range(2):
                    sp.wait_ge(read_done, NT * i + NT // 2 * (j + 1))
                    hd = bass.ds(2 * i + j, 1)
                    sp.dma_start(qh[:, j, :], qk[0, hd, :, 0:SEQ].rearrange("a p n -> (a p) n")).then_inc(k_in[j], 16)
                    sp.dma_start(kh[:, j, :], qk[1, hd, :, 0:SEQ].rearrange("a p n -> (a p) n")).then_inc(k_in[j], 16)
                    sp.dma_start(vh[:, j, :, :], vr[hd, :, :, :].rearrange("a p s n -> (a p) s n")).then_inc(k_in[j], 16)

        @block.tensor
        def _(pe):
            pe.sem_inc(read_done, NT)
            with pe.Fori(0, 4) as i:
                def score(n):
                    j, g, s, q0, nq, last, stream = ticks[n]
                    if n == 0 or ticks[n - 1][0] != j:
                        pe.wait_ge(k_in[j], 48 * i + 48)
                    if n >= 2:
                        pe.wait_ge(zb_done, NT * i + n - 1)
                    pe.matmul(ps[:, n % 2, 0:nq], kh[:, j, s * P:(s + 1) * P], qh[:, j, q0:q0 + nq], start=True,
                              stop=True).then_inc(z_done, 1)

                def own_sum(n):
                    j, g, s, q0, nq, last, stream = ticks[n]
                    c0 = q0 - g * HALF
                    pe.wait_ge(sp_done, NT * i + n + 1)
                    pe.matmul(ps[:, 2 + stream % 2, c0:c0 + nq], later, sp_[:, n % 2, 0:nq], start=(s == 4 * g + 3),
                              stop=True, skip_group_check=True).then_inc(cum_done, 1)

                def rest_sum(n):
                    j, g, s, q0, nq, last, stream = ticks[n]
                    c0 = q0 - g * HALF
                    pe.wait_ge(d_done, NT * i + n + 1)
                    if last:
                        pe.sem_inc(carried, 1)
                        return
                    pe.matmul(ps[:, 2 + stream % 2, c0:c0 + nq], earlier, sp_[:, n % 2, 0:nq], start=False,
                              stop=True, skip_group_check=True).then_inc(carried, 1)

                def read(n):
                    j, g, s, q0, nq, last, stream = ticks[n]
                    c0 = q0 - g * HALF
                    pe.wait_ge(w_done, NT * i + n + 1)
                    if s == 4 * g + 3:
                        pe.wait_ge(out_done, 4 * i + stream + 1)
                    r = slice(64 * j, 64 * j + 64)
                    pe.matmul(ps[r, 4 + stream % 2, c0:c0 + nq], vh[:, j, s, :], w[:, n % 2, 0:nq],
                              start=(s == 4 * g + 3), stop=True, skip_group_check=True).then_inc(read_done, 1)

                score(0)
                for n in range(NT + 2):
                    if n + 1 < NT:
                        score(n + 1)
                    if 0 <= n - 1 < NT:
                        own_sum(n - 1)
                    if n >= 2:
                        read(n - 2)
                    if 0 <= n - 1 < NT:
                        rest_sum(n - 1)

        @block.vector
        def _(dve):
            per = sum(1 for t in ticks if t[2] * P >= t[1] * HALF) * 2
            with dve.Fori(0, 4) as i:
                st = Steps(dve, step, per * i)

                def scores(n):
                    j, g, s, q0, nq, last, stream = ticks[n]
                    dve.wait_ge(z_done, NT * i + n + 1)
                    bias = T.vec("sb_bias")[:, bass.ds(2 * i + j, 1)]
                    dve.tensor_scalar(zb[:, n % 3, 0:nq], ps[:, n % 2, 0:nq], DH ** -0.5, bias, ALU.mult, ALU.add)\
                       .then_inc(zb_done, 1)
                    dve.wait_ge(zb_done, NT * i + n + 1)
                    dve.scalar_tensor_tensor(out=na[:, n % 2, 0:nq], in0=zb[:, n % 3, 0:nq], scalar=-1.0,
                                             in1=zb[:, n % 3, 0:nq], op0=ALU.mult, op1=ALU.min).then_inc(na_done, 1)

                def softplus(n):
                    j, g, s, q0, nq, last, stream = ticks[n]
                    dve.wait_ge(log_done, NT * i + n + 1)
                    if n >= 2:
                        dve.wait_ge(carried, NT * i + n - 1)
                    ins = dve.scalar_tensor_tensor(out=sp_[:, n % 2, 0:nq], in0=zb[:, n % 3, 0:nq], scalar=0.0,
                                                   in1=na[:, n % 2, 0:nq], op0=ALU.max, op1=ALU.add)
                    if s * P >= g * HALF:
                        st.link(ins)
                        ins = dve.tensor_tensor(sp_[:, n % 2, 0:P], sp_[:, n % 2, 0:P], earlier, ALU.mult)
                    ins.then_inc(sp_done, 1)

                def exponent(n):
                    j, g, s, q0, nq, last, stream = ticks[n]
                    c0 = q0 - g * HALF
                    dve.wait_ge(cum_done, NT * i + n + 1)
                    if n >= 2:
                        dve.wait_ge(w_done, NT * i + n - 1)
                    ins = dve.tensor_tensor(d[:, n % 2, 0:nq], zb[:, n % 3, 0:nq], ps[:, 2 + stream % 2, c0:c0 + nq],
                                            ALU.subtract)
                    if s * P >= g * HALF:
                        st.link(ins)
                        ins = dve.tensor_tensor(d[:, n % 2, 0:P], d[:, n % 2, 0:P], T.const("dcap"), ALU.min)
                    ins.then_inc(d_done, 1)

                for n in range(NT + 1):
                    if n < NT:
                        scores(n)
                    if n >= 1:
                        exponent(n - 1)
                    if n < NT:
                        softplus(n)
                assert st.n == per

        @block.scalar
        def _(act):
            act.sem_inc(out_done, 2)
            with act.Fori(0, 4) as i:
                for n in range(NT + 2):
                    if n < NT:
                        nq = ticks[n][4]
                        act.wait_ge(na_done, NT * i + n + 1)
                        act.activation(na[:, n % 2, 0:nq], na[:, n % 2, 0:nq], ACT.Exp).then_inc(exp_done, 1)
                        act.wait_ge(exp_done, NT * i + n + 1)
                        act.activation(na[:, n % 2, 0:nq], na[:, n % 2, 0:nq], ACT.Ln, bias=1.0).then_inc(log_done, 1)
                    if 0 <= n - 1 < NT:
                        m = n - 1
                        nq = ticks[m][4]
                        act.wait_ge(d_done, NT * i + m + 1)
                        if m >= 2:
                            act.wait_ge(read_done, NT * i + m - 1 + NT)
                        act.activation(w[:, m % 2, 0:nq], d[:, m % 2, 0:nq], ACT.Exp).then_inc(w_done, 1)
                    if n >= 2 and ticks[n - 2][5]:
                        j, g, s, q0, nq, last, stream = ticks[n - 2]
                        act.wait_ge(read_done, NT * i + n - 1 + NT)
                        r = slice(64 * j, 64 * j + 64)
                        act.activation(h[r, bass.ds(i, 1), g * HALF:(g + 1) * HALF].rearrange("p a n -> p (a n)"),
                                       ps[r, 4 + stream % 2, :], ACT.Copy).then_inc(out_done, 1)
    sems.clear()


def alone(eng, passed):
    eng.sem_inc(passed, 1)


def solve_levels_pe(pe, T, S, i, mtl, xm, xt, y, banks, passed):
    ps = T.ps
    yb, zb, ztb = banks
    for lv in range(1, 6):
        n = 5 * i + lv
        pe.wait_ge(S["x_ready"], n)
        if lv == 1:
            pe.wait_ge(S["blocks_ready"], i + 1)
        alone(pe, passed)
        for p in range(2):
            r = slice(64 * p, 64 * p + 64)
            for hd in range(8):
                c = slice(64 * hd, 64 * hd + 64)
                mm = pe.matmul(ps[r, yb, c], mtl[r, lv - 1, c], xm[r, c], start=True, stop=True)
        mm.then_inc(S["y_done"], 1)
        pe.wait_ge(S["y_ready"], n)
        alone(pe, passed)
        if lv < 5:
            for p in range(2):
                r = slice(64 * p, 64 * p + 64)
                for hd in range(8):
                    c = slice(64 * hd, 64 * hd + 64)
                    pe.matmul(ps[r, zb, c], xt[r, c], y[r, c], start=True, stop=True)
        for p in range(2):
            r = slice(64 * p, 64 * p + 64)
            for hd in range(8):
                c = slice(64 * hd, 64 * hd + 64)
                mm = pe.matmul(ps[r, ztb, c], y[r, c], xt[r, c], start=True, stop=True)
        mm.then_inc(S["z_done"], 1)


def solve_levels_act(act, T, S, i, y, banks):
    for lv in range(1, 6):
        act.wait_ge(S["y_done"], 5 * i + lv)
        act.activation(y[:, :], T.ps[:, banks[0], :], ACT.Copy).then_inc(S["y_ready"], 1)


def solve_levels_dve(dve, T, S, st, i, xm, xt, banks):
    ps = T.ps
    for lv in range(1, 6):
        dve.wait_ge(S["z_done"], 5 * i + lv)
        if lv < 5:
            st.do(dve.tensor_tensor(xm[:, :], xm[:, :], ps[:, banks[1], :], ALU.subtract))
        st.do(dve.tensor_tensor(xt[:, :], xt[:, :], ps[:, banks[2], :], ALU.subtract))
        st.settle()
        dve.sem_inc(S["x_ready"] if lv < 5 else S["solved"], 1)


def rwkv_phase(T):
    nc, h, ps, io = T.nc, T.h, T.ps, T.io
    sems = Sems(nc, "rwkv")
    S = {n: sems(n) for n in (
        "xs_in", "lora_in", "tanh_in", "gate_in", "lora_done", "w_sum", "w_exp", "a_sum", "a_exp", "k_sq", "k_sum",
        "k_rn", "l_ready", "decays", "prepped", "rkk", "bonus", "bonus_used", "turned", "tm_ready", "spread", "gram",
        "masked", "blocks_copied", "blocks_ready", "x_ready", "y_done", "y_ready", "z_done", "solved", "w_done", "w_copied",
        "u_done", "u_copied", "h_done", "h_ready", "o_done", "o_copied", "mean", "centered", "var", "rstd", "out_ready",
        "gate_copied", "step", "fin_step", "astep", "pstep", "cleared", "smp_turned", "smp_rows", "smp_out", "smp_in",
        "smp_done", "smp_back", "smp_step", "log_var",
        "pe_passed", "pool_passed")}
    halves, ident = T.const("halves"), T.const("ident")
    W = 2 * C
    with ExitStack() as ctx:
        sb = lambda n, s: ctx.enter_context(nc.sbuf_tensor("rw" + n, s, F32))
        lora = sb("_lora", [P, 2 * D_B])
        X = sb("_xs", [P, NB_T, W])
        th, sg = sb("_th", [P, W]), sb("_sg", [P, W])
        names = "yw rw ya ra kk t1 t2 L eL eN eX km A R K B g bon nm".split()
        t = {n: sb("_" + n, [P, 4, W]) for n in names}
        Ax, Rx, Bx = (sb(n, [P, 4, 2, W]) for n in ("_Ax", "_Rx", "_Bx"))
        ktm, btm, vtm, ak, rk, rb, mt, xm, xt, y, r0, u = (sb("_m" + n, [P, 512]) for n in
                                                           "ktm btm vtm ak rk rb mt xm xt y r0 u".split())
        mtl = sb("_mtl", [P, 6, 512])
        Hx, dh = sb("_Hx", [P, 4, 2, C]), sb("_dh", [P, 4, C])
        o, oc, rs = (sb("_" + n, [P, 4, W]) for n in ("o", "oc", "rs"))
        smp = mtl
        kv, vv, so, sa = sb("_kv", [P, 5, 64]), sb("_vv", [P, 32]), sb("_so", [P, 32]), sb("_sa", [P, 32])
        st8 = sb("_st", [P, 64, 32])
        tmp8 = sb("_tmp8", [P, 64, 32])
        orow = sb("_orow", [NS, 512])
        ocol = sb("_ocol", [P, 4, NS])
        scr = nc.dram_tensor("scratch_rw_rows", [6, NS, 512], F32, kind="Internal").ap()
        scr_o = nc.dram_tensor("scratch_rw_o", [NS, 512], F32, kind="Internal").ap()
        block = ctx.enter_context(nc.Block())
        bc = lambda v, n: T.vec(v).unsqueeze(2).to_broadcast([P, 4, n])
        m8 = lambda name: T.const(name).unsqueeze(1).to_broadcast([P, 8, C])
        h8 = lambda a: a.rearrange("p (h i) -> p h i", h=8)
        cut = lambda a, n: a[:, :, 0:n]

        @block.sync
        def _(sp):
            sp.dma_start(lora[:, :], io["w_lora"]).then_inc(S["lora_in"], 16)
            sp.dma_start(st8[:, :, :], io["wkv_in"].rearrange("p (k v) -> p k v", k=64)).then_inc(S["lora_in"], 16)
            xs = T.xs_rows.rearrange("t p n -> p t n")
            sp.dma_start(X[:, :, :], xs[:, :, 0:W]).then_inc(S["xs_in"], 16)
            with sp.Fori(1, NPAIR) as i:
                sp.wait_ge(S["out_ready"], i)
                sp.dma_start(X[:, :, :], xs[:, :, bass.ds(i * W, W)]).then_inc(S["xs_in"], 16)
            sp.wait_ge(S["out_ready"], NPAIR)
            sp.dma_start(X[:, :, 0:NS], xs[:, :, SEQ:TOK]).then_inc(S["xs_in"], 16)
            sp.wait_ge(S["h_ready"], 2 * NPAIR + 1)
            for e in range(2):
                sp.dma_start(io["wkv_prompt"][e], Hx[64 * e:64 * e + 64, :, e, :]).then_inc(S["smp_out"], 16)
            sp.wait_ge(S["smp_rows"], 1)
            sp.dma_start(scr.rearrange("a b n -> b a n"), smp[0:NS, :, :]).then_inc(S["smp_out"], 16)
            sp.wait_ge(S["smp_out"], 48)
            for e in range(2):
                r = slice(64 * e, 64 * e + 64)
                sp.dma_start(kv[r, :, :], scr[0:5].rearrange("a b (h k) -> (b h) a k", h=8)).then_inc(S["smp_in"], 16)
                sp.dma_start(vv[r, :], scr[5].rearrange("b (h e v) -> e (b h) v", h=8, e=2)[e]).then_inc(S["smp_in"], 16)
            sp.wait_ge(S["smp_done"], 1)
            for e in range(2):
                sp.dma_start(scr_o.rearrange("b (h e v) -> e (b h) v", h=8, e=2)[e], so[64 * e:64 * e + 64, :])\
                  .then_inc(S["smp_out"], 16)
            sp.dma_start(io["wkv_new"].rearrange("p (k v) -> p k v", k=64), st8[:, :, :]).then_inc(S["smp_out"], 16)
            sp.wait_ge(S["smp_out"], 96)
            sp.dma_start(orow[:, :], scr_o).then_inc(S["smp_back"], 16)

        def prep_pe(pe, i, n):
            pe.wait_ge(S["tanh_in"], i + 1)
            for k in range(4):
                pe.matmul(ps[:, 0, k * W:k * W + n], lora[0:64, k * P:(k + 1) * P], th[0:64, 0:n], start=True, stop=True)
            for k in range(4):
                pe.matmul(ps[:, 1, k * W:k * W + n], lora[64:P, k * P:(k + 1) * P], X[64:P, 12, 0:n], start=True, stop=True)
            pe.wait_ge(S["gate_in"], i + 1)
            for k in range(4):
                mm = pe.matmul(ps[:, 2, k * W:k * W + n], lora[:, D_B + k * P:D_B + (k + 1) * P], sg[:, 0:n], start=True,
                               stop=True)
            mm.then_inc(S["lora_done"], 1)
            pe.wait_ge(S["k_sq"], i + 1)
            pe.matmul(ps[:, 3, 0:4 * n], halves, cut(t["t1"], n), start=True, stop=True).then_inc(S["k_sum"], 1)
            pe.wait_ge(S["rkk"], i + 1)
            pe.matmul(ps[:, 4, 0:4 * n], halves, cut(t["t2"], n), start=True, stop=True).then_inc(S["bonus"], 1)

        def prep_act(act, i, n):
            st = Steps(act, S["astep"], 3 * i)
            act.wait_ge(S["xs_in"], 16 * i + 16)
            act.activation(th[0:64, 0:n], X[0:64, 12, 0:n], ACT.Exp, scale=2.0)
            act.activation(sg[:, 0:n], X[:, 13, 0:n], ACT.Exp, scale=-1.0).then_inc(S["w_exp"], 1)
            act.wait_ge(S["lora_done"], i + 1)
            act.activation(cut(t["g"], n), ps[:, 2, :].rearrange("p (k w) -> p k w", k=4)[:, :, 0:n], ACT.Copy)\
               .then_inc(S["gate_copied"], 1)
            act.wait_ge(S["w_sum"], i + 1)
            act.activation(cut(t["rw"], n), cut(t["yw"], n), ACT.Exp, scale=-1.0)
            act.activation(cut(t["ra"], n), cut(t["ya"], n), ACT.Exp, scale=-1.0).then_inc(S["a_exp"], 1)
            act.wait_ge(S["k_sum"], i + 1)
            st.link(act.activation(cut(t["nm"], n), ps[:, 3, 0:4 * n].rearrange("p (k w) -> p k w", k=4), ACT.Ln,
                                   bias=T.vec("eps_rms")))
            st.do(act.activation(cut(t["nm"], n), cut(t["nm"], n), ACT.Exp, scale=-0.5))
            st.settle()
            act.sem_inc(S["k_rn"], 1)
            act.wait_ge(S["l_ready"], i + 1)
            act.activation(cut(t["eL"], n), cut(t["L"], n), ACT.Exp, scale=-DECAY)
            act.activation(cut(t["eN"], n), cut(t["L"], n), ACT.Exp, scale=DECAY)
            st.do(act.activation(cut(t["eX"], n), cut(t["t1"], n), ACT.Exp, scale=-DECAY))
            st.settle()
            act.sem_inc(S["decays"], 1)
            assert st.n == 3

        PREP = 20

        def prep_dve(dve, i, n, prompt):
            st = Steps(dve, S["step"], PREP * i)
            r, k, v = X[:, 0:4, 0:n], X[:, 4:8, 0:n], X[:, 8:12, 0:n]
            part = lambda b: ps[:, b, :].rearrange("p (k w) -> p k w", k=4)[:, :, 0:n]
            tt = lambda o, a, b, op: dve.tensor_tensor(o, a, b, op)
            dve.wait_ge(S["w_exp"], i + 1)
            st.do(dve.tensor_scalar(th[0:64, 0:n], th[0:64, 0:n], 1.0, None, ALU.add))
            st.link(dve.tensor_scalar(sg[:, 0:n], sg[:, 0:n], 1.0, None, ALU.add))
            st.do(dve.reciprocal(th[0:64, 0:n], th[0:64, 0:n]))
            dve.reciprocal(sg[:, 0:n], sg[:, 0:n]).then_inc(S["gate_in"], 1)
            st.settle()
            dve.tensor_scalar(th[0:64, 0:n], th[0:64, 0:n], -2.0, 1.0, ALU.mult, ALU.add).then_inc(S["tanh_in"], 1)
            st.link(tt(cut(t["kk"], n), k, bc("kk", n), ALU.mult))
            dve.tensor_tensor(cut(t["t1"], n), cut(t["kk"], n), cut(t["kk"], n), ALU.mult).then_inc(S["k_sq"], 1)
            dve.wait_ge(S["lora_done"], i + 1)
            dve.tensor_tensor(cut(t["yw"], n), part(0), bc("w0", n), ALU.add)
            dve.tensor_tensor(cut(t["ya"], n), part(1), bc("a0", n), ALU.add).then_inc(S["w_sum"], 1)
            dve.wait_ge(S["a_exp"], i + 1)
            st.do(dve.tensor_scalar(cut(t["rw"], n), cut(t["rw"], n), 1.0, None, ALU.add))
            st.link(dve.tensor_scalar(cut(t["ra"], n), cut(t["ra"], n), 1.0, None, ALU.add))
            st.do(dve.reciprocal(cut(t["rw"], n), cut(t["rw"], n)))
            st.link(dve.reciprocal(cut(t["ra"], n), cut(t["ra"], n)))
            dve.wait_ge(S["k_sum"], i + 1)
            if prompt:
                st.link(dve.tensor_tensor_scan(t["L"][:, :, :].rearrange("p k w -> p (k w)"), T.const("scan64")[:, 0:512],
                                               t["rw"][:, :, :].rearrange("p k w -> p (k w)"), 0.0, ALU.mult, ALU.add))
                st.do(tt(cut(t["t1"], n), cut(t["L"], n), cut(t["rw"], n), ALU.subtract))
            else:
                st.link(dve.tensor_copy(cut(t["L"], n), cut(t["rw"], n)))
                st.do(tt(cut(t["t1"], n), cut(t["L"], n), cut(t["rw"], n), ALU.subtract))
            st.settle()
            dve.sem_inc(S["l_ready"], 1)
            st.link(dve.scalar_tensor_tensor(out=cut(t["km"], n), in0=cut(t["ra"], n), scalar=-1.0, in1=bc("ka", n),
                                             op0=ALU.add, op1=ALU.mult))
            st.link(dve.scalar_tensor_tensor(out=cut(t["km"], n), in0=cut(t["km"], n), scalar=1.0, in1=k, op0=ALU.add,
                                             op1=ALU.mult))
            st.link(tt(cut(t["t2"], n), r, cut(t["km"], n), ALU.mult))
            dve.tensor_tensor(cut(t["t2"], n), cut(t["t2"], n), bc("rk", n), ALU.mult).then_inc(S["rkk"], 1)
            dve.wait_ge(S["k_rn"], i + 1)
            st.link(tt(cut(t["kk"], n), cut(t["kk"], n), cut(t["nm"], n), ALU.mult))
            st.link(tt(cut(t["ra"], n), cut(t["kk"], n), cut(t["ra"], n), ALU.mult))
            dve.wait_ge(S["decays"], i + 1)
            if prompt:
                st.do(tt(t["A"][:, :, :], t["kk"][:, :, :], t["eX"][:, :, :], ALU.mult))
                st.do(tt(t["R"][:, :, :], r, t["eL"][:, :, :], ALU.mult))
                st.do(tt(t["K"][:, :, :], t["km"][:, :, :], t["eN"][:, :, :], ALU.mult))
                st.link(tt(t["B"][:, :, :], t["ra"][:, :, :], t["eN"][:, :, :], ALU.mult))
                dve.sem_inc(S["prepped"], 1)
            dve.wait_ge(S["bonus"], i + 1)
            st.link(tt(cut(t["bon"], n), ps[:, 4, 0:4 * n].rearrange("p (k w) -> p k w", k=4), v, ALU.mult))
            dve.sem_inc(S["bonus_used"], 1)
            if not prompt:
                dve.sem_inc(S["prepped"], 1)
            assert not prompt or st.n == PREP, st.n

        def finish_pe(pe, i, src, n):
            pe.wait_ge(S["o_copied"], i + 1)
            pe.matmul(ps[:, 7, 0:4 * n], halves, src, start=True, stop=True).then_inc(S["mean"], 1)
            pe.wait_ge(S["centered"], i + 1)
            pe.matmul(ps[:, 7, 0:4 * n], halves, cut(rs, n), start=True, stop=True).then_inc(S["var"], 1)

        def finish_dve(dve, i, src, n, out):
            st = Steps(dve, S["fin_step"], 6 * i)
            dve.wait_ge(S["mean"], i + 1)
            st.link(dve.scalar_tensor_tensor(out=cut(oc, n), in0=ps[:, 7, 0:4 * n].rearrange("p (k w) -> p k w", k=4),
                                             scalar=-1.0 / 64, in1=src, op0=ALU.mult, op1=ALU.add))
            dve.tensor_tensor(cut(rs, n), cut(oc, n), cut(oc, n), ALU.mult).then_inc(S["centered"], 1)
            dve.wait_ge(S["rstd"], i + 1)
            st.link(dve.tensor_tensor(cut(oc, n), cut(oc, n), cut(rs, n), ALU.mult))
            st.link(dve.tensor_tensor(cut(oc, n), cut(oc, n), bc("lnw", n), ALU.mult))
            st.link(dve.tensor_tensor(cut(oc, n), cut(oc, n), bc("lnb", n), ALU.add))
            st.link(dve.tensor_tensor(cut(oc, n), cut(oc, n), cut(t["bon"], n), ALU.add))
            st.link(dve.tensor_tensor(out, cut(oc, n), cut(t["g"], n), ALU.mult))
            dve.sem_inc(S["out_ready"], 1)
            assert st.n == 6

        def finish_act(act, i, n):
            act.wait_ge(S["var"], i + 1)
            act.activation(cut(rs, n), ps[:, 7, 0:4 * n].rearrange("p (k w) -> p k w", k=4), ACT.Ln, scale=1.0 / 64,
                           bias=T.vec("eps_gn")).then_inc(S["log_var"], 1)
            act.wait_ge(S["log_var"], i + 1)
            act.activation(cut(rs, n), cut(rs, n), ACT.Exp, scale=-0.5).then_inc(S["rstd"], 1)

        @block.gpsimd
        def _(pool):
            for a in (Ax, Rx, Bx):
                pool.memset(a[:, :, :, :], 0.0)
            pool.memset(Hx[:, :, :, :], 0.0).then_inc(S["cleared"], 1)
            pool.wait_ge(S["cleared"], 1)
            pool.sem_inc(S["h_ready"], 1)
            with pool.Fori(0, NPAIR) as i:
                pool.wait_ge(S["prepped"], i + 1)
                alone(pool, S["pool_passed"])
                for src, dst in ((t["A"], Ax), (t["B"], Bx), (t["R"], Rx)):
                    for e in range(2):
                        r = slice(64 * e, 64 * e + 64)
                        last = pool.tensor_copy(dst[r, :, e, :], src[r, :, :])
                last.then_inc(S["spread"], 1)
                pool.wait_ge(S["blocks_copied"], i + 1)
                for lv in range(1, 6):
                    last = pool.tensor_tensor(h8(mtl[:, lv - 1, :]), h8(mt[:, :]), m8(f"lev{lv}T"), ALU.mult)
                last.then_inc(S["blocks_ready"], 1)

        @block.tensor
        def _(pe):
            pe.wait_ge(S["lora_in"], 32)
            with pe.Fori(0, NPAIR) as i:
                prep_pe(pe, i, W)
                pe.wait_ge(S["prepped"], i + 1)
                for b, src in ((5, t["K"]), (6, t["B"]), (7, None)):
                    for k in range(4):
                        mm = pe.transpose(ps[:, b, k * P:(k + 1) * P], X[:, 8 + k, :] if src is None else src[:, k, :], ident)
                mm.then_inc(S["turned"], 1)
                pe.wait_ge(S["spread"], i + 1)
                pe.wait_ge(S["gate_copied"], i + 1)
                pe.wait_ge(S["bonus_used"], i + 1)

                def gram(bank, left, right):
                    for p in range(2):
                        for k in range(4):
                            c = slice(C * p, C * p + C)
                            mm = pe.matmul(ps[64 * p:64 * p + 64, bank, k * P:(k + 1) * P], left[:, k, c], right[:, k, :, c],
                                           start=True, stop=True)
                    mm.then_inc(S["gram"], 1)

                gram(1, t["B"], Ax)
                gram(2, t["A"], Bx)
                gram(0, t["K"], Ax)
                gram(3, t["K"], Rx)
                gram(4, t["B"], Rx)
                pe.wait_ge(S["tm_ready"], i + 1)
                solve_levels_pe(pe, T, S, i, mtl, xm, xt, y, (5, 6, 7), S["pe_passed"])
                pe.wait_ge(S["masked"], i + 1)
                pe.wait_ge(S["solved"], i + 1)
                for p in range(2):
                    r, c = slice(64 * p, 64 * p + 64), slice(C * p, C * p + C)
                    hc = lambda hd: slice(64 * hd, 64 * hd + 64)
                    pe.wait_ge(S["h_ready"], 2 * i + p + 1)
                    for k in range(4):
                        pe.matmul(ps[r, 0, k * P:(k + 1) * P], t["A"][:, k, c], Hx[:, k, :, :], start=True, stop=False,
                                  skip_group_check=True)
                        for hd in (2 * k, 2 * k + 1):
                            mm = pe.matmul(ps[r, 0, hc(hd)], ak[r, hc(hd)], vtm[r, hc(hd)], start=False, stop=True,
                                           skip_group_check=True)
                    mm.then_inc(S["w_done"], 1)
                    pe.wait_ge(S["w_copied"], 2 * i + p + 1)
                    alone(pe, S["pe_passed"])
                    for hd in range(8):
                        mm = pe.matmul(ps[r, 5, hc(hd)], xt[r, hc(hd)], r0[r, hc(hd)], start=True, stop=True)
                    mm.then_inc(S["u_done"], 1)
                    pe.wait_ge(S["u_copied"], 2 * i + p + 1)
                    alone(pe, S["pe_passed"])
                    for hd in range(8):
                        q = slice(64 * (hd % 2), 64 * (hd % 2) + 64)
                        k = hd // 2
                        pe.matmul(ps[q, 6, k * C:(k + 1) * C], ktm[r, hc(hd)], vtm[r, hc(hd)], start=True, stop=False,
                                  skip_group_check=True)
                        mm = pe.matmul(ps[q, 6, k * C:(k + 1) * C], btm[r, hc(hd)], u[r, hc(hd)], start=False, stop=True,
                                       skip_group_check=True)
                    for k in range(4):
                        oc_ = slice(k * P + C * p, k * P + C * p + C)
                        mm = pe.matmul(ps[:, 4, oc_], Hx[:, k, :, :].rearrange("p e v -> p (e v)"), t["R"][:, k, c],
                                       start=True, stop=False, skip_group_check=True)
                        for hd in (2 * k, 2 * k + 1):
                            q = slice(64 * (hd % 2), 64 * (hd % 2) + 64)
                            pe.matmul(ps[q, 4, oc_], vtm[r, hc(hd)], rk[r, hc(hd)], start=False, stop=False,
                                      skip_group_check=True)
                            mm = pe.matmul(ps[q, 4, oc_], u[r, hc(hd)], rb[r, hc(hd)], start=False, stop=True,
                                           skip_group_check=True)
                    mm.then_inc(S["h_done"], 1)
                finish_pe(pe, i, o[:, :, :], W)
            i = NPAIR
            prep_pe(pe, i, NS)
            pe.wait_ge(S["prepped"], i + 1)
            pe.wait_ge(S["gate_copied"], i + 1)
            for b, src in enumerate((t["kk"], t["eL"], t["ra"], t["km"], None, "v")):
                for k in range(4):
                    a = X[:, k, 0:NS] if src is None else X[:, 8 + k, 0:NS] if src == "v" else src[:, k, 0:NS]
                    mm = pe.transpose(ps[0:NS, b, k * P:(k + 1) * P], a, ident)
            mm.then_inc(S["smp_turned"], 1)
            pe.wait_ge(S["smp_back"], 16)
            pe.wait_ge(S["smp_rows"], 1)
            for k in range(4):
                mm = pe.transpose(ps[:, 6, k * NS:(k + 1) * NS], orow[:, k * P:(k + 1) * P], ident[0:NS, 0:NS])
            mm.then_inc(S["o_done"], 1)
            finish_pe(pe, i, ocol[:, :, :], NS)

        @block.scalar
        def _(act):
            with act.Fori(0, NPAIR) as i:
                prep_act(act, i, W)
                act.wait_ge(S["turned"], i + 1)
                act.activation(ktm[:, :], ps[:, 5, :], ACT.Copy)
                act.activation(btm[:, :], ps[:, 6, :], ACT.Copy, scale=-1.0)
                act.activation(vtm[:, :], ps[:, 7, :], ACT.Copy).then_inc(S["tm_ready"], 1)
                act.wait_ge(S["gram"], 5 * i + 1)
                act.activation(mt[:, :], ps[:, 1, :], ACT.Copy).then_inc(S["blocks_copied"], 1)
                solve_levels_act(act, T, S, i, y, (5, 6, 7))
                for p in range(2):
                    r = slice(64 * p, 64 * p + 64)
                    act.wait_ge(S["w_done"], 2 * i + p + 1)
                    act.activation(r0[r, :], ps[r, 0, :], ACT.Copy).then_inc(S["w_copied"], 1)
                    act.wait_ge(S["u_done"], 2 * i + p + 1)
                    act.activation(u[r, :], ps[r, 5, :], ACT.Copy).then_inc(S["u_copied"], 1)
                act.wait_ge(S["h_done"], 2 * i + 2)
                act.activation(o[:, :, :], ps[:, 4, :].rearrange("p (k w) -> p k w", k=4), ACT.Copy)\
                   .then_inc(S["o_copied"], 1)
                finish_act(act, i, W)
            i = NPAIR
            prep_act(act, i, NS)
            act.wait_ge(S["smp_turned"], 1)
            act.activation(smp[0:NS, :, :], ps[0:NS, 0:6, :], ACT.Copy).then_inc(S["smp_rows"], 1)
            act.wait_ge(S["o_done"], 1)
            act.activation(ocol[:, :, :], ps[:, 6, 0:4 * NS].rearrange("p (k w) -> p k w", k=4), ACT.Copy)\
               .then_inc(S["o_copied"], 1)
            finish_act(act, i, NS)

        @block.vector
        def _(dve):
            with dve.Fori(0, NPAIR) as i:
                prep_dve(dve, i, W, True)
                loop = Steps(dve, S["pstep"], 20 * i)
                dve.wait_ge(S["blocks_copied"], i + 1)
                loop.link(dve.tensor_tensor(h8(xt[:, :]), h8(ps[:, 1, :]), m8("lev0T"), ALU.mult))
                loop.do(dve.tensor_tensor(h8(xt[:, :]), m8("eye64"), h8(xt[:, :]), ALU.subtract))
                dve.wait_ge(S["gram"], 5 * i + 2)
                loop.link(dve.tensor_tensor(h8(xm[:, :]), h8(ps[:, 2, :]), m8("lev0"), ALU.mult))
                loop.link(dve.tensor_tensor(h8(xm[:, :]), m8("eye64"), h8(xm[:, :]), ALU.subtract))
                dve.sem_inc(S["x_ready"], 1)
                dve.wait_ge(S["gram"], 5 * i + 5)
                loop.do(dve.tensor_tensor(h8(ak[:, :]), h8(ps[:, 0, :]), m8("strictT"), ALU.mult))
                loop.do(dve.tensor_tensor(h8(rk[:, :]), h8(ps[:, 3, :]), m8("inclT"), ALU.mult))
                loop.link(dve.tensor_tensor(h8(rb[:, :]), h8(ps[:, 4, :]), m8("ninclT"), ALU.mult))
                dve.sem_inc(S["masked"], 1)
                solve_levels_dve(dve, T, S, loop, i, xm, xt, (5, 6, 7))
                for p in range(2):
                    dve.wait_ge(S["h_done"], 2 * i + p + 1)
                    for e in range(2):
                        r = slice(64 * e, 64 * e + 64)
                        st = dve.tensor_tensor(dh[r, :, :], Hx[r, :, e, :], ps[r, 6, 0:4 * C].rearrange("p (k v) -> p k v", k=4),
                                               ALU.add)
                        loop.do(st)
                    loop.settle()
                    end = C * p + C - 1
                    for e in range(2):
                        r = slice(64 * e, 64 * e + 64)
                        last = dve.tensor_tensor(Hx[r, :, e, :], dh[r, :, :],
                                                 t["eL"][r, :, end:end + 1].to_broadcast([64, 4, C]), ALU.mult)
                    last.then_inc(S["h_ready"], 1)
                assert loop.n == 20, loop.n
                finish_dve(dve, i, o[:, :, :], W, h[:, 4:8, bass.ds(i * W, W)])
            i = NPAIR
            prep_dve(dve, i, NS, False)
            st = Steps(dve, S["smp_step"])
            dve.wait_ge(S["smp_in"], 64)
            dve.wait_ge(S["lora_in"], 32)
            k3 = lambda n: kv[:, n, :].unsqueeze(2).to_broadcast([P, 64, 32])
            v3 = lambda a: a[:, :].unsqueeze(1).to_broadcast([P, 64, 32])
            s3, t3 = st8[:, :, :], tmp8[:, :, :]
            tt = lambda o_, a, b, op: st.link(dve.tensor_tensor(o_, a, b, op))
            tt(t3, s3, k3(0), ALU.mult)
            st.link(dve.tensor_reduce(sa[:, :], tmp8[:, :, :].rearrange("p k v -> p v k"), AX.X, ALU.add))
            tt(s3, s3, k3(1), ALU.mult)
            tt(t3, k3(2), v3(sa), ALU.mult)
            tt(s3, s3, t3, ALU.subtract)
            tt(t3, k3(3), v3(vv), ALU.mult)
            tt(s3, s3, t3, ALU.add)
            tt(t3, s3, k3(4), ALU.mult)
            st.link(dve.tensor_reduce(so[:, :], tmp8[:, :, :].rearrange("p k v -> p v k"), AX.X, ALU.add))
            dve.sem_inc(S["smp_done"], 1)
            finish_dve(dve, i, ocol[:, :, :], NS, h[:, 4:8, SEQ:TOK])
    sems.clear()


def odd_phase(T, ba):
    nc, h, ps, io = T.nc, T.h, T.ps, T.io
    sems = Sems(nc, "odd")
    w_in = [sems("w_in0"), sems("w_in1")]
    (row_out, row_free, product, row_in, conv_done, silu_done, step, cleared, ba_in, ba_exp, ba_log, ba_abs, ba_neg) = (
        sems(n) for n in ("row_out", "row_free", "product", "row_in", "conv_done", "silu_done", "step", "cleared",
                          "ba_in", "ba_exp", "ba_log", "ba_abs", "ba_neg"))
    PAR, NT = KT * P, ODD_T - 1
    with ExitStack() as ctx:
        sb = lambda n, s: ctx.enter_context(nc.sbuf_tensor("odd" + n, s, F32))
        w, row, cv = sb("_w", [P, 2, ODD_BLK]), sb("_row", [P, 2, 3 + TOK]), sb("_cv", [P, 2, TOK])
        sp1, sp2 = sb("_sp1", [P, TOK]), sb("_sp2", [P, TOK])
        block = ctx.enter_context(nc.Block())
        B8, A8 = slice(BETA_ROW, BETA_ROW + 8), slice(A_ROW, A_ROW + 8)

        @block.sync
        def _(sp):
            with sp.Fori(0, NT // 2) as i:
                for j in range(2):
                    sp.wait_ge(silu_done, 2 * i + j + 1)
                    sp.dma_start(w[:, j, :], io["w_odd"][bass.ds(2 * i + j, 1), :, :].rearrange("a p n -> (a p) n"))\
                      .then_inc(w_in[j], 16)
            sp.wait_ge(silu_done, NT + 1)
            sp.dma_start(w[:, 0, :], io["w_odd"][NT]).then_inc(w_in[0], 16)

        @block.tensor
        def _(pe):
            with pe.Fori(0, NT // 2) as i:
                for j in range(2):
                    pe.wait_ge(w_in[j], 16 * i + 16)
                    for c in range(GRP):
                        pe.wait_ge(row_in, 6 * i + 3 * j + c + 1)
                        group_products(pe, T, 3 * j + c, w[:, j, :], h, KT, c).then_inc(product, 1)
            pe.wait_ge(w_in[0], 16 * (NT // 2) + 16)
            for c in range(GRP):
                pe.wait_ge(row_in, 3 * NT + c + 1)
                group_products(pe, T, c, w[:, 0, :], h, KT, c).then_inc(product, 1)

        @block.scalar
        def _(act):
            act.sem_inc(row_in, 6)
            act.sem_inc(silu_done, 2)
            with act.Fori(0, NT // 2) as i:
                for j in range(2):
                    act.wait_ge(row_free, 2 * i + j + 1)
                    for c in range(GRP):
                        act.wait_ge(product, 6 * i + 3 * j + c + 1)
                        act.activation(row[:, j, 3 + c * GC:3 + (c + 1) * GC], ps[:, 3 * j + c, 0:GC], ACT.Copy)\
                           .then_inc(row_in, 1)
                    act.wait_ge(conv_done, 2 * i + j + 1)
                    act.activation(cv[:, j, :], cv[:, j, :], ACT.Silu).then_inc(silu_done, 1)
            for c in range(GRP):
                act.wait_ge(product, 3 * NT + c + 1)
                last = act.activation(ba[:, c * GC:(c + 1) * GC], ps[:, c, 0:GC], ACT.Copy)
            last.then_inc(ba_in, 1)
            act.wait_ge(ba_in, 1)
            act.activation(ba[B8, :], ba[B8, :], ACT.Exp, scale=-1.0)
            act.activation(sp1[A8, :], ba[A8, :], ACT.Identity, bias=T.vec("dt_bias")[A8, :]).then_inc(ba_exp, 1)
            act.wait_ge(ba_exp, 1)
            act.activation(sp2[A8, :], sp1[A8, :], ACT.Abs).then_inc(ba_abs, 1)
            act.wait_ge(ba_abs, 1)
            act.activation(sp2[A8, :], sp2[A8, :], ACT.Exp, scale=-1.0).then_inc(ba_abs, 1)
            act.wait_ge(ba_abs, 2)
            act.activation(sp2[A8, :], sp2[A8, :], ACT.Ln, bias=1.0)
            act.activation(row[A8, 0, 0:1], T.vec("a_log")[A8, :], ACT.Exp).then_inc(ba_log, 1)

        @block.vector
        def _(dve):
            dve.wait_ge(cleared, 1)
            per = 2 * 6
            with dve.Fori(0, NT // 2) as i:
                st = Steps(dve, step, i * per)
                for j in range(2):
                    tap = [w[:, j, PAR + n:PAR + n + 1] for n in range(4)]
                    kept = w[:, j, PAR + 4:PAR + 4 + 3 * NS].rearrange("p (r b) -> p r b", r=3)
                    dve.wait_ge(row_in, 6 * i + 3 * j + 3 + 6)
                    s = cv[:, j, SEQ:TOK]
                    o = cv[:, j, 0:SEQ]
                    st.do(dve.tensor_scalar(s, kept[:, 0, :], tap[0], None, ALU.mult))
                    st.link(dve.tensor_scalar(o, row[:, j, 0:SEQ], tap[0], None, ALU.mult))
                    for n in (1, 2):
                        st.do(dve.scalar_tensor_tensor(out=s, in0=kept[:, n, :], scalar=tap[n], in1=s, op0=ALU.mult,
                                                       op1=ALU.add))
                        st.link(dve.scalar_tensor_tensor(out=o, in0=row[:, j, n:n + SEQ], scalar=tap[n], in1=o,
                                                         op0=ALU.mult, op1=ALU.add))
                    dve.scalar_tensor_tensor(out=cv[:, j, :], in0=row[:, j, 3:3 + TOK], scalar=tap[3], in1=cv[:, j, :],
                                             op0=ALU.mult, op1=ALU.add).then_inc(conv_done, 1)
                assert st.n == per
            st = Steps(dve, step, per * NT // 2)
            dve.wait_ge(ba_exp, 1)
            st.link(dve.tensor_scalar(ba[B8, :], ba[B8, :], 1.0, None, ALU.add))
            st.do(dve.reciprocal(ba[B8, :], ba[B8, :]))
            dve.wait_ge(ba_log, 1)
            st.link(dve.scalar_tensor_tensor(out=sp1[A8, :], in0=sp1[A8, :], scalar=0.0, in1=sp2[A8, :], op0=ALU.max,
                                             op1=ALU.add))
            st.link(dve.tensor_scalar(sp1[A8, :], sp1[A8, :], row[A8, 0, 0:1], -1.0, ALU.mult, ALU.mult))
            st.do(dve.tensor_tensor_scan(ba[A8, 0:SEQ], T.const("scan64")[A8, :], sp1[A8, 0:SEQ], 0.0, ALU.mult, ALU.add))
            st.link(dve.tensor_copy(ba[A8, SEQ:TOK], sp1[A8, SEQ:TOK]))

        @block.gpsimd
        def _(pool):
            pool.memset(row[:, :, 0:3], 0.0).then_inc(cleared, 1)
            pool.sem_inc(row_free, 2)
            with pool.Fori(0, NT // 2) as i:
                for j in range(2):
                    pool.wait_ge(silu_done, 2 * i + j + 3)
                    pool.dma_start(T.odd_rows[bass.ds(2 * i + j, 1), :, :].rearrange("a p n -> (a p) n"),
                                   cv[:, j, :]).then_inc(row_out, 16)
                    pool.dma_start(io["dnconv_new"][bass.ds(2 * i + j, 1), :, :].rearrange("a p n -> (a p) n"),
                                   row[:, j, SEQ:SEQ + 3 + NS]).then_inc(row_out, 16)
                    pool.wait_ge(row_out, 64 * i + 32 * j + 32)
                    pool.sem_inc(row_free, 1)
    sems.clear()


def delta_phase(T, ba):
    nc, h, ps, io = T.nc, T.h, T.ps, T.io
    sems = Sems(nc, "dn")
    S = {n: sems(n) for n in (
        "rows_in", "squared", "sq_sum", "rn_log", "rn", "ba_cut", "spread", "l_copied", "l_exp", "unit", "turned", "k_copied",
        "ba_turned", "tm_ready", "kd_ready", "diff", "diff_exp", "keyed", "gram", "blocks_copied", "blocks_ready", "x_ready",
        "y_done", "y_ready", "z_done", "solved", "masked", "w_done", "r_ready", "u_done", "u_copied", "s_done", "s_ready",
        "o_copied", "o_sq", "o_sum", "rs_log", "rs", "out_ready", "step", "cleared", "pe_passed", "end_diff", "end_exp",
        "state_out")}
    ones, ident, sel = T.const("ones"), T.const("ident"), T.const("sel")
    W = 2 * C
    with ExitStack() as ctx:
        sb = lambda n, s: ctx.enter_context(nc.sbuf_tensor("dn" + n, s, F32))
        X = sb("_x", [P, 32, W])
        sq = sb("_sq", [P, 16, W])
        bs, bt, ek = sb("_bs", [P, W]), sb("_bt", [P, W]), sb("_ek", [P, 8])
        Lb, eL, kb, kbe, qe, ktm, bv, r0, vn, st_, tmp, o, rs = (sb("_" + n, [P, 8, W]) for n in
                                                              "Lb eL kb kbe qe ktm bv r0 vn S tmp o rs".split())
        dt_, dn, mt, xm, xt, y, at = (sb("_m" + n, [P, 512]) for n in "dt dn mt xm xt y at".split())
        mtl = sb("_mtl", [P, 5, 512])
        block = ctx.enter_context(nc.Block())
        m8 = lambda name: T.const(name).unsqueeze(1).to_broadcast([P, 8, C])
        h8 = lambda a: a.rearrange("p (h i) -> p h i", h=8)
        two = lambda b: ps[:, b:b + 2, :].rearrange("p b (h w) -> p (b h) w", h=4)
        bank = lambda b, hd: b + hd // 4
        col = lambda hd, a=0, n=W: slice((hd % 4) * W + a, (hd % 4) * W + a + n)
        hc = lambda hd: slice(64 * hd, 64 * hd + 64)

        @block.sync
        def _(sp):
            rows = T.odd_rows[0:32].rearrange("t p n -> p t n")
            sp.dma_start(X[:, :, :], rows[:, :, 0:W]).then_inc(S["rows_in"], 16)
            with sp.Fori(1, NPAIR) as i:
                sp.wait_ge(S["out_ready"], i)
                sp.dma_start(X[:, :, :], rows[:, :, bass.ds(i * W, W)]).then_inc(S["rows_in"], 16)
            sp.wait_ge(S["s_ready"], 2 * NPAIR + 1)
            sp.dma_start(io["dn_prompt"], st_[:, :, :]).then_inc(S["state_out"], 16)
            sp.wait_ge(S["state_out"], 16)

        @block.gpsimd
        def _(pool):
            pool.memset(st_[:, :, :], 0.0).then_inc(S["cleared"], 1)
            pool.wait_ge(S["cleared"], 1)
            pool.sem_inc(S["s_ready"], 1)
            with pool.Fori(0, NPAIR) as i:
                pool.wait_ge(S["blocks_copied"], i + 1)
                for lv in range(1, 6):
                    last = pool.tensor_tensor(h8(mtl[:, lv - 1, :]), h8(mt[:, :]), m8(f"lev{lv}T"), ALU.mult)
                last.then_inc(S["blocks_ready"], 1)

        @block.tensor
        def _(pe):
            with pe.Fori(0, NPAIR) as i:
                pe.wait_ge(S["squared"], i + 1)
                for b in range(4):
                    mm = pe.matmul(ps[:, b, :], ones, sq[:, 4 * b:4 * b + 4, :], start=True, stop=True)
                mm.then_inc(S["sq_sum"], 1)
                pe.wait_ge(S["ba_cut"], i + 1)
                for b, r in ((4, slice(A_ROW, A_ROW + 8)), (6, slice(BETA_ROW, BETA_ROW + 8))):
                    for hd in range(8):
                        mm = pe.matmul(ps[:, bank(b, hd), col(hd)], sel[r, hd * P:(hd + 1) * P], bs[r, :], start=True, stop=True)
                mm.then_inc(S["spread"], 1)
                pe.wait_ge(S["unit"], i + 1)
                for b, t0 in ((0, 8), (2, 16)):
                    for hd in range(8):
                        mm = pe.transpose(ps[:, bank(b, hd), col(hd)], X[:, t0 + hd, :], ident)
                pe.wait_ge(S["l_copied"], i + 1)
                mm = pe.transpose(ps[:, 4, 0:P], bs[:, :], ident)
                mm.then_inc(S["turned"], 1)
                pe.wait_ge(S["keyed"], i + 1)

                def gram(b, left, right):
                    for p in range(2):
                        c = slice(C * p, C * p + C)
                        for hd in range(8):
                            mm = pe.matmul(ps[64 * p:64 * p + 64, b, hc(hd)], left(hd)[:, c], right(hd)[:, c], start=True,
                                           stop=True)
                    mm.then_inc(S["gram"], 1)

                k_, q_, kb_ = (lambda hd: X[:, 8 + hd, :]), (lambda hd: X[:, hd, :]), (lambda hd: kb[:, hd, :])
                gram(5, k_, kb_)
                gram(6, kb_, k_)
                gram(7, k_, q_)
                pe.wait_ge(S["tm_ready"], i + 1)
                solve_levels_pe(pe, T, S, i, mtl, xm, xt, y, (0, 1, 2), S["pe_passed"])
                pe.wait_ge(S["masked"], i + 1)
                pe.wait_ge(S["solved"], i + 1)
                for p in range(2):
                    r, a = slice(64 * p, 64 * p + 64), C * p
                    c = slice(a, a + C)
                    pe.wait_ge(S["s_ready"], 2 * i + p + 1)
                    for hd in range(8):
                        mm = pe.matmul(ps[r, bank(0, hd), col(hd)], kbe[:, hd, c], st_[:, hd, :], start=True, stop=True)
                    mm.then_inc(S["w_done"], 1)
                    pe.wait_ge(S["r_ready"], 2 * i + p + 1)
                    alone(pe, S["pe_passed"])
                    for hd in range(8):
                        mm = pe.matmul(ps[r, bank(2, hd), col(hd)], xt[r, hc(hd)], r0[r, hd, :], start=True, stop=True)
                    mm.then_inc(S["u_done"], 1)
                    pe.wait_ge(S["u_copied"], 2 * i + p + 1)
                    alone(pe, S["pe_passed"])
                    for hd in range(8):
                        pe.matmul(ps[:, bank(6, hd), col(hd)], ktm[r, hd, :], vn[r, hd, :], start=True, stop=True)
                    for hd in range(8):
                        pe.matmul(ps[:, bank(4, hd), col(hd, a, C)], st_[:, hd, :], qe[:, hd, c], start=True, stop=False,
                                  skip_group_check=True)
                        mm = pe.matmul(ps[:, bank(4, hd), col(hd, a, C)], vn[r, hd, :], at[r, hc(hd)], start=False, stop=True,
                                       skip_group_check=True)
                    mm.then_inc(S["s_done"], 1)
                pe.wait_ge(S["o_sq"], i + 1)
                for b in range(2):
                    mm = pe.matmul(ps[:, b, :], ones, rs[:, 4 * b:4 * b + 4, :], start=True, stop=True)
                mm.then_inc(S["o_sum"], 1)

        @block.scalar
        def _(act):
            with act.Fori(0, NPAIR) as i:
                act.wait_ge(S["rows_in"], 16 * i + 16)
                act.activation(sq[:, :, :], X[:, 0:16, :], ACT.Square).then_inc(S["squared"], 1)
                act.wait_ge(S["sq_sum"], i + 1)
                act.activation(sq[:, :, :], ps[:, 0:4, :].rearrange("p b (h w) -> p (b h) w", h=4), ACT.Ln,
                               bias=T.vec("eps_rms")).then_inc(S["rn_log"], 1)
                act.wait_ge(S["rn_log"], i + 1)
                act.activation(sq[:, :, :], sq[:, :, :], ACT.Exp, scale=-0.5).then_inc(S["rn"], 1)
                act.wait_ge(S["spread"], i + 1)
                act.activation(Lb[:, :, :], two(4), ACT.Copy).then_inc(S["l_copied"], 1)
                act.wait_ge(S["l_copied"], i + 1)
                act.activation(eL[:, :, :], Lb[:, :, :], ACT.Exp).then_inc(S["l_exp"], 1)
                act.wait_ge(S["turned"], i + 1)
                act.activation(bt[:, :], ps[:, 4, 0:P], ACT.Copy).then_inc(S["ba_turned"], 1)
                act.wait_ge(S["end_diff"], i + 1)
                act.activation(ek[:, :], ek[:, :], ACT.Exp).then_inc(S["end_exp"], 1)
                act.wait_ge(S["diff"], i + 1)
                act.activation(dt_[:, :], dt_[:, :], ACT.Exp)
                act.activation(dn[:, :], dn[:, :], ACT.Exp).then_inc(S["diff_exp"], 1)
                solve_levels_act(act, T, S, i, y, (0, 1, 2))
                for p in range(2):
                    r = slice(64 * p, 64 * p + 64)
                    act.wait_ge(S["u_done"], 2 * i + p + 1)
                    act.activation(vn[r, :, :], ps[r, 2:4, :].rearrange("p b (h w) -> p (b h) w", h=4), ACT.Copy)\
                       .then_inc(S["u_copied"], 1)
                act.wait_ge(S["s_done"], 2 * i + 2)
                act.activation(o[:, :, :], two(4), ACT.Copy).then_inc(S["o_copied"], 1)
                act.wait_ge(S["o_copied"], i + 1)
                act.activation(rs[:, :, :], o[:, :, :], ACT.Square).then_inc(S["o_sq"], 1)
                act.wait_ge(S["o_sum"], i + 1)
                act.activation(rs[:, :, :], two(0), ACT.Ln, scale=1.0 / P, bias=T.vec("eps_rms")).then_inc(S["rs_log"], 1)
                act.wait_ge(S["rs_log"], i + 1)
                act.activation(rs[:, :, :], rs[:, :, :], ACT.Exp, scale=-0.5).then_inc(S["rs"], 1)

        @block.vector
        def _(dve):
            per = DN_STEPS
            with dve.Fori(0, NPAIR) as i:
                st = Steps(dve, S["step"], per * i)
                q_, k_ = X[:, 0:8, :], X[:, 8:16, :]
                dve.tensor_copy(bs[:, :], ba[:, bass.ds(i * W, W)]).then_inc(S["ba_cut"], 1)
                dve.wait_ge(S["rn"], i + 1)
                st.do(dve.scalar_tensor_tensor(out=q_, in0=q_, scalar=P ** -0.5, in1=sq[:, 0:8, :], op0=ALU.mult,
                                               op1=ALU.mult))
                st.link(dve.tensor_tensor(k_, k_, sq[:, 8:16, :], ALU.mult))
                dve.sem_inc(S["unit"], 1)
                dve.wait_ge(S["spread"], i + 1)
                st.link(dve.tensor_tensor(kb[:, :, :], k_, two(6), ALU.mult))
                dve.wait_ge(S["l_exp"], i + 1)
                st.do(dve.tensor_tensor(kbe[:, :, :], kb[:, :, :], eL[:, :, :], ALU.mult))
                st.link(dve.tensor_tensor(qe[:, :, :], q_, eL[:, :, :], ALU.mult))
                dve.sem_inc(S["keyed"], 1)
                dve.wait_ge(S["ba_turned"], i + 1)
                for p in range(2):
                    r = slice(64 * p, 64 * p + 64)
                    end = C * p + C - 1
                    lt = bt[r, A_ROW:A_ROW + 8]
                    st.do(dve.tensor_tensor(ek[r, :].unsqueeze(2), Lb[r, :, end:end + 1], lt.unsqueeze(2), ALU.subtract))
                    st.do(dve.tensor_tensor(h8(dt_[r, :]), Lb[r, :, C * p:C * p + C], lt.unsqueeze(2).to_broadcast([64, 8, C]),
                                            ALU.subtract))
                st.settle()
                dve.sem_inc(S["end_diff"], 1)
                st.link(dve.tensor_scalar(dn[:, :], dt_[:, :], -1.0, 0.0, ALU.mult, ALU.min))
                st.link(dve.tensor_scalar(dt_[:, :], dt_[:, :], 0.0, None, ALU.min))
                dve.sem_inc(S["diff"], 1)
                b8 = bt[:, BETA_ROW:BETA_ROW + 8].unsqueeze(2).to_broadcast([P, 8, W])
                st.do(dve.tensor_tensor(bv[:, :, :], two(2), b8, ALU.mult))
                dve.wait_ge(S["end_exp"], i + 1)
                st.do(dve.tensor_tensor(ktm[:, :, :], two(0), ek[:, :].unsqueeze(2).to_broadcast([P, 8, W]), ALU.mult))
                st.settle()
                dve.sem_inc(S["tm_ready"], 1)
                dve.wait_ge(S["gram"], 3 * i + 3)
                dve.wait_ge(S["diff_exp"], i + 1)
                st.do(dve.tensor_tensor(mt[:, :], dt_[:, :], ps[:, 5, :], ALU.mult))
                st.do(dve.tensor_tensor(xm[:, :], dn[:, :], ps[:, 6, :], ALU.mult))
                st.link(dve.tensor_tensor(at[:, :], dt_[:, :], ps[:, 7, :], ALU.mult))
                dve.sem_inc(S["blocks_copied"], 1)
                st.do(dve.tensor_tensor(h8(xt[:, :]), h8(mt[:, :]), m8("lev0T"), ALU.mult))
                st.link(dve.tensor_tensor(h8(xm[:, :]), h8(xm[:, :]), m8("lev0"), ALU.mult))
                st.do(dve.tensor_tensor(h8(xt[:, :]), m8("eye64"), h8(xt[:, :]), ALU.subtract))
                st.link(dve.tensor_tensor(h8(xm[:, :]), m8("eye64"), h8(xm[:, :]), ALU.subtract))
                dve.sem_inc(S["x_ready"], 1)
                st.link(dve.tensor_tensor(h8(at[:, :]), h8(at[:, :]), m8("inclT"), ALU.mult))
                dve.sem_inc(S["masked"], 1)
                solve_levels_dve(dve, T, S, st, i, xm, xt, (0, 1, 2))
                for p in range(2):
                    r = slice(64 * p, 64 * p + 64)
                    dve.wait_ge(S["w_done"], 2 * i + p + 1)
                    st.link(dve.tensor_tensor(r0[r, :, :], bv[r, :, :],
                                              ps[r, 0:2, :].rearrange("p b (h w) -> p (b h) w", h=4), ALU.subtract))
                    dve.sem_inc(S["r_ready"], 1)
                    end = C * p + C - 1
                    dve.wait_ge(S["u_copied"], 2 * i + p + 1)
                    st.link(dve.tensor_tensor(tmp[:, :, :], st_[:, :, :], eL[:, :, end:end + 1].to_broadcast([P, 8, W]),
                                              ALU.mult))
                    dve.wait_ge(S["s_done"], 2 * i + p + 1)
                    st.link(dve.tensor_tensor(st_[:, :, :], tmp[:, :, :], two(6), ALU.add))
                    dve.sem_inc(S["s_ready"], 1)
                dve.wait_ge(S["rs"], i + 1)
                st.link(dve.scalar_tensor_tensor(out=o[:, :, :], in0=o[:, :, :], scalar=T.vec("onorm"), in1=rs[:, :, :],
                                                 op0=ALU.mult, op1=ALU.mult))
                st.link(dve.tensor_tensor(h[:, :, bass.ds(i * W, W)], o[:, :, :], X[:, 24:32, :], ALU.mult))
                dve.sem_inc(S["out_ready"], 1)
                assert st.n == per, st.n
    sems.clear()


DN_STEPS = 38


def delta_samples_phase(T, ba):
    nc, h, ps, io = T.nc, T.h, T.ps, T.io
    sems = Sems(nc, "ds")
    S = {n: sems(n) for n in ("rows_in", "state_in", "squared", "sq_sum", "rn_log", "rn", "unit", "turned", "copied",
                              "stored", "loaded", "decay", "o_ready", "o_stored", "o_back", "o_turned", "o_copied", "o_sq",
                              "o_sum", "rs_log", "rs", "step")}
    ones, ident = T.const("ones"), T.const("ident")
    with ExitStack() as ctx:
        sb = lambda n, s: ctx.enter_context(nc.sbuf_tensor("ds" + n, s, F32))
        X, sq = sb("_x", [P, 32, NS]), sb("_sq", [P, 16, NS])
        rows, barow = sb("_rows", [NS, 3 * 1024]), sb("_barow", [NS, P])
        kr, qr, vr, br, gr = sb("_kr", [P, P]), sb("_qr", [P, P]), sb("_vr", [P, 64]), sb("_br", [P, 1]), sb("_gr", [P, 1])
        s3, t3 = sb("_s", [P, P, 64]), sb("_t", [P, P, 64])
        sa, so = sb("_sa", [P, 64]), sb("_so", [P, 64])
        orow, o, rs = sb("_orow", [NS, 1024]), sb("_o", [P, 8, NS]), sb("_rs", [P, 8, NS])
        scr = nc.dram_tensor("scratch_dn_rows", [3, NS, 1024], F32, kind="Internal").ap()
        scr_b = nc.dram_tensor("scratch_dn_ba", [2, NS, 8], F32, kind="Internal").ap()
        scr_o = nc.dram_tensor("scratch_dn_o", [NS, 1024], F32, kind="Internal").ap()
        block = ctx.enter_context(nc.Block())

        @block.sync
        def _(sp):
            sp.dma_start(X[:, :, :], T.odd_rows[0:32, :, SEQ:TOK].rearrange("t p n -> p t n")).then_inc(S["rows_in"], 16)
            sp.dma_start(s3[:, :, :], io["dn_in"].rearrange("p (k v) -> p k v", k=P)).then_inc(S["state_in"], 16)
            sp.wait_ge(S["copied"], 1)
            sp.dma_start(scr.rearrange("a b n -> b a n"), rows[:, :].rearrange("b (a n) -> b a n", a=3)).then_inc(S["stored"], 16)
            sp.dma_start(scr_b[0], barow[:, BETA_ROW:BETA_ROW + 8]).then_inc(S["stored"], 16)
            sp.dma_start(scr_b[1], barow[:, A_ROW:A_ROW + 8]).then_inc(S["stored"], 16)
            sp.wait_ge(S["stored"], 48)
            for e in range(2):
                r = slice(64 * e, 64 * e + 64)
                for dst, src in ((qr[r, :], scr[0].rearrange("b (h k) -> (b h) k", h=8)),
                                 (kr[r, :], scr[1].rearrange("b (h k) -> (b h) k", h=8)),
                                 (vr[r, :], scr[2].rearrange("b (h e v) -> e (b h) v", h=8, e=2)[e]),
                                 (br[r, :], scr_b[0].rearrange("b (h a) -> (b h) a", a=1)),
                                 (gr[r, :], scr_b[1].rearrange("b (h a) -> (b h) a", a=1))):
                    sp.dma_start(dst, src).then_inc(S["loaded"], 16)
            sp.wait_ge(S["o_ready"], 1)
            for e in range(2):
                sp.dma_start(scr_o.rearrange("b (h e v) -> e (b h) v", h=8, e=2)[e], so[64 * e:64 * e + 64, :])\
                  .then_inc(S["o_stored"], 16)
            sp.wait_ge(S["o_stored"], 32)
            sp.dma_start(orow[:, :], scr_o).then_inc(S["o_back"], 16)
            sp.dma_start(io["dn_new"].rearrange("p (k v) -> p k v", k=P), s3[:, :, :]).then_inc(S["o_stored"], 16)
            sp.wait_ge(S["o_stored"], 48)

        @block.tensor
        def _(pe):
            pe.wait_ge(S["squared"], 1)
            pe.matmul(ps[:, 0, 0:16 * NS], ones, sq[:, :, :], start=True, stop=True).then_inc(S["sq_sum"], 1)
            pe.wait_ge(S["unit"], 1)
            for k in range(24):
                pe.transpose(ps[0:NS, 1 + k // 4, (k % 4) * P:(k % 4 + 1) * P], X[:, k, :], ident)
            pe.transpose(ps[0:NS, 7, 0:P], ba[:, SEQ:TOK], ident).then_inc(S["turned"], 1)
            pe.wait_ge(S["o_back"], 16)
            for k in range(8):
                mm = pe.transpose(ps[:, 0, k * NS:(k + 1) * NS], orow[:, k * P:(k + 1) * P], ident[0:NS, 0:NS])
            mm.then_inc(S["o_turned"], 1)
            pe.wait_ge(S["o_sq"], 1)
            pe.matmul(ps[:, 1, 0:8 * NS], ones, rs[:, :, :], start=True, stop=True).then_inc(S["o_sum"], 1)

        @block.scalar
        def _(act):
            act.wait_ge(S["rows_in"], 16)
            act.activation(sq[:, :, :], X[:, 0:16, :], ACT.Square).then_inc(S["squared"], 1)
            act.wait_ge(S["sq_sum"], 1)
            act.activation(sq[:, :, :], ps[:, 0, 0:16 * NS].rearrange("p (h w) -> p h w", h=16), ACT.Ln,
                           bias=T.vec("eps_rms")).then_inc(S["rn_log"], 1)
            act.wait_ge(S["rn_log"], 1)
            act.activation(sq[:, :, :], sq[:, :, :], ACT.Exp, scale=-0.5).then_inc(S["rn"], 1)
            act.wait_ge(S["turned"], 1)
            act.activation(rows[:, :].rearrange("b (a n) -> b a n", a=6), ps[0:NS, 1:7, :], ACT.Copy)
            act.activation(barow[:, :], ps[0:NS, 7, 0:P], ACT.Copy).then_inc(S["copied"], 1)
            act.wait_ge(S["loaded"], 160)
            act.activation(gr[:, :], gr[:, :], ACT.Exp).then_inc(S["decay"], 1)
            act.wait_ge(S["o_turned"], 1)
            act.activation(o[:, :, :], ps[:, 0, 0:8 * NS].rearrange("p (h w) -> p h w", h=8), ACT.Copy).then_inc(S["o_copied"], 1)
            act.wait_ge(S["o_copied"], 1)
            act.activation(rs[:, :, :], o[:, :, :], ACT.Square).then_inc(S["o_sq"], 1)
            act.wait_ge(S["o_sum"], 1)
            act.activation(rs[:, :, :], ps[:, 1, 0:8 * NS].rearrange("p (h w) -> p h w", h=8), ACT.Ln, scale=1.0 / P,
                           bias=T.vec("eps_rms")).then_inc(S["rs_log"], 1)
            act.wait_ge(S["rs_log"], 1)
            act.activation(rs[:, :, :], rs[:, :, :], ACT.Exp, scale=-0.5).then_inc(S["rs"], 1)

        @block.vector
        def _(dve):
            st = Steps(dve, S["step"])
            dve.wait_ge(S["rn"], 1)
            st.do(dve.scalar_tensor_tensor(out=X[:, 0:8, :], in0=X[:, 0:8, :], scalar=P ** -0.5, in1=sq[:, 0:8, :],
                                           op0=ALU.mult, op1=ALU.mult))
            st.link(dve.tensor_tensor(X[:, 8:16, :], X[:, 8:16, :], sq[:, 8:16, :], ALU.mult))
            dve.sem_inc(S["unit"], 1)
            dve.wait_ge(S["decay"], 1)
            dve.wait_ge(S["state_in"], 16)
            k3, q3 = (a[:, :].unsqueeze(2).to_broadcast([P, P, 64]) for a in (kr, qr))
            s, t = s3[:, :, :], t3[:, :, :]
            over_k = t3[:, :, :].rearrange("p k v -> p v k")
            st.link(dve.tensor_tensor(t, s, k3, ALU.mult))
            st.link(dve.tensor_reduce(sa[:, :], over_k, AX.X, ALU.add))
            st.link(dve.tensor_scalar(sa[:, :], sa[:, :], gr[:, 0:1], None, ALU.mult))
            st.link(dve.tensor_tensor(sa[:, :], vr[:, :], sa[:, :], ALU.subtract))
            st.link(dve.tensor_scalar(sa[:, :], sa[:, :], br[:, 0:1], None, ALU.mult))
            st.link(dve.tensor_tensor(t, k3, sa[:, :].unsqueeze(1).to_broadcast([P, P, 64]), ALU.mult))
            st.link(dve.scalar_tensor_tensor(out=s, in0=s, scalar=gr[:, 0:1], in1=t, op0=ALU.mult, op1=ALU.add))
            st.link(dve.tensor_tensor(t, s, q3, ALU.mult))
            st.link(dve.tensor_reduce(so[:, :], over_k, AX.X, ALU.add))
            dve.sem_inc(S["o_ready"], 1)
            dve.wait_ge(S["rs"], 1)
            st.link(dve.scalar_tensor_tensor(out=o[:, :, :], in0=o[:, :, :], scalar=T.vec("onorm"), in1=rs[:, :, :],
                                             op0=ALU.mult, op1=ALU.mult))
            st.link(dve.tensor_tensor(h[:, :, SEQ:TOK], o[:, :, :], X[:, 24:32, :], ALU.mult))
    sems.clear()


def store_phase(T):
    sems = Sems(T.nc, "store")
    stored = sems("stored")
    with T.nc.Block() as block:
        @block.sync
        def _(sp):
            sp.dma_start(T.io["y"].rearrange("(k p) t -> p k t", p=P), T.x[:, :, :]).then_inc(stored, 16)
            sp.wait_ge(stored, 16)
    sems.clear()


def trunk_program(nc, io):
    with ExitStack() as ctx:
        T = Trunk(nc, io, ctx)
        T.n_phys = io["k_pages"].shape[0]
        T.xs_rows = nc.dram_tensor("scratch_xs_rows", [NB_T, P, TOK], F32, kind="Internal").ap()
        T.odd_rows = nc.dram_tensor("scratch_odd_rows", [ODD_T - 1, P, TOK], F32, kind="Internal").ap()
        load_phase(T)
        norm_phase(T, "norm0", "norm_even")
        qk_phase(T)
        v_phase(T)
        pb_phase(T)
        pages_phase(T)
        attention_phase(T)
        rwkv_phase(T)
        residual_phase(T, "out0", io["w_out_even"], T.h, KT)
        ffn(T, 0)
        norm_phase(T, "norm1", "norm_odd")
        with nc.sbuf_tensor("ba", [P, TOK], F32) as ba:
            odd_phase(T, ba)
            delta_phase(T, ba)
            delta_samples_phase(T, ba)
        residual_phase(T, "out1", io["w_out_odd"], T.h, KT)
        ffn(T, 1)
        store_phase(T)


def ffn(T, l):
    norm_phase(T, f"normf{l}", f"norm_ffn{l}")
    with T.nc.sbuf_tensor(f"ffn_a{l}", [P, FT, TOK], F32) as a:
        ffn_up_phase(T, f"up{l}", l, a)
        residual_phase(T, f"down{l}", T.io["w_down"][l], a, FT)


OUTS = {
    "y": (D_MODEL, TOK), "qk_rows": (8, P, TOK), "v_rows": (TOK, D_A), "shift_new": (NB_T, P, 1 + NS),
    "wkv_prompt": (2, 64, 4, 64), "wkv_new": (P, 64 * 32), "dn_prompt": (P, 8, P), "dn_new": (P, P * 64),
    "dnconv_new": (ODD_T - 1, P, 3 + NS), "dnconv_old": (NS, 2, QKV_T * P), "ffnconv_new": (2, FT, P, 2 + NS),
    "ffnconv_old": (2, NS, 1, D_FF),
}


def outputs(r):
    y = r["y"].T
    kk = r["qk_rows"][4:].reshape(D_A, TOK).T
    v = r["v_rows"]
    shift = r["shift_new"].reshape(NB_COLS, 1 + NS).T
    dnc = r["dnconv_new"][:QKV_T].reshape(QKV_T * P, 3 + NS).T
    ffc = r["ffnconv_new"].reshape(2, D_FF, 2 + NS).transpose(0, 2, 1)
    return (
        y[:SEQ].reshape(1, SEQ, D_MODEL), y[SEQ:].reshape(NS, 1, D_MODEL),
        kk[:SEQ].reshape(1, 1, SEQ, H_A, DH), v[:SEQ].reshape(1, 1, SEQ, H_A, DH),
        kk[SEQ:].reshape(1, NS, 1, H_A, DH), v[SEQ:].reshape(1, NS, 1, H_A, DH),
        r["wkv_prompt"].transpose(2, 0, 3, 1).reshape(1, 1, 8, 64, 64),
        r["wkv_new"].reshape(2, NS, 8, 64, 32).transpose(1, 2, 0, 4, 3).reshape(1, NS, 8, 64, 64),
        shift[:1].reshape(1, 1, NB_COLS), shift[1:].reshape(1, NS, NB_COLS),
        r["dn_prompt"].transpose(1, 0, 2).reshape(1, 1, 8, P, P),
        r["dn_new"].reshape(2, NS, 8, P, 64).transpose(1, 2, 3, 0, 4).reshape(1, NS, 8, P, P),
        dnc[:3].reshape(1, 1, 3, QKV_T * P),
        np.concatenate([r["dnconv_old"], dnc[3:, None]], 1)[None],
        ffc[:, None, :2], np.concatenate([r["ffnconv_old"], ffc[:, 2:, None]], 2),
    )


def layouts(inputs):
    A = {k: np.asarray(v) for k, v in inputs.items()}
    f = np.float32

    def blocks(w, nt=None):
        k, n = w.shape
        return w.reshape(k // P, P, n // P, P).transpose(2, 1, 0, 3).reshape(n // P, P, k)

    def cols(v):
        return v.reshape(-1, P).T

    def tiles(rows):
        return rows.T.reshape(-1, P, rows.shape[0])

    L = {"consts": CONSTS}
    L["x"] = np.concatenate([A["x_prompt"][0], A["x_sample"][:, 0]], 0).T
    one = np.ones((P, 1), f)
    row32 = lambda v: np.concatenate([np.zeros(A_ROW, f), v, np.zeros(P - A_ROW - 8, f)])[:, None]
    vec = {
        "norm_even": cols(A["norm_mix_even"][0]), "norm_ffn0": cols(A["norm_ffn"][0]),
        "norm_odd": cols(A["norm_mix_odd"][0]), "norm_ffn1": cols(A["norm_ffn"][1]),
        "w0": cols(A["w0_b"][0]), "a0": cols(A["a0_b"][0]), "kk": cols(A["kk_b"][0]), "ka": cols(A["ka_b"][0]),
        "rk": cols(A["rk_b"][0]), "lnw": cols(A["lnx_w_b"][0]), "lnb": cols(A["lnx_b_b"][0]),
        "onorm": A["onorm_dn"][0][:, None], "sb_bias": np.broadcast_to(A["sb_bias"][0], (P, 8)),
        "a_log": row32(A["a_log_dn"][0]), "dt_bias": row32(A["dt_bias_dn"][0]),
        "eps_rms": one * f(RMS_EPS), "eps_gn": one * f(GN_EPS),
    }
    L["vecs"] = np.concatenate([vec[n] for n in VEC_COLS], 1)
    we = A["w_in_even"][0]
    gain = np.concatenate([np.tile(A["qnorm_a"][0], (8,)), np.tile(A["knorm_a"][0], (8,))])
    L["w_qk"] = np.concatenate([blocks(we[:, :2 * D_A]), tiles(gain[None])], 2)
    L["w_v"] = we[:, 2 * D_A:3 * D_A].reshape(KT, P, D_A).transpose(1, 0, 2)
    L["w_pb"] = np.concatenate([blocks(we[:, 3 * D_A:]), tiles(A["mu_b"]), tiles(A["state_shift"][0])], 2)
    L["w_lora"] = np.concatenate([np.concatenate([A["w_up_b"][0], A["a_up_b"][0]], 0), A["g_up_b"][0]], 1)
    L["w_out_even"] = blocks(A["w_out_even"][0])
    wo = A["w_in_odd"][0]
    n = QKV_T * P + 8 * P
    ba = np.zeros((D_MODEL, P), f)
    ba[:, BETA_ROW:BETA_ROW + 8] = wo[:, n:n + 8]
    ba[:, A_ROW:A_ROW + 8] = wo[:, n + 8:]
    par = np.zeros((ODD_T, P, 4 + 3 * NS), f)
    par[:QKV_T, :, :4] = tiles(A["conv_dn"][0])
    par[QKV_T:ODD_T - 1, :, 3] = 1.0
    par[:QKV_T, :, 4:] = tiles(A["state_dn_conv"][0].transpose(1, 0, 2).reshape(3 * NS, -1))
    L["w_odd"] = np.concatenate([blocks(np.concatenate([wo[:, :n], ba], 1)), par], 2)
    L["w_out_odd"] = blocks(A["w_out_odd"][0])
    L["w_ff"] = np.stack([np.concatenate([
        blocks(A["w_gate"][l]), blocks(A["w_up"][l]), tiles(A["conv_ffn"][l]), tiles(A["conv_ffn_b"][l][None]),
        tiles(A["state_ffn_conv"][l].transpose(1, 0, 2).reshape(2 * NS, -1))], 2) for l in range(2)])
    L["w_down"] = np.stack([blocks(A["w_down"][l]) for l in range(2)])
    L["k_pages"] = A["cache_k"][0].reshape(-1, PAGE, D_A)
    L["v_pages"] = A["cache_v"][0].reshape(-1, PAGE, D_A)
    L["page_table"] = A["page_table"][:, ::-1].reshape(1, -1)
    L["wkv_in"] = A["state_wkv"][0].reshape(NS, 8, 2, 32, 64).transpose(2, 0, 1, 4, 3).reshape(P, 64 * 32)
    L["dn_in"] = A["state_dn"][0].reshape(NS, 8, 128, 2, 64).transpose(3, 0, 1, 2, 4).reshape(P, 128 * 64)
    L["dn_conv_rows"] = A["state_dn_conv"][0, :, 1:]
    L["ffn_conv_rows"] = A["state_ffn_conv"][:, :, 1:]
    return {k: np.ascontiguousarray(v) for k, v in L.items()}


def kernel(**inputs):
    import concourse.bacc as bacc
    from concourse.bass_utils import run_bass_kernel_spmd

    nc = bacc.Bacc("TRN2", target_bir_lowering=False, num_devices=1)
    arrays, io = {}, {}
    for name, a in layouts(inputs).items():
        arrays[f"in_{name}"] = a
        io[name] = nc.dram_tensor(f"in_{name}", a.shape, mybir.dt.from_np(a.dtype), kind="ExternalInput").ap()
    for name, shape in OUTS.items():
        io[name] = nc.dram_tensor(f"out_{name}", shape, F32, kind="ExternalOutput").ap()
    trunk_program(nc, io)
    r = run_bass_kernel_spmd(nc, [arrays], core_ids=[0]).results[0]
    return tuple(np.ascontiguousarray(a) for a in outputs({n: r[f"out_{n}"] for n in OUTS}))
```

```python
from contextlib import ExitStack

import concourse.bass as bass
import numpy as np
from concourse import mybir

F32 = mybir.dt.float32
F32R = mybir.dt.float32r
I32 = mybir.dt.int32
ALU = mybir.AluOpType
ACT = mybir.ActivationFunctionType
AX = mybir.AxisListType

P = 128
D_MODEL = 1024
SEQ = 1024
NS = 8
TOK = SEQ + NS
GRP = 3
GC = TOK // GRP
KT = D_MODEL // P
H_A, DH = 8, 64
D_A = H_A * DH
PAST, PAGE = 8192, 128
NPG = PAST // PAGE
D_B = 512
NB_COLS = 3 * D_B + 256
NB_T = NB_COLS // P
H_C = 8
QKV_T = 24
ODD_T = QKV_T + 8 + 1
BETA_ROW, A_ROW = 0, 32
D_FF = 2816
FT = D_FF // P
C = 64
NPAIR = SEQ // (2 * C)
RMS_EPS = 1e-6
GN_EPS = 64e-5
DECAY = float(np.exp(-0.5))

EXP_LN_SET = "natural_log_exp_and_others"

QK_BLK = KT * P + 1
PB_BLK = KT * P + 1 + NS
ODD_BLK = KT * P + 4 + 3 * NS
FF_BLK = 2 * KT * P + 4 + 2 * NS

CONST_COLS = {}


def _constants():
    parts = {}
    r = np.arange(P)
    parts["ident"] = np.eye(P)
    parts["halves"] = (r[:, None] // 64 == r[None, :] // 64) * 1.0
    parts["later"] = (r[:, None] >= r[None, :]) * 1.0
    parts["earlier"] = (r[:, None] < r[None, :]) * 1.0
    parts["dcap"] = np.where(r[:, None] < r[None, :], 3e38, -1e30)
    j, i = r[:, None] % C, np.arange(C)[None, :]
    parts["strictT"] = (j < i) * 1.0
    parts["inclT"] = (j <= i) * 1.0
    parts["ninclT"] = (j <= i) * -1.0
    parts["eye64"] = (j == i) * 1.0
    for lv in range(6):
        b = 1 << lv
        parts[f"lev{lv}T"] = ((j // (2 * b) == i // (2 * b)) & (j % (2 * b) < b) & (i % (2 * b) >= b)) * 1.0
    b = 1
    parts["lev0"] = ((j // 2 == i // 2) & (i % 2 < 1) & (j % 2 >= 1)) * 1.0
    parts["scan64"] = np.broadcast_to((np.arange(SEQ) % C != 0) * 1.0, (P, SEQ))
    parts["scanhead"] = np.broadcast_to((np.arange(512) % NPG != 0) * 1.0, (P, 512))
    sel = np.zeros((P, 8 * P))
    for h in range(8):
        sel[A_ROW + h, h * P:(h + 1) * P] = 1.0
        sel[BETA_ROW + h, h * P:(h + 1) * P] = 1.0
    parts["sel"] = sel
    at = 0
    for n, a in parts.items():
        CONST_COLS[n] = (at, a.shape[1])
        at += a.shape[1]
    return np.concatenate(list(parts.values()), axis=1).astype(np.float32)


CONSTS = _constants()
CONSTS_0 = CONST_COLS["sel"][0]
ONES = np.ones((P, P), np.float32)
VEC_COLS = {}
for _n, _w in (("norm_even", 8), ("norm_ffn0", 8), ("norm_odd", 8), ("norm_ffn1", 8), ("w0", 4), ("a0", 4),
               ("kk", 4), ("ka", 4), ("rk", 4), ("lnw", 4), ("lnb", 4), ("onorm", 1), ("sb_bias", 8),
               ("a_log", 1), ("dt_bias", 1), ("eps_rms", 1), ("eps_gn", 1)):
    VEC_COLS[_n] = (sum(w for _, w in VEC_COLS.values()), _w)
NVEC = sum(w for _, w in VEC_COLS.values())


class Sems:

    def __init__(self, nc, phase):
        self.nc, self.phase, self.all = nc, phase, []

    def __call__(self, name):
        s = self.nc.alloc_semaphore(f"{self.phase}_{name}")
        self.all.append(s)
        return s

    def clear(self):
        self.nc.clear_and_free_semaphores(self.all)
        self.nc.all_engine_barrier()


class Steps:

    def __init__(self, eng, sem, at=0):
        self.eng, self.sem, self.at, self.n = eng, sem, at, 0

    def do(self, ins):
        ins.then_inc(self.sem, 1)
        self.n += 1

    def settle(self):
        self.eng.wait_ge(self.sem, self.at + self.n)

    def link(self, ins):
        self.do(ins)
        self.settle()


class Trunk:

    def __init__(self, nc, io, ctx):
        self.nc, self.io = nc, io
        self.ones = ctx.enter_context(nc.sbuf_tensor("ones_sb", [P, P], F32))
        self.vecs = ctx.enter_context(nc.sbuf_tensor("vecs_sb", [P, NVEC], F32))
        self.ps = ctx.enter_context(nc.psum_tensor("ps", [P, 8, 512], F32))

    def const(self, name):
        if name == "ones":
            return self.ones[:, :]
        a, w = CONST_COLS[name]
        return self.consts[:, a:a + w]

    def vec(self, name):
        a, w = VEC_COLS[name]
        return self.vecs[:, a:a + w]


def load_phase(T):
    nc, io = T.nc, T.io
    sems = Sems(nc, "load")
    loaded = sems("loaded")
    with nc.Block() as block:
        @block.sync
        def _(sp):
            sp.dma_start(T.ones[:, :], io["ones"]).then_inc(loaded, 16)
            sp.dma_start(T.vecs[:, :], io["vecs"]).then_inc(loaded, 16)
            sp.dma_start(io["dnconv_old"], io["dn_conv_rows"]).then_inc(loaded, 16)
            sp.dma_start(io["ffnconv_old"], io["ffn_conv_rows"]).then_inc(loaded, 16)
            sp.wait_ge(loaded, 64)
    sems.clear()


def norm_phase(T, name, gain, x_dram, consts=False):
    nc, ps, hh, hl = T.nc, T.ps, T.hh, T.hl
    sems = Sems(nc, name)
    x_in = [sems(f"x_in{k}") for k in range(KT)]
    squared, summed, logged, rooted, sq_used, scaled, rounded, consts_in = (
        sems(n) for n in ("squared", "summed", "logged", "rooted", "sq_used", "scaled", "rounded", "consts_in"))
    ones, g = T.const("ones"), T.vec(gain)
    with ExitStack() as ctx:
        sb = lambda n, s: ctx.enter_context(nc.sbuf_tensor(name + n, s, F32))
        x, sq, rinv = sb("_x", [P, KT, TOK]), sb("_sq", [P, 2, TOK]), sb("_r", [P, TOK])
        block = ctx.enter_context(nc.Block())

        @block.sync
        def _(sp):
            for k in range(KT):
                sp.dma_start(x[:, k, :], x_dram[k]).then_inc(x_in[k], 16)
            if consts:
                sp.dma_start(T.consts[:, :], T.io["consts"][:, 0:T.consts.shape[1]]).then_inc(consts_in, 16)
                sp.wait_ge(consts_in, 16)

        @block.scalar
        def _(act):
            act.preload_act_table_set(EXP_LN_SET)
            for k in range(KT):
                act.wait_ge(x_in[k], 16)
                if k >= 2:
                    act.wait_ge(sq_used, k - 1)
                act.activation(sq[:, k % 2, :], x[:, k, :], ACT.Square).then_inc(squared, 1)
            act.wait_ge(summed, 1)
            act.activation(rinv[:, :].rearrange("p (c n) -> p c n", c=GRP), ps[:, 0:GRP, 0:GC], ACT.Ln,
                           scale=1.0 / D_MODEL, bias=T.vec("eps_rms")).then_inc(logged, 1)
            act.wait_ge(logged, 1)
            act.activation(rinv[:, :], rinv[:, :], ACT.Exp, scale=-0.5).then_inc(rooted, 1)
            for k in range(KT):
                act.wait_ge(scaled, k + 1)
                act.activation(hh[:, k, :], x[:, k, :], ACT.Copy).then_inc(rounded, 1)

        @block.tensor
        def _(pe):
            for k in range(KT):
                pe.wait_ge(squared, k + 1)
                for c in range(GRP):
                    mm = pe.matmul(ps[:, c, 0:GC], ones, sq[:, k % 2, c * GC:(c + 1) * GC], start=(k == 0),
                                   stop=(k == KT - 1))
                mm.then_inc(sq_used, 1)
            pe.wait_ge(sq_used, KT)
            pe.sem_inc(summed, 1)

        @block.vector
        def _(dve):
            dve.wait_ge(rooted, 1)
            for k in range(KT + 1):
                if k < KT:
                    dve.scalar_tensor_tensor(out=x[:, k, :], in0=x[:, k, :], scalar=g[:, k:k + 1], in1=rinv[:, :],
                                             op0=ALU.mult, op1=ALU.mult).then_inc(scaled, 1)
                if k >= 1:
                    dve.wait_ge(rounded, k)
                    dve.tensor_tensor(hl[:, k - 1, :], x[:, k - 1, :], hh[:, k - 1, :].bitcast(F32), ALU.subtract)
    sems.clear()


def round_weights(act, hi, w, rounded):
    act.activation(hi, w, ACT.Copy).then_inc(rounded, 1)


def rest_weights(dve, lo, w, hi, rest_ready):
    dve.tensor_tensor(lo, w, hi.bitcast(F32), ALU.subtract).then_inc(rest_ready, 1)


def split_products(pe, out, parts, last=None):
    n = len(parts)
    for k, (wh, wl, xh, xl) in enumerate(parts):
        pe.matmul(out, wh, xh, start=(k == 0), stop=False)
        pe.matmul(out, wl, xh, start=False, stop=False)
        mm = pe.matmul(out, wh, xl, start=False, stop=(k == n - 1))
    return mm


def group_products(pe, T, bank, hi, lo, c):
    g = slice(c * GC, (c + 1) * GC)
    return split_products(pe, T.ps[:, bank, 0:GC],
                          [(hi[:, k * P:(k + 1) * P], lo[:, k * P:(k + 1) * P], T.hh[:, k, g], T.hl[:, k, g])
                           for k in range(KT)])


def residual_phase(T, name, w_dram, src, x_dram, out_dram):
    nc, ps = T.nc, T.ps
    sems = Sems(nc, name)
    w_in = [sems("w_in0"), sems("w_in1")]
    x_in = [sems("x_in0"), sems("x_in1")]
    product, added, stored, x_free = sems("product"), sems("added"), sems("stored"), sems("x_free")
    with nc.sbuf_tensor(name + "_w", [P, 2, KT * P], F32) as w, nc.sbuf_tensor(name + "_x", [P, 2, TOK], F32) as x, \
            nc.Block() as block:
        @block.sync
        def _(sp):
            with sp.Fori(0, KT // 2) as i:
                for j in range(2):
                    tile = bass.ds(2 * i + j, 1)
                    sp.wait_ge(product, 6 * i + 3 * j + 3)
                    sp.dma_start(w[:, j, :], w_dram[tile, :, :].rearrange("a p n -> (a p) n")).then_inc(w_in[j], 16)
                    sp.wait_ge(x_free, 2 * i + j + 1)
                    sp.dma_start(x[:, j, :], x_dram[tile, :, :].rearrange("a p n -> (a p) n")).then_inc(x_in[j], 16)

        @block.tensor
        def _(pe):
            pe.sem_inc(product, 6)
            with pe.Fori(0, KT // 2) as i:
                for j in range(2):
                    pe.wait_ge(w_in[j], 16 * i + 16)
                    for c in range(GRP):
                        pe.wait_ge(added, 6 * i + 3 * j + c + 1)
                        for k in range(KT):
                            mm = pe.matmul(ps[:, 3 * j + c, 0:GC], w[:, j, k * P:(k + 1) * P],
                                           src[:, k, c * GC:(c + 1) * GC], start=(k == 0), stop=(k == KT - 1))
                        mm.then_inc(product, 1)

        @block.vector
        def _(dve):
            dve.sem_inc(added, 6)
            with dve.Fori(0, KT // 2) as i:
                for j in range(2):
                    dve.wait_ge(x_in[j], 16 * i + 16)
                    for c in range(GRP):
                        dve.wait_ge(product, 6 * i + 3 * j + c + 7)
                        row = x[:, j, c * GC:(c + 1) * GC]
                        dve.tensor_tensor(row, ps[:, 3 * j + c, 0:GC], row, ALU.add).then_inc(added, 1)

        @block.gpsimd
        def _(pool):
            pool.sem_inc(x_free, 2)
            with pool.Fori(0, KT // 2) as i:
                for j in range(2):
                    pool.wait_ge(added, 6 * i + 3 * j + 9)
                    pool.dma_start(out_dram[bass.ds(2 * i + j, 1), :, :].rearrange("a p n -> (a p) n"), x[:, j, :])\
                        .then_inc(stored, 16)
                    pool.wait_ge(stored, 32 * i + 16 * j + 16)
                    pool.sem_inc(x_free, 1)
    sems.clear()


def down_phase(T, name, w_dram, a, x_dram, out_dram):
    nc, ps = T.nc, T.ps
    sems = Sems(nc, name)
    HK = FT // 2
    w_in, x_in = [sems("w_in0"), sems("w_in1")], [sems("x_in0"), sems("x_in1")]
    (w_rounded, w_split, w_used, a_rounded, a_split, product, added, stored, x_free) = (
        sems(n) for n in ("w_rounded", "w_split", "w_used", "a_rounded", "a_split", "product", "added", "stored",
                          "x_free"))
    with ExitStack() as ctx:
        sb = lambda n, s, d=F32: ctx.enter_context(nc.sbuf_tensor(name + n, s, d))
        w, wh, wl = sb("_w", [P, 2, HK * P]), sb("_wh", [P, 2, HK * P], F32R), sb("_wl", [P, 2, HK * P], F32R)
        ah, al = sb("_ah", [P, FT, GC], F32R), sb("_al", [P, FT, GC], F32R)
        x = sb("_x", [P, 2, GC])
        block = ctx.enter_context(nc.Block())

        @block.sync
        def _(sp):
            for c in range(GRP):
                with sp.Fori(0, KT // 2) as i:
                    for j in range(2):
                        tile = bass.ds(2 * i + j, 1)
                        n = KT * c + 2 * i + j
                        for v in range(2):
                            sp.wait_ge(w_split, 2 * n + v + 1)
                            sp.dma_start(w[:, v, :], w_dram[tile, :, v * HK * P:(v + 1) * HK * P]
                                         .rearrange("a p n -> (a p) n")).then_inc(w_in[v], 16)
                        sp.wait_ge(x_free, n + 1)
                        sp.dma_start(x[:, j, :], x_dram[tile, :, c * GC:(c + 1) * GC].rearrange("a p n -> (a p) n"))\
                          .then_inc(x_in[j], 16)

        @block.scalar
        def _(act):
            for c in range(GRP):
                if c:
                    act.wait_ge(product, KT * c)
                for k in range(FT):
                    act.activation(ah[:, k, :], a[:, k, c * GC:(c + 1) * GC], ACT.Copy).then_inc(a_rounded, 1)
                    if k in (3, 7):
                        v = k // 4
                        act.wait_ge(w_in[v], 16 * KT * c + 16)
                        act.wait_ge(w_used, 2 * KT * c + v + 1)
                        round_weights(act, wh[:, v, :], w[:, v, :], w_rounded)
                with act.Fori(1, KT) as o:
                    for v in range(2):
                        act.wait_ge(w_in[v], 16 * (KT * c + o) + 16)
                        act.wait_ge(w_used, 2 * (KT * c + o) + v + 1)
                        round_weights(act, wh[:, v, :], w[:, v, :], w_rounded)

        @block.tensor
        def _(pe):
            pe.sem_inc(w_used, 2)
            for c in range(GRP):
                def tile(i, j, first=False):
                    n = KT * c + 2 * i + j
                    pe.wait_ge(added, n + 1)
                    for v in range(2):
                        pe.wait_ge(w_split, 2 * n + v + 3)
                        for k in range(HK):
                            kk = HK * v + k
                            if first:
                                pe.wait_ge(a_split, FT * c + kk + 1)
                            wk = slice(k * P, (k + 1) * P)
                            pe.matmul(ps[:, j, 0:GC], wh[:, v, wk], ah[:, kk, :], start=(kk == 0), stop=False)
                            pe.matmul(ps[:, j, 0:GC], wl[:, v, wk], ah[:, kk, :], start=False, stop=False)
                            mm = pe.matmul(ps[:, j, 0:GC], wh[:, v, wk], al[:, kk, :], start=False, stop=(kk == FT - 1))
                        mm.then_inc(w_used, 1)
                    pe.wait_ge(w_used, 2 * n + 4)
                    pe.sem_inc(product, 1)

                tile(0, 0, True)
                tile(0, 1)
                with pe.Fori(1, KT // 2) as i:
                    for j in range(2):
                        tile(i, j)

        @block.vector
        def _(dve):
            dve.sem_inc(added, 2)
            dve.sem_inc(w_split, 2)

            def rest(n, v):
                dve.wait_ge(w_rounded, 2 * n + v + 1)
                rest_weights(dve, wl[:, v, :], w[:, v, :], wh[:, v, :], w_split)

            def add(c, i, j):
                n = KT * c + 2 * i + j
                dve.wait_ge(x_in[j], 16 * (KT // 2 * c + i) + 16)
                dve.wait_ge(product, n + 1)
                dve.tensor_tensor(x[:, j, :], ps[:, j, 0:GC], x[:, j, :], ALU.add).then_inc(added, 1)

            for c in range(GRP):
                for k in range(FT):
                    dve.wait_ge(a_rounded, FT * c + k + 1)
                    dve.tensor_tensor(al[:, k, :], a[:, k, c * GC:(c + 1) * GC], ah[:, k, :].bitcast(F32), ALU.subtract)\
                       .then_inc(a_split, 1)
                    if k in (3, 7):
                        rest(KT * c, k // 4)
                with dve.Fori(0, KT // 2 - 1) as i:
                    for j in range(2):
                        for v in range(2):
                            rest(KT * c + 2 * i + j + 1, v)
                        add(c, i, j)
                for v in range(2):
                    rest(KT * c + KT - 1, v)
                add(c, KT // 2 - 1, 0)
                add(c, KT // 2 - 1, 1)

        @block.gpsimd
        def _(pool):
            pool.sem_inc(x_free, 2)
            for c in range(GRP):
                with pool.Fori(0, KT // 2) as i:
                    for j in range(2):
                        n = KT * c + 2 * i + j
                        pool.wait_ge(added, n + 3)
                        pool.dma_start(out_dram[bass.ds(2 * i + j, 1), :, c * GC:(c + 1) * GC]
                                       .rearrange("a p n -> (a p) n"), x[:, j, :]).then_inc(stored, 16)
                        pool.wait_ge(stored, 16 * n + 16)
                        pool.sem_inc(x_free, 1)
    sems.clear()


def ffn_up_phase(T, name, l, a):
    nc, ps, io = T.nc, T.ps, T.io
    sems = Sems(nc, name)
    w_in = [sems("w_in0"), sems("w_in1")]
    tail_out, tail_free = sems("tail_out"), sems("tail_free")
    gate_done, up_done, row_in, conv_done, silu_done, multiplied, step, cleared, w_rounded, w_split = (
        sems(n) for n in ("gate_done", "up_done", "row_in", "conv_done", "silu_done", "multiplied", "step", "cleared",
                          "w_rounded", "w_split"))
    w_dram, tail = io["w_ff"][l], io["ffnconv_new"][l]
    UP, PAR = KT * P, 2 * KT * P
    LAST = FT // 2 - 1
    with ExitStack() as ctx:
        sb = lambda n, s, d=F32: ctx.enter_context(nc.sbuf_tensor(name + n, s, d))
        w = sb("_w", [P, 2, FF_BLK])
        wh, wl = sb("_wh", [P, 2, KT * P], F32R), sb("_wl", [P, 2, KT * P], F32R)
        row = sb("_row", [P, 2, 2 + TOK])
        cv = sb("_cv", [P, 2, TOK])
        block = ctx.enter_context(nc.Block())

        @block.sync
        def _(sp):
            with sp.Fori(0, FT // 2) as i:
                for j in range(2):
                    sp.wait_ge(multiplied, 6 * i + 3 * j + 3)
                    sp.dma_start(w[:, j, :], w_dram[bass.ds(2 * i + j, 1), :, :].rearrange("a p n -> (a p) n"))\
                      .then_inc(w_in[j], 16)

        @block.gpsimd
        def _(pool):
            pool.memset(row[:, :, 0:2], 0.0).then_inc(cleared, 1)
            pool.sem_inc(tail_free, 2)
            with pool.Fori(0, FT // 2) as i:
                for j in range(2):
                    pool.wait_ge(row_in, 6 * i + 3 * j + 3 + 3)
                    pool.dma_start(tail[bass.ds(2 * i + j, 1), :, :].rearrange("a p n -> (a p) n"),
                                   row[:, j, SEQ:SEQ + 2 + NS]).then_inc(tail_out, 16)
                    pool.wait_ge(tail_out, 32 * i + 16 * j + 16)
                    pool.sem_inc(tail_free, 1)

        @block.tensor
        def _(pe):
            with pe.Fori(0, FT // 2) as i:
                for j in range(2):
                    t = 2 * i + j
                    pe.wait_ge(w_split, 2 * t + 1)
                    for c in range(GRP):
                        pe.wait_ge(row_in, 3 * t + c + 1)
                        group_products(pe, T, c, wh[:, 0, :], wl[:, 0, :], c).then_inc(gate_done, 1)
                    pe.wait_ge(w_split, 2 * t + 2)
                    for c in range(GRP):
                        pe.wait_ge(multiplied, 3 * t + c + 4)
                        group_products(pe, T, 3 + c, wh[:, 1, :], wl[:, 1, :], c).then_inc(up_done, 1)

        @block.scalar
        def _(act):
            act.sem_inc(row_in, 3)

            def round_gate(i, j):
                act.wait_ge(w_in[j], 16 * i + 16)
                act.wait_ge(gate_done, 3 * (2 * i + j))
                round_weights(act, wh[:, 0, :], w[:, j, 0:UP], w_rounded)

            def tile(i, j, last=False):
                t = 2 * i + j
                for c in range(GRP):
                    n = 3 * t + c
                    act.wait_ge(gate_done, n + 1)
                    act.wait_ge(conv_done, n + (2 if c < 2 else 1))
                    if c == 2:
                        act.wait_ge(tail_free, t + 1)
                    act.activation(row[:, j, 2 + c * GC:2 + (c + 1) * GC], ps[:, c, 0:GC], ACT.Copy)\
                       .then_inc(row_in, 1)
                    if c == 2 and not last:
                        round_gate(i + (j == 1), 1 - j)
                for c in range(GRP):
                    n = 3 * t + c
                    act.wait_ge(conv_done, n + 7)
                    act.activation(cv[:, j, c * GC:(c + 1) * GC], cv[:, j, c * GC:(c + 1) * GC], ACT.Silu,
                                   bias=w[:, j, PAR + 3:PAR + 4]).then_inc(silu_done, 1)
                if not last:
                    act.wait_ge(up_done, 3 * t + 3)
                    round_weights(act, wh[:, 1, :], w[:, 1 - j, UP:PAR], w_rounded)

            act.preload_act_table(ACT.Silu)
            act.wait_ge(w_in[0], 16)
            for g in range(2):
                round_weights(act, wh[:, g, :], w[:, 0, g * UP:(g + 1) * UP], w_rounded)
            with act.Fori(0, LAST) as i:
                for j in range(2):
                    tile(i, j)
            tile(LAST, 0)
            tile(LAST, 1, True)

        @block.vector
        def _(dve):
            dve.sem_inc(multiplied, 6)
            dve.sem_inc(conv_done, 6)
            dve.wait_ge(cleared, 1)
            per = 2 * (2 * GRP + 3)

            def rest(t, j, g):
                dve.wait_ge(w_rounded, 2 * t + g + 1)
                rest_weights(dve, wl[:, g, :], w[:, j, g * UP:(g + 1) * UP], wh[:, g, :], w_split)

            def tile(i, st, j, last=False):
                t = 2 * i + j
                tap = [w[:, j, PAR + n:PAR + n + 1] for n in range(3)]
                kept = w[:, j, PAR + 4:PAR + 4 + 2 * NS].rearrange("p (r b) -> p r b", r=2)
                for c in range(GRP):
                    n = 3 * t + c
                    a0, a1 = c * GC, min((c + 1) * GC, SEQ)
                    dve.wait_ge(row_in, n + 4)
                    dve.wait_ge(multiplied, n + 1)
                    if c == 2 and not last:
                        rest(t + 1, 1 - j, 0)
                    o = cv[:, j, a0:a1]
                    st.link(dve.tensor_scalar(o, row[:, j, a0:a1], tap[0], None, ALU.mult))
                    st.link(dve.scalar_tensor_tensor(out=o, in0=row[:, j, a0 + 1:a1 + 1], scalar=tap[1],
                                                     in1=o, op0=ALU.mult, op1=ALU.add))
                    if c == 2:
                        s = cv[:, j, SEQ:TOK]
                        st.link(dve.tensor_scalar(s, kept[:, 0, :], tap[0], None, ALU.mult))
                        st.link(dve.scalar_tensor_tensor(out=s, in0=kept[:, 1, :], scalar=tap[1], in1=s,
                                                         op0=ALU.mult, op1=ALU.add))
                        st.link(dve.scalar_tensor_tensor(out=s, in0=row[:, j, 2 + SEQ:2 + TOK], scalar=tap[2],
                                                         in1=s, op0=ALU.mult, op1=ALU.add))
                    dve.scalar_tensor_tensor(out=o, in0=row[:, j, a0 + 2:a1 + 2], scalar=tap[2], in1=o,
                                             op0=ALU.mult, op1=ALU.add).then_inc(conv_done, 1)
                for c in range(GRP):
                    n = 3 * t + c
                    dve.wait_ge(silu_done, n + 1)
                    dve.wait_ge(up_done, n + 1)
                    col = slice(c * GC, (c + 1) * GC)
                    dve.tensor_tensor(a[:, bass.ds(2 * i + j, 1), col].rearrange("p a t -> p (a t)"), cv[:, j, col],
                                      ps[:, 3 + c, 0:GC], ALU.mult).then_inc(multiplied, 1)
                if not last:
                    rest(t + 1, 1 - j, 1)

            for g in range(2):
                rest(0, 0, g)
            with dve.Fori(0, LAST) as i:
                st = Steps(dve, step, i * per)
                for j in range(2):
                    tile(i, st, j)
                assert st.n == per
            st = Steps(dve, step, LAST * per)
            tile(LAST, st, 0)
            tile(LAST, st, 1, True)
    sems.clear()


def qk_phase(T):
    nc, ps, io = T.nc, T.ps, T.io
    sems = Sems(nc, "qk")
    w_in = [sems("w_in0"), sems("w_in1")]
    row_out, row_free, product, raw_in, squared, summed, logged, rooted, scaled, w_rounded, w_split = (
        sems(n) for n in ("row_out", "row_free", "product", "raw_in", "squared", "summed", "logged", "rooted", "scaled",
                          "w_rounded", "w_split"))
    halves = T.const("halves")
    with ExitStack() as ctx:
        sb = lambda n, s, d=F32: ctx.enter_context(nc.sbuf_tensor("qk" + n, s, d))
        w, raw, sq, rt = sb("_w", [P, 2, QK_BLK]), sb("_raw", [P, 2, TOK]), sb("_sq", [P, 2, TOK]), sb("_rt", [P, 2, TOK])
        wh, wl = sb("_wh", [P, 2, KT * P], F32R), sb("_wl", [P, 2, KT * P], F32R)
        block = ctx.enter_context(nc.Block())

        @block.sync
        def _(sp):
            with sp.Fori(0, 4) as i:
                for j in range(2):
                    sp.wait_ge(scaled, 2 * i + j + 1)
                    sp.dma_start(w[:, j, :], io["w_qk"][bass.ds(2 * i + j, 1), :, :].rearrange("a p n -> (a p) n"))\
                      .then_inc(w_in[j], 16)

        @block.tensor
        def _(pe):
            def sums(i, j):
                for c in range(GRP):
                    pe.wait_ge(squared, 6 * i + 3 * j + c + 1)
                    pe.matmul(ps[:, 3 * j + c, 0:GC], halves, sq[:, j, c * GC:(c + 1) * GC], start=True, stop=True)\
                      .then_inc(summed, 1)

            with pe.Fori(0, 4) as i:
                for j in range(2):
                    pe.wait_ge(w_split, 2 * i + j + 1)
                    pe.wait_ge(logged, 2 * i + j + 1)
                    for c in range(GRP):
                        group_products(pe, T, 3 * j + c, wh[:, j, :], wl[:, j, :], c).then_inc(product, 1)
                    sums(i, j)

        @block.scalar
        def _(act):
            act.preload_act_table_set(EXP_LN_SET)
            act.sem_inc(logged, 2)

            def tile(i, j, last=False):
                t = 2 * i + j
                if not last:
                    act.wait_ge(w_in[1 - j], 16 * (i + j) + 16)
                    round_weights(act, wh[:, 1 - j, :], w[:, 1 - j, 0:KT * P], w_rounded)
                act.wait_ge(row_free, t + 1)
                for c in range(GRP):
                    act.wait_ge(product, 3 * t + c + 1)
                    act.activation(raw[:, j, c * GC:(c + 1) * GC], ps[:, 3 * j + c, 0:GC], ACT.Copy)\
                       .then_inc(raw_in, 1)
                    act.activation(sq[:, j, c * GC:(c + 1) * GC], ps[:, 3 * j + c, 0:GC], ACT.Square)\
                       .then_inc(squared, 1)
                act.wait_ge(summed, 3 * t + 3)
                act.activation(rt[:, j, :].rearrange("p (c n) -> p c n", c=GRP), ps[:, 3 * j:3 * j + 3, 0:GC],
                               ACT.Ln, scale=1.0 / DH, bias=T.vec("eps_rms")).then_inc(logged, 1)
                act.wait_ge(logged, t + 3)
                act.activation(rt[:, j, :], rt[:, j, :], ACT.Exp, scale=-0.5).then_inc(rooted, 1)

            act.wait_ge(w_in[0], 16)
            round_weights(act, wh[:, 0, :], w[:, 0, 0:KT * P], w_rounded)
            with act.Fori(0, 3) as i:
                tile(i, 0)
                tile(i, 1)
            tile(3, 0)
            tile(3, 1, True)

        @block.vector
        def _(dve):
            dve.sem_inc(scaled, 2)

            def rest(t, j):
                dve.wait_ge(w_rounded, t + 1)
                rest_weights(dve, wl[:, j, :], w[:, j, 0:KT * P], wh[:, j, :], w_split)

            def tile(i, j, last=False):
                t = 2 * i + j
                if not last:
                    rest(t + 1, 1 - j)
                dve.wait_ge(raw_in, 3 * t + 3)
                dve.wait_ge(rooted, t + 1)
                dve.scalar_tensor_tensor(out=raw[:, j, :], in0=raw[:, j, :], scalar=w[:, j, KT * P:KT * P + 1],
                                         in1=rt[:, j, :], op0=ALU.mult, op1=ALU.mult).then_inc(scaled, 1)

            rest(0, 0)
            with dve.Fori(0, 3) as i:
                tile(i, 0)
                tile(i, 1)
            tile(3, 0)
            tile(3, 1, True)

        @block.gpsimd
        def _(pool):
            pool.sem_inc(row_free, 2)
            with pool.Fori(0, 4) as i:
                for j in range(2):
                    pool.wait_ge(scaled, 2 * i + j + 3)
                    pool.dma_start(io["qk_rows"][bass.ds(2 * i + j, 1), :, :].rearrange("a p n -> (a p) n"),
                                   raw[:, j, :]).then_inc(row_out, 16)
                    pool.wait_ge(row_out, 32 * i + 16 * j + 16)
                    pool.sem_inc(row_free, 1)
    sems.clear()


def v_phase(T):
    nc, ps, io = T.nc, T.ps, T.io
    sems = Sems(nc, "v")
    w_in, w_rounded, w_split, product, copied, out = (
        sems(n) for n in ("w_in", "w_rounded", "w_split", "product", "copied", "out"))
    starts = [s * P for s in range(8)] + [TOK - P]
    with ExitStack() as ctx:
        sb = lambda n, s, d=F32: ctx.enter_context(nc.sbuf_tensor("v" + n, s, d))
        w, v = sb("_w", [P, KT, D_A]), sb("_sb", [P, 9, D_A])
        wh, wl = sb("_wh", [P, KT, D_A], F32R), sb("_wl", [P, KT, D_A], F32R)
        block = ctx.enter_context(nc.Block())

        @block.sync
        def _(sp):
            sp.dma_start(w[:, :, :], io["w_v"]).then_inc(w_in, 16)
            sp.wait_ge(copied, 8)
            sp.dma_start(io["v_rows"][0:SEQ, :].rearrange("(s p) n -> p s n", p=P), v[:, 0:8, :]).then_inc(out, 16)
            sp.wait_ge(copied, 9)
            sp.dma_start(io["v_rows"][SEQ:TOK, :], v[P - NS:P, 8, :]).then_inc(out, 16)
            sp.wait_ge(out, 32)

        @block.tensor
        def _(pe):
            for s in range(9):
                if s >= 8:
                    pe.wait_ge(copied, s - 7)
                tok = slice(starts[s], starts[s] + P)
                for k in range(KT):
                    if s == 0:
                        pe.wait_ge(w_split, k + 1)
                    pe.matmul(ps[:, s % 8, :], T.hh[:, k, tok], wh[:, k, :], start=(k == 0), stop=False)
                    pe.matmul(ps[:, s % 8, :], T.hh[:, k, tok], wl[:, k, :], start=False, stop=False)
                    mm = pe.matmul(ps[:, s % 8, :], T.hl[:, k, tok], wh[:, k, :], start=False, stop=(k == KT - 1))
                mm.then_inc(product, 1)

        @block.scalar
        def _(act):
            act.wait_ge(w_in, 16)
            for k in range(KT):
                round_weights(act, wh[:, k, :], w[:, k, :], w_rounded)
            for s in range(9):
                act.wait_ge(product, s + 1)
                act.activation(v[:, s, :], ps[:, s % 8, :], ACT.Copy).then_inc(copied, 1)

        @block.vector
        def _(dve):
            for k in range(KT):
                dve.wait_ge(w_rounded, k + 1)
                rest_weights(dve, wl[:, k, :], w[:, k, :], wh[:, k, :], w_split)
    sems.clear()


def pb_phase(T):
    nc, ps, io = T.nc, T.ps, T.io
    sems = Sems(nc, "pb")
    w_in = [sems("w_in0"), sems("w_in1")]
    out_sem, row_free, product, row_in, mixed, step, cleared, w_rounded, w_split = (
        sems(n) for n in ("out", "row_free", "product", "row_in", "mixed", "step", "cleared", "w_rounded", "w_split"))
    MU, LAST = KT * P, NB_T // 2 - 1
    with ExitStack() as ctx:
        sb = lambda n, s, d=F32: ctx.enter_context(nc.sbuf_tensor("pb" + n, s, d))
        w, row, xs = sb("_w", [P, 2, PB_BLK]), sb("_row", [P, 2, 1 + TOK]), sb("_xs", [P, 2, TOK])
        wh, wl = sb("_wh", [P, 2, KT * P], F32R), sb("_wl", [P, 2, KT * P], F32R)
        block = ctx.enter_context(nc.Block())

        @block.sync
        def _(sp):
            with sp.Fori(0, NB_T // 2) as i:
                for j in range(2):
                    sp.wait_ge(mixed, 2 * i + j + 1)
                    sp.dma_start(w[:, j, :], io["w_pb"][bass.ds(2 * i + j, 1), :, :].rearrange("a p n -> (a p) n"))\
                      .then_inc(w_in[j], 16)

        @block.tensor
        def _(pe):
            with pe.Fori(0, NB_T // 2) as i:
                for j in range(2):
                    pe.wait_ge(w_split, 2 * i + j + 1)
                    for c in range(GRP):
                        pe.wait_ge(row_in, 6 * i + 3 * j + c + 1)
                        group_products(pe, T, 3 * j + c, wh[:, j, :], wl[:, j, :], c).then_inc(product, 1)

        @block.scalar
        def _(act):
            act.sem_inc(row_in, 6)

            def tile(i, j, last=False):
                if not last:
                    act.wait_ge(w_in[1 - j], 16 * (i + j) + 16)
                    round_weights(act, wh[:, 1 - j, :], w[:, 1 - j, 0:KT * P], w_rounded)
                act.wait_ge(row_free, 2 * i + j + 1)
                for c in range(GRP):
                    act.wait_ge(product, 6 * i + 3 * j + c + 1)
                    act.activation(row[:, j, 1 + c * GC:1 + (c + 1) * GC], ps[:, 3 * j + c, 0:GC], ACT.Copy)\
                       .then_inc(row_in, 1)

            act.wait_ge(w_in[0], 16)
            round_weights(act, wh[:, 0, :], w[:, 0, 0:KT * P], w_rounded)
            with act.Fori(0, LAST) as i:
                tile(i, 0)
                tile(i, 1)
            tile(LAST, 0)
            tile(LAST, 1, True)

        @block.vector
        def _(dve):
            dve.sem_inc(mixed, 2)
            dve.wait_ge(cleared, 1)

            def rest(t, j):
                dve.wait_ge(w_rounded, t + 1)
                rest_weights(dve, wl[:, j, :], w[:, j, 0:KT * P], wh[:, j, :], w_split)

            def tile(i, st, j, last=False):
                if not last:
                    rest(2 * i + j + 1, 1 - j)
                dve.wait_ge(row_in, 6 * i + 3 * j + 3 + 6)
                st.do(dve.tensor_tensor(xs[:, j, 0:SEQ], row[:, j, 0:SEQ], row[:, j, 1:1 + SEQ], ALU.subtract))
                st.link(dve.tensor_tensor(xs[:, j, SEQ:TOK], w[:, j, MU + 1:MU + 1 + NS], row[:, j, 1 + SEQ:1 + TOK],
                                          ALU.subtract))
                dve.scalar_tensor_tensor(out=xs[:, j, :], in0=xs[:, j, :], scalar=w[:, j, MU:MU + 1],
                                         in1=row[:, j, 1:1 + TOK], op0=ALU.mult, op1=ALU.add).then_inc(mixed, 1)

            rest(0, 0)
            with dve.Fori(0, LAST) as i:
                st = Steps(dve, step, 4 * i)
                tile(i, st, 0)
                tile(i, st, 1)
            st = Steps(dve, step, 4 * LAST)
            tile(LAST, st, 0)
            tile(LAST, st, 1, True)

        @block.gpsimd
        def _(pool):
            pool.memset(row[:, :, 0:1], 0.0).then_inc(cleared, 1)
            pool.sem_inc(row_free, 2)
            with pool.Fori(0, NB_T // 2) as i:
                for j in range(2):
                    pool.wait_ge(mixed, 2 * i + j + 3)
                    pool.dma_start(T.xs_rows[bass.ds(2 * i + j, 1), :, :].rearrange("a p n -> (a p) n"),
                                   xs[:, j, :]).then_inc(out_sem, 16)
                    pool.dma_start(io["shift_new"][bass.ds(2 * i + j, 1), :, :].rearrange("a p n -> (a p) n"),
                                   row[:, j, SEQ:SEQ + 1 + NS]).then_inc(out_sem, 16)
                    pool.wait_ge(out_sem, 64 * i + 32 * j + 32)
                    pool.sem_inc(row_free, 1)
    sems.clear()


class Pages:
    RING = 8

    def __init__(self, T, sems, ctx):
        nc = T.nc
        self.T, self.nc = T, nc
        self.k_in = [sems(f"k_in{n}") for n in range(self.RING)]
        self.v_in = [sems(f"v_in{n}") for n in range(self.RING)]
        (self.qc_in, self.q_turned, self.q_copied, self.q_stored, self.q_in, self.table_in, self.k_used, self.v_used,
         self.reduced, self.biased, self.logged, self.softplus_ready, self.summed, self.z_ready, self.w_ready, self.read,
         self.picked, self.step, self.act_step) = (
            sems(n) for n in ("qc_in", "q_turned", "q_copied", "q_stored", "q_in", "table_in", "k_used", "v_used",
                              "reduced", "biased", "logged", "softplus_ready", "summed", "z_ready", "w_ready",
                              "read", "picked", "page_step", "page_act_step"))
        sb = lambda n, s, d=F32: ctx.enter_context(nc.sbuf_tensor("pg" + n, s, d))
        self.kp, self.vp = sb("_k", [P, self.RING, D_A]), sb("_v", [P, self.RING, D_A])
        self.qc, self.qr, self.q = sb("_qc", [P, 4, NS]), sb("_qr", [NS, D_A]), sb("_q", [P, D_A])
        self.prod = sb("_prod", [P, 2, D_A])
        self.z = sb("_z", [P, H_A, NPG])
        self.zb, self.sp, self.tmp, self.cum, self.wts = (sb(n, [P, H_A * NPG]) for n in ("_zb", "_sp", "_tmp", "_cum", "_w"))
        self.table = sb("_table", [1, NS * NPG], I32)
        self.q_rows = nc.dram_tensor("scratch_pg_q", [NS, D_A], F32, kind="Internal").ap()
        self.loads = NPG // self.RING

    def start_sp(self, sp):
        sp.dma_start(self.table[:, :], self.T.io["page_table"]).then_inc(self.table_in, 16)
        sp.dma_start(self.qc[:, :, :], self.T.io["qk_rows"][0:4, :, SEQ:TOK].rearrange("t p b -> p t b"))\
          .then_inc(self.qc_in, 16)
        sp.wait_ge(self.q_copied, 1)
        sp.dma_start(self.q_rows, self.qr[:, :]).then_inc(self.q_stored, 16)
        sp.wait_ge(self.q_stored, 16)
        sp.wait_ge(self.table_in, 16)

    def load_q(self, sp, b):
        sp.wait_ge(self.k_used, self.RING + NPG * b)
        sp.dma_start(self.q[:, :], self.q_rows[bass.ds(b, 1), :].to_broadcast([P, D_A])).then_inc(self.q_in, 16)

    def load_key_page(self, sp, b, m, n):
        g = NPG * b + self.RING * m + n
        sp.wait_ge(self.k_used, g + 1)
        page = sp.value_load(self.table[0:1, bass.ds(g, 1)], min_val=0, max_val=self.T.n_phys - 1)
        sp.dma_start(self.kp[:, n, :], self.T.io["k_pages"][bass.ds(page, 1), :, :].rearrange("a p n -> (a p) n"))\
          .then_inc(self.k_in[n], 16)

    def load_keys(self, sp, b):
        for n in range(self.RING):
            self.load_key_page(sp, b, 0, n)
        self.load_q(sp, b)
        with sp.Fori(1, self.loads) as m:
            for n in range(self.RING):
                self.load_key_page(sp, b, m, n)

    def start_pe(self, pe):
        pe.wait_ge(self.qc_in, 16)
        for t in range(4):
            mm = pe.transpose(self.T.ps[0:NS, 7, t * P:(t + 1) * P], self.qc[:, t, :], self.T.const("ident"))
        mm.then_inc(self.q_turned, 1)
        pe.sem_inc(self.v_used, self.RING)

    def sums_pe(self, pe, b):
        pe.wait_ge(self.softplus_ready, b + 1)
        pe.wait_ge(self.picked, b + 1)
        pe.matmul(self.T.ps[:, 6, :], self.T.const("later"), self.sp[:, :], start=True, stop=True)
        pe.matmul(self.T.ps[:, 7, :], self.T.const("ones"), self.sp[:, :], start=True, stop=True).then_inc(self.summed, 1)

    def values_pe(self, pe, b, pages):
        for g in pages:
            if g == 0:
                pe.wait_ge(self.w_ready, b + 1)
            n = g % self.RING
            pe.wait_ge(self.v_in[n], 16 * self.loads * b + 16 * (g // self.RING) + 16)
            for t in range(4):
                mm = pe.matmul(self.T.ps[:, 7, 2 * t:2 * t + 2], self.vp[:, n, t * P:(t + 1) * P],
                               self.wts[:, :].rearrange("p (h n) -> p h n", h=H_A)[:, 2 * t:2 * t + 2, g],
                               start=(g == 0 and t == 0), stop=False, skip_group_check=True)
            mm.then_inc(self.v_used, 1)
        if g == NPG - 1:
            pe.wait_ge(self.v_used, self.RING + NPG * b + NPG)
            pe.sem_inc(self.read, 1)

    def start_act(self, act):
        act.wait_ge(self.q_turned, 1)
        act.activation(self.qr[:, :], self.T.ps[0:NS, 7, :], ACT.Copy, scale=DH ** -0.5).then_inc(self.q_copied, 1)
        act.sem_inc(self.picked, 1)
        act.wait_ge(self.table_in, 16)

    def load_values(self, act, b, g):
        act.wait_ge(self.v_used, NPG * b + g + 1)
        page = act.value_load(self.table[0:1, bass.ds(NPG * b + g, 1)], min_val=0, max_val=self.T.n_phys - 1)
        act.dma_start(self.vp[:, g % self.RING, :], self.T.io["v_pages"][bass.ds(page, 1), :, :]
                      .rearrange("a p n -> (a p) n")).then_inc(self.v_in[g % self.RING], 16)

    def logs_act(self, act, b):
        st = Steps(act, self.act_step, 2 * b)
        act.wait_ge(self.biased, b + 1)
        st.link(act.activation(self.tmp[:, :], self.zb[:, :], ACT.Abs))
        st.link(act.activation(self.tmp[:, :], self.tmp[:, :], ACT.Exp, scale=-1.0))
        act.activation(self.tmp[:, :], self.tmp[:, :], ACT.Ln, bias=1.0).then_inc(self.logged, 1)

    def weights_act(self, act, b):
        act.wait_ge(self.z_ready, b + 1)
        act.activation(self.wts[:, :], self.cum[:, :], ACT.Exp).then_inc(self.w_ready, 1)

    def pick_act(self, act, b):
        act.wait_ge(self.read, b + 1)
        for e in range(2):
            r = slice(64 * e, 64 * e + 64)
            last = act.activation(self.T.h[r, 0:4, bass.ds(SEQ + b, 1)].rearrange("p t a -> p (t a)"),
                                  self.T.ps[r, 7, e:8:2], ACT.Copy)
        last.then_inc(self.picked, 1)

    def keys_dve(self, dve, b, m, n):
        g = self.RING * m + n
        if not isinstance(m, int) or g == 0:
            dve.wait_ge(self.q_in, 16 * b + 16)
        for e in range(2):
            dve.wait_ge(self.k_in[n + e], 16 * self.loads * b + 16 * m + 16)
        dve.wait_ge(self.reduced, NPG // 2 * b + self.RING // 2 * m + n // 2 + 1)
        dve.tensor_tensor(self.prod[:, :, :], self.kp[:, n:n + 2, :], self.q[:, :].unsqueeze(1).to_broadcast([P, 2, D_A]),
                          ALU.mult).then_inc(self.k_used, 2)
        dve.wait_ge(self.k_used, self.RING + NPG * b + g + 2)
        z = self.z[:, :, g:g + 2] if isinstance(g, int) else self.z[:, :, bass.ds(g, 2)]
        dve.tensor_reduce(z.rearrange("p h n -> p n h"), self.prod[:, :, :].rearrange("p n (h d) -> p n h d", h=H_A),
                          AX.X, ALU.add).then_inc(self.reduced, 1)

    def first_keys_dve(self, dve):
        dve.sem_inc(self.k_used, self.RING)
        dve.sem_inc(self.reduced, 1)
        with dve.Fori(0, self.loads) as m:
            for n in range(0, self.RING, 2):
                self.keys_dve(dve, 0, m, n)

    def bias_dve(self, dve, b):
        dve.wait_ge(self.reduced, NPG // 2 * b + NPG // 2 + 1)
        dve.tensor_tensor(self.zb[:, :].rearrange("p (h n) -> p h n", h=H_A), self.z[:, :, :],
                          self.T.vec("sb_bias").unsqueeze(2).to_broadcast([P, H_A, NPG]), ALU.add).then_inc(self.biased, 1)

    def softplus_dve(self, dve, b):
        dve.wait_ge(self.logged, b + 1)
        dve.scalar_tensor_tensor(out=self.sp[:, :], in0=self.zb[:, :], scalar=0.0, in1=self.tmp[:, :], op0=ALU.max,
                                 op1=ALU.add).then_inc(self.softplus_ready, 1)

    def exponents_dve(self, dve, b):
        st, ps, run = Steps(dve, self.step, 3 * b), self.T.ps, self.tmp[:, :]
        dve.wait_ge(self.summed, b + 1)
        st.do(dve.tensor_tensor(self.cum[:, :], self.zb[:, :], ps[:, 6, :], ALU.subtract))
        st.link(dve.tensor_tensor_scan(run, self.T.const("scanhead"), ps[:, 7, :], 0.0, ALU.mult, ALU.add))
        st.link(dve.tensor_tensor(run, run, ps[:, 7, :], ALU.subtract))
        dve.tensor_tensor(self.cum[:, :], self.cum[:, :], run, ALU.subtract).then_inc(self.z_ready, 1)


def attention_phase(T):
    nc, h, ps, io = T.nc, T.h, T.ps, T.io
    sems = Sems(nc, "attn")
    later, earlier = T.const("later"), T.const("earlier")
    HALF = 512
    ticks = []
    for j in range(2):
        for g in range(2):
            for s in reversed(range(4 * g + 4)):
                q0 = max(s * P, g * HALF)
                ticks.append((j, g, s, q0, (g + 1) * HALF - q0, s == 0, 2 * j + g))
    NT = len(ticks)
    k_in = [sems("heads_in0"), sems("heads_in1")]
    (z_done, zb_done, na_done, log_done, sp_done, cum_done, d_done, w_done, read_done, carried, out_done, step) = (
        sems(n) for n in ("z_done", "zb_done", "na_done", "log_done", "sp_done", "cum_done", "d_done", "w_done",
                          "read_done", "carried", "out_done", "step"))
    exp_done = sems("exp_done")
    with ExitStack() as ctx:
        sb = lambda n, s: ctx.enter_context(nc.sbuf_tensor("at" + n, s, F32))
        kh, qh, vh = sb("_k", [64, 2, SEQ]), sb("_q", [64, 2, SEQ]), sb("_v", [P, 2, 8, DH])
        zb, na, sp_, d, w = sb("_zb", [P, 3, HALF]), sb("_na", [P, 2, HALF]), sb("_sp", [P, 2, HALF]), \
            sb("_d", [P, 2, HALF]), sb("_w", [P, 2, HALF])
        block = ctx.enter_context(nc.Block())
        qk = io["qk_rows"].rearrange("(a t) (e p) n -> a (t e) p n", a=2, e=2)
        vr = io["v_rows"][0:SEQ, :].rearrange("(s p) (h n) -> h p s n", p=P, n=DH)

        @block.sync
        def _(sp):
            with sp.Fori(0, 4) as i:
                for j in range(2):
                    sp.wait_ge(read_done, NT * i + NT // 2 * (j + 1))
                    hd = bass.ds(2 * i + j, 1)
                    sp.dma_start(qh[:, j, :], qk[0, hd, :, 0:SEQ].rearrange("a p n -> (a p) n")).then_inc(k_in[j], 16)
                    sp.dma_start(kh[:, j, :], qk[1, hd, :, 0:SEQ].rearrange("a p n -> (a p) n")).then_inc(k_in[j], 16)
                    sp.dma_start(vh[:, j, :, :], vr[hd, :, :, :].rearrange("a p s n -> (a p) s n")).then_inc(k_in[j], 16)

        @block.tensor
        def _(pe):
            pe.sem_inc(read_done, NT)
            with pe.Fori(0, 4) as i:
                def score(n):
                    j, g, s, q0, nq, last, stream = ticks[n]
                    if n == 0 or ticks[n - 1][0] != j:
                        pe.wait_ge(k_in[j], 48 * i + 48)
                    if n >= 2:
                        pe.wait_ge(zb_done, NT * i + n - 1)
                    pe.matmul(ps[:, n % 2, 0:nq], kh[:, j, s * P:(s + 1) * P], qh[:, j, q0:q0 + nq], start=True,
                              stop=True).then_inc(z_done, 1)

                def own_sum(n):
                    j, g, s, q0, nq, last, stream = ticks[n]
                    c0 = q0 - g * HALF
                    pe.wait_ge(sp_done, NT * i + n + 1)
                    pe.matmul(ps[:, 2 + stream % 2, c0:c0 + nq], later, sp_[:, n % 2, 0:nq], start=(s == 4 * g + 3),
                              stop=True, skip_group_check=True).then_inc(cum_done, 1)

                def rest_sum(n):
                    j, g, s, q0, nq, last, stream = ticks[n]
                    c0 = q0 - g * HALF
                    pe.wait_ge(d_done, NT * i + n + 1)
                    if last:
                        pe.sem_inc(carried, 1)
                        return
                    pe.matmul(ps[:, 2 + stream % 2, c0:c0 + nq], earlier, sp_[:, n % 2, 0:nq], start=False,
                              stop=True, skip_group_check=True).then_inc(carried, 1)

                def read(n):
                    j, g, s, q0, nq, last, stream = ticks[n]
                    c0 = q0 - g * HALF
                    pe.wait_ge(w_done, NT * i + n + 1)
                    if s == 4 * g + 3:
                        pe.wait_ge(out_done, 4 * i + stream + 1)
                    r = slice(64 * j, 64 * j + 64)
                    pe.matmul(ps[r, 4 + stream % 2, c0:c0 + nq], vh[:, j, s, :], w[:, n % 2, 0:nq],
                              start=(s == 4 * g + 3), stop=True, skip_group_check=True).then_inc(read_done, 1)

                score(0)
                for n in range(NT + 2):
                    if n + 1 < NT:
                        score(n + 1)
                    if 0 <= n - 1 < NT:
                        own_sum(n - 1)
                    if n >= 2:
                        read(n - 2)
                    if 0 <= n - 1 < NT:
                        rest_sum(n - 1)

        @block.vector
        def _(dve):
            per = sum(1 for t in ticks if t[2] * P >= t[1] * HALF) * 2
            with dve.Fori(0, 4) as i:
                st = Steps(dve, step, per * i)

                def scores(n):
                    j, g, s, q0, nq, last, stream = ticks[n]
                    dve.wait_ge(z_done, NT * i + n + 1)
                    bias = T.vec("sb_bias")[:, bass.ds(2 * i + j, 1)]
                    dve.tensor_scalar(zb[:, n % 3, 0:nq], ps[:, n % 2, 0:nq], DH ** -0.5, bias, ALU.mult, ALU.add)\
                       .then_inc(zb_done, 1)
                    dve.wait_ge(zb_done, NT * i + n + 1)
                    dve.scalar_tensor_tensor(out=na[:, n % 2, 0:nq], in0=zb[:, n % 3, 0:nq], scalar=-1.0,
                                             in1=zb[:, n % 3, 0:nq], op0=ALU.mult, op1=ALU.min).then_inc(na_done, 1)

                def softplus(n):
                    j, g, s, q0, nq, last, stream = ticks[n]
                    dve.wait_ge(log_done, NT * i + n + 1)
                    if n >= 2:
                        dve.wait_ge(carried, NT * i + n - 1)
                    ins = dve.scalar_tensor_tensor(out=sp_[:, n % 2, 0:nq], in0=zb[:, n % 3, 0:nq], scalar=0.0,
                                                   in1=na[:, n % 2, 0:nq], op0=ALU.max, op1=ALU.add)
                    if s * P >= g * HALF:
                        st.link(ins)
                        ins = dve.tensor_tensor(sp_[:, n % 2, 0:P], sp_[:, n % 2, 0:P], earlier, ALU.mult)
                    ins.then_inc(sp_done, 1)

                def exponent(n):
                    j, g, s, q0, nq, last, stream = ticks[n]
                    c0 = q0 - g * HALF
                    dve.wait_ge(cum_done, NT * i + n + 1)
                    if n >= 2:
                        dve.wait_ge(w_done, NT * i + n - 1)
                    ins = dve.tensor_tensor(d[:, n % 2, 0:nq], zb[:, n % 3, 0:nq], ps[:, 2 + stream % 2, c0:c0 + nq],
                                            ALU.subtract)
                    if s * P >= g * HALF:
                        st.link(ins)
                        ins = dve.tensor_tensor(d[:, n % 2, 0:P], d[:, n % 2, 0:P], T.const("dcap"), ALU.min)
                    ins.then_inc(d_done, 1)

                for n in range(NT + 1):
                    if n < NT:
                        scores(n)
                    if n >= 1:
                        exponent(n - 1)
                    if n < NT:
                        softplus(n)
                assert st.n == per

        @block.scalar
        def _(act):
            act.preload_act_table_set(EXP_LN_SET)
            act.sem_inc(out_done, 2)
            with act.Fori(0, 4) as i:
                for n in range(NT + 2):
                    if n < NT:
                        nq = ticks[n][4]
                        act.wait_ge(na_done, NT * i + n + 1)
                        act.activation(na[:, n % 2, 0:nq], na[:, n % 2, 0:nq], ACT.Exp).then_inc(exp_done, 1)
                        act.wait_ge(exp_done, NT * i + n + 1)
                        act.activation(na[:, n % 2, 0:nq], na[:, n % 2, 0:nq], ACT.Ln, bias=1.0).then_inc(log_done, 1)
                    if 0 <= n - 1 < NT:
                        m = n - 1
                        nq = ticks[m][4]
                        act.wait_ge(d_done, NT * i + m + 1)
                        if m >= 2:
                            act.wait_ge(read_done, NT * i + m - 1 + NT)
                        act.activation(w[:, m % 2, 0:nq], d[:, m % 2, 0:nq], ACT.Exp).then_inc(w_done, 1)
                    if n >= 2 and ticks[n - 2][5]:
                        j, g, s, q0, nq, last, stream = ticks[n - 2]
                        act.wait_ge(read_done, NT * i + n - 1 + NT)
                        r = slice(64 * j, 64 * j + 64)
                        act.activation(h[r, bass.ds(i, 1), g * HALF:(g + 1) * HALF].rearrange("p a n -> p (a n)"),
                                       ps[r, 4 + stream % 2, :], ACT.Copy).then_inc(out_done, 1)
    sems.clear()


def alone(eng, passed):
    eng.sem_inc(passed, 1)


def solve_levels_pe(pe, T, S, i, mtl, xm, xt, y, banks, passed, between=lambda: None):
    ps = T.ps
    yb, zb, ztb = banks
    for lv in range(1, 6):
        n = 5 * i + lv
        pe.wait_ge(S["x_ready"], n)
        if lv == 1:
            pe.wait_ge(S["blocks_ready"], i + 1)
        alone(pe, passed)
        for p in range(2):
            r = slice(64 * p, 64 * p + 64)
            for hd in range(8):
                c = slice(64 * hd, 64 * hd + 64)
                mm = pe.matmul(ps[r, yb, c], mtl[r, lv - 1, c], xm[r, c], start=True, stop=True)
        mm.then_inc(S["y_done"], 1)
        between()
        pe.wait_ge(S["y_ready"], n)
        alone(pe, passed)
        if lv < 5:
            for p in range(2):
                r = slice(64 * p, 64 * p + 64)
                for hd in range(8):
                    c = slice(64 * hd, 64 * hd + 64)
                    pe.matmul(ps[r, zb, c], xt[r, c], y[r, c], start=True, stop=True)
        for p in range(2):
            r = slice(64 * p, 64 * p + 64)
            for hd in range(8):
                c = slice(64 * hd, 64 * hd + 64)
                mm = pe.matmul(ps[r, ztb, c], y[r, c], xt[r, c], start=True, stop=True)
        mm.then_inc(S["z_done"], 1)
        between()


def solve_levels_act(act, T, S, i, y, banks, between=lambda lv: None):
    for lv in range(1, 6):
        act.wait_ge(S["y_done"], 5 * i + lv)
        act.activation(y[:, :], T.ps[:, banks[0], :], ACT.Copy).then_inc(S["y_ready"], 1)
        between(lv)


def solve_levels_dve(dve, T, S, st, i, xm, xt, banks, between=lambda: None):
    ps = T.ps
    for lv in range(1, 6):
        between()
        dve.wait_ge(S["z_done"], 5 * i + lv)
        if lv < 5:
            st.do(dve.tensor_tensor(xm[:, :], xm[:, :], ps[:, banks[1], :], ALU.subtract))
        st.do(dve.tensor_tensor(xt[:, :], xt[:, :], ps[:, banks[2], :], ALU.subtract))
        st.settle()
        dve.sem_inc(S["x_ready"] if lv < 5 else S["solved"], 1)


def rwkv_phase(T):
    nc, h, ps, io = T.nc, T.h, T.ps, T.io
    sems = Sems(nc, "rwkv")
    S = {n: sems(n) for n in (
        "xs_in", "lora_in", "tanh_in", "gate_in", "lora_done", "w_sum", "w_exp", "a_sum", "a_exp", "k_sq", "k_sum",
        "k_rn", "l_ready", "decays", "prepped", "rkk", "bonus", "bonus_used", "turned", "tm_ready", "spread", "gram",
        "masked", "blocks_copied", "blocks_ready", "x_ready", "y_done", "y_ready", "z_done", "solved", "w_done", "w_copied",
        "u_done", "u_copied", "h_done", "h_ready", "o_done", "o_copied", "mean", "centered", "var", "rstd", "out_ready",
        "gate_copied", "step", "fin_step", "astep", "pstep", "cleared", "state_in", "smp_turned", "smp_rows", "smp_out", "smp_in",
        "smp_done", "smp_back", "smp_step", "log_var",
        "pe_passed", "pool_passed")}
    halves, ident = T.const("halves"), T.const("ident")
    W = 2 * C
    LAST = NPAIR - 1
    with ExitStack() as ctx:
        sb = lambda n, s: ctx.enter_context(nc.sbuf_tensor("rw" + n, s, F32))
        lora = sb("_lora", [P, 2 * D_B])
        X = sb("_xs", [P, NB_T, W])
        th, sg = sb("_th", [P, W]), sb("_sg", [P, W])
        names = "yw rw ya ra kk t1 t2 L eL eN eX km A R K B g bon nm".split()
        t = {n: sb("_" + n, [P, 4, W]) for n in names}
        Ax, Rx, Bx = (sb(n, [P, 4, 2, W]) for n in ("_Ax", "_Rx", "_Bx"))
        ktm, btm, vtm, ak, rk, rb, mt, xm, xt, y, r0, u = (sb("_m" + n, [P, 512]) for n in
                                                           "ktm btm vtm ak rk rb mt xm xt y r0 u".split())
        mtl = sb("_mtl", [P, 6, 512])
        Hx, dh = sb("_Hx", [P, 4, 2, C]), sb("_dh", [P, 4, C])
        o, oc, rs = (sb("_" + n, [P, 4, W]) for n in ("o", "oc", "rs"))
        smp = mtl
        kv, vv, so, sa = sb("_kv", [P, 5, 64]), sb("_vv", [P, 32]), sb("_so", [P, 32]), sb("_sa", [P, 32])
        pages = Pages(T, sems, ctx)
        st8, tmp8 = (b[:, 0:4, :].rearrange("p n (k v) -> p (n k) v", v=32) for b in (pages.kp, pages.vp))
        orow = pages.qr
        ocol = sb("_ocol", [P, 4, NS])
        scr = nc.dram_tensor("scratch_rw_rows", [6, NS, 512], F32, kind="Internal").ap()
        scr_o = nc.dram_tensor("scratch_rw_o", [NS, 512], F32, kind="Internal").ap()
        block = ctx.enter_context(nc.Block())
        bc = lambda v, n: T.vec(v).unsqueeze(2).to_broadcast([P, 4, n])
        m8 = lambda name: T.const(name).unsqueeze(1).to_broadcast([P, 8, C])
        h8 = lambda a: a.rearrange("p (h i) -> p h i", h=8)
        cut = lambda a, n: a[:, :, 0:n]

        @block.sync
        def _(sp):
            sp.dma_start(lora[:, :], io["w_lora"]).then_inc(S["lora_in"], 16)
            pages.start_sp(sp)
            with sp.Fori(0, NS) as b:
                pages.load_keys(sp, b)
            sp.wait_ge(pages.k_used, Pages.RING + NS * NPG)
            sp.dma_start(st8, io["wkv_in"].rearrange("p (k v) -> p k v", k=64)).then_inc(S["state_in"], 16)
            sp.wait_ge(S["h_ready"], 2 * NPAIR + 1)
            for e in range(2):
                sp.dma_start(io["wkv_prompt"][e], Hx[64 * e:64 * e + 64, :, e, :]).then_inc(S["smp_out"], 16)
            sp.wait_ge(S["smp_rows"], 1)
            sp.dma_start(scr.rearrange("a b n -> b a n"), smp[0:NS, :, :]).then_inc(S["smp_out"], 16)
            sp.wait_ge(S["smp_out"], 48)
            for e in range(2):
                r = slice(64 * e, 64 * e + 64)
                sp.dma_start(kv[r, :, :], scr[0:5].rearrange("a b (h k) -> (b h) a k", h=8)).then_inc(S["smp_in"], 16)
                sp.dma_start(vv[r, :], scr[5].rearrange("b (h e v) -> e (b h) v", h=8, e=2)[e]).then_inc(S["smp_in"], 16)
            sp.wait_ge(S["smp_done"], 1)
            for e in range(2):
                sp.dma_start(scr_o.rearrange("b (h e v) -> e (b h) v", h=8, e=2)[e], so[64 * e:64 * e + 64, :])\
                  .then_inc(S["smp_out"], 16)
            sp.dma_start(io["wkv_new"].rearrange("p (k v) -> p k v", k=64), st8).then_inc(S["smp_out"], 16)
            sp.wait_ge(S["smp_out"], 96)
            sp.dma_start(orow[:, :], scr_o).then_inc(S["smp_back"], 16)

        def prep_pe(pe, i, n, sample=None):
            pe.wait_ge(S["tanh_in"], i + 1)
            for k in range(4):
                pe.matmul(ps[:, 0, k * W:k * W + n], lora[0:64, k * P:(k + 1) * P], th[0:64, 0:n], start=True, stop=True)
            for k in range(4):
                pe.matmul(ps[:, 1, k * W:k * W + n], lora[64:P, k * P:(k + 1) * P], X[64:P, 12, 0:n], start=True, stop=True)
            pe.wait_ge(S["gate_in"], i + 1)
            for k in range(4):
                mm = pe.matmul(ps[:, 2, k * W:k * W + n], lora[:, D_B + k * P:D_B + (k + 1) * P], sg[:, 0:n], start=True,
                               stop=True)
            mm.then_inc(S["lora_done"], 1)
            if sample is not None:
                pages.sums_pe(pe, sample)
            pe.wait_ge(S["k_sq"], i + 1)
            pe.matmul(ps[:, 3, 0:4 * n], halves, cut(t["t1"], n), start=True, stop=True).then_inc(S["k_sum"], 1)
            pe.wait_ge(S["rkk"], i + 1)
            pe.matmul(ps[:, 4, 0:4 * n], halves, cut(t["t2"], n), start=True, stop=True).then_inc(S["bonus"], 1)

        xs = T.xs_rows.rearrange("t p n -> p t n")

        def prep_act(act, i, n, sample=None, fetch=None):
            st = Steps(act, S["astep"], 3 * i)
            act.wait_ge(S["out_ready"], i + 1)
            at = SEQ if n == NS else i * W
            act.dma_start(X[:, :, 0:n], xs[:, :, bass.ds(at, n)]).then_inc(S["xs_in"], 16)
            if sample is not None:
                fetch(8)
                pages.logs_act(act, sample)
            act.wait_ge(S["xs_in"], 16 * i + 16)
            act.activation(th[0:64, 0:n], X[0:64, 12, 0:n], ACT.Exp, scale=2.0)
            act.activation(sg[:, 0:n], X[:, 13, 0:n], ACT.Exp, scale=-1.0).then_inc(S["w_exp"], 1)
            act.wait_ge(S["lora_done"], i + 1)
            act.activation(cut(t["g"], n), ps[:, 2, :].rearrange("p (k w) -> p k w", k=4)[:, :, 0:n], ACT.Copy)\
               .then_inc(S["gate_copied"], 1)
            act.wait_ge(S["w_sum"], i + 1)
            act.activation(cut(t["rw"], n), cut(t["yw"], n), ACT.Exp, scale=-1.0)
            act.activation(cut(t["ra"], n), cut(t["ya"], n), ACT.Exp, scale=-1.0).then_inc(S["a_exp"], 1)
            if sample is not None:
                pages.weights_act(act, sample)
            act.wait_ge(S["k_sum"], i + 1)
            st.link(act.activation(cut(t["nm"], n), ps[:, 3, 0:4 * n].rearrange("p (k w) -> p k w", k=4), ACT.Ln,
                                   bias=T.vec("eps_rms")))
            st.do(act.activation(cut(t["nm"], n), cut(t["nm"], n), ACT.Exp, scale=-0.5))
            st.settle()
            act.sem_inc(S["k_rn"], 1)
            act.wait_ge(S["l_ready"], i + 1)
            act.activation(cut(t["eL"], n), cut(t["L"], n), ACT.Exp, scale=-DECAY)
            act.activation(cut(t["eN"], n), cut(t["L"], n), ACT.Exp, scale=DECAY)
            st.do(act.activation(cut(t["eX"], n), cut(t["t1"], n), ACT.Exp, scale=-DECAY))
            st.settle()
            act.sem_inc(S["decays"], 1)
            assert st.n == 3

        PREP = 20

        def prep_dve(dve, i, n, prompt, more=lambda units: None, sample=None):
            st = Steps(dve, S["step"], PREP * i)
            r, k, v = X[:, 0:4, 0:n], X[:, 4:8, 0:n], X[:, 8:12, 0:n]
            part = lambda b: ps[:, b, :].rearrange("p (k w) -> p k w", k=4)[:, :, 0:n]
            tt = lambda o, a, b, op: dve.tensor_tensor(o, a, b, op)
            if sample is not None:
                pages.bias_dve(dve, sample)
                dve.wait_ge(pages.biased, sample + 1)
            more(2)
            dve.wait_ge(S["w_exp"], i + 1)
            st.do(dve.tensor_scalar(th[0:64, 0:n], th[0:64, 0:n], 1.0, None, ALU.add))
            st.link(dve.tensor_scalar(sg[:, 0:n], sg[:, 0:n], 1.0, None, ALU.add))
            st.do(dve.reciprocal(th[0:64, 0:n], th[0:64, 0:n]))
            dve.reciprocal(sg[:, 0:n], sg[:, 0:n]).then_inc(S["gate_in"], 1)
            st.settle()
            dve.tensor_scalar(th[0:64, 0:n], th[0:64, 0:n], -2.0, 1.0, ALU.mult, ALU.add).then_inc(S["tanh_in"], 1)
            st.link(tt(cut(t["kk"], n), k, bc("kk", n), ALU.mult))
            dve.tensor_tensor(cut(t["t1"], n), cut(t["kk"], n), cut(t["kk"], n), ALU.mult).then_inc(S["k_sq"], 1)
            if sample is not None:
                pages.softplus_dve(dve, sample)
            more(2)
            dve.wait_ge(S["lora_done"], i + 1)
            dve.tensor_tensor(cut(t["yw"], n), part(0), bc("w0", n), ALU.add)
            dve.tensor_tensor(cut(t["ya"], n), part(1), bc("a0", n), ALU.add).then_inc(S["w_sum"], 1)
            if sample is not None:
                pages.exponents_dve(dve, sample)
            more(1)
            dve.wait_ge(S["a_exp"], i + 1)
            st.do(dve.tensor_scalar(cut(t["rw"], n), cut(t["rw"], n), 1.0, None, ALU.add))
            st.link(dve.tensor_scalar(cut(t["ra"], n), cut(t["ra"], n), 1.0, None, ALU.add))
            st.do(dve.reciprocal(cut(t["rw"], n), cut(t["rw"], n)))
            st.link(dve.reciprocal(cut(t["ra"], n), cut(t["ra"], n)))
            dve.wait_ge(S["k_sum"], i + 1)
            if prompt:
                st.link(dve.tensor_tensor_scan(t["L"][:, :, :].rearrange("p k w -> p (k w)"), T.const("scan64")[:, 0:512],
                                               t["rw"][:, :, :].rearrange("p k w -> p (k w)"), 0.0, ALU.mult, ALU.add))
                st.do(tt(cut(t["t1"], n), cut(t["L"], n), cut(t["rw"], n), ALU.subtract))
            else:
                st.link(dve.tensor_copy(cut(t["L"], n), cut(t["rw"], n)))
                st.do(tt(cut(t["t1"], n), cut(t["L"], n), cut(t["rw"], n), ALU.subtract))
            st.settle()
            dve.sem_inc(S["l_ready"], 1)
            st.link(dve.scalar_tensor_tensor(out=cut(t["km"], n), in0=cut(t["ra"], n), scalar=-1.0, in1=bc("ka", n),
                                             op0=ALU.add, op1=ALU.mult))
            st.link(dve.scalar_tensor_tensor(out=cut(t["km"], n), in0=cut(t["km"], n), scalar=1.0, in1=k, op0=ALU.add,
                                             op1=ALU.mult))
            st.link(tt(cut(t["t2"], n), r, cut(t["km"], n), ALU.mult))
            dve.tensor_tensor(cut(t["t2"], n), cut(t["t2"], n), bc("rk", n), ALU.mult).then_inc(S["rkk"], 1)
            more(1)
            dve.wait_ge(S["k_rn"], i + 1)
            st.link(tt(cut(t["kk"], n), cut(t["kk"], n), cut(t["nm"], n), ALU.mult))
            st.link(tt(cut(t["ra"], n), cut(t["kk"], n), cut(t["ra"], n), ALU.mult))
            dve.wait_ge(S["decays"], i + 1)
            if prompt:
                st.do(tt(t["A"][:, :, :], t["kk"][:, :, :], t["eX"][:, :, :], ALU.mult))
                st.do(tt(t["R"][:, :, :], r, t["eL"][:, :, :], ALU.mult))
                st.do(tt(t["K"][:, :, :], t["km"][:, :, :], t["eN"][:, :, :], ALU.mult))
                st.link(tt(t["B"][:, :, :], t["ra"][:, :, :], t["eN"][:, :, :], ALU.mult))
                dve.sem_inc(S["prepped"], 1)
            dve.wait_ge(S["bonus"], i + 1)
            st.link(tt(cut(t["bon"], n), ps[:, 4, 0:4 * n].rearrange("p (k w) -> p k w", k=4), v, ALU.mult))
            dve.sem_inc(S["bonus_used"], 1)
            if not prompt:
                dve.sem_inc(S["prepped"], 1)
            assert not prompt or st.n == PREP, st.n

        def finish_pe(pe, i, src, n, more=lambda pages: None):
            more(2)
            pe.wait_ge(S["o_copied"], i + 1)
            pe.matmul(ps[:, 1, 0:4 * n], halves, src, start=True, stop=True).then_inc(S["mean"], 1)
            more(3)
            pe.wait_ge(S["centered"], i + 1)
            pe.matmul(ps[:, 1, 0:4 * n], halves, cut(rs, n), start=True, stop=True).then_inc(S["var"], 1)

        def finish_dve(dve, i, src, n, out, more=lambda units: None):
            st = Steps(dve, S["fin_step"], 6 * i)
            dve.wait_ge(S["mean"], i + 1)
            st.link(dve.scalar_tensor_tensor(out=cut(oc, n), in0=ps[:, 1, 0:4 * n].rearrange("p (k w) -> p k w", k=4),
                                             scalar=-1.0 / 64, in1=src, op0=ALU.mult, op1=ALU.add))
            dve.tensor_tensor(cut(rs, n), cut(oc, n), cut(oc, n), ALU.mult).then_inc(S["centered"], 1)
            more(1)
            dve.wait_ge(S["rstd"], i + 1)
            st.link(dve.tensor_tensor(cut(oc, n), cut(oc, n), cut(rs, n), ALU.mult))
            st.link(dve.tensor_tensor(cut(oc, n), cut(oc, n), bc("lnw", n), ALU.mult))
            st.link(dve.tensor_tensor(cut(oc, n), cut(oc, n), bc("lnb", n), ALU.add))
            st.link(dve.tensor_tensor(cut(oc, n), cut(oc, n), cut(t["bon"], n), ALU.add))
            st.link(dve.tensor_tensor(out, cut(oc, n), cut(t["g"], n), ALU.mult))
            dve.sem_inc(S["out_ready"], 1)
            assert st.n == 6

        def finish_act(act, i, n):
            act.wait_ge(S["var"], i + 1)
            act.activation(cut(rs, n), ps[:, 1, 0:4 * n].rearrange("p (k w) -> p k w", k=4), ACT.Ln, scale=1.0 / 64,
                           bias=T.vec("eps_gn")).then_inc(S["log_var"], 1)
            act.wait_ge(S["log_var"], i + 1)
            act.activation(cut(rs, n), cut(rs, n), ACT.Exp, scale=-0.5).then_inc(S["rstd"], 1)

        @block.gpsimd
        def _(pool):
            for a in (Ax, Rx, Bx):
                pool.memset(a[:, :, :, :], 0.0)
            pool.memset(Hx[:, :, :, :], 0.0).then_inc(S["cleared"], 1)
            pool.wait_ge(S["cleared"], 1)
            pool.sem_inc(S["h_ready"], 1)
            with pool.Fori(0, NPAIR) as i:
                pool.wait_ge(S["prepped"], i + 1)
                alone(pool, S["pool_passed"])
                for src, dst in ((t["A"], Ax), (t["B"], Bx), (t["R"], Rx)):
                    for e in range(2):
                        r = slice(64 * e, 64 * e + 64)
                        last = pool.tensor_copy(dst[r, :, e, :], src[r, :, :])
                last.then_inc(S["spread"], 1)
                pool.wait_ge(S["blocks_copied"], i + 1)
                for lv in range(1, 6):
                    last = pool.tensor_tensor(h8(mtl[:, lv - 1, :]), h8(mt[:, :]), m8(f"lev{lv}T"), ALU.mult)
                last.then_inc(S["blocks_ready"], 1)

        @block.tensor
        def _(pe):
            pages.start_pe(pe)
            pe.wait_ge(pages.q_copied, 1)
            pe.wait_ge(S["lora_in"], 16)
            def pair(i):
                read = iter(range(NPG))
                more = lambda n: pages.values_pe(pe, i, [g for _, g in zip(range(n), read)])
                prep_pe(pe, i, W, sample=i)
                pe.wait_ge(S["prepped"], i + 1)
                pe.wait_ge(S["gate_copied"], i + 1)
                for b, src in ((5, t["K"]), (0, t["B"]), (3, None)):
                    for k in range(4):
                        mm = pe.transpose(ps[:, b, k * P:(k + 1) * P], X[:, 8 + k, :] if src is None else src[:, k, :], ident)
                mm.then_inc(S["turned"], 1)
                more(4)
                pe.wait_ge(S["spread"], i + 1)

                def gram(bank, left, right):
                    for p in range(2):
                        for k in range(4):
                            c = slice(C * p, C * p + C)
                            mm = pe.matmul(ps[64 * p:64 * p + 64, bank, k * P:(k + 1) * P], left[:, k, c], right[:, k, :, c],
                                           start=True, stop=True)
                    mm.then_inc(S["gram"], 1)

                gram(1, t["B"], Ax)
                gram(2, t["A"], Bx)
                pe.wait_ge(S["bonus_used"], i + 1)
                pe.wait_ge(S["tm_ready"], i + 1)
                gram(0, t["K"], Ax)
                gram(3, t["K"], Rx)
                gram(4, t["B"], Rx)
                more(2)
                solve_levels_pe(pe, T, S, i, mtl, xm, xt, y, (5, 2, 1), S["pe_passed"], lambda: more(3))
                pe.wait_ge(S["masked"], i + 1)
                pe.wait_ge(S["solved"], i + 1)
                for p in range(2):
                    r, c = slice(64 * p, 64 * p + 64), slice(C * p, C * p + C)
                    hc = lambda hd: slice(64 * hd, 64 * hd + 64)
                    pe.wait_ge(S["h_ready"], 2 * i + p + 1)
                    for k in range(4):
                        pe.matmul(ps[r, 0, k * P:(k + 1) * P], t["A"][:, k, c], Hx[:, k, :, :], start=True, stop=False,
                                  skip_group_check=True)
                        for hd in (2 * k, 2 * k + 1):
                            mm = pe.matmul(ps[r, 0, hc(hd)], ak[r, hc(hd)], vtm[r, hc(hd)], start=False, stop=True,
                                           skip_group_check=True)
                    mm.then_inc(S["w_done"], 1)
                    more(3)
                    pe.wait_ge(S["w_copied"], 2 * i + p + 1)
                    alone(pe, S["pe_passed"])
                    for hd in range(8):
                        mm = pe.matmul(ps[r, 5, hc(hd)], xt[r, hc(hd)], r0[r, hc(hd)], start=True, stop=True)
                    mm.then_inc(S["u_done"], 1)
                    more(3)
                    pe.wait_ge(S["u_copied"], 2 * i + p + 1)
                    alone(pe, S["pe_passed"])
                    for hd in range(8):
                        q = slice(64 * (hd % 2), 64 * (hd % 2) + 64)
                        k = hd // 2
                        pe.matmul(ps[q, 2, k * C:(k + 1) * C], ktm[r, hc(hd)], vtm[r, hc(hd)], start=True, stop=False,
                                  skip_group_check=True)
                        mm = pe.matmul(ps[q, 2, k * C:(k + 1) * C], btm[r, hc(hd)], u[r, hc(hd)], start=False, stop=True,
                                       skip_group_check=True)
                    for k in range(4):
                        oc_ = slice(k * P + C * p, k * P + C * p + C)
                        mm = pe.matmul(ps[:, 4, oc_], Hx[:, k, :, :].rearrange("p e v -> p (e v)"), t["R"][:, k, c],
                                       start=True, stop=False, skip_group_check=True)
                        for hd in (2 * k, 2 * k + 1):
                            q = slice(64 * (hd % 2), 64 * (hd % 2) + 64)
                            pe.matmul(ps[q, 4, oc_], vtm[r, hc(hd)], rk[r, hc(hd)], start=False, stop=False,
                                      skip_group_check=True)
                            mm = pe.matmul(ps[q, 4, oc_], u[r, hc(hd)], rb[r, hc(hd)], start=False, stop=True,
                                           skip_group_check=True)
                    mm.then_inc(S["h_done"], 1)
                    more(3)
                finish_pe(pe, i, o[:, :, :], W, more)
                more(NPG)

            with pe.Fori(0, LAST) as i:
                pair(i)
            pair(LAST)
            i = NPAIR
            prep_pe(pe, i, NS)
            pe.wait_ge(S["prepped"], i + 1)
            pe.wait_ge(S["gate_copied"], i + 1)
            for b, src in enumerate((t["kk"], t["eL"], t["ra"], t["km"], None, "v")):
                for k in range(4):
                    a = X[:, k, 0:NS] if src is None else X[:, 8 + k, 0:NS] if src == "v" else src[:, k, 0:NS]
                    mm = pe.transpose(ps[0:NS, b, k * P:(k + 1) * P], a, ident)
            mm.then_inc(S["smp_turned"], 1)
            pe.wait_ge(S["smp_back"], 16)
            pe.wait_ge(S["smp_rows"], 1)
            for k in range(4):
                mm = pe.transpose(ps[:, 6, k * NS:(k + 1) * NS], orow[:, k * P:(k + 1) * P], ident[0:NS, 0:NS])
            mm.then_inc(S["o_done"], 1)
            finish_pe(pe, i, ocol[:, :, :], NS)

        @block.scalar
        def _(act):
            act.preload_act_table_set(EXP_LN_SET)
            pages.start_act(act)

            def pair(i):
                asked = iter(range(NPG))

                def fetch(to):
                    for g in asked:
                        pages.load_values(act, i, g)
                        if g >= to - 1:
                            break

                prep_act(act, i, W, sample=i, fetch=fetch)
                act.wait_ge(S["turned"], i + 1)
                act.activation(ktm[:, :], ps[:, 5, :], ACT.Copy)
                act.activation(btm[:, :], ps[:, 0, :], ACT.Copy, scale=-1.0)
                act.activation(vtm[:, :], ps[:, 3, :], ACT.Copy).then_inc(S["tm_ready"], 1)
                act.wait_ge(S["gram"], 5 * i + 1)
                act.activation(mt[:, :], ps[:, 1, :], ACT.Copy).then_inc(S["blocks_copied"], 1)
                fetch(12)
                solve_levels_act(act, T, S, i, y, (5, 2, 1), lambda lv: fetch(8 + 6 * lv))
                for p in range(2):
                    r = slice(64 * p, 64 * p + 64)
                    act.wait_ge(S["w_done"], 2 * i + p + 1)
                    act.activation(r0[r, :], ps[r, 0, :], ACT.Copy).then_inc(S["w_copied"], 1)
                    fetch(44 + 9 * p)
                    act.wait_ge(S["u_done"], 2 * i + p + 1)
                    act.activation(u[r, :], ps[r, 5, :], ACT.Copy).then_inc(S["u_copied"], 1)
                    fetch(47 + 9 * p)
                act.wait_ge(S["h_done"], 2 * i + 2)
                act.activation(o[:, :, :], ps[:, 4, :].rearrange("p (k w) -> p k w", k=4), ACT.Copy)\
                   .then_inc(S["o_copied"], 1)
                fetch(59)
                finish_act(act, i, W)
                fetch(NPG)
                pages.pick_act(act, i)

            with act.Fori(0, LAST) as i:
                pair(i)
            pair(LAST)
            i = NPAIR
            prep_act(act, i, NS)
            act.wait_ge(S["smp_turned"], 1)
            act.activation(smp[0:NS, :, :], ps[0:NS, 0:6, :], ACT.Copy).then_inc(S["smp_rows"], 1)
            act.wait_ge(S["o_done"], 1)
            act.activation(ocol[:, :, :], ps[:, 6, 0:4 * NS].rearrange("p (k w) -> p k w", k=4), ACT.Copy)\
               .then_inc(S["o_copied"], 1)
            finish_act(act, i, NS)

        @block.vector
        def _(dve):
            dve.sem_inc(S["out_ready"], 1)
            pages.first_keys_dve(dve)

            def pair(i, keys=True):
                units = iter(range(0, NPG, 2))

                def more(n):
                    for _, g in zip(range(n if keys else 0), units):
                        pages.keys_dve(dve, i + 1, g // Pages.RING, g % Pages.RING)

                prep_dve(dve, i, W, True, more, sample=i)
                loop = Steps(dve, S["pstep"], 20 * i)
                dve.wait_ge(S["blocks_copied"], i + 1)
                loop.link(dve.tensor_tensor(h8(xt[:, :]), h8(ps[:, 1, :]), m8("lev0T"), ALU.mult))
                loop.do(dve.tensor_tensor(h8(xt[:, :]), m8("eye64"), h8(xt[:, :]), ALU.subtract))
                dve.wait_ge(S["gram"], 5 * i + 2)
                loop.link(dve.tensor_tensor(h8(xm[:, :]), h8(ps[:, 2, :]), m8("lev0"), ALU.mult))
                loop.link(dve.tensor_tensor(h8(xm[:, :]), m8("eye64"), h8(xm[:, :]), ALU.subtract))
                dve.sem_inc(S["x_ready"], 1)
                dve.wait_ge(S["gram"], 5 * i + 5)
                more(1)
                loop.do(dve.tensor_tensor(h8(ak[:, :]), h8(ps[:, 0, :]), m8("strictT"), ALU.mult))
                loop.do(dve.tensor_tensor(h8(rk[:, :]), h8(ps[:, 3, :]), m8("inclT"), ALU.mult))
                loop.link(dve.tensor_tensor(h8(rb[:, :]), h8(ps[:, 4, :]), m8("ninclT"), ALU.mult))
                dve.sem_inc(S["masked"], 1)
                solve_levels_dve(dve, T, S, loop, i, xm, xt, (5, 2, 1), lambda: more(2))
                for p in range(2):
                    more(4)
                    dve.wait_ge(S["h_done"], 2 * i + p + 1)
                    for e in range(2):
                        r = slice(64 * e, 64 * e + 64)
                        st = dve.tensor_tensor(dh[r, :, :], Hx[r, :, e, :], ps[r, 2, 0:4 * C].rearrange("p (k v) -> p k v", k=4),
                                               ALU.add)
                        loop.do(st)
                    loop.settle()
                    end = C * p + C - 1
                    for e in range(2):
                        r = slice(64 * e, 64 * e + 64)
                        last = dve.tensor_tensor(Hx[r, :, e, :], dh[r, :, :],
                                                 t["eL"][r, :, end:end + 1].to_broadcast([64, 4, C]), ALU.mult)
                    last.then_inc(S["h_ready"], 1)
                assert loop.n == 20, loop.n
                more(2)
                finish_dve(dve, i, o[:, :, :], W, h[:, 4:8, bass.ds(i * W, W)], more)
                more(NPG)

            with dve.Fori(0, LAST) as i:
                pair(i)
            pair(LAST, keys=False)
            i = NPAIR
            prep_dve(dve, i, NS, False)
            st = Steps(dve, S["smp_step"])
            dve.wait_ge(S["smp_in"], 64)
            dve.wait_ge(S["state_in"], 16)
            k3 = lambda n: kv[:, n, :].unsqueeze(2).to_broadcast([P, 64, 32])
            v3 = lambda a: a[:, :].unsqueeze(1).to_broadcast([P, 64, 32])
            s3, t3 = st8, tmp8
            tt = lambda o_, a, b, op: st.link(dve.tensor_tensor(o_, a, b, op))
            tt(t3, s3, k3(0), ALU.mult)
            st.link(dve.tensor_reduce(sa[:, :], tmp8.rearrange("p k v -> p v k"), AX.X, ALU.add))
            tt(s3, s3, k3(1), ALU.mult)
            tt(t3, k3(2), v3(sa), ALU.mult)
            tt(s3, s3, t3, ALU.subtract)
            tt(t3, k3(3), v3(vv), ALU.mult)
            tt(s3, s3, t3, ALU.add)
            tt(t3, s3, k3(4), ALU.mult)
            st.link(dve.tensor_reduce(so[:, :], tmp8.rearrange("p k v -> p v k"), AX.X, ALU.add))
            dve.sem_inc(S["smp_done"], 1)
            finish_dve(dve, i, ocol[:, :, :], NS, h[:, 4:8, SEQ:TOK])
    sems.clear()


def odd_phase(T, ba):
    nc, ps, io = T.nc, T.ps, T.io
    sems = Sems(nc, "odd")
    w_in = [sems("w_in0"), sems("w_in1")]
    (row_out, row_free, product, row_in, conv_done, silu_done, step, cleared, ba_in, ba_exp, ba_log, ba_abs, ba_neg) = (
        sems(n) for n in ("row_out", "row_free", "product", "row_in", "conv_done", "silu_done", "step", "cleared",
                          "ba_in", "ba_exp", "ba_log", "ba_abs", "ba_neg"))
    w_rounded, w_split = sems("w_rounded"), sems("w_split")
    PAR, NT = KT * P, ODD_T - 1
    with ExitStack() as ctx:
        sb = lambda n, s, d=F32: ctx.enter_context(nc.sbuf_tensor("odd" + n, s, d))
        wh, wl = sb("_wh", [P, 2, KT * P], F32R), sb("_wl", [P, 2, KT * P], F32R)
        w, row, cv = sb("_w", [P, 2, ODD_BLK]), sb("_row", [P, 2, 3 + TOK]), sb("_cv", [P, 2, TOK])
        sp1, sp2 = sb("_sp1", [P, TOK]), sb("_sp2", [P, TOK])
        block = ctx.enter_context(nc.Block())
        B8, A8 = slice(BETA_ROW, BETA_ROW + 8), slice(A_ROW, A_ROW + 8)

        @block.sync
        def _(sp):
            with sp.Fori(0, NT // 2) as i:
                for j in range(2):
                    sp.wait_ge(silu_done, 2 * i + j + 1)
                    sp.dma_start(w[:, j, :], io["w_odd"][bass.ds(2 * i + j, 1), :, :].rearrange("a p n -> (a p) n"))\
                      .then_inc(w_in[j], 16)
            sp.wait_ge(silu_done, NT + 1)
            sp.dma_start(w[:, 0, :], io["w_odd"][NT]).then_inc(w_in[0], 16)

        @block.tensor
        def _(pe):
            with pe.Fori(0, NT // 2) as i:
                for j in range(2):
                    pe.wait_ge(w_split, 2 * i + j + 1)
                    for c in range(GRP):
                        pe.wait_ge(row_in, 6 * i + 3 * j + c + 1)
                        group_products(pe, T, 3 * j + c, wh[:, j, :], wl[:, j, :], c).then_inc(product, 1)
            pe.wait_ge(w_split, NT + 1)
            for c in range(GRP):
                pe.wait_ge(row_in, 3 * NT + c + 1)
                group_products(pe, T, c, wh[:, 0, :], wl[:, 0, :], c).then_inc(product, 1)

        @block.scalar
        def _(act):
            act.sem_inc(row_in, 6)
            act.sem_inc(silu_done, 2)
            act.preload_act_table(ACT.Silu)
            act.wait_ge(w_in[0], 16)
            round_weights(act, wh[:, 0, :], w[:, 0, 0:KT * P], w_rounded)
            with act.Fori(0, NT // 2) as i:
                for j in range(2):
                    act.wait_ge(w_in[1 - j], 16 * (i + j) + 16)
                    round_weights(act, wh[:, 1 - j, :], w[:, 1 - j, 0:KT * P], w_rounded)
                    act.wait_ge(row_free, 2 * i + j + 1)
                    for c in range(GRP):
                        act.wait_ge(product, 6 * i + 3 * j + c + 1)
                        act.activation(row[:, j, 3 + c * GC:3 + (c + 1) * GC], ps[:, 3 * j + c, 0:GC], ACT.Copy)\
                           .then_inc(row_in, 1)
                    act.wait_ge(conv_done, 2 * i + j + 1)
                    act.activation(cv[:, j, :], cv[:, j, :], ACT.Silu).then_inc(silu_done, 1)
            for c in range(GRP):
                act.wait_ge(product, 3 * NT + c + 1)
                last = act.activation(ba[:, c * GC:(c + 1) * GC], ps[:, c, 0:GC], ACT.Copy)
            last.then_inc(ba_in, 1)
            act.preload_act_table_set(EXP_LN_SET)
            act.wait_ge(ba_in, 1)
            act.activation(ba[B8, :], ba[B8, :], ACT.Exp, scale=-1.0)
            act.activation(sp1[A8, :], ba[A8, :], ACT.Identity, bias=T.vec("dt_bias")[A8, :]).then_inc(ba_exp, 1)
            act.wait_ge(ba_exp, 1)
            act.activation(sp2[A8, :], sp1[A8, :], ACT.Abs).then_inc(ba_abs, 1)
            act.wait_ge(ba_abs, 1)
            act.activation(sp2[A8, :], sp2[A8, :], ACT.Exp, scale=-1.0).then_inc(ba_abs, 1)
            act.wait_ge(ba_abs, 2)
            act.activation(sp2[A8, :], sp2[A8, :], ACT.Ln, bias=1.0)
            act.activation(row[A8, 0, 0:1], T.vec("a_log")[A8, :], ACT.Exp).then_inc(ba_log, 1)

        @block.vector
        def _(dve):
            dve.wait_ge(cleared, 1)
            per = 2 * 6

            def rest(t, j):
                dve.wait_ge(w_rounded, t + 1)
                rest_weights(dve, wl[:, j, :], w[:, j, 0:KT * P], wh[:, j, :], w_split)

            rest(0, 0)
            with dve.Fori(0, NT // 2) as i:
                st = Steps(dve, step, i * per)
                for j in range(2):
                    rest(2 * i + j + 1, 1 - j)
                    tap = [w[:, j, PAR + n:PAR + n + 1] for n in range(4)]
                    kept = w[:, j, PAR + 4:PAR + 4 + 3 * NS].rearrange("p (r b) -> p r b", r=3)
                    dve.wait_ge(row_in, 6 * i + 3 * j + 3 + 6)
                    s = cv[:, j, SEQ:TOK]
                    o = cv[:, j, 0:SEQ]
                    st.do(dve.tensor_scalar(s, kept[:, 0, :], tap[0], None, ALU.mult))
                    st.link(dve.tensor_scalar(o, row[:, j, 0:SEQ], tap[0], None, ALU.mult))
                    for n in (1, 2):
                        st.do(dve.scalar_tensor_tensor(out=s, in0=kept[:, n, :], scalar=tap[n], in1=s, op0=ALU.mult,
                                                       op1=ALU.add))
                        st.link(dve.scalar_tensor_tensor(out=o, in0=row[:, j, n:n + SEQ], scalar=tap[n], in1=o,
                                                         op0=ALU.mult, op1=ALU.add))
                    dve.scalar_tensor_tensor(out=cv[:, j, :], in0=row[:, j, 3:3 + TOK], scalar=tap[3], in1=cv[:, j, :],
                                             op0=ALU.mult, op1=ALU.add).then_inc(conv_done, 1)
                assert st.n == per
            st = Steps(dve, step, per * NT // 2)
            dve.wait_ge(ba_exp, 1)
            st.link(dve.tensor_scalar(ba[B8, :], ba[B8, :], 1.0, None, ALU.add))
            st.do(dve.reciprocal(ba[B8, :], ba[B8, :]))
            dve.wait_ge(ba_log, 1)
            st.link(dve.scalar_tensor_tensor(out=sp1[A8, :], in0=sp1[A8, :], scalar=0.0, in1=sp2[A8, :], op0=ALU.max,
                                             op1=ALU.add))
            st.link(dve.tensor_scalar(sp1[A8, :], sp1[A8, :], row[A8, 0, 0:1], -1.0, ALU.mult, ALU.mult))
            st.do(dve.tensor_tensor_scan(ba[A8, 0:SEQ], T.const("scan64")[A8, :], sp1[A8, 0:SEQ], 0.0, ALU.mult, ALU.add))
            st.link(dve.tensor_copy(ba[A8, SEQ:TOK], sp1[A8, SEQ:TOK]))

        @block.gpsimd
        def _(pool):
            pool.memset(row[:, :, 0:3], 0.0).then_inc(cleared, 1)
            pool.sem_inc(row_free, 2)
            with pool.Fori(0, NT // 2) as i:
                for j in range(2):
                    pool.wait_ge(silu_done, 2 * i + j + 3)
                    pool.dma_start(T.odd_rows[bass.ds(2 * i + j, 1), :, :].rearrange("a p n -> (a p) n"),
                                   cv[:, j, :]).then_inc(row_out, 16)
                    pool.dma_start(io["dnconv_new"][bass.ds(2 * i + j, 1), :, :].rearrange("a p n -> (a p) n"),
                                   row[:, j, SEQ:SEQ + 3 + NS]).then_inc(row_out, 16)
                    pool.wait_ge(row_out, 64 * i + 32 * j + 32)
                    pool.sem_inc(row_free, 1)
    sems.clear()


def delta_phase(T, ba):
    nc, h, ps, io = T.nc, T.h, T.ps, T.io
    sems = Sems(nc, "dn")
    S = {n: sems(n) for n in (
        "rows_in", "squared", "sq_sum", "rn_log", "rn", "ba_cut", "spread", "l_copied", "l_exp", "unit", "turned", "k_copied",
        "ba_turned", "tm_ready", "kd_ready", "diff", "diff_exp", "keyed", "gram", "blocks_copied", "blocks_ready", "x_ready",
        "y_done", "y_ready", "z_done", "solved", "masked", "w_done", "r_ready", "u_done", "u_copied", "s_done", "s_ready",
        "o_copied", "o_sq", "o_sum", "rs_log", "rs", "out_ready", "step", "cleared", "pe_passed", "end_diff", "end_exp",
        "state_out")}
    ones, ident, sel = T.const("ones"), T.const("ident"), T.const("sel")
    W = 2 * C
    with ExitStack() as ctx:
        sb = lambda n, s: ctx.enter_context(nc.sbuf_tensor("dn" + n, s, F32))
        X = sb("_x", [P, 32, W])
        sq = sb("_sq", [P, 16, W])
        bs, bt, ek = sb("_bs", [P, W]), sb("_bt", [P, W]), sb("_ek", [P, 8])
        Lb, eL, kb, kbe, qe, ktm, bv, r0, vn, st_, tmp, o, rs = (sb("_" + n, [P, 8, W]) for n in
                                                              "Lb eL kb kbe qe ktm bv r0 vn S tmp o rs".split())
        dt_, dn, mt, xm, xt, y, at = (sb("_m" + n, [P, 512]) for n in "dt dn mt xm xt y at".split())
        mtl = sb("_mtl", [P, 5, 512])
        block = ctx.enter_context(nc.Block())
        m8 = lambda name: T.const(name).unsqueeze(1).to_broadcast([P, 8, C])
        h8 = lambda a: a.rearrange("p (h i) -> p h i", h=8)
        two = lambda b: ps[:, b:b + 2, :].rearrange("p b (h w) -> p (b h) w", h=4)
        bank = lambda b, hd: b + hd // 4
        col = lambda hd, a=0, n=W: slice((hd % 4) * W + a, (hd % 4) * W + a + n)
        hc = lambda hd: slice(64 * hd, 64 * hd + 64)

        @block.sync
        def _(sp):
            rows = T.odd_rows[0:32].rearrange("t p n -> p t n")
            sp.dma_start(X[:, :, :], rows[:, :, 0:W]).then_inc(S["rows_in"], 16)
            with sp.Fori(1, NPAIR) as i:
                sp.wait_ge(S["out_ready"], i)
                sp.dma_start(X[:, :, :], rows[:, :, bass.ds(i * W, W)]).then_inc(S["rows_in"], 16)
            sp.wait_ge(S["s_ready"], 2 * NPAIR + 1)
            sp.dma_start(io["dn_prompt"], st_[:, :, :]).then_inc(S["state_out"], 16)
            sp.wait_ge(S["state_out"], 16)

        @block.gpsimd
        def _(pool):
            pool.memset(st_[:, :, :], 0.0).then_inc(S["cleared"], 1)
            pool.wait_ge(S["cleared"], 1)
            pool.sem_inc(S["s_ready"], 1)
            with pool.Fori(0, NPAIR) as i:
                pool.wait_ge(S["blocks_copied"], i + 1)
                for lv in range(1, 6):
                    last = pool.tensor_tensor(h8(mtl[:, lv - 1, :]), h8(mt[:, :]), m8(f"lev{lv}T"), ALU.mult)
                last.then_inc(S["blocks_ready"], 1)

        @block.tensor
        def _(pe):
            with pe.Fori(0, NPAIR) as i:
                pe.wait_ge(S["squared"], i + 1)
                for b in range(4):
                    mm = pe.matmul(ps[:, b, :], ones, sq[:, 4 * b:4 * b + 4, :], start=True, stop=True)
                mm.then_inc(S["sq_sum"], 1)
                pe.wait_ge(S["ba_cut"], i + 1)
                for b, r in ((4, slice(A_ROW, A_ROW + 8)), (6, slice(BETA_ROW, BETA_ROW + 8))):
                    for hd in range(8):
                        mm = pe.matmul(ps[:, bank(b, hd), col(hd)], sel[r, hd * P:(hd + 1) * P], bs[r, :], start=True, stop=True)
                mm.then_inc(S["spread"], 1)
                pe.wait_ge(S["unit"], i + 1)
                for b, t0 in ((0, 8), (2, 16)):
                    for hd in range(8):
                        mm = pe.transpose(ps[:, bank(b, hd), col(hd)], X[:, t0 + hd, :], ident)
                pe.wait_ge(S["l_copied"], i + 1)
                mm = pe.transpose(ps[:, 4, 0:P], bs[:, :], ident)
                mm.then_inc(S["turned"], 1)
                pe.wait_ge(S["keyed"], i + 1)

                def gram(b, left, right):
                    for p in range(2):
                        c = slice(C * p, C * p + C)
                        for hd in range(8):
                            mm = pe.matmul(ps[64 * p:64 * p + 64, b, hc(hd)], left(hd)[:, c], right(hd)[:, c], start=True,
                                           stop=True)
                    mm.then_inc(S["gram"], 1)

                k_, q_, kb_ = (lambda hd: X[:, 8 + hd, :]), (lambda hd: X[:, hd, :]), (lambda hd: kb[:, hd, :])
                gram(5, k_, kb_)
                gram(6, kb_, k_)
                gram(7, k_, q_)
                pe.wait_ge(S["tm_ready"], i + 1)
                solve_levels_pe(pe, T, S, i, mtl, xm, xt, y, (0, 1, 2), S["pe_passed"])
                pe.wait_ge(S["masked"], i + 1)
                pe.wait_ge(S["solved"], i + 1)
                for p in range(2):
                    r, a = slice(64 * p, 64 * p + 64), C * p
                    c = slice(a, a + C)
                    pe.wait_ge(S["s_ready"], 2 * i + p + 1)
                    for hd in range(8):
                        mm = pe.matmul(ps[r, bank(0, hd), col(hd)], kbe[:, hd, c], st_[:, hd, :], start=True, stop=True)
                    mm.then_inc(S["w_done"], 1)
                    pe.wait_ge(S["r_ready"], 2 * i + p + 1)
                    alone(pe, S["pe_passed"])
                    for hd in range(8):
                        mm = pe.matmul(ps[r, bank(2, hd), col(hd)], xt[r, hc(hd)], r0[r, hd, :], start=True, stop=True)
                    mm.then_inc(S["u_done"], 1)
                    pe.wait_ge(S["u_copied"], 2 * i + p + 1)
                    alone(pe, S["pe_passed"])
                    for hd in range(8):
                        pe.matmul(ps[:, bank(6, hd), col(hd)], ktm[r, hd, :], vn[r, hd, :], start=True, stop=True)
                    for hd in range(8):
                        pe.matmul(ps[:, bank(4, hd), col(hd, a, C)], st_[:, hd, :], qe[:, hd, c], start=True, stop=False,
                                  skip_group_check=True)
                        mm = pe.matmul(ps[:, bank(4, hd), col(hd, a, C)], vn[r, hd, :], at[r, hc(hd)], start=False, stop=True,
                                       skip_group_check=True)
                    mm.then_inc(S["s_done"], 1)
                pe.wait_ge(S["o_sq"], i + 1)
                for b in range(2):
                    mm = pe.matmul(ps[:, b, :], ones, rs[:, 4 * b:4 * b + 4, :], start=True, stop=True)
                mm.then_inc(S["o_sum"], 1)

        @block.scalar
        def _(act):
            act.preload_act_table_set(EXP_LN_SET)
            with act.Fori(0, NPAIR) as i:
                act.wait_ge(S["rows_in"], 16 * i + 16)
                act.activation(sq[:, :, :], X[:, 0:16, :], ACT.Square).then_inc(S["squared"], 1)
                act.wait_ge(S["sq_sum"], i + 1)
                act.activation(sq[:, :, :], ps[:, 0:4, :].rearrange("p b (h w) -> p (b h) w", h=4), ACT.Ln,
                               bias=T.vec("eps_rms")).then_inc(S["rn_log"], 1)
                act.wait_ge(S["rn_log"], i + 1)
                act.activation(sq[:, :, :], sq[:, :, :], ACT.Exp, scale=-0.5).then_inc(S["rn"], 1)
                act.wait_ge(S["spread"], i + 1)
                act.activation(Lb[:, :, :], two(4), ACT.Copy).then_inc(S["l_copied"], 1)
                act.wait_ge(S["l_copied"], i + 1)
                act.activation(eL[:, :, :], Lb[:, :, :], ACT.Exp).then_inc(S["l_exp"], 1)
                act.wait_ge(S["turned"], i + 1)
                act.activation(bt[:, :], ps[:, 4, 0:P], ACT.Copy).then_inc(S["ba_turned"], 1)
                act.wait_ge(S["end_diff"], i + 1)
                act.activation(ek[:, :], ek[:, :], ACT.Exp).then_inc(S["end_exp"], 1)
                act.wait_ge(S["diff"], i + 1)
                act.activation(dt_[:, :], dt_[:, :], ACT.Exp)
                act.activation(dn[:, :], dn[:, :], ACT.Exp).then_inc(S["diff_exp"], 1)
                solve_levels_act(act, T, S, i, y, (0, 1, 2))
                for p in range(2):
                    r = slice(64 * p, 64 * p + 64)
                    act.wait_ge(S["u_done"], 2 * i + p + 1)
                    act.activation(vn[r, :, :], ps[r, 2:4, :].rearrange("p b (h w) -> p (b h) w", h=4), ACT.Copy)\
                       .then_inc(S["u_copied"], 1)
                act.wait_ge(S["s_done"], 2 * i + 2)
                act.activation(o[:, :, :], two(4), ACT.Copy).then_inc(S["o_copied"], 1)
                act.wait_ge(S["o_copied"], i + 1)
                act.activation(rs[:, :, :], o[:, :, :], ACT.Square).then_inc(S["o_sq"], 1)
                act.wait_ge(S["o_sum"], i + 1)
                act.activation(rs[:, :, :], two(0), ACT.Ln, scale=1.0 / P, bias=T.vec("eps_rms")).then_inc(S["rs_log"], 1)
                act.wait_ge(S["rs_log"], i + 1)
                act.activation(rs[:, :, :], rs[:, :, :], ACT.Exp, scale=-0.5).then_inc(S["rs"], 1)

        @block.vector
        def _(dve):
            per = DN_STEPS
            with dve.Fori(0, NPAIR) as i:
                st = Steps(dve, S["step"], per * i)
                q_, k_ = X[:, 0:8, :], X[:, 8:16, :]
                dve.tensor_copy(bs[:, :], ba[:, bass.ds(i * W, W)]).then_inc(S["ba_cut"], 1)
                dve.wait_ge(S["rn"], i + 1)
                st.do(dve.scalar_tensor_tensor(out=q_, in0=q_, scalar=P ** -0.5, in1=sq[:, 0:8, :], op0=ALU.mult,
                                               op1=ALU.mult))
                st.link(dve.tensor_tensor(k_, k_, sq[:, 8:16, :], ALU.mult))
                dve.sem_inc(S["unit"], 1)
                dve.wait_ge(S["spread"], i + 1)
                st.link(dve.tensor_tensor(kb[:, :, :], k_, two(6), ALU.mult))
                dve.wait_ge(S["l_exp"], i + 1)
                st.do(dve.tensor_tensor(kbe[:, :, :], kb[:, :, :], eL[:, :, :], ALU.mult))
                st.link(dve.tensor_tensor(qe[:, :, :], q_, eL[:, :, :], ALU.mult))
                dve.sem_inc(S["keyed"], 1)
                dve.wait_ge(S["ba_turned"], i + 1)
                for p in range(2):
                    r = slice(64 * p, 64 * p + 64)
                    end = C * p + C - 1
                    lt = bt[r, A_ROW:A_ROW + 8]
                    st.do(dve.tensor_tensor(ek[r, :].unsqueeze(2), Lb[r, :, end:end + 1], lt.unsqueeze(2), ALU.subtract))
                    st.do(dve.tensor_tensor(h8(dt_[r, :]), Lb[r, :, C * p:C * p + C], lt.unsqueeze(2).to_broadcast([64, 8, C]),
                                            ALU.subtract))
                st.settle()
                dve.sem_inc(S["end_diff"], 1)
                st.link(dve.tensor_scalar(dn[:, :], dt_[:, :], -1.0, 0.0, ALU.mult, ALU.min))
                st.link(dve.tensor_scalar(dt_[:, :], dt_[:, :], 0.0, None, ALU.min))
                dve.sem_inc(S["diff"], 1)
                b8 = bt[:, BETA_ROW:BETA_ROW + 8].unsqueeze(2).to_broadcast([P, 8, W])
                st.do(dve.tensor_tensor(bv[:, :, :], two(2), b8, ALU.mult))
                dve.wait_ge(S["end_exp"], i + 1)
                st.do(dve.tensor_tensor(ktm[:, :, :], two(0), ek[:, :].unsqueeze(2).to_broadcast([P, 8, W]), ALU.mult))
                st.settle()
                dve.sem_inc(S["tm_ready"], 1)
                dve.wait_ge(S["gram"], 3 * i + 3)
                dve.wait_ge(S["diff_exp"], i + 1)
                st.do(dve.tensor_tensor(mt[:, :], dt_[:, :], ps[:, 5, :], ALU.mult))
                st.do(dve.tensor_tensor(xm[:, :], dn[:, :], ps[:, 6, :], ALU.mult))
                st.link(dve.tensor_tensor(at[:, :], dt_[:, :], ps[:, 7, :], ALU.mult))
                dve.sem_inc(S["blocks_copied"], 1)
                st.do(dve.tensor_tensor(h8(xt[:, :]), h8(mt[:, :]), m8("lev0T"), ALU.mult))
                st.link(dve.tensor_tensor(h8(xm[:, :]), h8(xm[:, :]), m8("lev0"), ALU.mult))
                st.do(dve.tensor_tensor(h8(xt[:, :]), m8("eye64"), h8(xt[:, :]), ALU.subtract))
                st.link(dve.tensor_tensor(h8(xm[:, :]), m8("eye64"), h8(xm[:, :]), ALU.subtract))
                dve.sem_inc(S["x_ready"], 1)
                st.link(dve.tensor_tensor(h8(at[:, :]), h8(at[:, :]), m8("inclT"), ALU.mult))
                dve.sem_inc(S["masked"], 1)
                solve_levels_dve(dve, T, S, st, i, xm, xt, (0, 1, 2))
                for p in range(2):
                    r = slice(64 * p, 64 * p + 64)
                    dve.wait_ge(S["w_done"], 2 * i + p + 1)
                    st.link(dve.tensor_tensor(r0[r, :, :], bv[r, :, :],
                                              ps[r, 0:2, :].rearrange("p b (h w) -> p (b h) w", h=4), ALU.subtract))
                    dve.sem_inc(S["r_ready"], 1)
                    end = C * p + C - 1
                    dve.wait_ge(S["u_copied"], 2 * i + p + 1)
                    st.link(dve.tensor_tensor(tmp[:, :, :], st_[:, :, :], eL[:, :, end:end + 1].to_broadcast([P, 8, W]),
                                              ALU.mult))
                    dve.wait_ge(S["s_done"], 2 * i + p + 1)
                    st.link(dve.tensor_tensor(st_[:, :, :], tmp[:, :, :], two(6), ALU.add))
                    dve.sem_inc(S["s_ready"], 1)
                dve.wait_ge(S["rs"], i + 1)
                st.link(dve.scalar_tensor_tensor(out=o[:, :, :], in0=o[:, :, :], scalar=T.vec("onorm"), in1=rs[:, :, :],
                                                 op0=ALU.mult, op1=ALU.mult))
                st.link(dve.tensor_tensor(h[:, :, bass.ds(i * W, W)], o[:, :, :], X[:, 24:32, :], ALU.mult))
                dve.sem_inc(S["out_ready"], 1)
                assert st.n == per, st.n
    sems.clear()


DN_STEPS = 38


def delta_samples_phase(T, ba):
    nc, h, ps, io = T.nc, T.h, T.ps, T.io
    sems = Sems(nc, "ds")
    S = {n: sems(n) for n in ("rows_in", "state_in", "squared", "sq_sum", "rn_log", "rn", "unit", "turned", "copied",
                              "stored", "loaded", "decay", "o_ready", "o_stored", "o_back", "o_turned", "o_copied", "o_sq",
                              "o_sum", "rs_log", "rs", "step")}
    ones, ident = T.const("ones"), T.const("ident")
    with ExitStack() as ctx:
        sb = lambda n, s: ctx.enter_context(nc.sbuf_tensor("ds" + n, s, F32))
        X, sq = sb("_x", [P, 32, NS]), sb("_sq", [P, 16, NS])
        rows, barow = sb("_rows", [NS, 3 * 1024]), sb("_barow", [NS, P])
        kr, qr, vr, br, gr = sb("_kr", [P, P]), sb("_qr", [P, P]), sb("_vr", [P, 64]), sb("_br", [P, 1]), sb("_gr", [P, 1])
        s3, t3 = sb("_s", [P, P, 64]), sb("_t", [P, P, 64])
        sa, so = sb("_sa", [P, 64]), sb("_so", [P, 64])
        orow, o, rs = sb("_orow", [NS, 1024]), sb("_o", [P, 8, NS]), sb("_rs", [P, 8, NS])
        scr = nc.dram_tensor("scratch_dn_rows", [3, NS, 1024], F32, kind="Internal").ap()
        scr_b = nc.dram_tensor("scratch_dn_ba", [2, NS, 8], F32, kind="Internal").ap()
        scr_o = nc.dram_tensor("scratch_dn_o", [NS, 1024], F32, kind="Internal").ap()
        block = ctx.enter_context(nc.Block())

        @block.sync
        def _(sp):
            sp.dma_start(X[:, :, :], T.odd_rows[0:32, :, SEQ:TOK].rearrange("t p n -> p t n")).then_inc(S["rows_in"], 16)
            sp.dma_start(s3[:, :, :], io["dn_in"].rearrange("p (k v) -> p k v", k=P)).then_inc(S["state_in"], 16)
            sp.wait_ge(S["copied"], 1)
            sp.dma_start(scr.rearrange("a b n -> b a n"), rows[:, :].rearrange("b (a n) -> b a n", a=3)).then_inc(S["stored"], 16)
            sp.dma_start(scr_b[0], barow[:, BETA_ROW:BETA_ROW + 8]).then_inc(S["stored"], 16)
            sp.dma_start(scr_b[1], barow[:, A_ROW:A_ROW + 8]).then_inc(S["stored"], 16)
            sp.wait_ge(S["stored"], 48)
            for e in range(2):
                r = slice(64 * e, 64 * e + 64)
                for dst, src in ((qr[r, :], scr[0].rearrange("b (h k) -> (b h) k", h=8)),
                                 (kr[r, :], scr[1].rearrange("b (h k) -> (b h) k", h=8)),
                                 (vr[r, :], scr[2].rearrange("b (h e v) -> e (b h) v", h=8, e=2)[e]),
                                 (br[r, :], scr_b[0].rearrange("b (h a) -> (b h) a", a=1)),
                                 (gr[r, :], scr_b[1].rearrange("b (h a) -> (b h) a", a=1))):
                    sp.dma_start(dst, src).then_inc(S["loaded"], 16)
            sp.wait_ge(S["o_ready"], 1)
            for e in range(2):
                sp.dma_start(scr_o.rearrange("b (h e v) -> e (b h) v", h=8, e=2)[e], so[64 * e:64 * e + 64, :])\
                  .then_inc(S["o_stored"], 16)
            sp.wait_ge(S["o_stored"], 32)
            sp.dma_start(orow[:, :], scr_o).then_inc(S["o_back"], 16)
            sp.dma_start(io["dn_new"].rearrange("p (k v) -> p k v", k=P), s3[:, :, :]).then_inc(S["o_stored"], 16)
            sp.wait_ge(S["o_stored"], 48)

        @block.tensor
        def _(pe):
            pe.wait_ge(S["squared"], 1)
            pe.matmul(ps[:, 0, 0:16 * NS], ones, sq[:, :, :], start=True, stop=True).then_inc(S["sq_sum"], 1)
            pe.wait_ge(S["unit"], 1)
            for k in range(24):
                pe.transpose(ps[0:NS, 1 + k // 4, (k % 4) * P:(k % 4 + 1) * P], X[:, k, :], ident)
            pe.transpose(ps[0:NS, 7, 0:P], ba[:, SEQ:TOK], ident).then_inc(S["turned"], 1)
            pe.wait_ge(S["o_back"], 16)
            for k in range(8):
                mm = pe.transpose(ps[:, 0, k * NS:(k + 1) * NS], orow[:, k * P:(k + 1) * P], ident[0:NS, 0:NS])
            mm.then_inc(S["o_turned"], 1)
            pe.wait_ge(S["o_sq"], 1)
            pe.matmul(ps[:, 1, 0:8 * NS], ones, rs[:, :, :], start=True, stop=True).then_inc(S["o_sum"], 1)

        @block.scalar
        def _(act):
            act.preload_act_table_set(EXP_LN_SET)
            act.wait_ge(S["rows_in"], 16)
            act.activation(sq[:, :, :], X[:, 0:16, :], ACT.Square).then_inc(S["squared"], 1)
            act.wait_ge(S["sq_sum"], 1)
            act.activation(sq[:, :, :], ps[:, 0, 0:16 * NS].rearrange("p (h w) -> p h w", h=16), ACT.Ln,
                           bias=T.vec("eps_rms")).then_inc(S["rn_log"], 1)
            act.wait_ge(S["rn_log"], 1)
            act.activation(sq[:, :, :], sq[:, :, :], ACT.Exp, scale=-0.5).then_inc(S["rn"], 1)
            act.wait_ge(S["turned"], 1)
            act.activation(rows[:, :].rearrange("b (a n) -> b a n", a=6), ps[0:NS, 1:7, :], ACT.Copy)
            act.activation(barow[:, :], ps[0:NS, 7, 0:P], ACT.Copy).then_inc(S["copied"], 1)
            act.wait_ge(S["loaded"], 160)
            act.activation(gr[:, :], gr[:, :], ACT.Exp).then_inc(S["decay"], 1)
            act.wait_ge(S["o_turned"], 1)
            act.activation(o[:, :, :], ps[:, 0, 0:8 * NS].rearrange("p (h w) -> p h w", h=8), ACT.Copy).then_inc(S["o_copied"], 1)
            act.wait_ge(S["o_copied"], 1)
            act.activation(rs[:, :, :], o[:, :, :], ACT.Square).then_inc(S["o_sq"], 1)
            act.wait_ge(S["o_sum"], 1)
            act.activation(rs[:, :, :], ps[:, 1, 0:8 * NS].rearrange("p (h w) -> p h w", h=8), ACT.Ln, scale=1.0 / P,
                           bias=T.vec("eps_rms")).then_inc(S["rs_log"], 1)
            act.wait_ge(S["rs_log"], 1)
            act.activation(rs[:, :, :], rs[:, :, :], ACT.Exp, scale=-0.5).then_inc(S["rs"], 1)

        @block.vector
        def _(dve):
            st = Steps(dve, S["step"])
            dve.wait_ge(S["rn"], 1)
            st.do(dve.scalar_tensor_tensor(out=X[:, 0:8, :], in0=X[:, 0:8, :], scalar=P ** -0.5, in1=sq[:, 0:8, :],
                                           op0=ALU.mult, op1=ALU.mult))
            st.link(dve.tensor_tensor(X[:, 8:16, :], X[:, 8:16, :], sq[:, 8:16, :], ALU.mult))
            dve.sem_inc(S["unit"], 1)
            dve.wait_ge(S["decay"], 1)
            dve.wait_ge(S["state_in"], 16)
            k3, q3 = (a[:, :].unsqueeze(2).to_broadcast([P, P, 64]) for a in (kr, qr))
            s, t = s3[:, :, :], t3[:, :, :]
            over_k = t3[:, :, :].rearrange("p k v -> p v k")
            st.link(dve.tensor_tensor(t, s, k3, ALU.mult))
            st.link(dve.tensor_reduce(sa[:, :], over_k, AX.X, ALU.add))
            st.link(dve.tensor_scalar(sa[:, :], sa[:, :], gr[:, 0:1], None, ALU.mult))
            st.link(dve.tensor_tensor(sa[:, :], vr[:, :], sa[:, :], ALU.subtract))
            st.link(dve.tensor_scalar(sa[:, :], sa[:, :], br[:, 0:1], None, ALU.mult))
            st.link(dve.tensor_tensor(t, k3, sa[:, :].unsqueeze(1).to_broadcast([P, P, 64]), ALU.mult))
            st.link(dve.scalar_tensor_tensor(out=s, in0=s, scalar=gr[:, 0:1], in1=t, op0=ALU.mult, op1=ALU.add))
            st.link(dve.tensor_tensor(t, s, q3, ALU.mult))
            st.link(dve.tensor_reduce(so[:, :], over_k, AX.X, ALU.add))
            dve.sem_inc(S["o_ready"], 1)
            dve.wait_ge(S["rs"], 1)
            st.link(dve.scalar_tensor_tensor(out=o[:, :, :], in0=o[:, :, :], scalar=T.vec("onorm"), in1=rs[:, :, :],
                                             op0=ALU.mult, op1=ALU.mult))
            st.link(dve.tensor_tensor(h[:, :, SEQ:TOK], o[:, :, :], X[:, 24:32, :], ALU.mult))
    sems.clear()


def ffn(T, l, x_dram, out_dram):
    nc = T.nc
    with nc.sbuf_tensor(f"ffn_a{l}", [P, FT, TOK], F32) as a:
        with nc.sbuf_tensor(f"ffn_hh{l}", [P, KT, TOK], F32R) as T.hh, nc.sbuf_tensor(f"ffn_hl{l}", [P, KT, TOK], F32R) as T.hl:
            norm_phase(T, f"normf{l}", f"norm_ffn{l}", x_dram)
            ffn_up_phase(T, f"up{l}", l, a)
        down_phase(T, f"down{l}", T.io["w_down"][l], a, x_dram, out_dram)


def trunk_program(nc, io):
    with ExitStack() as ctx:
        T = Trunk(nc, io, ctx)
        T.n_phys = io["k_pages"].shape[0]
        scratch = lambda n, s: nc.dram_tensor("scratch_" + n, s, F32, kind="Internal").ap()
        T.xs_rows = scratch("xs_rows", [NB_T, P, TOK])
        T.odd_rows = scratch("odd_rows", [ODD_T - 1, P, TOK])
        x1, x2, x3 = (scratch(n, [KT, P, TOK]) for n in ("x1", "x2", "x3"))
        load_phase(T)
        with nc.sbuf_tensor("consts0", [P, CONSTS_0], F32) as T.consts:
            with nc.sbuf_tensor("hh0", [P, KT, TOK], F32R) as T.hh, nc.sbuf_tensor("hl0", [P, KT, TOK], F32R) as T.hl:
                norm_phase(T, "norm0", "norm_even", io["x"], consts=True)
                qk_phase(T)
                v_phase(T)
                pb_phase(T)
            with nc.sbuf_tensor("h0", [P, KT, TOK], F32) as T.h:
                attention_phase(T)
                rwkv_phase(T)
                residual_phase(T, "out0", io["w_out_even"], T.h, io["x"], x1)
        ffn(T, 0, x1, x2)
        with nc.sbuf_tensor("consts1", [P, CONSTS.shape[1]], F32) as T.consts, nc.sbuf_tensor("ba", [P, TOK], F32) as ba:
            with nc.sbuf_tensor("hh1", [P, KT, TOK], F32R) as T.hh, nc.sbuf_tensor("hl1", [P, KT, TOK], F32R) as T.hl:
                norm_phase(T, "norm1", "norm_odd", x2, consts=True)
                odd_phase(T, ba)
            with nc.sbuf_tensor("h1", [P, KT, TOK], F32) as T.h:
                delta_phase(T, ba)
                delta_samples_phase(T, ba)
                residual_phase(T, "out1", io["w_out_odd"], T.h, x2, x3)
        ffn(T, 1, x3, io["y"])


OUTS = {
    "y": (KT, P, TOK), "qk_rows": (8, P, TOK), "v_rows": (TOK, D_A), "shift_new": (NB_T, P, 1 + NS),
    "wkv_prompt": (2, 64, 4, 64), "wkv_new": (P, 64 * 32), "dn_prompt": (P, 8, P), "dn_new": (P, P * 64),
    "dnconv_new": (ODD_T - 1, P, 3 + NS), "dnconv_old": (NS, 2, QKV_T * P), "ffnconv_new": (2, FT, P, 2 + NS),
    "ffnconv_old": (2, NS, 1, D_FF),
}


def outputs(r):
    y = r["y"].reshape(D_MODEL, TOK).T
    kk = r["qk_rows"][4:].reshape(D_A, TOK).T
    v = r["v_rows"]
    shift = r["shift_new"].reshape(NB_COLS, 1 + NS).T
    dnc = r["dnconv_new"][:QKV_T].reshape(QKV_T * P, 3 + NS).T
    ffc = r["ffnconv_new"].reshape(2, D_FF, 2 + NS).transpose(0, 2, 1)
    return (
        y[:SEQ].reshape(1, SEQ, D_MODEL), y[SEQ:].reshape(NS, 1, D_MODEL),
        kk[:SEQ].reshape(1, 1, SEQ, H_A, DH), v[:SEQ].reshape(1, 1, SEQ, H_A, DH),
        kk[SEQ:].reshape(1, NS, 1, H_A, DH), v[SEQ:].reshape(1, NS, 1, H_A, DH),
        r["wkv_prompt"].transpose(2, 0, 3, 1).reshape(1, 1, 8, 64, 64),
        r["wkv_new"].reshape(2, NS, 8, 64, 32).transpose(1, 2, 0, 4, 3).reshape(1, NS, 8, 64, 64),
        shift[:1].reshape(1, 1, NB_COLS), shift[1:].reshape(1, NS, NB_COLS),
        r["dn_prompt"].transpose(1, 0, 2).reshape(1, 1, 8, P, P),
        r["dn_new"].reshape(2, NS, 8, P, 64).transpose(1, 2, 3, 0, 4).reshape(1, NS, 8, P, P),
        dnc[:3].reshape(1, 1, 3, QKV_T * P),
        np.concatenate([r["dnconv_old"], dnc[3:, None]], 1)[None],
        ffc[:, None, :2], np.concatenate([r["ffnconv_old"], ffc[:, 2:, None]], 2),
    )


def layouts(inputs):
    A = {k: np.asarray(v) for k, v in inputs.items()}
    f = np.float32

    def blocks(w, nt=None):
        k, n = w.shape
        return w.reshape(k // P, P, n // P, P).transpose(2, 1, 0, 3).reshape(n // P, P, k)

    def cols(v):
        return v.reshape(-1, P).T

    def tiles(rows):
        return rows.T.reshape(-1, P, rows.shape[0])

    L = {"consts": CONSTS, "ones": ONES}
    L["x"] = np.concatenate([A["x_prompt"][0], A["x_sample"][:, 0]], 0).T.reshape(KT, P, TOK)
    one = np.ones((P, 1), f)
    row32 = lambda v: np.concatenate([np.zeros(A_ROW, f), v, np.zeros(P - A_ROW - 8, f)])[:, None]
    vec = {
        "norm_even": cols(A["norm_mix_even"][0]), "norm_ffn0": cols(A["norm_ffn"][0]),
        "norm_odd": cols(A["norm_mix_odd"][0]), "norm_ffn1": cols(A["norm_ffn"][1]),
        "w0": cols(A["w0_b"][0]), "a0": cols(A["a0_b"][0]), "kk": cols(A["kk_b"][0]), "ka": cols(A["ka_b"][0]),
        "rk": cols(A["rk_b"][0]), "lnw": cols(A["lnx_w_b"][0]), "lnb": cols(A["lnx_b_b"][0]),
        "onorm": A["onorm_dn"][0][:, None], "sb_bias": np.broadcast_to(A["sb_bias"][0], (P, 8)),
        "a_log": row32(A["a_log_dn"][0]), "dt_bias": row32(A["dt_bias_dn"][0]),
        "eps_rms": one * f(RMS_EPS), "eps_gn": one * f(GN_EPS),
    }
    L["vecs"] = np.concatenate([vec[n] for n in VEC_COLS], 1)
    we = A["w_in_even"][0]
    gain = np.concatenate([np.tile(A["qnorm_a"][0], (8,)), np.tile(A["knorm_a"][0], (8,))])
    L["w_qk"] = np.concatenate([blocks(we[:, :2 * D_A]), tiles(gain[None])], 2)
    L["w_v"] = we[:, 2 * D_A:3 * D_A].reshape(KT, P, D_A).transpose(1, 0, 2)
    L["w_pb"] = np.concatenate([blocks(we[:, 3 * D_A:]), tiles(A["mu_b"]), tiles(A["state_shift"][0])], 2)
    L["w_lora"] = np.concatenate([np.concatenate([A["w_up_b"][0], A["a_up_b"][0]], 0), A["g_up_b"][0]], 1)
    L["w_out_even"] = blocks(A["w_out_even"][0])
    wo = A["w_in_odd"][0]
    n = QKV_T * P + 8 * P
    ba = np.zeros((D_MODEL, P), f)
    ba[:, BETA_ROW:BETA_ROW + 8] = wo[:, n:n + 8]
    ba[:, A_ROW:A_ROW + 8] = wo[:, n + 8:]
    par = np.zeros((ODD_T, P, 4 + 3 * NS), f)
    par[:QKV_T, :, :4] = tiles(A["conv_dn"][0])
    par[QKV_T:ODD_T - 1, :, 3] = 1.0
    par[:QKV_T, :, 4:] = tiles(A["state_dn_conv"][0].transpose(1, 0, 2).reshape(3 * NS, -1))
    L["w_odd"] = np.concatenate([blocks(np.concatenate([wo[:, :n], ba], 1)), par], 2)
    L["w_out_odd"] = blocks(A["w_out_odd"][0])
    L["w_ff"] = np.stack([np.concatenate([
        blocks(A["w_gate"][l]), blocks(A["w_up"][l]), tiles(A["conv_ffn"][l]), tiles(A["conv_ffn_b"][l][None]),
        tiles(A["state_ffn_conv"][l].transpose(1, 0, 2).reshape(2 * NS, -1))], 2) for l in range(2)])
    L["w_down"] = np.stack([blocks(A["w_down"][l]) for l in range(2)])
    L["k_pages"] = A["cache_k"][0].reshape(-1, PAGE, D_A)
    L["v_pages"] = A["cache_v"][0].reshape(-1, PAGE, D_A)
    L["page_table"] = A["page_table"][:, ::-1].reshape(1, -1)
    L["wkv_in"] = A["state_wkv"][0].reshape(NS, 8, 2, 32, 64).transpose(2, 0, 1, 4, 3).reshape(P, 64 * 32)
    L["dn_in"] = A["state_dn"][0].reshape(NS, 8, 128, 2, 64).transpose(3, 0, 1, 2, 4).reshape(P, 128 * 64)
    L["dn_conv_rows"] = A["state_dn_conv"][0, :, 1:]
    L["ffn_conv_rows"] = A["state_ffn_conv"][:, :, 1:]
    return {k: np.ascontiguousarray(v) for k, v in L.items()}


def kernel(**inputs):
    import concourse.bacc as bacc
    from concourse.bass_utils import run_bass_kernel_spmd

    nc = bacc.Bacc("TRN2", target_bir_lowering=False, num_devices=1)
    arrays, io = {}, {}
    for name, a in layouts(inputs).items():
        arrays[f"in_{name}"] = a
        io[name] = nc.dram_tensor(f"in_{name}", a.shape, mybir.dt.from_np(a.dtype), kind="ExternalInput").ap()
    for name, shape in OUTS.items():
        io[name] = nc.dram_tensor(f"out_{name}", shape, F32, kind="ExternalOutput").ap()
    trunk_program(nc, io)
    r = run_bass_kernel_spmd(nc, [arrays], core_ids=[0]).results[0]
    return tuple(np.ascontiguousarray(a) for a in outputs({n: r[f"out_{n}"] for n in OUTS}))
```

```python
from contextlib import ExitStack

import concourse.bass as bass
import numpy as np
from concourse import mybir

F32 = mybir.dt.float32
F32R = mybir.dt.float32r
I32 = mybir.dt.int32
ALU = mybir.AluOpType
ACT = mybir.ActivationFunctionType
AX = mybir.AxisListType

P = 128
D_MODEL = 1024
SEQ = 1024
NS = 8
TOK = SEQ + NS
GRP = 3
GC = TOK // GRP
KT = D_MODEL // P
H_A, DH = 8, 64
D_A = H_A * DH
PAST, PAGE = 8192, 128
NPG = PAST // PAGE
D_B = 512
NB_COLS = 3 * D_B + 256
NB_T = NB_COLS // P
H_C = 8
QKV_T = 24
ODD_T = QKV_T + 8 + 1
BETA_ROW, A_ROW = 0, 32
D_FF = 2816
FT = D_FF // P
C = 64
NPAIR = SEQ // (2 * C)
RMS_EPS = 1e-6
GN_EPS = 64e-5
DECAY = float(np.exp(-0.5))

EXP_LN_SET = "natural_log_exp_and_others"

QK_BLK = KT * P + 1
PB_BLK = KT * P + 1 + NS
ODD_BLK = KT * P + 4 + 3 * NS
FF_BLK = 2 * KT * P + 4 + 2 * NS

CONST_COLS = {}


def _constants():
    parts = {}
    r = np.arange(P)
    parts["ident"] = np.eye(P)
    parts["headrow"] = (r[:, None] % 32 == np.arange(8)[None, :]) * 1.0
    parts["halves"] = (r[:, None] // 64 == r[None, :] // 64) * 1.0
    parts["later"] = (r[:, None] >= r[None, :]) * 1.0
    parts["earlier"] = (r[:, None] < r[None, :]) * 1.0
    parts["dcap"] = np.where(r[:, None] < r[None, :], 3e38, -1e30)
    j, i = r[:, None] % C, np.arange(C)[None, :]
    parts["strictT"] = (j < i) * 1.0
    parts["inclT"] = (j <= i) * 1.0
    parts["ninclT"] = (j <= i) * -1.0
    parts["eye64"] = (j == i) * 1.0
    for lv in range(6):
        b = 1 << lv
        parts[f"lev{lv}T"] = ((j // (2 * b) == i // (2 * b)) & (j % (2 * b) < b) & (i % (2 * b) >= b)) * 1.0
    b = 1
    parts["lev0"] = ((j // 2 == i // 2) & (i % 2 < 1) & (j % 2 >= 1)) * 1.0
    parts["scan64"] = np.broadcast_to((np.arange(SEQ) % C != 0) * 1.0, (P, SEQ))
    parts["scanhead"] = np.broadcast_to((np.arange(512) % NPG != 0) * 1.0, (P, 512))
    sel = np.zeros((P, 8 * P))
    for h in range(8):
        sel[A_ROW + h, h * P:(h + 1) * P] = 1.0
        sel[BETA_ROW + h, h * P:(h + 1) * P] = 1.0
    parts["sel"] = sel
    at = 0
    for n, a in parts.items():
        CONST_COLS[n] = (at, a.shape[1])
        at += a.shape[1]
    return np.concatenate(list(parts.values()), axis=1).astype(np.float32)


CONSTS = _constants()
CONSTS_0 = CONST_COLS["sel"][0]
ONES = np.ones((P, P), np.float32)
VEC_COLS = {}
for _n, _w in (("norm_even", 8), ("norm_ffn0", 8), ("norm_odd", 8), ("norm_ffn1", 8), ("w0", 4), ("a0", 4),
               ("kk", 4), ("ka", 4), ("rk", 4), ("lnw", 4), ("lnb", 4), ("onorm", 1), ("sb_bias", 8),
               ("a_log", 1), ("dt_bias", 1), ("eps_rms", 1), ("eps_gn", 1)):
    VEC_COLS[_n] = (sum(w for _, w in VEC_COLS.values()), _w)
NVEC = sum(w for _, w in VEC_COLS.values())


class Sems:

    def __init__(self, nc, phase):
        self.nc, self.phase, self.all = nc, phase, []

    def __call__(self, name):
        s = self.nc.alloc_semaphore(f"{self.phase}_{name}")
        self.all.append(s)
        return s

    def clear(self):
        self.nc.clear_and_free_semaphores(self.all)
        self.nc.all_engine_barrier()


class Steps:

    def __init__(self, eng, sem, at=0):
        self.eng, self.sem, self.at, self.n = eng, sem, at, 0

    def do(self, ins):
        ins.then_inc(self.sem, 1)
        self.n += 1

    def settle(self):
        self.eng.wait_ge(self.sem, self.at + self.n)

    def link(self, ins):
        self.do(ins)
        self.settle()


class Trunk:

    def __init__(self, nc, io, ctx):
        self.nc, self.io = nc, io
        self.ones = ctx.enter_context(nc.sbuf_tensor("ones_sb", [P, P], F32))
        self.vecs = ctx.enter_context(nc.sbuf_tensor("vecs_sb", [P, NVEC], F32))
        self.ps = ctx.enter_context(nc.psum_tensor("ps", [P, 8, 512], F32))

    def const(self, name):
        if name == "ones":
            return self.ones[:, :]
        a, w = CONST_COLS[name]
        return self.consts[:, a:a + w]

    def vec(self, name):
        a, w = VEC_COLS[name]
        return self.vecs[:, a:a + w]


def load_phase(T):
    nc, io = T.nc, T.io
    sems = Sems(nc, "load")
    loaded = sems("loaded")
    with nc.Block() as block:
        @block.sync
        def _(sp):
            sp.dma_start(T.ones[:, :], io["ones"]).then_inc(loaded, 16)
            sp.dma_start(T.vecs[:, :], io["vecs"]).then_inc(loaded, 16)
            sp.dma_start(io["dnconv_old"], io["dn_conv_rows"]).then_inc(loaded, 16)
            sp.dma_start(io["ffnconv_old"], io["ffn_conv_rows"]).then_inc(loaded, 16)
            sp.wait_ge(loaded, 64)
    sems.clear()


def norm_phase(T, name, gain, x_dram, consts=False):
    nc, ps, hh, hl = T.nc, T.ps, T.hh, T.hl
    sems = Sems(nc, name)
    x_in = [sems(f"x_in{k}") for k in range(KT)]
    squared, summed, logged, rooted, sq_used, scaled, rounded, consts_in = (
        sems(n) for n in ("squared", "summed", "logged", "rooted", "sq_used", "scaled", "rounded", "consts_in"))
    ones, g = T.const("ones"), T.vec(gain)
    with ExitStack() as ctx:
        sb = lambda n, s: ctx.enter_context(nc.sbuf_tensor(name + n, s, F32))
        x, sq, rinv = sb("_x", [P, KT, TOK]), sb("_sq", [P, 2, TOK]), sb("_r", [P, TOK])
        block = ctx.enter_context(nc.Block())

        @block.sync
        def _(sp):
            for k in range(KT):
                sp.dma_start(x[:, k, :], x_dram[k]).then_inc(x_in[k], 16)
            if consts:
                sp.dma_start(T.consts[:, :], T.io["consts"][:, 0:T.consts.shape[1]]).then_inc(consts_in, 16)
                sp.wait_ge(consts_in, 16)

        @block.scalar
        def _(act):
            act.preload_act_table_set(EXP_LN_SET)
            for k in range(KT):
                act.wait_ge(x_in[k], 16)
                if k >= 2:
                    act.wait_ge(sq_used, k - 1)
                act.activation(sq[:, k % 2, :], x[:, k, :], ACT.Square).then_inc(squared, 1)
            act.wait_ge(summed, 1)
            act.activation(rinv[:, :].rearrange("p (c n) -> p c n", c=GRP), ps[:, 0:GRP, 0:GC], ACT.Ln,
                           scale=1.0 / D_MODEL, bias=T.vec("eps_rms")).then_inc(logged, 1)
            act.wait_ge(logged, 1)
            act.activation(rinv[:, :], rinv[:, :], ACT.Exp, scale=-0.5).then_inc(rooted, 1)
            for k in range(KT):
                act.wait_ge(scaled, k + 1)
                act.activation(hh[:, k, :], x[:, k, :], ACT.Copy).then_inc(rounded, 1)

        @block.tensor
        def _(pe):
            for k in range(KT):
                pe.wait_ge(squared, k + 1)
                for c in range(GRP):
                    mm = pe.matmul(ps[:, c, 0:GC], ones, sq[:, k % 2, c * GC:(c + 1) * GC], start=(k == 0),
                                   stop=(k == KT - 1))
                mm.then_inc(sq_used, 1)
            pe.wait_ge(sq_used, KT)
            pe.sem_inc(summed, 1)

        @block.vector
        def _(dve):
            dve.wait_ge(rooted, 1)
            for k in range(KT + 1):
                if k < KT:
                    dve.scalar_tensor_tensor(out=x[:, k, :], in0=x[:, k, :], scalar=g[:, k:k + 1], in1=rinv[:, :],
                                             op0=ALU.mult, op1=ALU.mult).then_inc(scaled, 1)
                if k >= 1:
                    dve.wait_ge(rounded, k)
                    dve.tensor_tensor(hl[:, k - 1, :], x[:, k - 1, :], hh[:, k - 1, :].bitcast(F32), ALU.subtract)
    sems.clear()


def round_weights(act, hi, w, rounded):
    act.activation(hi, w, ACT.Copy).then_inc(rounded, 1)


def rest_weights(dve, lo, w, hi, rest_ready):
    dve.tensor_tensor(lo, w, hi.bitcast(F32), ALU.subtract).then_inc(rest_ready, 1)


def split_products(pe, out, parts, last=None):
    n = len(parts)
    for k, (wh, wl, xh, xl) in enumerate(parts):
        pe.matmul(out, wh, xh, start=(k == 0), stop=False)
        pe.matmul(out, wl, xh, start=False, stop=False)
        mm = pe.matmul(out, wh, xl, start=False, stop=(k == n - 1))
    return mm


def group_products(pe, T, bank, hi, lo, c):
    g = slice(c * GC, (c + 1) * GC)
    return split_products(pe, T.ps[:, bank, 0:GC],
                          [(hi[:, k * P:(k + 1) * P], lo[:, k * P:(k + 1) * P], T.hh[:, k, g], T.hl[:, k, g])
                           for k in range(KT)])


def residual_phase(T, name, w_dram, src, x_dram, out_dram):
    nc, ps = T.nc, T.ps
    sems = Sems(nc, name)
    w_in = [sems("w_in0"), sems("w_in1")]
    x_in = [sems("x_in0"), sems("x_in1")]
    (product, added, stored, x_free, w_rounded, w_split, src_rounded, src_split) = (
        sems(n) for n in ("product", "added", "stored", "x_free", "w_rounded", "w_split", "src_rounded", "src_split"))
    with ExitStack() as ctx:
        sb = lambda n, s, d=F32: ctx.enter_context(nc.sbuf_tensor(name + n, s, d))
        w, x = sb("_w", [P, 2, KT * P]), sb("_x", [P, 2, TOK])
        wh, wl = sb("_wh", [P, 2, KT * P], F32R), sb("_wl", [P, 2, KT * P], F32R)
        sh, sl = sb("_sh", [P, KT, TOK], F32R), sb("_sl", [P, KT, TOK], F32R)
        block = ctx.enter_context(nc.Block())
        LAST = KT // 2 - 1

        @block.sync
        def _(sp):
            with sp.Fori(0, KT // 2) as i:
                for j in range(2):
                    tile = bass.ds(2 * i + j, 1)
                    sp.wait_ge(w_split, 2 * i + j + 1)
                    sp.dma_start(w[:, j, :], w_dram[tile, :, :].rearrange("a p n -> (a p) n")).then_inc(w_in[j], 16)
                    sp.wait_ge(x_free, 2 * i + j + 1)
                    sp.dma_start(x[:, j, :], x_dram[tile, :, :].rearrange("a p n -> (a p) n")).then_inc(x_in[j], 16)

        @block.scalar
        def _(act):
            def weights(i, j):
                act.wait_ge(w_in[j], 16 * i + 16)
                act.wait_ge(product, 6 * i + 3 * j + 3)
                round_weights(act, wh[:, j, :], w[:, j, :], w_rounded)

            weights(0, 0)
            for k in range(KT):
                act.activation(sh[:, k, :], src[:, k, :], ACT.Copy).then_inc(src_rounded, 1)
            weights(0, 1)
            with act.Fori(1, KT // 2) as i:
                weights(i, 0)
                weights(i, 1)

        @block.tensor
        def _(pe):
            pe.sem_inc(product, 6)

            def tile(i, j, first=False):
                pe.wait_ge(w_split, 2 * i + j + 3)
                for c in range(GRP):
                    pe.wait_ge(added, 6 * i + 3 * j + c + 1)
                    g = slice(c * GC, (c + 1) * GC)
                    for k in range(KT):
                        if first and c == 0:
                            pe.wait_ge(src_split, k + 1)
                        wk = slice(k * P, (k + 1) * P)
                        out = ps[:, 3 * j + c, 0:GC]
                        pe.matmul(out, wh[:, j, wk], sh[:, k, g], start=(k == 0), stop=False)
                        pe.matmul(out, wl[:, j, wk], sh[:, k, g], start=False, stop=False)
                        mm = pe.matmul(out, wh[:, j, wk], sl[:, k, g], start=False, stop=(k == KT - 1))
                    mm.then_inc(product, 1)

            tile(0, 0, True)
            tile(0, 1)
            with pe.Fori(1, KT // 2) as i:
                tile(i, 0)
                tile(i, 1)

        @block.vector
        def _(dve):
            dve.sem_inc(added, 6)
            dve.sem_inc(w_split, 2)

            def rest(t, j):
                dve.wait_ge(w_rounded, t + 1)
                rest_weights(dve, wl[:, j, :], w[:, j, :], wh[:, j, :], w_split)

            def add(i, j):
                dve.wait_ge(x_in[j], 16 * i + 16)
                for c in range(GRP):
                    dve.wait_ge(product, 6 * i + 3 * j + c + 7)
                    row = x[:, j, c * GC:(c + 1) * GC]
                    dve.tensor_tensor(row, ps[:, 3 * j + c, 0:GC], row, ALU.add).then_inc(added, 1)

            rest(0, 0)
            for k in range(KT):
                dve.wait_ge(src_rounded, k + 1)
                dve.tensor_tensor(sl[:, k, :], src[:, k, :], sh[:, k, :].bitcast(F32), ALU.subtract).then_inc(src_split, 1)
            with dve.Fori(0, LAST) as i:
                rest(2 * i + 1, 1)
                add(i, 0)
                rest(2 * i + 2, 0)
                add(i, 1)
            rest(2 * LAST + 1, 1)
            add(LAST, 0)
            add(LAST, 1)

        @block.gpsimd
        def _(pool):
            pool.sem_inc(x_free, 2)
            with pool.Fori(0, KT // 2) as i:
                for j in range(2):
                    pool.wait_ge(added, 6 * i + 3 * j + 9)
                    pool.dma_start(out_dram[bass.ds(2 * i + j, 1), :, :].rearrange("a p n -> (a p) n"), x[:, j, :])\
                        .then_inc(stored, 16)
                    pool.wait_ge(stored, 32 * i + 16 * j + 16)
                    pool.sem_inc(x_free, 1)
    sems.clear()


def down_phase(T, name, w_dram, a, x_dram, out_dram):
    nc, ps = T.nc, T.ps
    sems = Sems(nc, name)
    HK = FT // 2
    w_in, x_in = [sems("w_in0"), sems("w_in1")], [sems("x_in0"), sems("x_in1")]
    (w_rounded, w_split, w_used, a_rounded, a_split, product, added, stored, x_free) = (
        sems(n) for n in ("w_rounded", "w_split", "w_used", "a_rounded", "a_split", "product", "added", "stored",
                          "x_free"))
    with ExitStack() as ctx:
        sb = lambda n, s, d=F32: ctx.enter_context(nc.sbuf_tensor(name + n, s, d))
        w, wh, wl = sb("_w", [P, 2, HK * P]), sb("_wh", [P, 2, HK * P], F32R), sb("_wl", [P, 2, HK * P], F32R)
        ah, al = sb("_ah", [P, FT, GC], F32R), sb("_al", [P, FT, GC], F32R)
        x = sb("_x", [P, 2, GC])
        block = ctx.enter_context(nc.Block())

        @block.sync
        def _(sp):
            for c in range(GRP):
                with sp.Fori(0, KT // 2) as i:
                    for j in range(2):
                        tile = bass.ds(2 * i + j, 1)
                        n = KT * c + 2 * i + j
                        for v in range(2):
                            sp.wait_ge(w_split, 2 * n + v + 1)
                            sp.dma_start(w[:, v, :], w_dram[tile, :, v * HK * P:(v + 1) * HK * P]
                                         .rearrange("a p n -> (a p) n")).then_inc(w_in[v], 16)
                        sp.wait_ge(x_free, n + 1)
                        sp.dma_start(x[:, j, :], x_dram[tile, :, c * GC:(c + 1) * GC].rearrange("a p n -> (a p) n"))\
                          .then_inc(x_in[j], 16)

        @block.scalar
        def _(act):
            def weights(c, o, v):
                act.wait_ge(w_in[v], 16 * (KT * c + o) + 16)
                act.wait_ge(w_used, 2 * (KT * c + o) + v + 1)
                round_weights(act, wh[:, v, :], w[:, v, :], w_rounded)

            for c in range(GRP):
                weights(c, 0, 0)
                if c:
                    act.wait_ge(product, KT * c)
                for k in range(FT):
                    act.activation(ah[:, k, :], a[:, k, c * GC:(c + 1) * GC], ACT.Copy).then_inc(a_rounded, 1)
                    if k == 3:
                        weights(c, 0, 1)
                with act.Fori(1, KT) as o:
                    for v in range(2):
                        weights(c, o, v)

        @block.tensor
        def _(pe):
            pe.sem_inc(w_used, 2)
            for c in range(GRP):
                def tile(i, j, first=False):
                    n = KT * c + 2 * i + j
                    pe.wait_ge(added, n + 1)
                    for v in range(2):
                        pe.wait_ge(w_split, 2 * n + v + 3)
                        for k in range(HK):
                            kk = HK * v + k
                            if first:
                                pe.wait_ge(a_split, FT * c + kk + 1)
                            wk = slice(k * P, (k + 1) * P)
                            pe.matmul(ps[:, j, 0:GC], wh[:, v, wk], ah[:, kk, :], start=(kk == 0), stop=False)
                            pe.matmul(ps[:, j, 0:GC], wl[:, v, wk], ah[:, kk, :], start=False, stop=False)
                            mm = pe.matmul(ps[:, j, 0:GC], wh[:, v, wk], al[:, kk, :], start=False, stop=(kk == FT - 1))
                        mm.then_inc(w_used, 1)
                    pe.wait_ge(w_used, 2 * n + 4)
                    pe.sem_inc(product, 1)

                tile(0, 0, True)
                tile(0, 1)
                with pe.Fori(1, KT // 2) as i:
                    for j in range(2):
                        tile(i, j)

        @block.vector
        def _(dve):
            dve.sem_inc(added, 2)
            dve.sem_inc(w_split, 2)

            def rest(n, v):
                dve.wait_ge(w_rounded, 2 * n + v + 1)
                rest_weights(dve, wl[:, v, :], w[:, v, :], wh[:, v, :], w_split)

            def add(c, i, j):
                n = KT * c + 2 * i + j
                dve.wait_ge(x_in[j], 16 * (KT // 2 * c + i) + 16)
                dve.wait_ge(product, n + 1)
                dve.tensor_tensor(x[:, j, :], ps[:, j, 0:GC], x[:, j, :], ALU.add).then_inc(added, 1)

            rest(0, 0)
            for c in range(GRP):
                for k in range(FT):
                    dve.wait_ge(a_rounded, FT * c + k + 1)
                    dve.tensor_tensor(al[:, k, :], a[:, k, c * GC:(c + 1) * GC], ah[:, k, :].bitcast(F32), ALU.subtract)\
                       .then_inc(a_split, 1)
                    if k == 3:
                        rest(KT * c, 1)
                with dve.Fori(0, KT // 2 - 1) as i:
                    for j in range(2):
                        for v in range(2):
                            rest(KT * c + 2 * i + j + 1, v)
                        add(c, i, j)
                for v in range(2):
                    rest(KT * c + KT - 1, v)
                add(c, KT // 2 - 1, 0)
                if c < GRP - 1:
                    rest(KT * (c + 1), 0)
                add(c, KT // 2 - 1, 1)

        @block.gpsimd
        def _(pool):
            pool.sem_inc(x_free, 2)
            for c in range(GRP):
                with pool.Fori(0, KT // 2) as i:
                    for j in range(2):
                        n = KT * c + 2 * i + j
                        pool.wait_ge(added, n + 3)
                        pool.dma_start(out_dram[bass.ds(2 * i + j, 1), :, c * GC:(c + 1) * GC]
                                       .rearrange("a p n -> (a p) n"), x[:, j, :]).then_inc(stored, 16)
                        pool.wait_ge(stored, 16 * n + 16)
                        pool.sem_inc(x_free, 1)
    sems.clear()


def ffn_up_phase(T, name, l, a):
    nc, ps, io = T.nc, T.ps, T.io
    sems = Sems(nc, name)
    w_in = [sems("w_in0"), sems("w_in1")]
    tail_out, tail_free = sems("tail_out"), sems("tail_free")
    gate_done, up_done, row_in, conv_done, silu_done, multiplied, step, cleared, w_rounded, w_split = (
        sems(n) for n in ("gate_done", "up_done", "row_in", "conv_done", "silu_done", "multiplied", "step", "cleared",
                          "w_rounded", "w_split"))
    w_dram, tail = io["w_ff"][l], io["ffnconv_new"][l]
    UP, PAR = KT * P, 2 * KT * P
    LAST = FT // 2 - 1
    with ExitStack() as ctx:
        sb = lambda n, s, d=F32: ctx.enter_context(nc.sbuf_tensor(name + n, s, d))
        w = sb("_w", [P, 2, FF_BLK])
        wh, wl = sb("_wh", [P, 2, KT * P], F32R), sb("_wl", [P, 2, KT * P], F32R)
        row = sb("_row", [P, 2, 2 + TOK])
        cv = sb("_cv", [P, 2, TOK])
        block = ctx.enter_context(nc.Block())

        @block.sync
        def _(sp):
            with sp.Fori(0, FT // 2) as i:
                for j in range(2):
                    sp.wait_ge(multiplied, 6 * i + 3 * j + 3)
                    sp.dma_start(w[:, j, :], w_dram[bass.ds(2 * i + j, 1), :, :].rearrange("a p n -> (a p) n"))\
                      .then_inc(w_in[j], 16)

        @block.gpsimd
        def _(pool):
            pool.memset(row[:, :, 0:2], 0.0).then_inc(cleared, 1)
            pool.sem_inc(tail_free, 2)
            with pool.Fori(0, FT // 2) as i:
                for j in range(2):
                    pool.wait_ge(row_in, 6 * i + 3 * j + 3 + 3)
                    pool.dma_start(tail[bass.ds(2 * i + j, 1), :, :].rearrange("a p n -> (a p) n"),
                                   row[:, j, SEQ:SEQ + 2 + NS]).then_inc(tail_out, 16)
                    pool.wait_ge(tail_out, 32 * i + 16 * j + 16)
                    pool.sem_inc(tail_free, 1)

        @block.tensor
        def _(pe):
            with pe.Fori(0, FT // 2) as i:
                for j in range(2):
                    t = 2 * i + j
                    pe.wait_ge(w_split, 2 * t + 1)
                    for c in range(GRP):
                        pe.wait_ge(row_in, 3 * t + c + 1)
                        group_products(pe, T, c, wh[:, 0, :], wl[:, 0, :], c).then_inc(gate_done, 1)
                    pe.wait_ge(w_split, 2 * t + 2)
                    for c in range(GRP):
                        pe.wait_ge(multiplied, 3 * t + c + 4)
                        group_products(pe, T, 3 + c, wh[:, 1, :], wl[:, 1, :], c).then_inc(up_done, 1)

        @block.scalar
        def _(act):
            act.sem_inc(row_in, 3)

            def round_gate(i, j):
                act.wait_ge(w_in[j], 16 * i + 16)
                act.wait_ge(gate_done, 3 * (2 * i + j))
                round_weights(act, wh[:, 0, :], w[:, j, 0:UP], w_rounded)

            def tile(i, j, last=False):
                t = 2 * i + j
                for c in range(GRP):
                    n = 3 * t + c
                    act.wait_ge(gate_done, n + 1)
                    act.wait_ge(conv_done, n + (2 if c < 2 else 1))
                    if c == 2:
                        act.wait_ge(tail_free, t + 1)
                    act.activation(row[:, j, 2 + c * GC:2 + (c + 1) * GC], ps[:, c, 0:GC], ACT.Copy)\
                       .then_inc(row_in, 1)
                    if c == 2 and not last:
                        round_gate(i + (j == 1), 1 - j)
                for c in range(GRP):
                    n = 3 * t + c
                    act.wait_ge(conv_done, n + 7)
                    act.activation(cv[:, j, c * GC:(c + 1) * GC], cv[:, j, c * GC:(c + 1) * GC], ACT.Silu,
                                   bias=w[:, j, PAR + 3:PAR + 4]).then_inc(silu_done, 1)
                if not last:
                    act.wait_ge(up_done, 3 * t + 3)
                    round_weights(act, wh[:, 1, :], w[:, 1 - j, UP:PAR], w_rounded)

            act.preload_act_table(ACT.Silu)
            act.wait_ge(w_in[0], 16)
            for g in range(2):
                round_weights(act, wh[:, g, :], w[:, 0, g * UP:(g + 1) * UP], w_rounded)
            with act.Fori(0, LAST) as i:
                for j in range(2):
                    tile(i, j)
            tile(LAST, 0)
            tile(LAST, 1, True)

        @block.vector
        def _(dve):
            dve.sem_inc(multiplied, 6)
            dve.sem_inc(conv_done, 6)
            dve.wait_ge(cleared, 1)
            per = 2 * (2 * GRP + 3)

            def rest(t, j, g):
                dve.wait_ge(w_rounded, 2 * t + g + 1)
                rest_weights(dve, wl[:, g, :], w[:, j, g * UP:(g + 1) * UP], wh[:, g, :], w_split)

            def tile(i, st, j, last=False):
                t = 2 * i + j
                tap = [w[:, j, PAR + n:PAR + n + 1] for n in range(3)]
                kept = w[:, j, PAR + 4:PAR + 4 + 2 * NS].rearrange("p (r b) -> p r b", r=2)
                for c in range(GRP):
                    n = 3 * t + c
                    a0, a1 = c * GC, min((c + 1) * GC, SEQ)
                    dve.wait_ge(row_in, n + 4)
                    dve.wait_ge(multiplied, n + 1)
                    if c == 2 and not last:
                        rest(t + 1, 1 - j, 0)
                    o = cv[:, j, a0:a1]
                    st.link(dve.tensor_scalar(o, row[:, j, a0:a1], tap[0], None, ALU.mult))
                    st.link(dve.scalar_tensor_tensor(out=o, in0=row[:, j, a0 + 1:a1 + 1], scalar=tap[1],
                                                     in1=o, op0=ALU.mult, op1=ALU.add))
                    if c == 2:
                        s = cv[:, j, SEQ:TOK]
                        st.link(dve.tensor_scalar(s, kept[:, 0, :], tap[0], None, ALU.mult))
                        st.link(dve.scalar_tensor_tensor(out=s, in0=kept[:, 1, :], scalar=tap[1], in1=s,
                                                         op0=ALU.mult, op1=ALU.add))
                        st.link(dve.scalar_tensor_tensor(out=s, in0=row[:, j, 2 + SEQ:2 + TOK], scalar=tap[2],
                                                         in1=s, op0=ALU.mult, op1=ALU.add))
                    dve.scalar_tensor_tensor(out=o, in0=row[:, j, a0 + 2:a1 + 2], scalar=tap[2], in1=o,
                                             op0=ALU.mult, op1=ALU.add).then_inc(conv_done, 1)
                for c in range(GRP):
                    n = 3 * t + c
                    dve.wait_ge(silu_done, n + 1)
                    dve.wait_ge(up_done, n + 1)
                    col = slice(c * GC, (c + 1) * GC)
                    dve.tensor_tensor(a[:, bass.ds(2 * i + j, 1), col].rearrange("p a t -> p (a t)"), cv[:, j, col],
                                      ps[:, 3 + c, 0:GC], ALU.mult).then_inc(multiplied, 1)
                if not last:
                    rest(t + 1, 1 - j, 1)

            for g in range(2):
                rest(0, 0, g)
            with dve.Fori(0, LAST) as i:
                st = Steps(dve, step, i * per)
                for j in range(2):
                    tile(i, st, j)
                assert st.n == per
            st = Steps(dve, step, LAST * per)
            tile(LAST, st, 0)
            tile(LAST, st, 1, True)
    sems.clear()


def qk_phase(T):
    nc, ps, io = T.nc, T.ps, T.io
    sems = Sems(nc, "qk")
    w_in = [sems("w_in0"), sems("w_in1")]
    row_out, row_free, product, raw_in, squared, summed, logged, rooted, scaled, w_rounded, w_split = (
        sems(n) for n in ("row_out", "row_free", "product", "raw_in", "squared", "summed", "logged", "rooted", "scaled",
                          "w_rounded", "w_split"))
    halves = T.const("halves")
    with ExitStack() as ctx:
        sb = lambda n, s, d=F32: ctx.enter_context(nc.sbuf_tensor("qk" + n, s, d))
        w, raw, sq, rt = sb("_w", [P, 2, QK_BLK]), sb("_raw", [P, 2, TOK]), sb("_sq", [P, 2, TOK]), sb("_rt", [P, 2, TOK])
        wh, wl = sb("_wh", [P, 2, KT * P], F32R), sb("_wl", [P, 2, KT * P], F32R)
        block = ctx.enter_context(nc.Block())

        @block.sync
        def _(sp):
            with sp.Fori(0, 4) as i:
                for j in range(2):
                    sp.wait_ge(scaled, 2 * i + j + 1)
                    sp.dma_start(w[:, j, :], io["w_qk"][bass.ds(2 * i + j, 1), :, :].rearrange("a p n -> (a p) n"))\
                      .then_inc(w_in[j], 16)

        @block.tensor
        def _(pe):
            def sums(i, j):
                for c in range(GRP):
                    pe.wait_ge(squared, 6 * i + 3 * j + c + 1)
                    pe.matmul(ps[:, 3 * j + c, 0:GC], halves, sq[:, j, c * GC:(c + 1) * GC], start=True, stop=True)\
                      .then_inc(summed, 1)

            with pe.Fori(0, 4) as i:
                for j in range(2):
                    pe.wait_ge(w_split, 2 * i + j + 1)
                    pe.wait_ge(logged, 2 * i + j + 1)
                    for c in range(GRP):
                        group_products(pe, T, 3 * j + c, wh[:, j, :], wl[:, j, :], c).then_inc(product, 1)
                    sums(i, j)

        @block.scalar
        def _(act):
            act.preload_act_table_set(EXP_LN_SET)
            act.sem_inc(logged, 2)

            def tile(i, j, last=False):
                t = 2 * i + j
                if not last:
                    act.wait_ge(w_in[1 - j], 16 * (i + j) + 16)
                    round_weights(act, wh[:, 1 - j, :], w[:, 1 - j, 0:KT * P], w_rounded)
                act.wait_ge(row_free, t + 1)
                for c in range(GRP):
                    act.wait_ge(product, 3 * t + c + 1)
                    act.activation(raw[:, j, c * GC:(c + 1) * GC], ps[:, 3 * j + c, 0:GC], ACT.Copy)\
                       .then_inc(raw_in, 1)
                    act.activation(sq[:, j, c * GC:(c + 1) * GC], ps[:, 3 * j + c, 0:GC], ACT.Square)\
                       .then_inc(squared, 1)
                act.wait_ge(summed, 3 * t + 3)
                act.activation(rt[:, j, :].rearrange("p (c n) -> p c n", c=GRP), ps[:, 3 * j:3 * j + 3, 0:GC],
                               ACT.Ln, scale=1.0 / DH, bias=T.vec("eps_rms")).then_inc(logged, 1)
                act.wait_ge(logged, t + 3)
                act.activation(rt[:, j, :], rt[:, j, :], ACT.Exp, scale=-0.5).then_inc(rooted, 1)

            act.wait_ge(w_in[0], 16)
            round_weights(act, wh[:, 0, :], w[:, 0, 0:KT * P], w_rounded)
            with act.Fori(0, 3) as i:
                tile(i, 0)
                tile(i, 1)
            tile(3, 0)
            tile(3, 1, True)

        @block.vector
        def _(dve):
            dve.sem_inc(scaled, 2)

            def rest(t, j):
                dve.wait_ge(w_rounded, t + 1)
                rest_weights(dve, wl[:, j, :], w[:, j, 0:KT * P], wh[:, j, :], w_split)

            def tile(i, j, last=False):
                t = 2 * i + j
                if not last:
                    rest(t + 1, 1 - j)
                dve.wait_ge(raw_in, 3 * t + 3)
                dve.wait_ge(rooted, t + 1)
                dve.scalar_tensor_tensor(out=raw[:, j, :], in0=raw[:, j, :], scalar=w[:, j, KT * P:KT * P + 1],
                                         in1=rt[:, j, :], op0=ALU.mult, op1=ALU.mult).then_inc(scaled, 1)

            rest(0, 0)
            with dve.Fori(0, 3) as i:
                tile(i, 0)
                tile(i, 1)
            tile(3, 0)
            tile(3, 1, True)

        @block.gpsimd
        def _(pool):
            pool.sem_inc(row_free, 2)
            with pool.Fori(0, 4) as i:
                for j in range(2):
                    pool.wait_ge(scaled, 2 * i + j + 3)
                    pool.dma_start(io["qk_rows"][bass.ds(2 * i + j, 1), :, :].rearrange("a p n -> (a p) n"),
                                   raw[:, j, :]).then_inc(row_out, 16)
                    pool.wait_ge(row_out, 32 * i + 16 * j + 16)
                    pool.sem_inc(row_free, 1)
    sems.clear()


def v_phase(T):
    nc, ps, io = T.nc, T.ps, T.io
    sems = Sems(nc, "v")
    w_in, w_rounded, w_split, product, copied, out = (
        sems(n) for n in ("w_in", "w_rounded", "w_split", "product", "copied", "out"))
    starts = [s * P for s in range(8)] + [TOK - P]
    with ExitStack() as ctx:
        sb = lambda n, s, d=F32: ctx.enter_context(nc.sbuf_tensor("v" + n, s, d))
        w, v = sb("_w", [P, KT, D_A]), sb("_sb", [P, 9, D_A])
        wh, wl = sb("_wh", [P, KT, D_A], F32R), sb("_wl", [P, KT, D_A], F32R)
        block = ctx.enter_context(nc.Block())

        @block.sync
        def _(sp):
            sp.dma_start(w[:, :, :], io["w_v"]).then_inc(w_in, 16)
            sp.wait_ge(copied, 8)
            sp.dma_start(io["v_rows"][0:SEQ, :].rearrange("(s p) n -> p s n", p=P), v[:, 0:8, :]).then_inc(out, 16)
            sp.wait_ge(copied, 9)
            sp.dma_start(io["v_rows"][SEQ:TOK, :], v[P - NS:P, 8, :]).then_inc(out, 16)
            sp.wait_ge(out, 32)

        @block.tensor
        def _(pe):
            for s in range(9):
                if s >= 8:
                    pe.wait_ge(copied, s - 7)
                tok = slice(starts[s], starts[s] + P)
                for k in range(KT):
                    if s == 0:
                        pe.wait_ge(w_split, k + 1)
                    pe.matmul(ps[:, s % 8, :], T.hh[:, k, tok], wh[:, k, :], start=(k == 0), stop=False)
                    pe.matmul(ps[:, s % 8, :], T.hh[:, k, tok], wl[:, k, :], start=False, stop=False)
                    mm = pe.matmul(ps[:, s % 8, :], T.hl[:, k, tok], wh[:, k, :], start=False, stop=(k == KT - 1))
                mm.then_inc(product, 1)

        @block.scalar
        def _(act):
            act.wait_ge(w_in, 16)
            for k in range(KT):
                round_weights(act, wh[:, k, :], w[:, k, :], w_rounded)
            for s in range(9):
                act.wait_ge(product, s + 1)
                act.activation(v[:, s, :], ps[:, s % 8, :], ACT.Copy).then_inc(copied, 1)

        @block.vector
        def _(dve):
            for k in range(KT):
                dve.wait_ge(w_rounded, k + 1)
                rest_weights(dve, wl[:, k, :], w[:, k, :], wh[:, k, :], w_split)
    sems.clear()


def pb_phase(T):
    nc, ps, io = T.nc, T.ps, T.io
    sems = Sems(nc, "pb")
    pages = T.pages
    RING = Pages.RING
    w_in = [sems("w_in0"), sems("w_in1")]
    out_sem, row_free, product, row_in, mixed, step, cleared, w_rounded, w_split = (
        sems(n) for n in ("out", "row_free", "product", "row_in", "mixed", "step", "cleared", "w_rounded", "w_split"))
    MU, LAST = KT * P, NB_T // 2 - 1
    with ExitStack() as ctx:
        sb = lambda n, s, d=F32: ctx.enter_context(nc.sbuf_tensor("pb" + n, s, d))
        w, row, xs = sb("_w", [P, 2, PB_BLK]), sb("_row", [P, 2, 1 + TOK]), sb("_xs", [P, 2, TOK])
        wh, wl = sb("_wh", [P, 2, KT * P], F32R), sb("_wl", [P, 2, KT * P], F32R)
        block = ctx.enter_context(nc.Block())

        @block.sync
        def _(sp):
            def weights(i, j):
                sp.wait_ge(mixed, 2 * i + j + 1)
                sp.dma_start(w[:, j, :], io["w_pb"][bass.ds(2 * i + j, 1), :, :].rearrange("a p n -> (a p) n"))\
                  .then_inc(w_in[j], 16)

            def keys(m):
                for n in range(RING):
                    pages.load_key_page(sp, 0, m, n)

            pages.ask_sp(sp)
            weights(0, 0)
            weights(0, 1)
            pages.start_sp(sp)
            keys(0)
            with sp.Fori(1, NB_T // 2) as i:
                weights(i, 0)
                keys(i)
                weights(i, 1)
            keys(NB_T // 2)

        @block.tensor
        def _(pe):
            pages.start_pe(pe)
            with pe.Fori(0, NB_T // 2) as i:
                for j in range(2):
                    pe.wait_ge(w_split, 2 * i + j + 1)
                    for c in range(GRP):
                        pe.wait_ge(row_in, 6 * i + 3 * j + c + 1)
                        group_products(pe, T, 3 * j + c, wh[:, j, :], wl[:, j, :], c).then_inc(product, 1)

        @block.scalar
        def _(act):
            act.sem_inc(row_in, 6)
            pages.start_act(act)

            def tile(i, j, last=False):
                if not last:
                    act.wait_ge(w_in[1 - j], 16 * (i + j) + 16)
                    round_weights(act, wh[:, 1 - j, :], w[:, 1 - j, 0:KT * P], w_rounded)
                act.wait_ge(row_free, 2 * i + j + 1)
                for c in range(GRP):
                    act.wait_ge(product, 6 * i + 3 * j + c + 1)
                    act.activation(row[:, j, 1 + c * GC:1 + (c + 1) * GC], ps[:, 3 * j + c, 0:GC], ACT.Copy)\
                       .then_inc(row_in, 1)

            act.wait_ge(w_in[0], 16)
            round_weights(act, wh[:, 0, :], w[:, 0, 0:KT * P], w_rounded)
            with act.Fori(0, LAST) as i:
                tile(i, 0)
                tile(i, 1)
            tile(LAST, 0)
            tile(LAST, 1, True)

        @block.vector
        def _(dve):
            dve.sem_inc(mixed, 2)
            pages.start_dve(dve)
            dve.wait_ge(cleared, 1)

            def rest(t, j):
                dve.wait_ge(w_rounded, t + 1)
                rest_weights(dve, wl[:, j, :], w[:, j, 0:KT * P], wh[:, j, :], w_split)

            def tile(i, st, j, last=False):
                if not last:
                    rest(2 * i + j + 1, 1 - j)
                first, units = (RING // 2 * j, RING // 4) if i is not LAST else (0, RING // 2)
                for n in range(units):
                    pages.keys_dve(dve, 0, i if i is not LAST else LAST + j, first + 2 * n)
                dve.wait_ge(row_in, 6 * i + 3 * j + 3 + 6)
                st.do(dve.tensor_tensor(xs[:, j, 0:SEQ], row[:, j, 0:SEQ], row[:, j, 1:1 + SEQ], ALU.subtract))
                st.link(dve.tensor_tensor(xs[:, j, SEQ:TOK], w[:, j, MU + 1:MU + 1 + NS], row[:, j, 1 + SEQ:1 + TOK],
                                          ALU.subtract))
                dve.scalar_tensor_tensor(out=xs[:, j, :], in0=xs[:, j, :], scalar=w[:, j, MU:MU + 1],
                                         in1=row[:, j, 1:1 + TOK], op0=ALU.mult, op1=ALU.add).then_inc(mixed, 1)

            rest(0, 0)
            with dve.Fori(0, LAST) as i:
                st = Steps(dve, step, 4 * i)
                tile(i, st, 0)
                tile(i, st, 1)
            st = Steps(dve, step, 4 * LAST)
            tile(LAST, st, 0)
            tile(LAST, st, 1, True)

        @block.gpsimd
        def _(pool):
            pool.memset(pages.fold[:, :], 0.0).then_inc(pages.cleared, 1)
            pool.memset(row[:, :, 0:1], 0.0).then_inc(cleared, 1)
            pool.sem_inc(row_free, 2)
            with pool.Fori(0, NB_T // 2) as i:
                for j in range(2):
                    pool.wait_ge(mixed, 2 * i + j + 3)
                    pool.dma_start(T.xs_rows[bass.ds(2 * i + j, 1), :, :].rearrange("a p n -> (a p) n"),
                                   xs[:, j, :]).then_inc(out_sem, 16)
                    pool.dma_start(io["shift_new"][bass.ds(2 * i + j, 1), :, :].rearrange("a p n -> (a p) n"),
                                   row[:, j, SEQ:SEQ + 1 + NS]).then_inc(out_sem, 16)
                    pool.wait_ge(out_sem, 64 * i + 32 * j + 32)
                    pool.sem_inc(row_free, 1)
    sems.clear()


class Pages:
    RING = 8

    def __init__(self, T, ctx):
        nc = T.nc
        self.T, self.nc = T, nc
        self.sems = sems = Sems(nc, "pages")
        self.k_in = [sems(f"k_in{n}") for n in range(self.RING)]
        self.v_in = [sems(f"v_in{n}") for n in range(self.RING)]
        (self.qc_in, self.q_turned, self.q_copied, self.q_stored, self.q_in, self.table_in, self.k_used, self.v_used,
         self.reduced, self.biased, self.logged, self.softplus_ready, self.summed, self.z_ready, self.w_ready,
         self.cleared, self.folded, self.selected, self.picked, self.step, self.act_step) = (
            sems(n) for n in ("qc_in", "q_turned", "q_copied", "q_stored", "q_in", "table_in", "k_used", "v_used",
                              "reduced", "biased", "logged", "softplus_ready", "summed", "z_ready", "w_ready",
                              "fold_cleared", "folded", "selected", "picked", "page_step", "page_act_step"))
        sb = lambda n, s, d=F32: ctx.enter_context(nc.sbuf_tensor("pg" + n, s, d))
        self.kp, self.vp = sb("_k", [P, self.RING, D_A]), sb("_v", [P, self.RING, D_A])
        self.qc, self.q = sb("_qc", [P, 4, NS]), sb("_q", [P, D_A])
        self.fold = sb("_fold", [P, D_A])
        self.qr = self.fold[0:NS, :]
        self.prod = sb("_prod", [P, 2, D_A])
        self.z = sb("_z", [P, H_A, NPG])
        self.zb, self.sp, self.tmp, self.cum, self.wts = (sb(n, [P, H_A * NPG]) for n in ("_zb", "_sp", "_tmp", "_cum", "_w"))
        self.table = sb("_table", [1, NS * NPG], I32)
        self.q_rows = nc.dram_tensor("scratch_pg_q", [NS, D_A], F32, kind="Internal").ap()
        self.loads = NPG // self.RING

    def ask_sp(self, sp):
        sp.dma_start(self.qc[:, :, :], self.T.io["qk_rows"][0:4, :, SEQ:TOK].rearrange("t p b -> p t b"))\
          .then_inc(self.qc_in, 16)
        sp.dma_start(self.table[:, :], self.T.io["page_table"]).then_inc(self.table_in, 16)

    def start_sp(self, sp):
        sp.wait_ge(self.q_copied, 1)
        sp.dma_start(self.q_rows, self.qr).then_inc(self.q_stored, 16)
        sp.wait_ge(self.q_stored, 16)
        sp.wait_ge(self.table_in, 16)
        self.load_q(sp, 0)

    def load_q(self, sp, b):
        sp.wait_ge(self.k_used, self.RING + NPG * b)
        sp.dma_start(self.q[:, :], self.q_rows[bass.ds(b, 1), :].to_broadcast([P, D_A])).then_inc(self.q_in, 16)

    def load_key_page(self, sp, b, m, n):
        g = NPG * b + self.RING * m + n
        sp.wait_ge(self.k_used, g + 1)
        page = sp.value_load(self.table[0:1, bass.ds(g, 1)], min_val=0, max_val=self.T.n_phys - 1)
        sp.dma_start(self.kp[:, n, :], self.T.io["k_pages"][bass.ds(page, 1), :, :].rearrange("a p n -> (a p) n"))\
          .then_inc(self.k_in[n], 16)

    def load_keys(self, sp, b):
        for n in range(self.RING):
            self.load_key_page(sp, b, 0, n)
        self.load_q(sp, b)
        with sp.Fori(1, self.loads) as m:
            for n in range(self.RING):
                self.load_key_page(sp, b, m, n)

    def start_pe(self, pe):
        pe.wait_ge(self.qc_in, 16)
        for t in range(4):
            mm = pe.transpose(self.T.ps[0:NS, 7, t * P:(t + 1) * P], self.qc[:, t, :], self.T.const("ident"))
        mm.then_inc(self.q_turned, 1)
        pe.sem_inc(self.v_used, self.RING)

    def sums_pe(self, pe, b):
        pe.wait_ge(self.softplus_ready, b + 1)
        pe.wait_ge(self.picked, b + 1)
        pe.matmul(self.T.ps[:, 6, :], self.T.const("later"), self.sp[:, :], start=True, stop=True)
        pe.matmul(self.T.ps[:, 7, :], self.T.const("ones"), self.sp[:, :], start=True, stop=True).then_inc(self.summed, 1)

    def values_pe(self, pe, b, pages):
        wts = self.wts[:, :].rearrange("p (h n) -> p h n", h=H_A)
        for g in pages:
            if g == 0:
                pe.wait_ge(self.w_ready, b + 1)
            n, c = g % self.RING, 32 * (g % 4)
            pe.wait_ge(self.v_in[n], 16 * self.loads * b + 16 * (g // self.RING) + 16)
            pe.matmul(self.T.ps[c:c + H_A, 7, :], wts[:, :, g], self.vp[:, n, :], start=(g < 4), stop=(g >= NPG - 4),
                      tile_position=(0, c), skip_group_check=True).then_inc(self.v_used, 1)

    def select_pe(self, pe, b):
        pe.wait_ge(self.folded, b + 1)
        for t in range(4):
            mm = pe.matmul(self.T.ps[:, 6, 2 * t:2 * t + 2], self.fold[:, t * P:(t + 1) * P],
                           self.T.const("headrow")[:, 2 * t:2 * t + 2], start=True, stop=True)
        mm.then_inc(self.selected, 1)

    def start_act(self, act):
        act.wait_ge(self.cleared, 1)
        act.wait_ge(self.q_turned, 1)
        act.activation(self.qr, self.T.ps[0:NS, 7, :], ACT.Copy, scale=DH ** -0.5).then_inc(self.q_copied, 1)
        act.sem_inc(self.picked, 1)

    def load_values(self, act, b, g):
        act.wait_ge(self.v_used, NPG * b + g + 1)
        page = act.value_load(self.table[0:1, bass.ds(NPG * b + g, 1)], min_val=0, max_val=self.T.n_phys - 1)
        act.dma_start(self.vp[:, g % self.RING, :], self.T.io["v_pages"][bass.ds(page, 1), :, :]
                      .rearrange("a p n -> (a p) n")).then_inc(self.v_in[g % self.RING], 16)

    def logs_act(self, act, b):
        st = Steps(act, self.act_step, 2 * b)
        act.wait_ge(self.biased, b + 1)
        st.link(act.activation(self.tmp[:, :], self.zb[:, :], ACT.Abs))
        st.link(act.activation(self.tmp[:, :], self.tmp[:, :], ACT.Exp, scale=-1.0))
        act.activation(self.tmp[:, :], self.tmp[:, :], ACT.Ln, bias=1.0).then_inc(self.logged, 1)

    def weights_act(self, act, b):
        act.wait_ge(self.z_ready, b + 1)
        act.activation(self.wts[:, :], self.cum[:, :], ACT.Exp).then_inc(self.w_ready, 1)

    def fold_act(self, act, b):
        act.wait_ge(self.v_used, self.RING + NPG * b + NPG)
        for c in range(0, P, 32):
            last = act.activation(self.fold[c:c + H_A, :], self.T.ps[c:c + H_A, 7, :], ACT.Copy)
        last.then_inc(self.folded, 1)

    def pick_act(self, act, b):
        act.wait_ge(self.selected, b + 1)
        for e in range(2):
            r = slice(64 * e, 64 * e + 64)
            last = act.activation(self.T.h[r, 0:4, bass.ds(SEQ + b, 1)].rearrange("p t a -> p (t a)"),
                                  self.T.ps[r, 6, e:8:2], ACT.Copy)
        last.then_inc(self.picked, 1)

    def keys_dve(self, dve, b, m, n):
        g = self.RING * m + n
        if not isinstance(g, int) or g == 0:
            dve.wait_ge(self.q_in, 16 * b + 16)
        for e in range(2):
            dve.wait_ge(self.k_in[n + e], 16 * self.loads * b + 16 * m + 16)
        dve.wait_ge(self.reduced, NPG // 2 * b + self.RING // 2 * m + n // 2 + 1)
        dve.tensor_tensor(self.prod[:, :, :], self.kp[:, n:n + 2, :], self.q[:, :].unsqueeze(1).to_broadcast([P, 2, D_A]),
                          ALU.mult).then_inc(self.k_used, 2)
        dve.wait_ge(self.k_used, self.RING + NPG * b + g + 2)
        z = self.z[:, :, g:g + 2] if isinstance(g, int) else self.z[:, :, bass.ds(g, 2)]
        dve.tensor_reduce(z.rearrange("p h n -> p n h"), self.prod[:, :, :].rearrange("p n (h d) -> p n h d", h=H_A),
                          AX.X, ALU.add).then_inc(self.reduced, 1)

    def start_dve(self, dve):
        dve.sem_inc(self.k_used, self.RING)
        dve.sem_inc(self.reduced, 1)

    def bias_dve(self, dve, b):
        dve.wait_ge(self.reduced, NPG // 2 * b + NPG // 2 + 1)
        dve.tensor_tensor(self.zb[:, :].rearrange("p (h n) -> p h n", h=H_A), self.z[:, :, :],
                          self.T.vec("sb_bias").unsqueeze(2).to_broadcast([P, H_A, NPG]), ALU.add).then_inc(self.biased, 1)

    def softplus_dve(self, dve, b):
        dve.wait_ge(self.logged, b + 1)
        dve.scalar_tensor_tensor(out=self.sp[:, :], in0=self.zb[:, :], scalar=0.0, in1=self.tmp[:, :], op0=ALU.max,
                                 op1=ALU.add).then_inc(self.softplus_ready, 1)

    def exponents_dve(self, dve, b):
        st, ps, run = Steps(dve, self.step, 3 * b), self.T.ps, self.tmp[:, :]
        dve.wait_ge(self.summed, b + 1)
        st.do(dve.tensor_tensor(self.cum[:, :], self.zb[:, :], ps[:, 6, :], ALU.subtract))
        st.link(dve.tensor_tensor_scan(run, self.T.const("scanhead"), ps[:, 7, :], 0.0, ALU.mult, ALU.add))
        st.link(dve.tensor_tensor(run, run, ps[:, 7, :], ALU.subtract))
        dve.tensor_tensor(self.cum[:, :], self.cum[:, :], run, ALU.subtract).then_inc(self.z_ready, 1)


def attention_phase(T):
    nc, h, ps, io = T.nc, T.h, T.ps, T.io
    sems = Sems(nc, "attn")
    later, earlier = T.const("later"), T.const("earlier")
    HALF = 512
    SCORE_BANK = (0, 1, 6, 7)
    ticks = []
    for g in range(2):
        for s in reversed(range(4 * g + 4)):
            for j in range(2):
                q0 = max(s * P, g * HALF)
                ticks.append((j, g, s, q0, (g + 1) * HALF - q0, s == 0))
    NT = len(ticks)
    STEPS = NT // 2
    heads_in = [sems("heads_in0"), sems("heads_in1")]
    (z_done, zb_done, na_done, log_done, sp_done, cum_done, d_done, w_done, read_done, carried, out_done, step,
     exp_done) = (
        sems(n) for n in ("z_done", "zb_done", "na_done", "log_done", "sp_done", "cum_done", "d_done", "w_done",
                          "read_done", "carried", "out_done", "step", "exp_done"))
    with ExitStack() as ctx:
        sb = lambda n, s: ctx.enter_context(nc.sbuf_tensor("at" + n, s, F32))
        kh, qh, vh = sb("_k", [P, 2, SEQ]), sb("_q", [P, 2, SEQ]), sb("_v", [P, 2, 8, 2 * DH])
        zb, na, sp_, d, w = sb("_zb", [P, 6, HALF]), sb("_na", [P, 4, HALF]), sb("_sp", [P, 4, HALF]), \
            sb("_d", [P, 4, HALF]), sb("_w", [P, 4, HALF])
        block = ctx.enter_context(nc.Block())
        vr = io["v_rows"][0:SEQ, :].rearrange("(s p) (t n) -> t p s n", p=P, n=2 * DH)

        @block.sync
        def _(sp):
            with sp.Fori(0, 2) as i:
                for u in range(2):
                    sp.wait_ge(read_done, NT * (2 * i + u + 1))
                    pair = bass.ds(2 * i + u, 1)
                    sp.dma_start(qh[:, u, :], io["qk_rows"][pair, :, 0:SEQ].rearrange("a p n -> (a p) n"))\
                      .then_inc(heads_in[u], 16)
                    pair_k = bass.ds(2 * i + u + 4, 1)
                    sp.dma_start(kh[:, u, :], io["qk_rows"][pair_k, :, 0:SEQ].rearrange("a p n -> (a p) n"))\
                      .then_inc(heads_in[u], 16)
                    sp.dma_start(vh[:, u, :, :], vr[pair, :, :, :].rearrange("a p s n -> (a p) s n"))\
                      .then_inc(heads_in[u], 16)

        @block.tensor
        def _(pe):
            pe.sem_inc(read_done, 2 * NT)

            def pair(i, u):
                at = NT * (2 * i + u)

                def score(n):
                    j, g, s, q0, nq, last = ticks[n]
                    if n == 0:
                        pe.wait_ge(heads_in[u], 48 * i + 48)
                    if n >= 4:
                        pe.wait_ge(zb_done, at + n - 3)
                    r = slice(64 * j, 64 * j + 64)
                    pe.matmul(ps[:, SCORE_BANK[n % 4], 0:nq], kh[r, u, s * P:(s + 1) * P], qh[r, u, q0:q0 + nq],
                              start=True, stop=True).then_inc(z_done, 1)

                def own_sum(n):
                    j, g, s, q0, nq, last = ticks[n]
                    c0 = q0 - g * HALF
                    pe.wait_ge(sp_done, at + n + 1)
                    pe.matmul(ps[:, 2 + j, c0:c0 + nq], later, sp_[:, n % 4, 0:nq], start=(s == 4 * g + 3),
                              stop=True, skip_group_check=True).then_inc(cum_done, 1)

                def rest_sum(n):
                    j, g, s, q0, nq, last = ticks[n]
                    c0 = q0 - g * HALF
                    pe.wait_ge(d_done, at + n + 1)
                    if last:
                        pe.sem_inc(carried, 1)
                        return
                    pe.matmul(ps[:, 2 + j, c0:c0 + nq], earlier, sp_[:, n % 4, 0:nq], start=False,
                              stop=True, skip_group_check=True).then_inc(carried, 1)

                def read(n):
                    j, g, s, q0, nq, last = ticks[n]
                    c0 = q0 - g * HALF
                    pe.wait_ge(w_done, at + n + 1)
                    if s == 4 * g + 3:
                        pe.wait_ge(out_done, 4 * (2 * i + u) + 2 * g + j + 1)
                    r = slice(64 * j, 64 * j + 64)
                    pe.matmul(ps[r, 4 + j, c0:c0 + nq], vh[:, u, s, r], w[:, n % 4, 0:nq],
                              start=(s == 4 * g + 3), stop=True, skip_group_check=True).then_inc(read_done, 1)

                def both(stage, m):
                    if 0 <= m < STEPS:
                        stage(2 * m)
                        stage(2 * m + 1)

                both(score, 0)
                for m in range(STEPS + 2):
                    both(score, m + 1)
                    both(own_sum, m - 1)
                    both(read, m - 2)
                    both(rest_sum, m - 1)

            with pe.Fori(0, 2) as i:
                for u in range(2):
                    pair(i, u)

        @block.vector
        def _(dve):
            per = sum(1 for t in ticks if t[2] * P >= t[1] * HALF) * 2

            def pair(i, u):
                at = NT * (2 * i + u)
                st = Steps(dve, step, per * (2 * i + u))

                def scores(n):
                    j, g, s, q0, nq, last = ticks[n]
                    dve.wait_ge(z_done, at + n + 1)
                    bias = T.vec("sb_bias")[:, bass.ds(4 * i + 2 * u + j, 1)]
                    dve.tensor_scalar(zb[:, n % 6, 0:nq], ps[:, SCORE_BANK[n % 4], 0:nq], DH ** -0.5, bias, ALU.mult,
                                      ALU.add).then_inc(zb_done, 1)

                def minus_abs(n):
                    nq = ticks[n][4]
                    dve.wait_ge(zb_done, at + n + 1)
                    dve.scalar_tensor_tensor(out=na[:, n % 4, 0:nq], in0=zb[:, n % 6, 0:nq], scalar=-1.0,
                                             in1=zb[:, n % 6, 0:nq], op0=ALU.mult, op1=ALU.min).then_inc(na_done, 1)

                def softplus(n):
                    j, g, s, q0, nq, last = ticks[n]
                    dve.wait_ge(log_done, at + n + 1)
                    if n >= 4:
                        dve.wait_ge(carried, at + n - 3)
                    ins = dve.scalar_tensor_tensor(out=sp_[:, n % 4, 0:nq], in0=zb[:, n % 6, 0:nq], scalar=0.0,
                                                   in1=na[:, n % 4, 0:nq], op0=ALU.max, op1=ALU.add)
                    if s * P >= g * HALF:
                        st.link(ins)
                        ins = dve.tensor_tensor(sp_[:, n % 4, 0:P], sp_[:, n % 4, 0:P], earlier, ALU.mult)
                    ins.then_inc(sp_done, 1)

                def exponent(n):
                    j, g, s, q0, nq, last = ticks[n]
                    c0 = q0 - g * HALF
                    dve.wait_ge(cum_done, at + n + 1)
                    if n >= 4:
                        dve.wait_ge(w_done, at + n - 3)
                    ins = dve.tensor_tensor(d[:, n % 4, 0:nq], zb[:, n % 6, 0:nq], ps[:, 2 + j, c0:c0 + nq],
                                            ALU.subtract)
                    if s * P >= g * HALF:
                        st.link(ins)
                        ins = dve.tensor_tensor(d[:, n % 4, 0:P], d[:, n % 4, 0:P], T.const("dcap"), ALU.min)
                    ins.then_inc(d_done, 1)

                def both(stage, m):
                    if 0 <= m < STEPS:
                        stage(2 * m)
                        stage(2 * m + 1)

                for m in range(STEPS + 1):
                    both(scores, m)
                    both(minus_abs, m)
                    both(exponent, m - 1)
                    both(softplus, m)
                assert st.n == per

            with dve.Fori(0, 2) as i:
                for u in range(2):
                    pair(i, u)

        @block.scalar
        def _(act):
            act.preload_act_table_set(EXP_LN_SET)
            act.sem_inc(out_done, 2)

            def pair(i, u):
                at = NT * (2 * i + u)

                def logs(m):
                    for n in (2 * m, 2 * m + 1):
                        nq = ticks[n][4]
                        act.wait_ge(na_done, at + n + 1)
                        act.activation(na[:, n % 4, 0:nq], na[:, n % 4, 0:nq], ACT.Exp).then_inc(exp_done, 1)
                    for n in (2 * m, 2 * m + 1):
                        nq = ticks[n][4]
                        act.wait_ge(exp_done, at + n + 1)
                        act.activation(na[:, n % 4, 0:nq], na[:, n % 4, 0:nq], ACT.Ln, bias=1.0).then_inc(log_done, 1)

                def weights(m):
                    for n in (2 * m, 2 * m + 1):
                        nq = ticks[n][4]
                        act.wait_ge(d_done, at + n + 1)
                        if n >= 4:
                            act.wait_ge(read_done, at + n - 3 + 2 * NT)
                        act.activation(w[:, n % 4, 0:nq], d[:, n % 4, 0:nq], ACT.Exp).then_inc(w_done, 1)

                def outputs_of(m):
                    for n in (2 * m, 2 * m + 1):
                        j, g, s, q0, nq, last = ticks[n]
                        if last:
                            act.wait_ge(read_done, at + n + 1 + 2 * NT)
                            r = slice(64 * j, 64 * j + 64)
                            act.activation(h[r, bass.ds(2 * i + u, 1), g * HALF:(g + 1) * HALF]
                                           .rearrange("p a n -> p (a n)"), ps[r, 4 + j, :], ACT.Copy).then_inc(out_done, 1)

                for m in range(STEPS + 2):
                    if m < STEPS:
                        logs(m)
                    if 0 <= m - 1 < STEPS:
                        weights(m - 1)
                    if m >= 2:
                        outputs_of(m - 2)

            with act.Fori(0, 2) as i:
                for u in range(2):
                    pair(i, u)
    sems.clear()


def alone(eng, passed):
    eng.sem_inc(passed, 1)


def solve_levels_pe(pe, T, S, i, mtl, xm, xt, y, banks, passed, between=lambda: None):
    ps = T.ps
    yb, zb, ztb = banks
    for lv in range(1, 6):
        n = 5 * i + lv
        pe.wait_ge(S["xm_ready"], n)
        pe.wait_ge(S["blocks_ready"], n)
        alone(pe, passed)
        for hd in range(8):
            c = slice(64 * hd, 64 * hd + 64)
            for p in range(2):
                r = slice(64 * p, 64 * p + 64)
                mm = pe.matmul(ps[r, yb, c], mtl[r, lv - 1, c], xm[r, c], start=True, stop=True)
        mm.then_inc(S["y_done"], 1)
        between()
        pe.wait_ge(S["y_ready"], n)
        pe.wait_ge(S["xt_ready"], n)
        alone(pe, passed)
        if lv < 5:
            for hd in range(8):
                c = slice(64 * hd, 64 * hd + 64)
                for p in range(2):
                    r = slice(64 * p, 64 * p + 64)
                    mm = pe.matmul(ps[r, zb, c], xt[r, c], y[r, c], start=True, stop=True)
            mm.then_inc(S["z_done"], 1)
        for hd in range(8):
            c = slice(64 * hd, 64 * hd + 64)
            for p in range(2):
                r = slice(64 * p, 64 * p + 64)
                mm = pe.matmul(ps[r, ztb, c], y[r, c], xt[r, c], start=True, stop=True)
        mm.then_inc(S["zt_done"], 1)
        between()


def solve_levels_act(act, T, S, i, y, banks, between=lambda lv: None):
    for lv in range(1, 6):
        act.wait_ge(S["y_done"], 5 * i + lv)
        act.activation(y[:, :], T.ps[:, banks[0], :], ACT.Copy).then_inc(S["y_ready"], 1)
        between(lv)


def solve_levels_dve(dve, T, S, st, i, xm, xt, banks, between=lambda lv: None):
    ps = T.ps
    for lv in range(1, 6):
        between(lv)
        if lv < 5:
            dve.wait_ge(S["z_done"], 4 * i + lv)
            st.link(dve.tensor_tensor(xm[:, :], xm[:, :], ps[:, banks[1], :], ALU.subtract))
            dve.sem_inc(S["xm_ready"], 1)
        dve.wait_ge(S["zt_done"], 5 * i + lv)
        st.link(dve.tensor_tensor(xt[:, :], xt[:, :], ps[:, banks[2], :], ALU.subtract))
        dve.sem_inc(S["xt_ready"] if lv < 5 else S["solved"], 1)


def rwkv_phase(T):
    nc, h, ps, io = T.nc, T.h, T.ps, T.io
    sems = Sems(nc, "rwkv")
    S = {n: sems(n) for n in (
        "xs_in", "lora_in", "tanh_in", "gate_in", "lora_done", "w_sum", "w_exp", "a_sum", "a_exp", "k_sq", "k_sum",
        "k_rn", "l_ready", "decays", "prepped", "rkk", "bonus", "bonus_used", "turned", "tm_ready", "spread", "gram",
        "masked", "blocks_copied", "blocks_ready", "xm_ready", "xt_ready", "y_done", "y_ready", "z_done", "zt_done", "solved", "w_done", "w_copied",
        "u_done", "u_copied", "h_done", "h_ready", "o_done", "o_copied", "mean", "centered", "var", "rstd",
        "gate_copied", "step", "fin_step", "astep", "pstep", "cleared", "state_in", "smp_turned", "smp_rows", "smp_out", "smp_in",
        "smp_done", "smp_back", "smp_step", "log_var",
        "pe_passed")}
    halves, ident = T.const("halves"), T.const("ident")
    W = 2 * C
    LAST = NPAIR - 1
    with ExitStack() as ctx:
        sb = lambda n, s: ctx.enter_context(nc.sbuf_tensor("rw" + n, s, F32))
        lora = sb("_lora", [P, 2 * D_B])
        X = sb("_xs", [P, NB_T, W])
        th, sg = sb("_th", [P, W]), sb("_sg", [P, W])
        names = "yw rw ya ra kk t1 t2 L eL eN eX km A R K B g bon nm".split()
        t = {n: sb("_" + n, [P, 4, W]) for n in names}
        Ax, Rx, Bx = (sb(n, [P, 4, 2, W]) for n in ("_Ax", "_Rx", "_Bx"))
        ktm, btm, vtm, ak, rk, rb, mt, xm, xt, y, r0, u = (sb("_m" + n, [P, 512]) for n in
                                                           "ktm btm vtm ak rk rb mt xm xt y r0 u".split())
        mtl = sb("_mtl", [P, 6, 512])
        Hx, dh = sb("_Hx", [P, 4, 2, C]), sb("_dh", [P, 4, C])
        o, oc, rs = (sb("_" + n, [P, 4, W]) for n in ("o", "oc", "rs"))
        smp = mtl
        kv, vv, so, sa = sb("_kv", [P, 5, 64]), sb("_vv", [P, 32]), sb("_so", [P, 32]), sb("_sa", [P, 32])
        pages = T.pages
        st8, tmp8 = (b[:, 0:4, :].rearrange("p n (k v) -> p (n k) v", v=32) for b in (pages.kp, pages.vp))
        orow = pages.qr
        ocol = sb("_ocol", [P, 4, NS])
        scr = nc.dram_tensor("scratch_rw_rows", [6, NS, 512], F32, kind="Internal").ap()
        scr_o = nc.dram_tensor("scratch_rw_o", [NS, 512], F32, kind="Internal").ap()
        block = ctx.enter_context(nc.Block())
        bc = lambda v, n: T.vec(v).unsqueeze(2).to_broadcast([P, 4, n])
        m8 = lambda name: T.const(name).unsqueeze(1).to_broadcast([P, 8, C])
        h8 = lambda a: a.rearrange("p (h i) -> p h i", h=8)
        cut = lambda a, n: a[:, :, 0:n]

        @block.sync
        def _(sp):
            sp.dma_start(lora[:, :], io["w_lora"]).then_inc(S["lora_in"], 16)
            with sp.Fori(1, NS) as b:
                pages.load_keys(sp, b)
            sp.wait_ge(pages.k_used, Pages.RING + NS * NPG)
            sp.dma_start(st8, io["wkv_in"].rearrange("p (k v) -> p k v", k=64)).then_inc(S["state_in"], 16)
            sp.wait_ge(S["h_ready"], 2 * NPAIR + 1)
            for e in range(2):
                sp.dma_start(io["wkv_prompt"][e], Hx[64 * e:64 * e + 64, :, e, :]).then_inc(S["smp_out"], 16)
            sp.wait_ge(S["smp_rows"], 1)
            sp.dma_start(scr.rearrange("a b n -> b a n"), smp[0:NS, :, :]).then_inc(S["smp_out"], 16)
            sp.wait_ge(S["smp_out"], 48)
            for e in range(2):
                r = slice(64 * e, 64 * e + 64)
                sp.dma_start(kv[r, :, :], scr[0:5].rearrange("a b (h k) -> (b h) a k", h=8)).then_inc(S["smp_in"], 16)
                sp.dma_start(vv[r, :], scr[5].rearrange("b (h e v) -> e (b h) v", h=8, e=2)[e]).then_inc(S["smp_in"], 16)
            sp.wait_ge(S["smp_done"], 1)
            for e in range(2):
                sp.dma_start(scr_o.rearrange("b (h e v) -> e (b h) v", h=8, e=2)[e], so[64 * e:64 * e + 64, :])\
                  .then_inc(S["smp_out"], 16)
            sp.dma_start(io["wkv_new"].rearrange("p (k v) -> p k v", k=64), st8).then_inc(S["smp_out"], 16)
            sp.wait_ge(S["smp_out"], 96)
            sp.dma_start(orow, scr_o).then_inc(S["smp_back"], 16)

        def prep_pe(pe, i, n, sample=None, more=lambda pages: None):
            pe.wait_ge(S["tanh_in"], i + 1)
            for k in range(4):
                pe.matmul(ps[:, 0, k * W:k * W + n], lora[0:64, k * P:(k + 1) * P], th[0:64, 0:n], start=True, stop=True)
            for k in range(4):
                pe.matmul(ps[:, 1, k * W:k * W + n], lora[64:P, k * P:(k + 1) * P], X[64:P, 12, 0:n], start=True, stop=True)
            pe.wait_ge(S["gate_in"], i + 1)
            for k in range(4):
                mm = pe.matmul(ps[:, 2, k * W:k * W + n], lora[:, D_B + k * P:D_B + (k + 1) * P], sg[:, 0:n], start=True,
                               stop=True)
            mm.then_inc(S["lora_done"], 1)
            if sample is not None:
                pages.sums_pe(pe, sample)
            pe.wait_ge(S["k_sq"], i + 1)
            pe.matmul(ps[:, 3, 0:4 * n], halves, cut(t["t1"], n), start=True, stop=True).then_inc(S["k_sum"], 1)
            more(8)
            pe.wait_ge(S["rkk"], i + 1)
            pe.matmul(ps[:, 4, 0:4 * n], halves, cut(t["t2"], n), start=True, stop=True).then_inc(S["bonus"], 1)
            more(4)

        xs = T.xs_rows.rearrange("t p n -> p t n")

        def prep_act(act, i, n, sample=None, fetch=None):
            st = Steps(act, S["astep"], 3 * i)
            act.wait_ge(S["xs_in"], 16 * i + 16)
            act.activation(th[0:64, 0:n], X[0:64, 12, 0:n], ACT.Exp, scale=2.0)
            act.activation(sg[:, 0:n], X[:, 13, 0:n], ACT.Exp, scale=-1.0).then_inc(S["w_exp"], 1)
            if sample is not None:
                pages.logs_act(act, sample)
                fetch(8)
            act.wait_ge(S["lora_done"], i + 1)
            act.activation(cut(t["g"], n), ps[:, 2, :].rearrange("p (k w) -> p k w", k=4)[:, :, 0:n], ACT.Copy)\
               .then_inc(S["gate_copied"], 1)
            act.wait_ge(S["w_sum"], i + 1)
            act.activation(cut(t["rw"], n), cut(t["yw"], n), ACT.Exp, scale=-1.0)
            act.activation(cut(t["ra"], n), cut(t["ya"], n), ACT.Exp, scale=-1.0).then_inc(S["a_exp"], 1)
            if sample is not None:
                pages.weights_act(act, sample)
            act.wait_ge(S["k_sum"], i + 1)
            st.link(act.activation(cut(t["nm"], n), ps[:, 3, 0:4 * n].rearrange("p (k w) -> p k w", k=4), ACT.Ln,
                                   bias=T.vec("eps_rms")))
            st.do(act.activation(cut(t["nm"], n), cut(t["nm"], n), ACT.Exp, scale=-0.5))
            st.settle()
            act.sem_inc(S["k_rn"], 1)
            if sample is not None:
                fetch(12)
            act.wait_ge(S["l_ready"], i + 1)
            act.activation(cut(t["eL"], n), cut(t["L"], n), ACT.Exp, scale=-DECAY)
            act.activation(cut(t["eN"], n), cut(t["L"], n), ACT.Exp, scale=DECAY)
            st.do(act.activation(cut(t["eX"], n), cut(t["t1"], n), ACT.Exp, scale=-DECAY))
            st.settle()
            act.sem_inc(S["decays"], 1)
            assert st.n == 3

        PREP = 20

        def prep_dve(dve, i, n, prompt, sample=None):
            st = Steps(dve, S["step"], PREP * i)
            r, k, v = X[:, 0:4, 0:n], X[:, 4:8, 0:n], X[:, 8:12, 0:n]
            part = lambda b: ps[:, b, :].rearrange("p (k w) -> p k w", k=4)[:, :, 0:n]
            tt = lambda o, a, b, op: dve.tensor_tensor(o, a, b, op)
            if sample is not None:
                pages.bias_dve(dve, sample)
                dve.wait_ge(pages.biased, sample + 1)
            dve.wait_ge(S["w_exp"], i + 1)
            st.do(dve.tensor_scalar(th[0:64, 0:n], th[0:64, 0:n], 1.0, None, ALU.add))
            st.link(dve.tensor_scalar(sg[:, 0:n], sg[:, 0:n], 1.0, None, ALU.add))
            st.do(dve.reciprocal(th[0:64, 0:n], th[0:64, 0:n]))
            dve.reciprocal(sg[:, 0:n], sg[:, 0:n]).then_inc(S["gate_in"], 1)
            st.settle()
            dve.tensor_scalar(th[0:64, 0:n], th[0:64, 0:n], -2.0, 1.0, ALU.mult, ALU.add).then_inc(S["tanh_in"], 1)
            st.link(tt(cut(t["kk"], n), k, bc("kk", n), ALU.mult))
            dve.tensor_tensor(cut(t["t1"], n), cut(t["kk"], n), cut(t["kk"], n), ALU.mult).then_inc(S["k_sq"], 1)
            if sample is not None:
                pages.softplus_dve(dve, sample)
            dve.wait_ge(S["lora_done"], i + 1)
            dve.tensor_tensor(cut(t["yw"], n), part(0), bc("w0", n), ALU.add)
            dve.tensor_tensor(cut(t["ya"], n), part(1), bc("a0", n), ALU.add).then_inc(S["w_sum"], 1)
            if sample is not None:
                pages.exponents_dve(dve, sample)
            dve.wait_ge(S["a_exp"], i + 1)
            st.do(dve.tensor_scalar(cut(t["rw"], n), cut(t["rw"], n), 1.0, None, ALU.add))
            st.link(dve.tensor_scalar(cut(t["ra"], n), cut(t["ra"], n), 1.0, None, ALU.add))
            st.do(dve.reciprocal(cut(t["rw"], n), cut(t["rw"], n)))
            st.link(dve.reciprocal(cut(t["ra"], n), cut(t["ra"], n)))
            dve.wait_ge(S["k_sum"], i + 1)
            if prompt:
                st.link(dve.tensor_tensor_scan(t["L"][:, :, :].rearrange("p k w -> p (k w)"), T.const("scan64")[:, 0:512],
                                               t["rw"][:, :, :].rearrange("p k w -> p (k w)"), 0.0, ALU.mult, ALU.add))
                st.do(tt(cut(t["t1"], n), cut(t["L"], n), cut(t["rw"], n), ALU.subtract))
            else:
                st.link(dve.tensor_copy(cut(t["L"], n), cut(t["rw"], n)))
                st.do(tt(cut(t["t1"], n), cut(t["L"], n), cut(t["rw"], n), ALU.subtract))
            st.settle()
            dve.sem_inc(S["l_ready"], 1)
            st.link(dve.scalar_tensor_tensor(out=cut(t["km"], n), in0=cut(t["ra"], n), scalar=-1.0, in1=bc("ka", n),
                                             op0=ALU.add, op1=ALU.mult))
            st.link(dve.scalar_tensor_tensor(out=cut(t["km"], n), in0=cut(t["km"], n), scalar=1.0, in1=k, op0=ALU.add,
                                             op1=ALU.mult))
            st.link(tt(cut(t["t2"], n), r, cut(t["km"], n), ALU.mult))
            dve.tensor_tensor(cut(t["t2"], n), cut(t["t2"], n), bc("rk", n), ALU.mult).then_inc(S["rkk"], 1)
            dve.wait_ge(S["k_rn"], i + 1)
            st.link(tt(cut(t["kk"], n), cut(t["kk"], n), cut(t["nm"], n), ALU.mult))
            st.link(tt(cut(t["ra"], n), cut(t["kk"], n), cut(t["ra"], n), ALU.mult))
            dve.wait_ge(S["decays"], i + 1)
            if prompt:
                st.do(tt(t["A"][:, :, :], t["kk"][:, :, :], t["eX"][:, :, :], ALU.mult))
                st.do(tt(t["R"][:, :, :], r, t["eL"][:, :, :], ALU.mult))
                st.do(tt(t["K"][:, :, :], t["km"][:, :, :], t["eN"][:, :, :], ALU.mult))
                st.link(tt(t["B"][:, :, :], t["ra"][:, :, :], t["eN"][:, :, :], ALU.mult))
                dve.sem_inc(S["prepped"], 1)
            dve.wait_ge(S["bonus"], i + 1)
            st.link(tt(cut(t["bon"], n), ps[:, 4, 0:4 * n].rearrange("p (k w) -> p k w", k=4), v, ALU.mult))
            dve.sem_inc(S["bonus_used"], 1)
            if not prompt:
                dve.sem_inc(S["prepped"], 1)
            assert not prompt or st.n == PREP, st.n

        def finish_pe(pe, i, src, n):
            pe.wait_ge(S["o_copied"], i + 1)
            pe.matmul(ps[:, 1, 0:4 * n], halves, src, start=True, stop=True).then_inc(S["mean"], 1)
            pe.wait_ge(S["centered"], i + 1)
            pe.matmul(ps[:, 1, 0:4 * n], halves, cut(rs, n), start=True, stop=True).then_inc(S["var"], 1)

        def finish_dve(dve, i, src, n, out, more=lambda units: None):
            st = Steps(dve, S["fin_step"], 6 * i)
            dve.wait_ge(S["mean"], i + 1)
            st.link(dve.scalar_tensor_tensor(out=cut(oc, n), in0=ps[:, 1, 0:4 * n].rearrange("p (k w) -> p k w", k=4),
                                             scalar=-1.0 / 64, in1=src, op0=ALU.mult, op1=ALU.add))
            dve.tensor_tensor(cut(rs, n), cut(oc, n), cut(oc, n), ALU.mult).then_inc(S["centered"], 1)
            more(1)
            dve.wait_ge(S["rstd"], i + 1)
            st.link(dve.tensor_tensor(cut(oc, n), cut(oc, n), cut(rs, n), ALU.mult))
            st.link(dve.tensor_tensor(cut(oc, n), cut(oc, n), bc("lnw", n), ALU.mult))
            st.link(dve.tensor_tensor(cut(oc, n), cut(oc, n), bc("lnb", n), ALU.add))
            st.link(dve.tensor_tensor(cut(oc, n), cut(oc, n), cut(t["bon"], n), ALU.add))
            st.link(dve.tensor_tensor(out, cut(oc, n), cut(t["g"], n), ALU.mult))
            assert st.n == 6

        def finish_act(act, i, n):
            act.wait_ge(S["var"], i + 1)
            act.activation(cut(rs, n), ps[:, 1, 0:4 * n].rearrange("p (k w) -> p k w", k=4), ACT.Ln, scale=1.0 / 64,
                           bias=T.vec("eps_gn")).then_inc(S["log_var"], 1)
            act.wait_ge(S["log_var"], i + 1)
            act.activation(cut(rs, n), cut(rs, n), ACT.Exp, scale=-0.5).then_inc(S["rstd"], 1)

        @block.gpsimd
        def _(pool):
            for a in (Ax, Rx, Bx):
                pool.memset(a[:, :, :, :], 0.0)
            pool.memset(Hx[:, :, :, :], 0.0).then_inc(S["cleared"], 1)
            pool.wait_ge(S["cleared"], 1)
            pool.sem_inc(S["h_ready"], 1)
            with pool.Fori(0, NPAIR) as i:
                pool.wait_ge(S["blocks_copied"], i + 1)
                for lv in range(1, 6):
                    pool.tensor_tensor(h8(mtl[:, lv - 1, :]), h8(mt[:, :]), m8(f"lev{lv}T"), ALU.mult)\
                        .then_inc(S["blocks_ready"], 1)

        @block.tensor
        def _(pe):
            pe.wait_ge(S["lora_in"], 16)
            def pair(i):
                read = iter(range(NPG))
                more = lambda n: pages.values_pe(pe, i, [g for _, g in zip(range(n), read)])
                prep_pe(pe, i, W, sample=i, more=more)
                pe.wait_ge(S["prepped"], i + 1)
                pe.wait_ge(S["gate_copied"], i + 1)
                for b, src in ((5, t["K"]), (0, t["B"]), (3, None)):
                    for k in range(4):
                        mm = pe.transpose(ps[:, b, k * P:(k + 1) * P], X[:, 8 + k, :] if src is None else src[:, k, :], ident)
                mm.then_inc(S["turned"], 1)
                pe.wait_ge(S["spread"], 3 * i + 2)

                def gram(bank, left, right):
                    for k in range(4):
                        for p in range(2):
                            c = slice(C * p, C * p + C)
                            mm = pe.matmul(ps[64 * p:64 * p + 64, bank, k * P:(k + 1) * P], left[:, k, c], right[:, k, :, c],
                                           start=True, stop=True)
                    mm.then_inc(S["gram"], 1)

                gram(1, t["B"], Ax)
                gram(2, t["A"], Bx)
                pe.wait_ge(S["bonus_used"], i + 1)
                pe.wait_ge(S["tm_ready"], i + 1)
                gram(0, t["K"], Ax)
                pe.wait_ge(S["spread"], 3 * i + 3)
                gram(3, t["K"], Rx)
                gram(4, t["B"], Rx)
                more(4)
                solve_levels_pe(pe, T, S, i, mtl, xm, xt, y, (5, 2, 1), S["pe_passed"], lambda: more(4))
                pe.wait_ge(S["masked"], i + 1)
                pe.wait_ge(S["solved"], i + 1)
                for p in range(2):
                    r, c = slice(64 * p, 64 * p + 64), slice(C * p, C * p + C)
                    hc = lambda hd: slice(64 * hd, 64 * hd + 64)
                    pe.wait_ge(S["h_ready"], 2 * i + p + 1)
                    for k in range(4):
                        pe.matmul(ps[r, 0, k * P:(k + 1) * P], t["A"][:, k, c], Hx[:, k, :, :], start=True, stop=False,
                                  skip_group_check=True)
                        for hd in (2 * k, 2 * k + 1):
                            mm = pe.matmul(ps[r, 0, hc(hd)], ak[r, hc(hd)], vtm[r, hc(hd)], start=False, stop=True,
                                           skip_group_check=True)
                    mm.then_inc(S["w_done"], 1)
                    pe.wait_ge(S["w_copied"], 2 * i + p + 1)
                    alone(pe, S["pe_passed"])
                    for hd in range(8):
                        mm = pe.matmul(ps[r, 5, hc(hd)], xt[r, hc(hd)], r0[r, hc(hd)], start=True, stop=True)
                    mm.then_inc(S["u_done"], 1)
                    pe.wait_ge(S["u_copied"], 2 * i + p + 1)
                    alone(pe, S["pe_passed"])
                    for hd in range(8):
                        q = slice(64 * (hd % 2), 64 * (hd % 2) + 64)
                        k = hd // 2
                        pe.matmul(ps[q, 2, k * C:(k + 1) * C], ktm[r, hc(hd)], vtm[r, hc(hd)], start=True, stop=False,
                                  skip_group_check=True)
                        mm = pe.matmul(ps[q, 2, k * C:(k + 1) * C], btm[r, hc(hd)], u[r, hc(hd)], start=False, stop=True,
                                       skip_group_check=True)
                    for k in range(4):
                        oc_ = slice(k * P + C * p, k * P + C * p + C)
                        mm = pe.matmul(ps[:, 4, oc_], Hx[:, k, :, :].rearrange("p e v -> p (e v)"), t["R"][:, k, c],
                                       start=True, stop=False, skip_group_check=True)
                        for hd in (2 * k, 2 * k + 1):
                            q = slice(64 * (hd % 2), 64 * (hd % 2) + 64)
                            pe.matmul(ps[q, 4, oc_], vtm[r, hc(hd)], rk[r, hc(hd)], start=False, stop=False,
                                      skip_group_check=True)
                            mm = pe.matmul(ps[q, 4, oc_], u[r, hc(hd)], rb[r, hc(hd)], start=False, stop=True,
                                           skip_group_check=True)
                    mm.then_inc(S["h_done"], 1)
                    more(4)
                finish_pe(pe, i, o[:, :, :], W)
                pages.select_pe(pe, i)

            with pe.Fori(0, LAST) as i:
                pair(i)
            pair(LAST)
            i = NPAIR
            prep_pe(pe, i, NS)
            pe.wait_ge(S["prepped"], i + 1)
            pe.wait_ge(S["gate_copied"], i + 1)
            for b, src in enumerate((t["kk"], t["eL"], t["ra"], t["km"], None, "v")):
                for k in range(4):
                    a = X[:, k, 0:NS] if src is None else X[:, 8 + k, 0:NS] if src == "v" else src[:, k, 0:NS]
                    mm = pe.transpose(ps[0:NS, b, k * P:(k + 1) * P], a, ident)
            mm.then_inc(S["smp_turned"], 1)
            pe.wait_ge(S["smp_back"], 16)
            pe.wait_ge(S["smp_rows"], 1)
            for k in range(4):
                mm = pe.transpose(ps[:, 6, k * NS:(k + 1) * NS], orow[:, k * P:(k + 1) * P], ident[0:NS, 0:NS])
            mm.then_inc(S["o_done"], 1)
            finish_pe(pe, i, ocol[:, :, :], NS)

        @block.scalar
        def _(act):
            act.preload_act_table_set(EXP_LN_SET)
            act.dma_start(X[:, :, :], xs[:, :, 0:W]).then_inc(S["xs_in"], 16)
            act.wait_ge(S["cleared"], 1)

            def pair(i, more_samples=True):
                asked = iter(range(4, NPG))

                def fetch(to):
                    for g in asked:
                        pages.load_values(act, i, g)
                        if g >= to - 1:
                            break

                prep_act(act, i, W, sample=i, fetch=fetch)
                act.wait_ge(S["prepped"], i + 1)
                for src, dst in ((t["A"], Ax), (t["B"], Bx), (t["R"], Rx)):
                    for e in range(2):
                        r = slice(64 * e, 64 * e + 64)
                        last = act.activation(dst[r, :, e, :], src[r, :, :], ACT.Copy)
                    last.then_inc(S["spread"], 1)
                act.wait_ge(S["turned"], i + 1)
                act.activation(ktm[:, :], ps[:, 5, :], ACT.Copy)
                act.activation(btm[:, :], ps[:, 0, :], ACT.Copy, scale=-1.0)
                act.activation(vtm[:, :], ps[:, 3, :], ACT.Copy).then_inc(S["tm_ready"], 1)
                act.wait_ge(S["gram"], 5 * i + 1)
                act.activation(mt[:, :], ps[:, 1, :], ACT.Copy).then_inc(S["blocks_copied"], 1)
                act.wait_ge(S["bonus_used"], i + 1)
                if more_samples:
                    act.dma_start(X[:, :, :], xs[:, :, bass.ds((i + 1) * W, W)]).then_inc(S["xs_in"], 16)
                else:
                    act.dma_start(X[:, :, 0:NS], xs[:, :, SEQ:TOK]).then_inc(S["xs_in"], 16)
                fetch(20)
                solve_levels_act(act, T, S, i, y, (5, 2, 1), lambda lv: fetch(20 + 8 * lv))
                for p in range(2):
                    r = slice(64 * p, 64 * p + 64)
                    act.wait_ge(S["w_done"], 2 * i + p + 1)
                    act.activation(r0[r, :], ps[r, 0, :], ACT.Copy).then_inc(S["w_copied"], 1)
                    act.wait_ge(S["u_done"], 2 * i + p + 1)
                    act.activation(u[r, :], ps[r, 5, :], ACT.Copy).then_inc(S["u_copied"], 1)
                    fetch(NPG)
                act.wait_ge(S["h_done"], 2 * i + 2)
                act.activation(o[:, :, :], ps[:, 4, :].rearrange("p (k w) -> p k w", k=4), ACT.Copy)\
                   .then_inc(S["o_copied"], 1)
                pages.fold_act(act, i)
                finish_act(act, i, W)
                pages.pick_act(act, i)
                if more_samples:
                    for g in range(4):
                        pages.load_values(act, i + 1, g)

            for g in range(4):
                pages.load_values(act, 0, g)
            with act.Fori(0, LAST) as i:
                pair(i)
            pair(LAST, more_samples=False)
            i = NPAIR
            prep_act(act, i, NS)
            act.wait_ge(S["smp_turned"], 1)
            act.activation(smp[0:NS, :, :], ps[0:NS, 0:6, :], ACT.Copy).then_inc(S["smp_rows"], 1)
            act.wait_ge(S["o_done"], 1)
            act.activation(ocol[:, :, :], ps[:, 6, 0:4 * NS].rearrange("p (k w) -> p k w", k=4), ACT.Copy)\
               .then_inc(S["o_copied"], 1)
            finish_act(act, i, NS)

        @block.vector
        def _(dve):

            def pair(i, keys=True):
                units = iter(range(0, NPG, 2))

                def more(n):
                    for _, g in zip(range(n if keys else 0), units):
                        pages.keys_dve(dve, i + 1, g // Pages.RING, g % Pages.RING)

                prep_dve(dve, i, W, True, sample=i)
                more(1)
                loop = Steps(dve, S["pstep"], 20 * i)
                dve.wait_ge(S["blocks_copied"], i + 1)
                loop.link(dve.tensor_tensor(h8(xt[:, :]), h8(ps[:, 1, :]), m8("lev0T"), ALU.mult))
                loop.do(dve.tensor_tensor(h8(xt[:, :]), m8("eye64"), h8(xt[:, :]), ALU.subtract))
                dve.wait_ge(S["gram"], 5 * i + 2)
                loop.link(dve.tensor_tensor(h8(xm[:, :]), h8(ps[:, 2, :]), m8("lev0"), ALU.mult))
                loop.link(dve.tensor_tensor(h8(xm[:, :]), m8("eye64"), h8(xm[:, :]), ALU.subtract))
                dve.sem_inc(S["xm_ready"], 1)
                dve.sem_inc(S["xt_ready"], 1)
                dve.wait_ge(S["gram"], 5 * i + 5)
                more(1)
                loop.do(dve.tensor_tensor(h8(ak[:, :]), h8(ps[:, 0, :]), m8("strictT"), ALU.mult))
                loop.do(dve.tensor_tensor(h8(rk[:, :]), h8(ps[:, 3, :]), m8("inclT"), ALU.mult))
                loop.link(dve.tensor_tensor(h8(rb[:, :]), h8(ps[:, 4, :]), m8("ninclT"), ALU.mult))
                dve.sem_inc(S["masked"], 1)
                solve_levels_dve(dve, T, S, loop, i, xm, xt, (5, 2, 1), lambda lv: more(1 if lv == 1 else 4))
                for p in range(2):
                    more(6 - 2 * p)
                    dve.wait_ge(S["h_done"], 2 * i + p + 1)
                    for e in range(2):
                        r = slice(64 * e, 64 * e + 64)
                        st = dve.tensor_tensor(dh[r, :, :], Hx[r, :, e, :], ps[r, 2, 0:4 * C].rearrange("p (k v) -> p k v", k=4),
                                               ALU.add)
                        loop.do(st)
                    loop.settle()
                    end = C * p + C - 1
                    for e in range(2):
                        r = slice(64 * e, 64 * e + 64)
                        last = dve.tensor_tensor(Hx[r, :, e, :], dh[r, :, :],
                                                 t["eL"][r, :, end:end + 1].to_broadcast([64, 4, C]), ALU.mult)
                    last.then_inc(S["h_ready"], 1)
                assert loop.n == 20, loop.n
                more(1)
                finish_dve(dve, i, o[:, :, :], W, h[:, 4:8, bass.ds(i * W, W)], more)
                more(NPG)

            with dve.Fori(0, LAST) as i:
                pair(i)
            pair(LAST, keys=False)
            i = NPAIR
            prep_dve(dve, i, NS, False)
            st = Steps(dve, S["smp_step"])
            dve.wait_ge(S["smp_in"], 64)
            dve.wait_ge(S["state_in"], 16)
            k3 = lambda n: kv[:, n, :].unsqueeze(2).to_broadcast([P, 64, 32])
            v3 = lambda a: a[:, :].unsqueeze(1).to_broadcast([P, 64, 32])
            s3, t3 = st8, tmp8
            tt = lambda o_, a, b, op: st.link(dve.tensor_tensor(o_, a, b, op))
            tt(t3, s3, k3(0), ALU.mult)
            st.link(dve.tensor_reduce(sa[:, :], tmp8.rearrange("p k v -> p v k"), AX.X, ALU.add))
            tt(s3, s3, k3(1), ALU.mult)
            tt(t3, k3(2), v3(sa), ALU.mult)
            tt(s3, s3, t3, ALU.subtract)
            tt(t3, k3(3), v3(vv), ALU.mult)
            tt(s3, s3, t3, ALU.add)
            tt(t3, s3, k3(4), ALU.mult)
            st.link(dve.tensor_reduce(so[:, :], tmp8.rearrange("p k v -> p v k"), AX.X, ALU.add))
            dve.sem_inc(S["smp_done"], 1)
            finish_dve(dve, i, ocol[:, :, :], NS, h[:, 4:8, SEQ:TOK])
    sems.clear()
    pages.sems.clear()


def odd_phase(T, ba):
    nc, ps, io = T.nc, T.ps, T.io
    sems = Sems(nc, "odd")
    w_in = [sems("w_in0"), sems("w_in1")]
    (row_out, row_free, product, row_in, conv_done, silu_done, step, cleared, ba_in, ba_exp, ba_log, ba_abs, ba_neg) = (
        sems(n) for n in ("row_out", "row_free", "product", "row_in", "conv_done", "silu_done", "step", "cleared",
                          "ba_in", "ba_exp", "ba_log", "ba_abs", "ba_neg"))
    w_rounded, w_split = sems("w_rounded"), sems("w_split")
    PAR, NT = KT * P, ODD_T - 1
    with ExitStack() as ctx:
        sb = lambda n, s, d=F32: ctx.enter_context(nc.sbuf_tensor("odd" + n, s, d))
        wh, wl = sb("_wh", [P, 2, KT * P], F32R), sb("_wl", [P, 2, KT * P], F32R)
        w, row, cv = sb("_w", [P, 2, ODD_BLK]), sb("_row", [P, 2, 3 + TOK]), sb("_cv", [P, 2, TOK])
        sp1, sp2 = sb("_sp1", [P, TOK]), sb("_sp2", [P, TOK])
        block = ctx.enter_context(nc.Block())
        B8, A8 = slice(BETA_ROW, BETA_ROW + 8), slice(A_ROW, A_ROW + 8)

        @block.sync
        def _(sp):
            with sp.Fori(0, NT // 2) as i:
                for j in range(2):
                    sp.wait_ge(silu_done, 2 * i + j + 1)
                    sp.dma_start(w[:, j, :], io["w_odd"][bass.ds(2 * i + j, 1), :, :].rearrange("a p n -> (a p) n"))\
                      .then_inc(w_in[j], 16)
            sp.wait_ge(silu_done, NT + 1)
            sp.dma_start(w[:, 0, :], io["w_odd"][NT]).then_inc(w_in[0], 16)

        @block.tensor
        def _(pe):
            with pe.Fori(0, NT // 2) as i:
                for j in range(2):
                    pe.wait_ge(w_split, 2 * i + j + 1)
                    for c in range(GRP):
                        pe.wait_ge(row_in, 6 * i + 3 * j + c + 1)
                        group_products(pe, T, 3 * j + c, wh[:, j, :], wl[:, j, :], c).then_inc(product, 1)
            pe.wait_ge(w_split, NT + 1)
            for c in range(GRP):
                pe.wait_ge(row_in, 3 * NT + c + 1)
                group_products(pe, T, c, wh[:, 0, :], wl[:, 0, :], c).then_inc(product, 1)

        @block.scalar
        def _(act):
            act.sem_inc(row_in, 6)
            act.sem_inc(silu_done, 2)
            act.preload_act_table(ACT.Silu)
            act.wait_ge(w_in[0], 16)
            round_weights(act, wh[:, 0, :], w[:, 0, 0:KT * P], w_rounded)
            with act.Fori(0, NT // 2) as i:
                for j in range(2):
                    act.wait_ge(w_in[1 - j], 16 * (i + j) + 16)
                    round_weights(act, wh[:, 1 - j, :], w[:, 1 - j, 0:KT * P], w_rounded)
                    act.wait_ge(row_free, 2 * i + j + 1)
                    for c in range(GRP):
                        act.wait_ge(product, 6 * i + 3 * j + c + 1)
                        act.activation(row[:, j, 3 + c * GC:3 + (c + 1) * GC], ps[:, 3 * j + c, 0:GC], ACT.Copy)\
                           .then_inc(row_in, 1)
                    act.wait_ge(conv_done, 2 * i + j + 1)
                    act.activation(cv[:, j, :], cv[:, j, :], ACT.Silu).then_inc(silu_done, 1)
            for c in range(GRP):
                act.wait_ge(product, 3 * NT + c + 1)
                last = act.activation(ba[:, c * GC:(c + 1) * GC], ps[:, c, 0:GC], ACT.Copy)
            last.then_inc(ba_in, 1)
            act.preload_act_table_set(EXP_LN_SET)
            act.wait_ge(ba_in, 1)
            act.activation(ba[B8, :], ba[B8, :], ACT.Exp, scale=-1.0)
            act.activation(sp1[A8, :], ba[A8, :], ACT.Identity, bias=T.vec("dt_bias")[A8, :]).then_inc(ba_exp, 1)
            act.wait_ge(ba_exp, 1)
            act.activation(sp2[A8, :], sp1[A8, :], ACT.Abs).then_inc(ba_abs, 1)
            act.wait_ge(ba_abs, 1)
            act.activation(sp2[A8, :], sp2[A8, :], ACT.Exp, scale=-1.0).then_inc(ba_abs, 1)
            act.wait_ge(ba_abs, 2)
            act.activation(sp2[A8, :], sp2[A8, :], ACT.Ln, bias=1.0)
            act.activation(row[A8, 0, 0:1], T.vec("a_log")[A8, :], ACT.Exp).then_inc(ba_log, 1)

        @block.vector
        def _(dve):
            dve.wait_ge(cleared, 1)
            per = 2 * 6

            def rest(t, j):
                dve.wait_ge(w_rounded, t + 1)
                rest_weights(dve, wl[:, j, :], w[:, j, 0:KT * P], wh[:, j, :], w_split)

            rest(0, 0)
            with dve.Fori(0, NT // 2) as i:
                st = Steps(dve, step, i * per)
                for j in range(2):
                    rest(2 * i + j + 1, 1 - j)
                    tap = [w[:, j, PAR + n:PAR + n + 1] for n in range(4)]
                    kept = w[:, j, PAR + 4:PAR + 4 + 3 * NS].rearrange("p (r b) -> p r b", r=3)
                    dve.wait_ge(row_in, 6 * i + 3 * j + 3 + 6)
                    s = cv[:, j, SEQ:TOK]
                    o = cv[:, j, 0:SEQ]
                    st.do(dve.tensor_scalar(s, kept[:, 0, :], tap[0], None, ALU.mult))
                    st.link(dve.tensor_scalar(o, row[:, j, 0:SEQ], tap[0], None, ALU.mult))
                    for n in (1, 2):
                        st.do(dve.scalar_tensor_tensor(out=s, in0=kept[:, n, :], scalar=tap[n], in1=s, op0=ALU.mult,
                                                       op1=ALU.add))
                        st.link(dve.scalar_tensor_tensor(out=o, in0=row[:, j, n:n + SEQ], scalar=tap[n], in1=o,
                                                         op0=ALU.mult, op1=ALU.add))
                    dve.scalar_tensor_tensor(out=cv[:, j, :], in0=row[:, j, 3:3 + TOK], scalar=tap[3], in1=cv[:, j, :],
                                             op0=ALU.mult, op1=ALU.add).then_inc(conv_done, 1)
                assert st.n == per
            st = Steps(dve, step, per * NT // 2)
            dve.wait_ge(ba_exp, 1)
            st.link(dve.tensor_scalar(ba[B8, :], ba[B8, :], 1.0, None, ALU.add))
            st.do(dve.reciprocal(ba[B8, :], ba[B8, :]))
            dve.wait_ge(ba_log, 1)
            st.link(dve.scalar_tensor_tensor(out=sp1[A8, :], in0=sp1[A8, :], scalar=0.0, in1=sp2[A8, :], op0=ALU.max,
                                             op1=ALU.add))
            st.link(dve.tensor_scalar(sp1[A8, :], sp1[A8, :], row[A8, 0, 0:1], -1.0, ALU.mult, ALU.mult))
            st.do(dve.tensor_tensor_scan(ba[A8, 0:SEQ], T.const("scan64")[A8, :], sp1[A8, 0:SEQ], 0.0, ALU.mult, ALU.add))
            st.link(dve.tensor_copy(ba[A8, SEQ:TOK], sp1[A8, SEQ:TOK]))

        @block.gpsimd
        def _(pool):
            pool.memset(row[:, :, 0:3], 0.0).then_inc(cleared, 1)
            pool.sem_inc(row_free, 2)
            with pool.Fori(0, NT // 2) as i:
                for j in range(2):
                    pool.wait_ge(silu_done, 2 * i + j + 3)
                    pool.dma_start(T.odd_rows[bass.ds(2 * i + j, 1), :, :].rearrange("a p n -> (a p) n"),
                                   cv[:, j, :]).then_inc(row_out, 16)
                    pool.dma_start(io["dnconv_new"][bass.ds(2 * i + j, 1), :, :].rearrange("a p n -> (a p) n"),
                                   row[:, j, SEQ:SEQ + 3 + NS]).then_inc(row_out, 16)
                    pool.wait_ge(row_out, 64 * i + 32 * j + 32)
                    pool.sem_inc(row_free, 1)
    sems.clear()


def delta_phase(T, ba):
    nc, h, ps, io = T.nc, T.h, T.ps, T.io
    sems = Sems(nc, "dn")
    S = {n: sems(n) for n in (
        "rows_in", "z_in", "squared", "sq_sum", "rn_log", "rn", "ba_cut", "spread", "l_copied", "l_exp", "unit", "turned", "k_copied",
        "ba_turned", "tm_ready", "kd_ready", "diff", "diff_exp", "keyed", "gram", "blocks_copied", "blocks_ready", "xm_ready", "xt_ready", "zt_done",
        "y_done", "y_ready", "z_done", "solved", "masked", "w_done", "r_ready", "u_done", "u_copied", "s_done", "s_ready",
        "o_copied", "o_sq", "o_sum", "rs_log", "rs", "out_ready", "step", "cleared", "pe_passed", "end_diff", "end_exp",
        "state_out")}
    ones, ident, sel = T.const("ones"), T.const("ident"), T.const("sel")
    W = 2 * C
    with ExitStack() as ctx:
        sb = lambda n, s: ctx.enter_context(nc.sbuf_tensor("dn" + n, s, F32))
        X, Z = sb("_x", [P, 24, W]), sb("_z", [P, 8, W])
        qk = sb("_qk", [P, 16, W])
        bs, bt, ek = sb("_bs", [P, W]), sb("_bt", [P, W]), sb("_ek", [P, 8])
        Lb, eL, kb, kbe, qe, ktm, bv, r0, vn, st_, tmp, o, rs = (sb("_" + n, [P, 8, W]) for n in
                                                              "Lb eL kb kbe qe ktm bv r0 vn S tmp o rs".split())
        dt_, dn, mt, xm, xt, y, at = (sb("_m" + n, [P, 512]) for n in "dt dn mt xm xt y at".split())
        mtl = sb("_mtl", [P, 5, 512])
        block = ctx.enter_context(nc.Block())
        m8 = lambda name: T.const(name).unsqueeze(1).to_broadcast([P, 8, C])
        h8 = lambda a: a.rearrange("p (h i) -> p h i", h=8)
        two = lambda b: ps[:, b:b + 2, :].rearrange("p b (h w) -> p (b h) w", h=4)
        bank = lambda b, hd: b + hd // 4
        col = lambda hd, a=0, n=W: slice((hd % 4) * W + a, (hd % 4) * W + a + n)
        hc = lambda hd: slice(64 * hd, 64 * hd + 64)

        @block.sync
        def _(sp):
            rows = T.odd_rows[0:32].rearrange("t p n -> p t n")
            sp.dma_start(X[:, :, :], rows[:, 0:24, 0:W]).then_inc(S["rows_in"], 16)
            sp.dma_start(Z[:, :, :], rows[:, 24:32, 0:W]).then_inc(S["z_in"], 16)
            with sp.Fori(1, NPAIR) as i:
                sp.wait_ge(S["turned"], i)
                sp.dma_start(X[:, :, :], rows[:, 0:24, bass.ds(i * W, W)]).then_inc(S["rows_in"], 16)
                sp.wait_ge(S["out_ready"], i)
                sp.dma_start(Z[:, :, :], rows[:, 24:32, bass.ds(i * W, W)]).then_inc(S["z_in"], 16)
            sp.wait_ge(S["s_ready"], 2 * NPAIR + 1)
            sp.dma_start(io["dn_prompt"], st_[:, :, :]).then_inc(S["state_out"], 16)
            sp.wait_ge(S["state_out"], 16)

        @block.gpsimd
        def _(pool):
            pool.memset(st_[:, :, :], 0.0).then_inc(S["cleared"], 1)
            pool.wait_ge(S["cleared"], 1)
            pool.sem_inc(S["s_ready"], 1)
            with pool.Fori(0, NPAIR) as i:
                pool.wait_ge(S["blocks_copied"], i + 1)
                for lv in range(1, 6):
                    pool.tensor_tensor(h8(mtl[:, lv - 1, :]), h8(mt[:, :]), m8(f"lev{lv}T"), ALU.mult)\
                        .then_inc(S["blocks_ready"], 1)

        @block.tensor
        def _(pe):
            with pe.Fori(0, NPAIR) as i:
                pe.wait_ge(S["squared"], i + 1)
                for b in range(4):
                    mm = pe.matmul(ps[:, b, :], ones, qk[:, 4 * b:4 * b + 4, :], start=True, stop=True)
                mm.then_inc(S["sq_sum"], 1)
                pe.wait_ge(S["ba_cut"], i + 1)
                for b, r in ((4, slice(A_ROW, A_ROW + 8)), (6, slice(BETA_ROW, BETA_ROW + 8))):
                    for hd in range(8):
                        mm = pe.matmul(ps[:, bank(b, hd), col(hd)], sel[r, hd * P:(hd + 1) * P], bs[r, :], start=True, stop=True)
                mm.then_inc(S["spread"], 1)
                pe.wait_ge(S["unit"], i + 1)
                for b, src in ((0, qk[:, 8:16, :]), (2, X[:, 16:24, :])):
                    for hd in range(8):
                        mm = pe.transpose(ps[:, bank(b, hd), col(hd)], src[:, hd, :], ident)
                pe.wait_ge(S["l_copied"], i + 1)
                mm = pe.transpose(ps[:, 4, 0:P], bs[:, :], ident)
                mm.then_inc(S["turned"], 1)
                pe.wait_ge(S["keyed"], i + 1)

                def gram(b, left, right):
                    for hd in range(8):
                        for p in range(2):
                            c = slice(C * p, C * p + C)
                            mm = pe.matmul(ps[64 * p:64 * p + 64, b, hc(hd)], left(hd)[:, c], right(hd)[:, c], start=True,
                                           stop=True)
                    mm.then_inc(S["gram"], 1)

                k_, q_, kb_ = (lambda hd: qk[:, 8 + hd, :]), (lambda hd: qk[:, hd, :]), (lambda hd: kb[:, hd, :])
                gram(5, k_, kb_)
                gram(6, kb_, k_)
                gram(7, k_, q_)
                pe.wait_ge(S["tm_ready"], i + 1)
                solve_levels_pe(pe, T, S, i, mtl, xm, xt, y, (0, 1, 2), S["pe_passed"])
                pe.wait_ge(S["masked"], i + 1)
                pe.wait_ge(S["solved"], i + 1)
                for p in range(2):
                    r, a = slice(64 * p, 64 * p + 64), C * p
                    c = slice(a, a + C)
                    pe.wait_ge(S["s_ready"], 2 * i + p + 1)
                    for hd in range(8):
                        mm = pe.matmul(ps[r, bank(0, hd), col(hd)], kbe[:, hd, c], st_[:, hd, :], start=True, stop=True)
                    mm.then_inc(S["w_done"], 1)
                    pe.wait_ge(S["r_ready"], 2 * i + p + 1)
                    alone(pe, S["pe_passed"])
                    for hd in range(8):
                        mm = pe.matmul(ps[r, bank(2, hd), col(hd)], xt[r, hc(hd)], r0[r, hd, :], start=True, stop=True)
                    mm.then_inc(S["u_done"], 1)
                    pe.wait_ge(S["u_copied"], 2 * i + p + 1)
                    alone(pe, S["pe_passed"])
                    for hd in range(8):
                        pe.matmul(ps[:, bank(6, hd), col(hd)], ktm[r, hd, :], vn[r, hd, :], start=True, stop=True)
                    for hd in range(8):
                        pe.matmul(ps[:, bank(4, hd), col(hd, a, C)], st_[:, hd, :], qe[:, hd, c], start=True, stop=False,
                                  skip_group_check=True)
                        mm = pe.matmul(ps[:, bank(4, hd), col(hd, a, C)], vn[r, hd, :], at[r, hc(hd)], start=False, stop=True,
                                       skip_group_check=True)
                    mm.then_inc(S["s_done"], 1)
                pe.wait_ge(S["o_sq"], i + 1)
                for b in range(2):
                    mm = pe.matmul(ps[:, b, :], ones, rs[:, 4 * b:4 * b + 4, :], start=True, stop=True)
                mm.then_inc(S["o_sum"], 1)

        @block.scalar
        def _(act):
            act.preload_act_table_set(EXP_LN_SET)
            with act.Fori(0, NPAIR) as i:
                act.wait_ge(S["rows_in"], 16 * i + 16)
                act.activation(qk[:, :, :], X[:, 0:16, :], ACT.Square).then_inc(S["squared"], 1)
                act.wait_ge(S["sq_sum"], i + 1)
                act.activation(qk[:, :, :], ps[:, 0:4, :].rearrange("p b (h w) -> p (b h) w", h=4), ACT.Ln,
                               bias=T.vec("eps_rms")).then_inc(S["rn_log"], 1)
                act.wait_ge(S["rn_log"], i + 1)
                act.activation(qk[:, :, :], qk[:, :, :], ACT.Exp, scale=-0.5).then_inc(S["rn"], 1)
                act.wait_ge(S["spread"], i + 1)
                act.activation(Lb[:, :, :], two(4), ACT.Copy).then_inc(S["l_copied"], 1)
                act.wait_ge(S["l_copied"], i + 1)
                act.activation(eL[:, :, :], Lb[:, :, :], ACT.Exp).then_inc(S["l_exp"], 1)
                act.wait_ge(S["turned"], i + 1)
                act.activation(bt[:, :], ps[:, 4, 0:P], ACT.Copy).then_inc(S["ba_turned"], 1)
                act.wait_ge(S["end_diff"], i + 1)
                act.activation(ek[:, :], ek[:, :], ACT.Exp).then_inc(S["end_exp"], 1)
                act.wait_ge(S["diff"], i + 1)
                act.activation(dt_[:, :], dt_[:, :], ACT.Exp)
                act.activation(dn[:, :], dn[:, :], ACT.Exp).then_inc(S["diff_exp"], 1)
                solve_levels_act(act, T, S, i, y, (0, 1, 2))
                for p in range(2):
                    r = slice(64 * p, 64 * p + 64)
                    act.wait_ge(S["u_done"], 2 * i + p + 1)
                    act.activation(vn[r, :, :], ps[r, 2:4, :].rearrange("p b (h w) -> p (b h) w", h=4), ACT.Copy)\
                       .then_inc(S["u_copied"], 1)
                act.wait_ge(S["s_done"], 2 * i + 2)
                act.activation(o[:, :, :], two(4), ACT.Copy).then_inc(S["o_copied"], 1)
                act.wait_ge(S["o_copied"], i + 1)
                act.activation(rs[:, :, :], o[:, :, :], ACT.Square).then_inc(S["o_sq"], 1)
                act.wait_ge(S["o_sum"], i + 1)
                act.activation(rs[:, :, :], two(0), ACT.Ln, scale=1.0 / P, bias=T.vec("eps_rms")).then_inc(S["rs_log"], 1)
                act.wait_ge(S["rs_log"], i + 1)
                act.activation(rs[:, :, :], rs[:, :, :], ACT.Exp, scale=-0.5).then_inc(S["rs"], 1)

        @block.vector
        def _(dve):
            per = DN_STEPS
            with dve.Fori(0, NPAIR) as i:
                st = Steps(dve, S["step"], per * i)
                q_, k_ = qk[:, 0:8, :], qk[:, 8:16, :]
                dve.tensor_copy(bs[:, :], ba[:, bass.ds(i * W, W)]).then_inc(S["ba_cut"], 1)
                dve.wait_ge(S["rn"], i + 1)
                st.do(dve.scalar_tensor_tensor(out=q_, in0=X[:, 0:8, :], scalar=P ** -0.5, in1=q_, op0=ALU.mult,
                                               op1=ALU.mult))
                st.link(dve.tensor_tensor(k_, X[:, 8:16, :], k_, ALU.mult))
                dve.sem_inc(S["unit"], 1)
                dve.wait_ge(S["spread"], i + 1)
                st.link(dve.tensor_tensor(kb[:, :, :], k_, two(6), ALU.mult))
                dve.wait_ge(S["l_exp"], i + 1)
                st.do(dve.tensor_tensor(kbe[:, :, :], kb[:, :, :], eL[:, :, :], ALU.mult))
                st.link(dve.tensor_tensor(qe[:, :, :], q_, eL[:, :, :], ALU.mult))
                dve.sem_inc(S["keyed"], 1)
                dve.wait_ge(S["ba_turned"], i + 1)
                for p in range(2):
                    r = slice(64 * p, 64 * p + 64)
                    end = C * p + C - 1
                    lt = bt[r, A_ROW:A_ROW + 8]
                    st.do(dve.tensor_tensor(ek[r, :].unsqueeze(2), Lb[r, :, end:end + 1], lt.unsqueeze(2), ALU.subtract))
                    st.do(dve.tensor_tensor(h8(dt_[r, :]), Lb[r, :, C * p:C * p + C], lt.unsqueeze(2).to_broadcast([64, 8, C]),
                                            ALU.subtract))
                st.settle()
                dve.sem_inc(S["end_diff"], 1)
                st.link(dve.tensor_scalar(dn[:, :], dt_[:, :], -1.0, 0.0, ALU.mult, ALU.min))
                st.link(dve.tensor_scalar(dt_[:, :], dt_[:, :], 0.0, None, ALU.min))
                dve.sem_inc(S["diff"], 1)
                b8 = bt[:, BETA_ROW:BETA_ROW + 8].unsqueeze(2).to_broadcast([P, 8, W])
                st.do(dve.tensor_tensor(bv[:, :, :], two(2), b8, ALU.mult))
                dve.wait_ge(S["end_exp"], i + 1)
                st.do(dve.tensor_tensor(ktm[:, :, :], two(0), ek[:, :].unsqueeze(2).to_broadcast([P, 8, W]), ALU.mult))
                st.settle()
                dve.sem_inc(S["tm_ready"], 1)
                dve.wait_ge(S["gram"], 3 * i + 3)
                dve.wait_ge(S["diff_exp"], i + 1)
                st.do(dve.tensor_tensor(mt[:, :], dt_[:, :], ps[:, 5, :], ALU.mult))
                st.do(dve.tensor_tensor(xm[:, :], dn[:, :], ps[:, 6, :], ALU.mult))
                st.link(dve.tensor_tensor(at[:, :], dt_[:, :], ps[:, 7, :], ALU.mult))
                dve.sem_inc(S["blocks_copied"], 1)
                st.do(dve.tensor_tensor(h8(xt[:, :]), h8(mt[:, :]), m8("lev0T"), ALU.mult))
                st.link(dve.tensor_tensor(h8(xm[:, :]), h8(xm[:, :]), m8("lev0"), ALU.mult))
                st.do(dve.tensor_tensor(h8(xt[:, :]), m8("eye64"), h8(xt[:, :]), ALU.subtract))
                st.link(dve.tensor_tensor(h8(xm[:, :]), m8("eye64"), h8(xm[:, :]), ALU.subtract))
                dve.sem_inc(S["xm_ready"], 1)
                dve.sem_inc(S["xt_ready"], 1)
                st.link(dve.tensor_tensor(h8(at[:, :]), h8(at[:, :]), m8("inclT"), ALU.mult))
                dve.sem_inc(S["masked"], 1)
                solve_levels_dve(dve, T, S, st, i, xm, xt, (0, 1, 2))
                for p in range(2):
                    r = slice(64 * p, 64 * p + 64)
                    dve.wait_ge(S["w_done"], 2 * i + p + 1)
                    st.link(dve.tensor_tensor(r0[r, :, :], bv[r, :, :],
                                              ps[r, 0:2, :].rearrange("p b (h w) -> p (b h) w", h=4), ALU.subtract))
                    dve.sem_inc(S["r_ready"], 1)
                    end = C * p + C - 1
                    dve.wait_ge(S["u_copied"], 2 * i + p + 1)
                    st.link(dve.tensor_tensor(tmp[:, :, :], st_[:, :, :], eL[:, :, end:end + 1].to_broadcast([P, 8, W]),
                                              ALU.mult))
                    dve.wait_ge(S["s_done"], 2 * i + p + 1)
                    st.link(dve.tensor_tensor(st_[:, :, :], tmp[:, :, :], two(6), ALU.add))
                    dve.sem_inc(S["s_ready"], 1)
                dve.wait_ge(S["rs"], i + 1)
                st.link(dve.scalar_tensor_tensor(out=o[:, :, :], in0=o[:, :, :], scalar=T.vec("onorm"), in1=rs[:, :, :],
                                                 op0=ALU.mult, op1=ALU.mult))
                dve.wait_ge(S["z_in"], 16 * i + 16)
                st.link(dve.tensor_tensor(h[:, :, bass.ds(i * W, W)], o[:, :, :], Z[:, :, :], ALU.mult))
                dve.sem_inc(S["out_ready"], 1)
                assert st.n == per, st.n
    sems.clear()


DN_STEPS = 38


def delta_samples_phase(T, ba):
    nc, h, ps, io = T.nc, T.h, T.ps, T.io
    sems = Sems(nc, "ds")
    S = {n: sems(n) for n in ("rows_in", "state_in", "squared", "sq_sum", "rn_log", "rn", "unit", "turned", "copied",
                              "stored", "loaded", "decay", "o_ready", "o_stored", "o_back", "o_turned", "o_copied", "o_sq",
                              "o_sum", "rs_log", "rs", "step")}
    ones, ident = T.const("ones"), T.const("ident")
    with ExitStack() as ctx:
        sb = lambda n, s: ctx.enter_context(nc.sbuf_tensor("ds" + n, s, F32))
        X, sq = sb("_x", [P, 32, NS]), sb("_sq", [P, 16, NS])
        rows, barow = sb("_rows", [NS, 3 * 1024]), sb("_barow", [NS, P])
        kr, qr, vr, br, gr = sb("_kr", [P, P]), sb("_qr", [P, P]), sb("_vr", [P, 64]), sb("_br", [P, 1]), sb("_gr", [P, 1])
        s3, t3 = sb("_s", [P, P, 64]), sb("_t", [P, P, 64])
        sa, so = sb("_sa", [P, 64]), sb("_so", [P, 64])
        orow, o, rs = sb("_orow", [NS, 1024]), sb("_o", [P, 8, NS]), sb("_rs", [P, 8, NS])
        scr = nc.dram_tensor("scratch_dn_rows", [3, NS, 1024], F32, kind="Internal").ap()
        scr_b = nc.dram_tensor("scratch_dn_ba", [2, NS, 8], F32, kind="Internal").ap()
        scr_o = nc.dram_tensor("scratch_dn_o", [NS, 1024], F32, kind="Internal").ap()
        block = ctx.enter_context(nc.Block())

        @block.sync
        def _(sp):
            sp.dma_start(X[:, :, :], T.odd_rows[0:32, :, SEQ:TOK].rearrange("t p n -> p t n")).then_inc(S["rows_in"], 16)
            sp.dma_start(s3[:, :, :], io["dn_in"].rearrange("p (k v) -> p k v", k=P)).then_inc(S["state_in"], 16)
            sp.wait_ge(S["copied"], 1)
            sp.dma_start(scr.rearrange("a b n -> b a n"), rows[:, :].rearrange("b (a n) -> b a n", a=3)).then_inc(S["stored"], 16)
            sp.dma_start(scr_b[0], barow[:, BETA_ROW:BETA_ROW + 8]).then_inc(S["stored"], 16)
            sp.dma_start(scr_b[1], barow[:, A_ROW:A_ROW + 8]).then_inc(S["stored"], 16)
            sp.wait_ge(S["stored"], 48)
            for e in range(2):
                r = slice(64 * e, 64 * e + 64)
                for dst, src in ((qr[r, :], scr[0].rearrange("b (h k) -> (b h) k", h=8)),
                                 (kr[r, :], scr[1].rearrange("b (h k) -> (b h) k", h=8)),
                                 (vr[r, :], scr[2].rearrange("b (h e v) -> e (b h) v", h=8, e=2)[e]),
                                 (br[r, :], scr_b[0].rearrange("b (h a) -> (b h) a", a=1)),
                                 (gr[r, :], scr_b[1].rearrange("b (h a) -> (b h) a", a=1))):
                    sp.dma_start(dst, src).then_inc(S["loaded"], 16)
            sp.wait_ge(S["o_ready"], 1)
            for e in range(2):
                sp.dma_start(scr_o.rearrange("b (h e v) -> e (b h) v", h=8, e=2)[e], so[64 * e:64 * e + 64, :])\
                  .then_inc(S["o_stored"], 16)
            sp.wait_ge(S["o_stored"], 32)
            sp.dma_start(orow[:, :], scr_o).then_inc(S["o_back"], 16)
            sp.dma_start(io["dn_new"].rearrange("p (k v) -> p k v", k=P), s3[:, :, :]).then_inc(S["o_stored"], 16)
            sp.wait_ge(S["o_stored"], 48)

        @block.tensor
        def _(pe):
            pe.wait_ge(S["squared"], 1)
            pe.matmul(ps[:, 0, 0:16 * NS], ones, sq[:, :, :], start=True, stop=True).then_inc(S["sq_sum"], 1)
            pe.wait_ge(S["unit"], 1)
            for k in range(24):
                pe.transpose(ps[0:NS, 1 + k // 4, (k % 4) * P:(k % 4 + 1) * P], X[:, k, :], ident)
            pe.transpose(ps[0:NS, 7, 0:P], ba[:, SEQ:TOK], ident).then_inc(S["turned"], 1)
            pe.wait_ge(S["o_back"], 16)
            for k in range(8):
                mm = pe.transpose(ps[:, 0, k * NS:(k + 1) * NS], orow[:, k * P:(k + 1) * P], ident[0:NS, 0:NS])
            mm.then_inc(S["o_turned"], 1)
            pe.wait_ge(S["o_sq"], 1)
            pe.matmul(ps[:, 1, 0:8 * NS], ones, rs[:, :, :], start=True, stop=True).then_inc(S["o_sum"], 1)

        @block.scalar
        def _(act):
            act.preload_act_table_set(EXP_LN_SET)
            act.wait_ge(S["rows_in"], 16)
            act.activation(sq[:, :, :], X[:, 0:16, :], ACT.Square).then_inc(S["squared"], 1)
            act.wait_ge(S["sq_sum"], 1)
            act.activation(sq[:, :, :], ps[:, 0, 0:16 * NS].rearrange("p (h w) -> p h w", h=16), ACT.Ln,
                           bias=T.vec("eps_rms")).then_inc(S["rn_log"], 1)
            act.wait_ge(S["rn_log"], 1)
            act.activation(sq[:, :, :], sq[:, :, :], ACT.Exp, scale=-0.5).then_inc(S["rn"], 1)
            act.wait_ge(S["turned"], 1)
            act.activation(rows[:, :].rearrange("b (a n) -> b a n", a=6), ps[0:NS, 1:7, :], ACT.Copy)
            act.activation(barow[:, :], ps[0:NS, 7, 0:P], ACT.Copy).then_inc(S["copied"], 1)
            act.wait_ge(S["loaded"], 160)
            act.activation(gr[:, :], gr[:, :], ACT.Exp).then_inc(S["decay"], 1)
            act.wait_ge(S["o_turned"], 1)
            act.activation(o[:, :, :], ps[:, 0, 0:8 * NS].rearrange("p (h w) -> p h w", h=8), ACT.Copy).then_inc(S["o_copied"], 1)
            act.wait_ge(S["o_copied"], 1)
            act.activation(rs[:, :, :], o[:, :, :], ACT.Square).then_inc(S["o_sq"], 1)
            act.wait_ge(S["o_sum"], 1)
            act.activation(rs[:, :, :], ps[:, 1, 0:8 * NS].rearrange("p (h w) -> p h w", h=8), ACT.Ln, scale=1.0 / P,
                           bias=T.vec("eps_rms")).then_inc(S["rs_log"], 1)
            act.wait_ge(S["rs_log"], 1)
            act.activation(rs[:, :, :], rs[:, :, :], ACT.Exp, scale=-0.5).then_inc(S["rs"], 1)

        @block.vector
        def _(dve):
            st = Steps(dve, S["step"])
            dve.wait_ge(S["rn"], 1)
            st.do(dve.scalar_tensor_tensor(out=X[:, 0:8, :], in0=X[:, 0:8, :], scalar=P ** -0.5, in1=sq[:, 0:8, :],
                                           op0=ALU.mult, op1=ALU.mult))
            st.link(dve.tensor_tensor(X[:, 8:16, :], X[:, 8:16, :], sq[:, 8:16, :], ALU.mult))
            dve.sem_inc(S["unit"], 1)
            dve.wait_ge(S["decay"], 1)
            dve.wait_ge(S["state_in"], 16)
            k3, q3 = (a[:, :].unsqueeze(2).to_broadcast([P, P, 64]) for a in (kr, qr))
            s, t = s3[:, :, :], t3[:, :, :]
            over_k = t3[:, :, :].rearrange("p k v -> p v k")
            st.link(dve.tensor_tensor(t, s, k3, ALU.mult))
            st.link(dve.tensor_reduce(sa[:, :], over_k, AX.X, ALU.add))
            st.link(dve.tensor_scalar(sa[:, :], sa[:, :], gr[:, 0:1], None, ALU.mult))
            st.link(dve.tensor_tensor(sa[:, :], vr[:, :], sa[:, :], ALU.subtract))
            st.link(dve.tensor_scalar(sa[:, :], sa[:, :], br[:, 0:1], None, ALU.mult))
            st.link(dve.tensor_tensor(t, k3, sa[:, :].unsqueeze(1).to_broadcast([P, P, 64]), ALU.mult))
            st.link(dve.scalar_tensor_tensor(out=s, in0=s, scalar=gr[:, 0:1], in1=t, op0=ALU.mult, op1=ALU.add))
            st.link(dve.tensor_tensor(t, s, q3, ALU.mult))
            st.link(dve.tensor_reduce(so[:, :], over_k, AX.X, ALU.add))
            dve.sem_inc(S["o_ready"], 1)
            dve.wait_ge(S["rs"], 1)
            st.link(dve.scalar_tensor_tensor(out=o[:, :, :], in0=o[:, :, :], scalar=T.vec("onorm"), in1=rs[:, :, :],
                                             op0=ALU.mult, op1=ALU.mult))
            st.link(dve.tensor_tensor(h[:, :, SEQ:TOK], o[:, :, :], X[:, 24:32, :], ALU.mult))
    sems.clear()


def ffn(T, l, x_dram, out_dram):
    nc = T.nc
    with nc.sbuf_tensor(f"ffn_a{l}", [P, FT, TOK], F32) as a:
        with nc.sbuf_tensor(f"ffn_hh{l}", [P, KT, TOK], F32R) as T.hh, nc.sbuf_tensor(f"ffn_hl{l}", [P, KT, TOK], F32R) as T.hl:
            norm_phase(T, f"normf{l}", f"norm_ffn{l}", x_dram)
            ffn_up_phase(T, f"up{l}", l, a)
        down_phase(T, f"down{l}", T.io["w_down"][l], a, x_dram, out_dram)


def trunk_program(nc, io):
    with ExitStack() as ctx:
        T = Trunk(nc, io, ctx)
        T.n_phys = io["k_pages"].shape[0]
        scratch = lambda n, s: nc.dram_tensor("scratch_" + n, s, F32, kind="Internal").ap()
        T.xs_rows = scratch("xs_rows", [NB_T, P, TOK])
        T.odd_rows = scratch("odd_rows", [ODD_T - 1, P, TOK])
        x1, x2, x3 = (scratch(n, [KT, P, TOK]) for n in ("x1", "x2", "x3"))
        load_phase(T)
        with nc.sbuf_tensor("consts0", [P, CONSTS_0], F32) as T.consts, ExitStack() as pages_ctx:
            T.pages = Pages(T, pages_ctx)
            with nc.sbuf_tensor("hh0", [P, KT, TOK], F32R) as T.hh, nc.sbuf_tensor("hl0", [P, KT, TOK], F32R) as T.hl:
                norm_phase(T, "norm0", "norm_even", io["x"], consts=True)
                qk_phase(T)
                v_phase(T)
                pb_phase(T)
            with nc.sbuf_tensor("h0", [P, KT, TOK], F32) as T.h:
                attention_phase(T)
                rwkv_phase(T)
                residual_phase(T, "out0", io["w_out_even"], T.h, io["x"], x1)
        ffn(T, 0, x1, x2)
        with nc.sbuf_tensor("consts1", [P, CONSTS.shape[1]], F32) as T.consts, nc.sbuf_tensor("ba", [P, TOK], F32) as ba:
            with nc.sbuf_tensor("hh1", [P, KT, TOK], F32R) as T.hh, nc.sbuf_tensor("hl1", [P, KT, TOK], F32R) as T.hl:
                norm_phase(T, "norm1", "norm_odd", x2, consts=True)
                odd_phase(T, ba)
            with nc.sbuf_tensor("h1", [P, KT, TOK], F32) as T.h:
                delta_phase(T, ba)
                delta_samples_phase(T, ba)
                residual_phase(T, "out1", io["w_out_odd"], T.h, x2, x3)
        ffn(T, 1, x3, io["y"])


OUTS = {
    "y": (KT, P, TOK), "qk_rows": (8, P, TOK), "v_rows": (TOK, D_A), "shift_new": (NB_T, P, 1 + NS),
    "wkv_prompt": (2, 64, 4, 64), "wkv_new": (P, 64 * 32), "dn_prompt": (P, 8, P), "dn_new": (P, P * 64),
    "dnconv_new": (ODD_T - 1, P, 3 + NS), "dnconv_old": (NS, 2, QKV_T * P), "ffnconv_new": (2, FT, P, 2 + NS),
    "ffnconv_old": (2, NS, 1, D_FF),
}


def outputs(r):
    y = r["y"].reshape(D_MODEL, TOK).T
    kk = r["qk_rows"][4:].reshape(D_A, TOK).T
    v = r["v_rows"]
    shift = r["shift_new"].reshape(NB_COLS, 1 + NS).T
    dnc = r["dnconv_new"][:QKV_T].reshape(QKV_T * P, 3 + NS).T
    ffc = r["ffnconv_new"].reshape(2, D_FF, 2 + NS).transpose(0, 2, 1)
    return (
        y[:SEQ].reshape(1, SEQ, D_MODEL), y[SEQ:].reshape(NS, 1, D_MODEL),
        kk[:SEQ].reshape(1, 1, SEQ, H_A, DH), v[:SEQ].reshape(1, 1, SEQ, H_A, DH),
        kk[SEQ:].reshape(1, NS, 1, H_A, DH), v[SEQ:].reshape(1, NS, 1, H_A, DH),
        r["wkv_prompt"].transpose(2, 0, 3, 1).reshape(1, 1, 8, 64, 64),
        r["wkv_new"].reshape(2, NS, 8, 64, 32).transpose(1, 2, 0, 4, 3).reshape(1, NS, 8, 64, 64),
        shift[:1].reshape(1, 1, NB_COLS), shift[1:].reshape(1, NS, NB_COLS),
        r["dn_prompt"].transpose(1, 0, 2).reshape(1, 1, 8, P, P),
        r["dn_new"].reshape(2, NS, 8, P, 64).transpose(1, 2, 3, 0, 4).reshape(1, NS, 8, P, P),
        dnc[:3].reshape(1, 1, 3, QKV_T * P),
        np.concatenate([r["dnconv_old"], dnc[3:, None]], 1)[None],
        ffc[:, None, :2], np.concatenate([r["ffnconv_old"], ffc[:, 2:, None]], 2),
    )


def layouts(inputs):
    A = {k: np.asarray(v) for k, v in inputs.items()}
    f = np.float32

    def blocks(w, nt=None):
        k, n = w.shape
        return w.reshape(k // P, P, n // P, P).transpose(2, 1, 0, 3).reshape(n // P, P, k)

    def cols(v):
        return v.reshape(-1, P).T

    def tiles(rows):
        return rows.T.reshape(-1, P, rows.shape[0])

    L = {"consts": CONSTS, "ones": ONES}
    L["x"] = np.concatenate([A["x_prompt"][0], A["x_sample"][:, 0]], 0).T.reshape(KT, P, TOK)
    one = np.ones((P, 1), f)
    row32 = lambda v: np.concatenate([np.zeros(A_ROW, f), v, np.zeros(P - A_ROW - 8, f)])[:, None]
    vec = {
        "norm_even": cols(A["norm_mix_even"][0]), "norm_ffn0": cols(A["norm_ffn"][0]),
        "norm_odd": cols(A["norm_mix_odd"][0]), "norm_ffn1": cols(A["norm_ffn"][1]),
        "w0": cols(A["w0_b"][0]), "a0": cols(A["a0_b"][0]), "kk": cols(A["kk_b"][0]), "ka": cols(A["ka_b"][0]),
        "rk": cols(A["rk_b"][0]), "lnw": cols(A["lnx_w_b"][0]), "lnb": cols(A["lnx_b_b"][0]),
        "onorm": A["onorm_dn"][0][:, None], "sb_bias": np.broadcast_to(A["sb_bias"][0], (P, 8)),
        "a_log": row32(A["a_log_dn"][0]), "dt_bias": row32(A["dt_bias_dn"][0]),
        "eps_rms": one * f(RMS_EPS), "eps_gn": one * f(GN_EPS),
    }
    L["vecs"] = np.concatenate([vec[n] for n in VEC_COLS], 1)
    we = A["w_in_even"][0]
    gain = np.concatenate([np.tile(A["qnorm_a"][0], (8,)), np.tile(A["knorm_a"][0], (8,))])
    L["w_qk"] = np.concatenate([blocks(we[:, :2 * D_A]), tiles(gain[None])], 2)
    L["w_v"] = we[:, 2 * D_A:3 * D_A].reshape(KT, P, D_A).transpose(1, 0, 2)
    L["w_pb"] = np.concatenate([blocks(we[:, 3 * D_A:]), tiles(A["mu_b"]), tiles(A["state_shift"][0])], 2)
    L["w_lora"] = np.concatenate([np.concatenate([A["w_up_b"][0], A["a_up_b"][0]], 0), A["g_up_b"][0]], 1)
    L["w_out_even"] = blocks(A["w_out_even"][0])
    wo = A["w_in_odd"][0]
    n = QKV_T * P + 8 * P
    ba = np.zeros((D_MODEL, P), f)
    ba[:, BETA_ROW:BETA_ROW + 8] = wo[:, n:n + 8]
    ba[:, A_ROW:A_ROW + 8] = wo[:, n + 8:]
    par = np.zeros((ODD_T, P, 4 + 3 * NS), f)
    par[:QKV_T, :, :4] = tiles(A["conv_dn"][0])
    par[QKV_T:ODD_T - 1, :, 3] = 1.0
    par[:QKV_T, :, 4:] = tiles(A["state_dn_conv"][0].transpose(1, 0, 2).reshape(3 * NS, -1))
    L["w_odd"] = np.concatenate([blocks(np.concatenate([wo[:, :n], ba], 1)), par], 2)
    L["w_out_odd"] = blocks(A["w_out_odd"][0])
    L["w_ff"] = np.stack([np.concatenate([
        blocks(A["w_gate"][l]), blocks(A["w_up"][l]), tiles(A["conv_ffn"][l]), tiles(A["conv_ffn_b"][l][None]),
        tiles(A["state_ffn_conv"][l].transpose(1, 0, 2).reshape(2 * NS, -1))], 2) for l in range(2)])
    L["w_down"] = np.stack([blocks(A["w_down"][l]) for l in range(2)])
    L["k_pages"] = A["cache_k"][0].reshape(-1, PAGE, D_A)
    L["v_pages"] = A["cache_v"][0].reshape(-1, PAGE, D_A)
    L["page_table"] = A["page_table"][:, ::-1].reshape(1, -1)
    L["wkv_in"] = A["state_wkv"][0].reshape(NS, 8, 2, 32, 64).transpose(2, 0, 1, 4, 3).reshape(P, 64 * 32)
    L["dn_in"] = A["state_dn"][0].reshape(NS, 8, 128, 2, 64).transpose(3, 0, 1, 2, 4).reshape(P, 128 * 64)
    L["dn_conv_rows"] = A["state_dn_conv"][0, :, 1:]
    L["ffn_conv_rows"] = A["state_ffn_conv"][:, :, 1:]
    return {k: np.ascontiguousarray(v) for k, v in L.items()}


def kernel(**inputs):
    import concourse.bacc as bacc
    from concourse.bass_utils import run_bass_kernel_spmd

    nc = bacc.Bacc("TRN2", target_bir_lowering=False, num_devices=1)
    arrays, io = {}, {}
    for name, a in layouts(inputs).items():
        arrays[f"in_{name}"] = a
        io[name] = nc.dram_tensor(f"in_{name}", a.shape, mybir.dt.from_np(a.dtype), kind="ExternalInput").ap()
    for name, shape in OUTS.items():
        io[name] = nc.dram_tensor(f"out_{name}", shape, F32, kind="ExternalOutput").ap()
    trunk_program(nc, io)
    r = run_bass_kernel_spmd(nc, [arrays], core_ids=[0]).results[0]
    return tuple(np.ascontiguousarray(a) for a in outputs({n: r[f"out_{n}"] for n in OUTS}))
```
